# Optimizing a Trainium2 kernel written in Bass

```python
import jax, jax.numpy as jnp
from jax import lax
import numpy as np
import math

D_MODEL = 1024
BATCH = 1
SEQ = 512
DEPTH = 1

MLA_HEADS = 4
QK_NOPE_DIM = 64
QK_ROPE_DIM = 32
V_HEAD_DIM = 64
Q_RANK = D_MODEL // 4
KV_RANK = D_MODEL // 8
ROPE_BASE = 10000.0
Q_BLOCK = 128
SG_GROUPS = 4
SG_WIDTH = D_MODEL // 4
SG_CHUNK = 128
CONV_WIDTH = D_MODEL // 4
CONV_K = 3
POOL_WINDOWS = (2, 4, 8, 16)
POOL_WIDTH = D_MODEL // 4
POOL_GROUP = POOL_WIDTH // 4
N_BRANCH = 4
D_FF = 4 * D_MODEL
EPS = 1e-6
N_IN = Q_RANK + KV_RANK + QK_ROPE_DIM + 2 * SG_WIDTH + 3 * CONV_WIDTH + POOL_WIDTH + N_BRANCH * D_MODEL


def rmsnorm(x, g):
    xf = x.astype(jnp.float32)
    y = xf * lax.rsqrt(jnp.mean(xf * xf, axis=-1, keepdims=True) + EPS)
    return (y * g.astype(jnp.float32)).astype(x.dtype)

def layernorm(x, g, b):
    xf = x.astype(jnp.float32)
    mu = jnp.mean(xf, axis=-1, keepdims=True)
    xc = xf - mu
    y = xc * lax.rsqrt(jnp.mean(xc * xc, axis=-1, keepdims=True) + EPS)
    return (y * g.astype(jnp.float32) + b.astype(jnp.float32)).astype(x.dtype)

def split_cols(proj):
    sizes = (Q_RANK, KV_RANK, QK_ROPE_DIM, SG_WIDTH, SG_WIDTH, CONV_WIDTH, CONV_WIDTH, CONV_WIDTH,
             POOL_WIDTH, N_BRANCH * D_MODEL)
    offs = []
    acc = 0
    for s in sizes[:-1]:
        acc += s
        offs.append(acc)
    return jnp.split(proj, offs, axis=-1)

def rope(x, cos, sin):
    x1, x2 = jnp.split(x, 2, axis=-1)
    return jnp.concatenate([x1 * cos - x2 * sin, x2 * cos + x1 * sin], axis=-1)

def mla(c_q, c_kv, k_rope, positions, q_norm, w_uq, kv_norm, w_ukv):
    B_, S_, _ = c_q.shape
    q = (rmsnorm(c_q, q_norm) @ w_uq).reshape(B_, S_, MLA_HEADS, QK_NOPE_DIM + QK_ROPE_DIM)
    q_nope, q_rope = q[..., :QK_NOPE_DIM], q[..., QK_NOPE_DIM:]
    kv = (rmsnorm(c_kv, kv_norm) @ w_ukv).reshape(B_, S_, MLA_HEADS, QK_NOPE_DIM + V_HEAD_DIM)
    k_nope, v = kv[..., :QK_NOPE_DIM], kv[..., QK_NOPE_DIM:]
    inv_freq = ROPE_BASE ** (-jnp.arange(0, QK_ROPE_DIM, 2, dtype=jnp.float32) / QK_ROPE_DIM)
    ang = positions.astype(jnp.float32)[..., None] * inv_freq
    cos = jnp.cos(ang).astype(q.dtype)
    sin = jnp.sin(ang).astype(q.dtype)
    q_rope = rope(q_rope, cos[:, :, None, :], sin[:, :, None, :])
    k_rope = rope(k_rope, cos, sin)
    scale = (QK_NOPE_DIM + QK_ROPE_DIM) ** -0.5
    nb = S_ // Q_BLOCK

    def to_blocks(a):
        return jnp.moveaxis(a.reshape((B_, nb, Q_BLOCK) + a.shape[2:]), 1, 0)

    k_idx = jnp.arange(S_)

    def block(args):
        qn, qr, start = args
        s = jnp.einsum('bqhd,bkhd->bhqk', qn, k_nope) + jnp.einsum('bqhr,bkr->bhqk', qr, k_rope)
        s = s.astype(jnp.float32) * scale
        q_idx = start + jnp.arange(Q_BLOCK)
        s = jnp.where(k_idx[None, :] <= q_idx[:, None], s, -jnp.inf)
        p = jax.nn.softmax(s, axis=-1).astype(v.dtype)
        return jnp.einsum('bhqk,bkhd->bqhd', p, v)

    starts = jnp.arange(nb, dtype=jnp.int32) * Q_BLOCK
    o = lax.map(block, (to_blocks(q_nope), to_blocks(q_rope), starts))
    return jnp.moveaxis(o, 0, 1).reshape(B_, S_, MLA_HEADS * V_HEAD_DIM)

def spatial_gating(u, v, ln_g, ln_b, w_s, b_s):
    B_, S_, _ = u.shape
    u = jax.nn.gelu(u)
    v = layernorm(jax.nn.gelu(v), ln_g, ln_b)
    n = S_ // SG_CHUNK
    vc = v.reshape(B_, n, SG_CHUNK, SG_GROUPS, SG_WIDTH // SG_GROUPS)
    mask = jnp.tril(jnp.ones((SG_CHUNK, SG_CHUNK), dtype=bool))
    w = jnp.where(mask, w_s, 0)
    s = jnp.einsum('gts,bnsgc->bntgc', w, vc) + b_s.T[:, :, None]
    return u * s.reshape(B_, S_, SG_WIDTH)

def short_conv(xin, bg, cg, conv_w):
    z = cg * xin
    S_ = z.shape[1]
    zp = jnp.pad(z, ((0, 0), (CONV_K - 1, 0), (0, 0)))
    y = sum(conv_w[k] * zp[:, k:k + S_] for k in range(CONV_K))
    return bg * y

def multiscale_pool(p, w_pool, scale):
    B_, S_, _ = p.shape
    pg = p.reshape(B_, S_, len(POOL_WINDOWS), POOL_GROUP).astype(jnp.float32)
    cs = jnp.cumsum(pg, axis=1)
    t = jnp.arange(S_)
    outs = []
    for g, win in enumerate(POOL_WINDOWS):
        c = cs[:, :, g]
        lagged = jnp.pad(c, ((0, 0), (win, 0), (0, 0)))[:, :S_]
        cnt = jnp.minimum(t + 1, win).astype(jnp.float32)[None, :, None]
        outs.append((c - lagged) / cnt - pg[:, :, g])
    pooled = jnp.stack(outs, axis=2).astype(p.dtype)
    mixed = jnp.einsum('bsgc,gcd->bsgd', pooled, w_pool)
    return mixed.reshape(B_, S_, POOL_WIDTH) * scale

def first_inputs(seed: int = 0) -> dict:
    key = jax.random.key(seed)
    ks = jax.random.split(key, 26)
    L = DEPTH

    def nrm(k, shape, fan_in):
        return jax.random.normal(k, shape, jnp.float32) * fan_in ** -0.5

    def gain(k, shape):
        return 1.0 + 0.05 * jax.random.normal(k, shape, jnp.float32)

    def small(k, shape, s):
        return s * jax.random.normal(k, shape, jnp.float32)

    x = jax.random.normal(ks[0], (BATCH, SEQ, D_MODEL), jnp.float32)
    positions = (jax.random.randint(ks[1], (BATCH, 1), 0, 4096, dtype=jnp.int32)
                 + jnp.arange(SEQ, dtype=jnp.int32)[None, :])
    return {
        'x': x,
        'positions': positions,
        'norm_mix_pre': gain(ks[2], (L, D_MODEL)),
        'w_in': nrm(ks[3], (L, D_MODEL, N_IN), D_MODEL),
        'gate_b': small(ks[4], (L, N_BRANCH * D_MODEL), 0.01),
        'q_norm': gain(ks[5], (L, Q_RANK)),
        'w_uq': nrm(ks[6], (L, Q_RANK, MLA_HEADS * (QK_NOPE_DIM + QK_ROPE_DIM)), Q_RANK),
        'kv_norm': gain(ks[7], (L, KV_RANK)),
        'w_ukv': nrm(ks[8], (L, KV_RANK, MLA_HEADS * (QK_NOPE_DIM + V_HEAD_DIM)), KV_RANK),
        'w_br_mla': nrm(ks[9], (L, MLA_HEADS * V_HEAD_DIM, D_MODEL), MLA_HEADS * V_HEAD_DIM),
        'sg_ln_g': gain(ks[10], (L, SG_WIDTH)),
        'sg_ln_b': small(ks[11], (L, SG_WIDTH), 0.02),
        'sg_w': nrm(ks[12], (L, SG_GROUPS, SG_CHUNK, SG_CHUNK), SG_CHUNK),
        'sg_b': gain(ks[13], (L, SG_GROUPS, SG_CHUNK)),
        'w_br_sg': nrm(ks[14], (L, SG_WIDTH, D_MODEL), SG_WIDTH),
        'conv_w': nrm(ks[15], (L, CONV_K, CONV_WIDTH), CONV_K),
        'w_br_conv': nrm(ks[16], (L, CONV_WIDTH, D_MODEL), CONV_WIDTH),
        'pool_w': nrm(ks[17], (L, len(POOL_WINDOWS), POOL_GROUP, POOL_GROUP), POOL_GROUP),
        'pool_scale': gain(ks[18], (L, POOL_WIDTH)),
        'w_br_pool': nrm(ks[19], (L, POOL_WIDTH, D_MODEL), POOL_WIDTH),
        'w_out': nrm(ks[20], (L, D_MODEL, D_MODEL), D_MODEL),
        'norm_mix_post': gain(ks[21], (L, D_MODEL)),
        'norm_ffn_pre': gain(ks[22], (L, D_MODEL)),
        'w_ff1': nrm(ks[23], (L, D_MODEL, D_FF), D_MODEL),
        'w_ff2': nrm(ks[24], (L, D_FF, D_MODEL), D_FF),
        'norm_ffn_post': gain(ks[25], (L, D_MODEL)),
    }

def first_block(x, positions, norm_mix_pre, w_in, gate_b, q_norm, w_uq, kv_norm, w_ukv, w_br_mla,
              sg_ln_g, sg_ln_b, sg_w, sg_b, w_br_sg, conv_w, w_br_conv, pool_w, pool_scale, w_br_pool,
              w_out, norm_mix_post, norm_ffn_pre, w_ff1, w_ff2, norm_ffn_post):
    B_, S_, D_ = x.shape
    for l in range(DEPTH):
        h = rmsnorm(x, norm_mix_pre[l])
        (c_q, c_kv, k_r, sg_u, sg_v, cv_x, cv_b, cv_c, pool_in, gate_pre) = split_cols(h @ w_in[l])
        gates = jax.nn.sigmoid(gate_pre + gate_b[l]).reshape(B_, S_, N_BRANCH, D_)
        y_a = mla(c_q, c_kv, k_r, positions, q_norm[l], w_uq[l], kv_norm[l], w_ukv[l]) @ w_br_mla[l]
        y_b = spatial_gating(sg_u, sg_v, sg_ln_g[l], sg_ln_b[l], sg_w[l], sg_b[l]) @ w_br_sg[l]
        y_c = short_conv(cv_x, cv_b, cv_c, conv_w[l]) @ w_br_conv[l]
        y_d = multiscale_pool(pool_in, pool_w[l], pool_scale[l]) @ w_br_pool[l]
        merged = (gates[:, :, 0] * y_a + gates[:, :, 1] * y_b
                  + gates[:, :, 2] * y_c + gates[:, :, 3] * y_d)
        x = x + rmsnorm(merged @ w_out[l], norm_mix_post[l])
        h = rmsnorm(x, norm_ffn_pre[l])
        f = jnp.square(jax.nn.relu(h @ w_ff1[l])) @ w_ff2[l]
        x = x + rmsnorm(f, norm_ffn_post[l])
    return x


_first_inputs = first_inputs


def first_inputs(seed=0):
    import zlib

    import numpy as np

    out = dict(_first_inputs(seed))
    spreads = {}
    factors = {'gate_b': 8.0,
     'q_norm': 8.0,
     'kv_norm': 8.0,
     'sg_ln_g': 4.952,
     'sg_ln_b': 8.0,
     'sg_b': 3.712,
     'pool_scale': 2.803}
    for name, (base, spread) in spreads.items():
        noise = np.random.default_rng([zlib.crc32(name.encode()), seed]).standard_normal(out[name].shape)
        drawn = base * np.exp(spread * noise) if base else spread * noise
        out[name] = __import__('jax').numpy.asarray(drawn.astype(out[name].dtype))
    for name, factor in factors.items():
        out[name] = (out[name] * factor).astype(out[name].dtype)
    return out


_narrow_inputs = first_inputs


def first_inputs(seed=0):

    out = dict(_narrow_inputs(seed))
    wider = {'sg_ln_g': 6.3, 'sg_ln_b': 10.56, 'sg_b': 6.23, 'pool_scale': 6.32}
    for name, times in wider.items():
        mean = out[name].mean()
        out[name] = (mean + times * (out[name] - mean)).astype(out[name].dtype)
    return out


N_HEADS_ATTN = 8
HEAD_DIM_ATTN = 64
V_DIM_ATTN = 2 * HEAD_DIM_ATTN
ATTN_WIDTH = N_HEADS_ATTN * V_DIM_ATTN
SSM_WIDTH = D_MODEL
SSM_HEADDIM = 64
N_HEADS_SSM = SSM_WIDTH // SSM_HEADDIM
SSM_GROUPS = 4
SSM_HEADS_PER_GROUP = N_HEADS_SSM // SSM_GROUPS
SSM_STATE = 128
CONV_WIDTH_2 = 5
CONV_CH = SSM_WIDTH + 2 * SSM_GROUPS * SSM_STATE
CHUNK = 128
D_MIX = ATTN_WIDTH + SSM_WIDTH
Q_COLS = N_HEADS_ATTN * 2 * HEAD_DIM_ATTN
K_COLS = N_HEADS_ATTN * 2 * HEAD_DIM_ATTN
V_COLS = ATTN_WIDTH
Z_COLS = SSM_WIDTH
XBC_COLS = CONV_CH
DT_COLS = N_HEADS_SSM
IN_COLS = Q_COLS + K_COLS + V_COLS + Z_COLS + XBC_COLS + DT_COLS
D_FF_2 = -(-8 * D_MODEL // (3 * 256)) * 256
DEEPNORM_ALPHA = (2 * DEPTH) ** 0.25
DEEPNORM_BETA = (8 * DEPTH) ** -0.25
LN_EPS = 1e-5
RMS_EPS = 1e-5


def layernorm_2(x, g, b):
    x32 = x.astype(jnp.float32)
    mu = jnp.mean(x32, axis=-1, keepdims=True)
    var = jnp.mean(jnp.square(x32 - mu), axis=-1, keepdims=True)
    y = (x32 - mu) * lax.rsqrt(var + LN_EPS)
    return (y * g.astype(jnp.float32) + b.astype(jnp.float32)).astype(x.dtype)

def rmsnorm_2(x, w):
    x32 = x.astype(jnp.float32)
    y = x32 * lax.rsqrt(jnp.mean(jnp.square(x32), axis=-1, keepdims=True) + RMS_EPS)
    return (y * w.astype(jnp.float32)).astype(x.dtype)

def alibi_slopes(n_heads):
    return jnp.exp2(-8.0 * jnp.arange(1, n_heads + 1, dtype=jnp.float32) / n_heads)

def diff_attention(q, k, v, lq1, lk1, lq2, lk2, subln_w, lambda_init):
    b, S = q.shape[0], q.shape[1]
    nblk = S // Q_BLOCK
    f32 = jnp.float32
    lam = (jnp.exp(jnp.sum(lq1.astype(f32) * lk1.astype(f32)))
           - jnp.exp(jnp.sum(lq2.astype(f32) * lk2.astype(f32))) + lambda_init)
    slopes = alibi_slopes(N_HEADS_ATTN)
    k_t = k.transpose(0, 2, 3, 1, 4)
    v_t = v.transpose(0, 2, 1, 3)
    q_blocks = q.reshape(b, nblk, Q_BLOCK, N_HEADS_ATTN, 2, HEAD_DIM_ATTN)
    q_blocks = q_blocks.transpose(1, 0, 3, 4, 2, 5)
    pos_k = jnp.arange(S, dtype=jnp.int32)
    starts = jnp.arange(nblk, dtype=jnp.int32) * Q_BLOCK
    scale = HEAD_DIM_ATTN ** -0.5

    def block(args):
        qb, start = args
        s = jnp.einsum('bhcqd,bhckd->bhcqk', qb, k_t).astype(f32) * scale
        pos_q = start + jnp.arange(Q_BLOCK, dtype=jnp.int32)
        dist = jnp.abs(pos_q[:, None] - pos_k[None, :]).astype(f32)
        s = s - slopes[:, None, None, None] * dist
        p = jax.nn.softmax(s, axis=-1)
        a = p[:, :, 0] - lam * p[:, :, 1]
        return jnp.einsum('bhqk,bhkd->bhqd', a.astype(v_t.dtype), v_t)

    o = lax.map(block, (q_blocks, starts))
    o = o.transpose(1, 0, 3, 2, 4).reshape(b, S, N_HEADS_ATTN, V_DIM_ATTN)
    o = rmsnorm_2(o, subln_w) * (1.0 - lambda_init)
    return o.reshape(b, S, ATTN_WIDTH)

def depthwise_conv_centred(u, w, bias):
    out = lax.conv_general_dilated(
        u, w[:, None, :].astype(u.dtype), window_strides=(1,),
        padding=[(CONV_WIDTH_2 // 2, CONV_WIDTH_2 // 2)],
        dimension_numbers=('NWC', 'WIO', 'NWC'),
        feature_group_count=u.shape[-1])
    return out + bias.astype(out.dtype)

def segsum_exp(cs):
    T = cs.shape[-1]
    diff = cs[..., :, None] - cs[..., None, :]
    mask = jnp.tril(jnp.ones((T, T), dtype=bool))
    return jnp.exp(jnp.where(mask, diff, -jnp.inf))

def ssd_scan(xh, dt, A, Bg, Cg):
    b, S, G, R, P = xh.shape
    nc = S // CHUNK
    dA = dt * A
    xc = (xh * dt[..., None].astype(xh.dtype)).reshape(b, nc, CHUNK, G, R, P)
    Bc = Bg.reshape(b, nc, CHUNK, G, SSM_STATE)
    Cc = Cg.reshape(b, nc, CHUNK, G, SSM_STATE)
    acs = jnp.cumsum(dA.reshape(b, nc, CHUNK, G, R).transpose(0, 3, 4, 1, 2), axis=-1)
    L = segsum_exp(acs)
    cb = jnp.einsum('bclgn,bcsgn->bcgls', Cc, Bc)
    y_diag = jnp.einsum('bcgls,bgrcls,bcsgrp->bclgrp', cb, L, xc)
    decay_states = jnp.exp(acs[..., -1:] - acs)
    states = jnp.einsum('bclgn,bgrcl,bclgrp->bcgrpn', Bc, decay_states, xc)
    states = jnp.concatenate([jnp.zeros_like(states[:, :1]), states], axis=1)
    chunk_tot = jnp.pad(acs[..., -1], ((0, 0), (0, 0), (0, 0), (1, 0)))
    decay_chunk = segsum_exp(jnp.cumsum(chunk_tot, axis=-1))
    new_states = jnp.einsum('bgrzc,bcgrpn->bzgrpn', decay_chunk, states)
    states = new_states[:, :-1]
    y_off = jnp.einsum('bclgn,bcgrpn,bgrcl->bclgrp', Cc, states, jnp.exp(acs))
    return (y_diag + y_off).reshape(b, S, G, R, P)

def ssd_mixer(z, xbc, dt_raw, conv_w, conv_b, dt_bias_fwd, dt_bias_bwd,
              a_log_fwd, a_log_bwd, d_skip, norm_w):
    b, S = z.shape[0], z.shape[1]
    xbc = jax.nn.silu(depthwise_conv_centred(xbc, conv_w, conv_b))
    xs = xbc[..., :SSM_WIDTH]
    Bg = xbc[..., SSM_WIDTH:SSM_WIDTH + SSM_GROUPS * SSM_STATE].reshape(b, S, SSM_GROUPS, SSM_STATE)
    Cg = xbc[..., SSM_WIDTH + SSM_GROUPS * SSM_STATE:].reshape(b, S, SSM_GROUPS, SSM_STATE)
    xh = xs.reshape(b, S, SSM_GROUPS, SSM_HEADS_PER_GROUP, SSM_HEADDIM)
    dt32 = dt_raw.astype(jnp.float32)

    def direction(xh_d, B_d, C_d, dt_d, dt_bias, a_log):
        dt = jax.nn.softplus(dt_d + dt_bias.astype(jnp.float32))
        dt = dt.reshape(b, S, SSM_GROUPS, SSM_HEADS_PER_GROUP)
        A = -jnp.exp(a_log.astype(jnp.float32)).reshape(SSM_GROUPS, SSM_HEADS_PER_GROUP)
        return ssd_scan(xh_d, dt, A, B_d, C_d)

    flip = lambda t: jnp.flip(t, axis=1)
    y_f = direction(xh, Bg, Cg, dt32, dt_bias_fwd, a_log_fwd)
    y_b = flip(direction(flip(xh), flip(Bg), flip(Cg), flip(dt32), dt_bias_bwd, a_log_bwd))
    D = d_skip.reshape(SSM_GROUPS, SSM_HEADS_PER_GROUP)[..., None]
    y = (y_f + y_b + D * xh).astype(z.dtype).reshape(b, S, SSM_WIDTH)
    g = (y * jax.nn.silu(z)).reshape(b, S, SSM_GROUPS, SSM_WIDTH // SSM_GROUPS)
    g32 = g.astype(jnp.float32)
    g32 = g32 * lax.rsqrt(jnp.mean(jnp.square(g32), axis=-1, keepdims=True) + RMS_EPS)
    return (g32.reshape(b, S, SSM_WIDTH) * norm_w.astype(jnp.float32)).astype(z.dtype)

def second_inputs(seed: int = 0) -> dict:
    key = jax.random.key(seed)
    ks = jax.random.split(key, 24)
    f32 = jnp.float32

    def nrm(k, shape, scale):
        return jax.random.normal(k, shape, f32) * scale

    def dt_bias(k):
        dt = jnp.exp(jax.random.uniform(k, (DEPTH, N_HEADS_SSM), f32, math.log(1e-3), math.log(1e-1)))
        return dt + jnp.log(-jnp.expm1(-dt))

    def a_log(k):
        return jnp.log(jax.random.uniform(k, (DEPTH, N_HEADS_SSM), f32, 1.0, 16.0))

    return {
        "x": nrm(ks[0], (BATCH, SEQ, D_MODEL), 1.0),
        "w_in": nrm(ks[1], (DEPTH, D_MODEL, IN_COLS), D_MODEL ** -0.5),
        "lambda_q1": nrm(ks[2], (DEPTH, HEAD_DIM_ATTN), 0.1),
        "lambda_k1": nrm(ks[3], (DEPTH, HEAD_DIM_ATTN), 0.1),
        "lambda_q2": nrm(ks[4], (DEPTH, HEAD_DIM_ATTN), 0.1),
        "lambda_k2": nrm(ks[5], (DEPTH, HEAD_DIM_ATTN), 0.1),
        "subln_w": 1.0 + nrm(ks[6], (DEPTH, V_DIM_ATTN), 0.02),
        "conv_w": nrm(ks[7], (DEPTH, CONV_WIDTH_2, CONV_CH), CONV_WIDTH_2 ** -0.5),
        "conv_b": nrm(ks[8], (DEPTH, CONV_CH), 0.02),
        "dt_bias_fwd": dt_bias(ks[9]),
        "dt_bias_bwd": dt_bias(ks[10]),
        "a_log_fwd": a_log(ks[11]),
        "a_log_bwd": a_log(ks[12]),
        "d_skip": 1.0 + nrm(ks[13], (DEPTH, N_HEADS_SSM), 0.02),
        "ssm_norm_w": 1.0 + nrm(ks[14], (DEPTH, SSM_WIDTH), 0.02),
        "w_out": nrm(ks[15], (DEPTH, D_MIX, D_MODEL), D_MIX ** -0.5 * DEEPNORM_BETA),
        "ln1_g": 1.0 + nrm(ks[16], (DEPTH, D_MODEL), 0.02),
        "ln1_b": nrm(ks[17], (DEPTH, D_MODEL), 0.02),
        "w_gate": nrm(ks[18], (DEPTH, D_MODEL, D_FF_2), D_MODEL ** -0.5),
        "w_up": nrm(ks[19], (DEPTH, D_MODEL, D_FF_2), D_MODEL ** -0.5),
        "w_down": nrm(ks[20], (DEPTH, D_FF_2, D_MODEL), D_FF_2 ** -0.5 * DEEPNORM_BETA),
        "ln2_g": 1.0 + nrm(ks[21], (DEPTH, D_MODEL), 0.02),
        "ln2_b": nrm(ks[22], (DEPTH, D_MODEL), 0.02),
    }

def second_block(x, w_in, lambda_q1, lambda_k1, lambda_q2, lambda_k2, subln_w, conv_w, conv_b,
              dt_bias_fwd, dt_bias_bwd, a_log_fwd, a_log_bwd, d_skip, ssm_norm_w, w_out,
              ln1_g, ln1_b, w_gate, w_up, w_down, ln2_g, ln2_b):
    b, S = x.shape[0], x.shape[1]
    splits = np.cumsum([Q_COLS, K_COLS, V_COLS, Z_COLS, XBC_COLS]).tolist()
    for l in range(DEPTH):
        lambda_init = 0.8 - 0.6 * math.exp(-0.3 * l)
        h = jnp.einsum('bsd,de->bse', x, w_in[l])
        q, k, v, z, xbc, dt_raw = jnp.split(h, splits, axis=-1)
        attn_out = diff_attention(
            q.reshape(b, S, N_HEADS_ATTN, 2, HEAD_DIM_ATTN),
            k.reshape(b, S, N_HEADS_ATTN, 2, HEAD_DIM_ATTN),
            v.reshape(b, S, N_HEADS_ATTN, V_DIM_ATTN),
            lambda_q1[l], lambda_k1[l], lambda_q2[l], lambda_k2[l], subln_w[l], lambda_init)
        ssd_out = ssd_mixer(z, xbc, dt_raw, conv_w[l], conv_b[l], dt_bias_fwd[l], dt_bias_bwd[l],
                            a_log_fwd[l], a_log_bwd[l], d_skip[l], ssm_norm_w[l])
        mix = jnp.einsum('bse,ed->bsd', jnp.concatenate([attn_out, ssd_out], axis=-1), w_out[l])
        x = layernorm_2(DEEPNORM_ALPHA * x + mix, ln1_g[l], ln1_b[l])
        hid = jax.nn.silu(jnp.einsum('bsd,df->bsf', x, w_gate[l])) * jnp.einsum('bsd,df->bsf', x, w_up[l])
        ffn = jnp.einsum('bsf,fd->bsd', hid, w_down[l])
        x = layernorm_2(DEEPNORM_ALPHA * x + ffn, ln2_g[l], ln2_b[l])
    return x


_first_inputs_2 = second_inputs


def second_inputs(seed=0):
    import zlib

    import numpy as np

    out = dict(_first_inputs_2(seed))
    spreads = {}
    factors = {'lambda_k2': 6.289,
     'subln_w': 8.0,
     'conv_b': 5.441,
     'd_skip': 8.0,
     'ssm_norm_w': 8.0,
     'ln1_g': 2.748,
     'ln1_b': 2.739,
     'ln2_g': 2.752,
     'ln2_b': 2.828}
    for name, (base, spread) in spreads.items():
        noise = np.random.default_rng([zlib.crc32(name.encode()), seed]).standard_normal(out[name].shape)
        drawn = base * np.exp(spread * noise) if base else spread * noise
        out[name] = __import__('jax').numpy.asarray(drawn.astype(out[name].dtype))
    for name, factor in factors.items():
        out[name] = (out[name] * factor).astype(out[name].dtype)
    return out


_narrow_inputs_2 = second_inputs


def second_inputs(seed=0):

    out = dict(_narrow_inputs_2(seed))
    wider = {'subln_w': 4.07, 'd_skip': 5.3, 'ssm_norm_w': 3.56, 'ln2_g': 3.09, 'ln2_b': 3.1}
    for name, times in wider.items():
        mean = out[name].mean()
        out[name] = (mean + times * (out[name] - mean)).astype(out[name].dtype)
    return out


N_MEM = 256

NSA_WIDTH = D_MODEL // 2
HG_WIDTH = D_MODEL - NSA_WIDTH

NSA_HEAD_DIM = 64
NSA_HEADS = NSA_WIDTH // NSA_HEAD_DIM
NSA_KV_GROUPS = 2
NSA_HPG = NSA_HEADS // NSA_KV_GROUPS
CMP_BLOCK = 32
CMP_STRIDE = 16
CMP_HIDDEN = 256
SEL_BLOCK = 64
SEL_TOP_N = 16
WINDOW = 512
FORCE_BONUS = 1.0e4

HG_KEY_DIM = 128
HG_VAL_DIM = 128
HG_HEADS = HG_WIDTH // HG_VAL_DIM
HG_CHUNK = 64

XA_HEADS = 4
XA_HEAD_DIM = D_MODEL // XA_HEADS

MOE_GROUPS = 4
MOE_EXPERTS_PER_GROUP = 8
MOE_N_EXPERTS = MOE_GROUPS * MOE_EXPERTS_PER_GROUP
MOE_TOP_K = 2
MOE_D_FF = 512
MOE_BLOCK = 128

DEEPNORM_ALPHA_3 = (2.0 * DEPTH) ** 0.25
DEEPNORM_BETA_3 = (8.0 * DEPTH) ** -0.25

RMS_EPS_3 = 1e-6
NEG_INF = -1e30

NSA_Q_COLS = NSA_HEADS * NSA_HEAD_DIM
NSA_KV_COLS = NSA_KV_GROUPS * NSA_HEAD_DIM
NSA_GATE_COLS = NSA_HEADS * 3
HG_QF_COLS = HG_HEADS * HG_KEY_DIM
HG_IV_COLS = HG_HEADS * HG_VAL_DIM
IN_SPLITS = (NSA_Q_COLS, NSA_KV_COLS, NSA_KV_COLS, NSA_KV_COLS, NSA_KV_COLS, NSA_KV_COLS, NSA_KV_COLS,
             NSA_GATE_COLS, HG_QF_COLS, HG_QF_COLS, HG_IV_COLS, HG_IV_COLS)
VALUE_SPLITS = (False, False, True, False, True, False, True, False, False, False, True, False)
IN_COLS_3 = NSA_Q_COLS + 6 * NSA_KV_COLS + NSA_GATE_COLS + 2 * HG_QF_COLS + 2 * HG_IV_COLS


def layer_norm(x, g, b):
    xf = x.astype(jnp.float32)
    mu = jnp.mean(xf, axis=-1, keepdims=True)
    var = jnp.mean(jnp.square(xf - mu), axis=-1, keepdims=True)
    return ((xf - mu) * lax.rsqrt(var + LN_EPS) * g + b).astype(x.dtype)

def rms_norm(x, g):
    xf = x.astype(jnp.float32)
    return xf * lax.rsqrt(jnp.mean(xf * xf, axis=-1, keepdims=True) + RMS_EPS_3) * g

def masked_softmax(s, mask):
    s = jnp.where(mask, s.astype(jnp.float32), NEG_INF)
    p = jax.nn.softmax(s, axis=-1)
    return jnp.where(mask, p, 0.0)

def split_cols_3(h):
    offs = np.cumsum((0,) + IN_SPLITS)
    return [h[..., int(offs[i]):int(offs[i + 1])] for i in range(len(IN_SPLITS))]

def nsa_compress(k, pe, w1, w2):
    b, s, g, d = k.shape
    n_sub = CMP_BLOCK // CMP_STRIDE
    n_ch = s // CMP_STRIDE
    ncmp = n_ch - n_sub + 1
    ch = k.reshape(b, n_ch, CMP_STRIDE, g, d)
    blocks = jnp.concatenate([ch[:, i:i + ncmp] for i in range(n_sub)], axis=2)
    blocks = blocks + pe[None, None, :, None, :]
    blocks = jnp.moveaxis(blocks, 3, 1).reshape(b, g, ncmp, CMP_BLOCK * d)
    return jax.nn.gelu(blocks @ w1) @ w2

def cmp_to_sel(p, n_sel):
    n_sub = CMP_BLOCK // CMP_STRIDE
    r = SEL_BLOCK // CMP_STRIDE
    ncmp = p.shape[-1]
    pp = jnp.pad(p, [(0, 0)] * (p.ndim - 1) + [(n_sub - 1, r * n_sel - ncmp)])
    return sum(pp[..., m:m + r * n_sel:r] for m in range(r + n_sub - 1))

def nsa_attention(q, kc, vc, ks, vs, kw, vw, gates):
    b, h, s, d = q.shape
    g = NSA_KV_GROUPS
    ncmp = kc.shape[2]
    n_sel = s // SEL_BLOCK
    top_n = min(SEL_TOP_N, n_sel)
    scale = d ** -0.5
    kw_pad = jnp.pad(kw, ((0, 0), (0, 0), (WINDOW, 0), (0, 0)))
    vw_pad = jnp.pad(vw, ((0, 0), (0, 0), (WINDOW, 0), (0, 0)))
    cmp_end = jnp.arange(ncmp) * CMP_STRIDE + CMP_BLOCK - 1
    blk_ids = jnp.arange(n_sel)
    bi = jnp.arange(b)[:, None, None, None]
    gi = jnp.arange(g)[None, :, None, None]
    offs = jnp.arange(SEL_BLOCK)

    def one_block(qb):
        s0 = qb * Q_BLOCK
        t = s0 + jnp.arange(Q_BLOCK)
        qq = lax.dynamic_slice_in_dim(q, s0, Q_BLOCK, axis=2)
        qq = qq.reshape(b, g, NSA_HPG, Q_BLOCK, d) * scale
        sc = jnp.einsum('bgrtd,bgnd->bgrtn', qq, kc)
        pc = masked_softmax(sc, cmp_end[None, :] <= t[:, None])
        o_c = jnp.einsum('bgrtn,bgnd->bgrtd', pc.astype(vc.dtype), vc)
        imp = cmp_to_sel(jnp.sum(pc, axis=2), n_sel)
        cur = t // SEL_BLOCK
        valid = blk_ids[None, :] <= cur[:, None]
        forced = ((blk_ids[None, :] == 0) | (blk_ids[None, :] == cur[:, None])
                  | (blk_ids[None, :] == cur[:, None] - 1))
        score = jnp.where(valid, imp + jnp.where(forced, FORCE_BONUS, 0.0), -1.0)
        _, idx = lax.top_k(score, top_n)
        pos = (idx[..., None] * SEL_BLOCK + offs).reshape(b, g, Q_BLOCK, top_n * SEL_BLOCK)
        k_sel = ks[bi, gi, pos]
        v_sel = vs[bi, gi, pos]
        ss = jnp.einsum('bgrtd,bgtkd->bgrtk', qq, k_sel)
        ps = masked_softmax(ss, (pos <= t[None, None, :, None])[:, :, None])
        o_s = jnp.einsum('bgrtk,bgtkd->bgrtd', ps.astype(v_sel.dtype), v_sel)
        kwb = lax.dynamic_slice_in_dim(kw_pad, s0, WINDOW + Q_BLOCK, axis=2)
        vwb = lax.dynamic_slice_in_dim(vw_pad, s0, WINDOW + Q_BLOCK, axis=2)
        kpos = s0 - WINDOW + jnp.arange(WINDOW + Q_BLOCK)
        m_w = ((kpos[None, :] <= t[:, None]) & (kpos[None, :] > t[:, None] - WINDOW)
               & (kpos[None, :] >= 0))
        sw = jnp.einsum('bgrtd,bgkd->bgrtk', qq, kwb)
        pw = masked_softmax(sw, m_w)
        o_w = jnp.einsum('bgrtk,bgkd->bgrtd', pw.astype(vwb.dtype), vwb)
        gb = lax.dynamic_slice_in_dim(gates, s0, Q_BLOCK, axis=2).reshape(b, g, NSA_HPG, Q_BLOCK, 3)
        o = gb[..., 0:1] * o_c + gb[..., 1:2] * o_s + gb[..., 2:3] * o_w
        return o.reshape(b, h, Q_BLOCK, d)

    out = lax.map(one_block, jnp.arange(s // Q_BLOCK))
    return jnp.transpose(out, (1, 0, 3, 2, 4)).reshape(b, s, h * d)

def hgrn2_recurrence(q, f_logit, i, lb):
    b, s, h, dk = q.shape
    dv = i.shape[-1]
    lb = lb.reshape(h, dk)
    log_f = jnp.logaddexp(jnp.log(lb), jnp.log1p(-lb) + jax.nn.log_sigmoid(f_logit.astype(jnp.float32)))
    k = -jnp.expm1(log_f)
    nc = s // HG_CHUNK

    def to_chunks(a):
        return jnp.transpose(a.astype(jnp.float32).reshape(b, nc, HG_CHUNK, h, a.shape[-1]), (1, 0, 3, 2, 4))

    qc, kc, vc, lc = to_chunks(q), to_chunks(k), to_chunks(i), to_chunks(log_f)
    bc = jnp.cumsum(lc, axis=3)
    causal = jnp.tril(jnp.ones((HG_CHUNK, HG_CHUNK), dtype=bool))

    def step(state, xs):
        qt, kt, vt, bt = xs
        inter = jnp.einsum('bhtk,bhkv->bhtv', qt * jnp.exp(bt), state)
        diff = bt[:, :, :, None, :] - bt[:, :, None, :, :]
        decay = jnp.where(causal[:, :, None], jnp.exp(jnp.minimum(diff, 0.0)), 0.0)
        att = jnp.einsum('bhtk,bhsk,bhtsk->bhts', qt, kt, decay)
        intra = jnp.einsum('bhts,bhsv->bhtv', att, vt)
        b_last = bt[:, :, -1:, :]
        new_state = (jnp.exp(b_last[:, :, 0, :])[..., None] * state
                     + jnp.einsum('bhsk,bhsv->bhkv', kt * jnp.exp(b_last - bt), vt))
        return new_state, inter + intra

    s_init = jnp.zeros((b, h, dk, dv), jnp.float32)
    _, o = lax.scan(step, s_init, (qc, kc, vc, bc))
    return jnp.transpose(o, (1, 0, 3, 2, 4)).reshape(b, s, h, dv)

def memory_cross_attention(x, mem, wq, wk, wv, wo):
    b, s, d = x.shape
    m = mem.shape[1]
    q = (x @ wq).reshape(b, s, XA_HEADS, XA_HEAD_DIM)
    k = (mem @ wk).reshape(b, m, XA_HEADS, XA_HEAD_DIM)
    v = (mem @ wv).reshape(b, m, XA_HEADS, XA_HEAD_DIM)
    sc = jnp.einsum('bshd,bmhd->bhsm', q, k).astype(jnp.float32) * (XA_HEAD_DIM ** -0.5)
    p = jax.nn.softmax(sc, axis=-1).astype(v.dtype)
    o = jnp.einsum('bhsm,bmhd->bshd', p, v).reshape(b, s, d)
    return o @ wo

def hierarchical_moe(x, w_group, b_group, w_expert, b_expert, w_gate, w_up, w_down):
    b, s, d = x.shape
    xt = x.reshape(-1, d)
    n_tok = xt.shape[0]
    g_prob = jax.nn.softmax((xt @ w_group + b_group).astype(jnp.float32), axis=-1)
    g_w, g_idx = lax.top_k(g_prob, 1)
    e_logits = (xt @ w_expert + b_expert).astype(jnp.float32).reshape(n_tok, MOE_GROUPS, MOE_EXPERTS_PER_GROUP)
    e_logits = e_logits[jnp.arange(n_tok), g_idx[:, 0]]
    top_p, top_i = lax.top_k(jax.nn.softmax(e_logits, axis=-1), MOE_TOP_K)
    top_p = top_p / jnp.sum(top_p, axis=-1, keepdims=True)
    weights = (g_w * top_p).reshape(-1)
    experts = (g_idx * MOE_EXPERTS_PER_GROUP + top_i).reshape(-1)
    tokens = jnp.repeat(jnp.arange(n_tok, dtype=jnp.int32), MOE_TOP_K)
    n_assign = n_tok * MOE_TOP_K
    order = jnp.argsort(experts)
    e_sorted, tok_sorted, w_sorted = experts[order], tokens[order], weights[order]
    counts = jnp.bincount(experts, length=MOE_N_EXPERTS)
    padded = ((counts + MOE_BLOCK - 1) // MOE_BLOCK) * MOE_BLOCK
    start = jnp.cumsum(counts) - counts
    pend = jnp.cumsum(padded)
    pstart = pend - padded
    dest = pstart[e_sorted] + (jnp.arange(n_assign) - start[e_sorted])
    cap = n_assign + MOE_N_EXPERTS * MOE_BLOCK
    n_blocks = cap // MOE_BLOCK
    slot_tok = jnp.full((cap,), n_tok, jnp.int32).at[dest].set(tok_sorted)
    slot_w = jnp.zeros((cap,), jnp.float32).at[dest].set(w_sorted)
    block_expert = jnp.minimum(jnp.searchsorted(pend, jnp.arange(n_blocks) * MOE_BLOCK, side='right'),
                               MOE_N_EXPERTS - 1)
    x_pad = jnp.concatenate([xt, jnp.zeros((1, d), xt.dtype)], axis=0)
    xb = x_pad[slot_tok].reshape(n_blocks, MOE_BLOCK, d)

    def run_block(args):
        xblk, e = args
        hid = jax.nn.silu(xblk @ w_gate[e]) * (xblk @ w_up[e])
        return hid @ w_down[e]

    yb = lax.map(run_block, (xb, block_expert)).reshape(cap, d)
    y = yb * slot_w[:, None].astype(yb.dtype)
    out = jax.ops.segment_sum(y, slot_tok, num_segments=n_tok + 1)[:n_tok]
    return out.reshape(b, s, d)

def third_inputs(seed: int = 0) -> dict:
    key = jax.random.key(seed)
    ks = jax.random.split(key, 32)
    f32 = jnp.float32
    nrm = lambda k, shape, sc: jax.random.normal(k, shape, f32) * sc
    beta = DEEPNORM_BETA_3
    col_scale = jnp.concatenate([jnp.full((n,), beta if v else 1.0, f32) for n, v in zip(IN_SPLITS, VALUE_SPLITS)])
    ln_g = lambda k: 1.0 + nrm(k, (DEPTH, D_MODEL), 0.02)
    ln_b = lambda k: nrm(k, (DEPTH, D_MODEL), 0.02)
    return {
        "x": nrm(ks[0], (BATCH, SEQ, D_MODEL), 1.0),
        "mem": nrm(ks[1], (BATCH, N_MEM, D_MODEL), 1.0),
        "w_in": nrm(ks[2], (DEPTH, D_MODEL, IN_COLS_3), D_MODEL ** -0.5) * col_scale,
        "cmp_pe_k": nrm(ks[3], (DEPTH, CMP_BLOCK, NSA_HEAD_DIM), 0.1),
        "cmp_pe_v": nrm(ks[4], (DEPTH, CMP_BLOCK, NSA_HEAD_DIM), 0.1),
        "cmp_w1_k": nrm(ks[5], (DEPTH, CMP_BLOCK * NSA_HEAD_DIM, CMP_HIDDEN), (CMP_BLOCK * NSA_HEAD_DIM) ** -0.5),
        "cmp_w2_k": nrm(ks[6], (DEPTH, CMP_HIDDEN, NSA_HEAD_DIM), CMP_HIDDEN ** -0.5),
        "cmp_w1_v": nrm(ks[7], (DEPTH, CMP_BLOCK * NSA_HEAD_DIM, CMP_HIDDEN), (CMP_BLOCK * NSA_HEAD_DIM) ** -0.5),
        "cmp_w2_v": nrm(ks[8], (DEPTH, CMP_HIDDEN, NSA_HEAD_DIM), CMP_HIDDEN ** -0.5),
        "nsa_norm_g": 1.0 + nrm(ks[9], (DEPTH, NSA_WIDTH), 0.02),
        "hg_lb_logits": nrm(ks[10], (DEPTH + 1, HG_HEADS * HG_KEY_DIM), 0.5),
        "hg_norm_g": 1.0 + nrm(ks[11], (DEPTH, HG_VAL_DIM), 0.02),
        "w_out": nrm(ks[12], (DEPTH, D_MODEL, D_MODEL), D_MODEL ** -0.5 * beta),
        "ln1_g": ln_g(ks[13]),
        "ln1_b": ln_b(ks[14]),
        "xa_wq": nrm(ks[15], (DEPTH, D_MODEL, D_MODEL), D_MODEL ** -0.5),
        "xa_wk": nrm(ks[16], (DEPTH, D_MODEL, D_MODEL), D_MODEL ** -0.5),
        "xa_wv": nrm(ks[17], (DEPTH, D_MODEL, D_MODEL), D_MODEL ** -0.5 * beta),
        "xa_wo": nrm(ks[18], (DEPTH, D_MODEL, D_MODEL), D_MODEL ** -0.5 * beta),
        "ln2_g": ln_g(ks[19]),
        "ln2_b": ln_b(ks[20]),
        "moe_w_group": nrm(ks[21], (DEPTH, D_MODEL, MOE_GROUPS), D_MODEL ** -0.5),
        "moe_b_group": nrm(ks[22], (DEPTH, MOE_GROUPS), 0.01),
        "moe_w_expert": nrm(ks[23], (DEPTH, D_MODEL, MOE_N_EXPERTS), D_MODEL ** -0.5),
        "moe_b_expert": nrm(ks[24], (DEPTH, MOE_N_EXPERTS), 0.01),
        "moe_w_gate": nrm(ks[25], (DEPTH, MOE_N_EXPERTS, D_MODEL, MOE_D_FF), D_MODEL ** -0.5),
        "moe_w_up": nrm(ks[26], (DEPTH, MOE_N_EXPERTS, D_MODEL, MOE_D_FF), D_MODEL ** -0.5 * beta),
        "moe_w_down": nrm(ks[27], (DEPTH, MOE_N_EXPERTS, MOE_D_FF, D_MODEL), MOE_D_FF ** -0.5 * beta),
        "ln3_g": ln_g(ks[28]),
        "ln3_b": ln_b(ks[29]),
    }

def third_block(x, mem, w_in, cmp_pe_k, cmp_pe_v, cmp_w1_k, cmp_w2_k, cmp_w1_v, cmp_w2_v, nsa_norm_g,
              hg_lb_logits, hg_norm_g, w_out, ln1_g, ln1_b, xa_wq, xa_wk, xa_wv, xa_wo, ln2_g, ln2_b,
              moe_w_group, moe_b_group, moe_w_expert, moe_b_expert, moe_w_gate, moe_w_up, moe_w_down,
              ln3_g, ln3_b):
    b, s, _ = x.shape
    lb_all = jnp.cumsum(jax.nn.softmax(hg_lb_logits.astype(jnp.float32), axis=0), axis=0)
    for l in range(DEPTH):
        h = x @ w_in[l]
        (nq, nkc, nvc, nks, nvs, nkw, nvw, ngate, hq, hf, hi, hgate) = split_cols_3(h)
        kv = lambda a: a.reshape(b, s, NSA_KV_GROUPS, NSA_HEAD_DIM)
        kc = nsa_compress(kv(nkc), cmp_pe_k[l], cmp_w1_k[l], cmp_w2_k[l])
        vc = nsa_compress(kv(nvc), cmp_pe_v[l], cmp_w1_v[l], cmp_w2_v[l])
        tr = lambda a: jnp.transpose(kv(a), (0, 2, 1, 3))
        q_nsa = jnp.transpose(nq.reshape(b, s, NSA_HEADS, NSA_HEAD_DIM), (0, 2, 1, 3))
        gates = jnp.transpose(jax.nn.sigmoid(ngate.reshape(b, s, NSA_HEADS, 3)), (0, 2, 1, 3))
        o_nsa = nsa_attention(q_nsa, kc, vc, tr(nks), tr(nvs), tr(nkw), tr(nvw), gates)
        o_nsa = rms_norm(o_nsa, nsa_norm_g[l])
        o_hg = hgrn2_recurrence(hq.reshape(b, s, HG_HEADS, HG_KEY_DIM),
                                hf.reshape(b, s, HG_HEADS, HG_KEY_DIM),
                                hi.reshape(b, s, HG_HEADS, HG_VAL_DIM), lb_all[l])
        o_hg = rms_norm(o_hg, hg_norm_g[l]) * jax.nn.silu(
            hgate.reshape(b, s, HG_HEADS, HG_VAL_DIM).astype(jnp.float32))
        o_hg = o_hg.reshape(b, s, HG_WIDTH)
        mix = jnp.concatenate([o_nsa.astype(x.dtype), o_hg.astype(x.dtype)], axis=-1) @ w_out[l]
        x = layer_norm(DEEPNORM_ALPHA_3 * x + mix, ln1_g[l], ln1_b[l])
        xa = memory_cross_attention(x, mem, xa_wq[l], xa_wk[l], xa_wv[l], xa_wo[l])
        x = layer_norm(DEEPNORM_ALPHA_3 * x + xa, ln2_g[l], ln2_b[l])
        ff = hierarchical_moe(x, moe_w_group[l], moe_b_group[l], moe_w_expert[l], moe_b_expert[l],
                              moe_w_gate[l], moe_w_up[l], moe_w_down[l])
        x = layer_norm(DEEPNORM_ALPHA_3 * x + ff, ln3_g[l], ln3_b[l])
    return x


_first_inputs_3 = third_inputs


def third_inputs(seed=0):
    import zlib

    import numpy as np

    out = dict(_first_inputs_3(seed))
    spreads = {}
    factors = {'cmp_pe_k': 6.677,
     'nsa_norm_g': 20.86,
     'hg_norm_g': 33.349,
     'ln1_b': 2.709,
     'ln2_b': 2.679,
     'moe_b_group': 25.525,
     'moe_b_expert': 28.689,
     'ln3_g': 7.517,
     'ln3_b': 8.039}
    for name, (base, spread) in spreads.items():
        noise = np.random.default_rng([zlib.crc32(name.encode()), seed]).standard_normal(out[name].shape)
        drawn = base * np.exp(spread * noise) if base else spread * noise
        out[name] = __import__('jax').numpy.asarray(drawn.astype(out[name].dtype))
    for name, factor in factors.items():
        out[name] = (out[name] * factor).astype(out[name].dtype)
    return out


_narrow_inputs_3 = third_inputs


def third_inputs(seed=0):

    out = dict(_narrow_inputs_3(seed))
    wider = {'nsa_norm_g': 4.12, 'hg_norm_g': 3.97, 'ln3_g': 3.08, 'ln3_b': 3.08}
    for name, times in wider.items():
        mean = out[name].mean()
        out[name] = (mean + times * (out[name] - mean)).astype(out[name].dtype)
    return out


def setup_inputs(seed=0):
    out = dict(first_inputs(seed))
    for name, value in second_inputs(seed + 1).items():
        if name != "x":
            out[name + "_2"] = value
    for name, value in third_inputs(seed + 2).items():
        if name != "x":
            out[name + "_3"] = value
    return out


def reference(
    x, positions, norm_mix_pre, w_in, gate_b, q_norm, w_uq, kv_norm, w_ukv, w_br_mla, sg_ln_g,
    sg_ln_b, sg_w, sg_b, w_br_sg, conv_w, w_br_conv, pool_w, pool_scale, w_br_pool, w_out,
    norm_mix_post, norm_ffn_pre, w_ff1, w_ff2, norm_ffn_post, w_in_2, lambda_q1_2, lambda_k1_2,
    lambda_q2_2, lambda_k2_2, subln_w_2, conv_w_2, conv_b_2, dt_bias_fwd_2, dt_bias_bwd_2,
    a_log_fwd_2, a_log_bwd_2, d_skip_2, ssm_norm_w_2, w_out_2, ln1_g_2, ln1_b_2, w_gate_2,
    w_up_2, w_down_2, ln2_g_2, ln2_b_2, mem_3, w_in_3, cmp_pe_k_3, cmp_pe_v_3, cmp_w1_k_3,
    cmp_w2_k_3, cmp_w1_v_3, cmp_w2_v_3, nsa_norm_g_3, hg_lb_logits_3, hg_norm_g_3, w_out_3,
    ln1_g_3, ln1_b_3, xa_wq_3, xa_wk_3, xa_wv_3, xa_wo_3, ln2_g_3, ln2_b_3, moe_w_group_3,
    moe_b_group_3, moe_w_expert_3, moe_b_expert_3, moe_w_gate_3, moe_w_up_3, moe_w_down_3,
    ln3_g_3, ln3_b_3,
):
    x = first_block(
        x, positions, norm_mix_pre, w_in, gate_b, q_norm, w_uq, kv_norm, w_ukv, w_br_mla,
        sg_ln_g, sg_ln_b, sg_w, sg_b, w_br_sg, conv_w, w_br_conv, pool_w, pool_scale, w_br_pool,
        w_out, norm_mix_post, norm_ffn_pre, w_ff1, w_ff2, norm_ffn_post,
    )
    x = second_block(
        x, w_in_2, lambda_q1_2, lambda_k1_2, lambda_q2_2, lambda_k2_2, subln_w_2, conv_w_2,
        conv_b_2, dt_bias_fwd_2, dt_bias_bwd_2, a_log_fwd_2, a_log_bwd_2, d_skip_2,
        ssm_norm_w_2, w_out_2, ln1_g_2, ln1_b_2, w_gate_2, w_up_2, w_down_2, ln2_g_2, ln2_b_2,
    )
    return third_block(
        x, mem_3, w_in_3, cmp_pe_k_3, cmp_pe_v_3, cmp_w1_k_3, cmp_w2_k_3, cmp_w1_v_3,
        cmp_w2_v_3, nsa_norm_g_3, hg_lb_logits_3, hg_norm_g_3, w_out_3, ln1_g_3, ln1_b_3,
        xa_wq_3, xa_wk_3, xa_wv_3, xa_wo_3, ln2_g_3, ln2_b_3, moe_w_group_3, moe_b_group_3,
        moe_w_expert_3, moe_b_expert_3, moe_w_gate_3, moe_w_up_3, moe_w_down_3, ln3_g_3,
        ln3_b_3,
    )


_drawn_inputs = setup_inputs


def setup_inputs(seed=0):
    import zlib

    import numpy as np

    out = dict(_drawn_inputs(seed))
    spreads = {}
    factors = {'cmp_pe_v_3': 4.774, 'ln1_g_3': 2.701, 'moe_b_group_3': 7.665}
    for name, (base, spread) in spreads.items():
        noise = np.random.default_rng([zlib.crc32(name.encode()), seed]).standard_normal(out[name].shape)
        drawn = base * np.exp(spread * noise) if base else spread * noise
        out[name] = __import__('jax').numpy.asarray(drawn.astype(out[name].dtype))
    for name, factor in factors.items():
        out[name] = (out[name] * factor).astype(out[name].dtype)
    return out
```

```python
import math
from contextlib import ExitStack

import numpy as np

import concourse.bass as bass
from concourse import mybir

F32 = mybir.dt.float32
I32 = mybir.dt.int32
U32 = mybir.dt.uint32
ALU = mybir.AluOpType
ACT = mybir.ActivationFunctionType
AX = mybir.AxisListType

P = 128
S = 512
D = 1024
NT = S // P
KD = D // P
UNIT = 4096
NEG = -1e30
RING = 3


class Signal:

    def __init__(self, sem):
        self.sem, self.base, self.sent = sem, 0, 0

    def up(self, by=1):
        self.sent += by
        return by

    def at(self, n):
        return self.base + n


class Core:

    def __init__(self, nc, ctx):
        self.nc, self.ctx = nc, ctx
        self.signals = {}
        self.arena = ctx.enter_context(nc.sbuf_tensor("arena", [P, 12 * UNIT], F32))
        self.banks = [ctx.enter_context(nc.psum_tensor(f"bank{i}", [P, 512], F32)) for i in range(8)]
        self.chunks = []
        self.at = {}
        self.loaded = [Signal(ctx.enter_context(nc.semaphore(f"weights_loaded{i}"))) for i in range(RING)]
        self.arrived = {}
        self.freed = {}
        self.issued = 0

    def sb(self, name, shape, dt=F32):
        return self.ctx.enter_context(self.nc.sbuf_tensor(name, shape, dt))

    def sig(self, name):
        if name not in self.signals:
            self.signals[name] = Signal(self.ctx.enter_context(self.nc.semaphore(name)))
        s = self.signals[name]
        s.base = s.sent
        return s

    def region(self, unit, off, *shape):
        n = int(np.prod(shape))
        v = self.arena[:, int(unit * UNIT) + off:int(unit * UNIT) + off + n]
        if len(shape) == 2:
            v = v.rearrange("p (a b) -> p a b", a=shape[0])
        if len(shape) == 3:
            v = v.rearrange("p (a b c) -> p a b c", a=shape[0], b=shape[1])
        return v

    def plan(self, key, *parts):
        self.at[key] = len(self.chunks)
        self.chunks.append((key, parts))

    def slot(self, key):
        n = self.at[key]
        out, off = [], (2 + n % RING) * UNIT
        for part in self.chunks[n][1]:
            a, b = part.shape[1], part.shape[2]
            out.append(self.arena[:, off:off + a * b].rearrange("p (a b) -> p a b", a=a))
            off += a * b
        assert off <= (3 + n % RING) * UNIT
        return out

    def load_weights(self, eng):
        while self.issued < len(self.chunks):
            n = self.issued
            if n >= RING:
                if n - RING not in self.freed:
                    return
                sem, count = self.freed[n - RING]
                eng.wait_ge(sem, count)
            for dst, src in zip(self.slot(self.chunks[n][0]), self.chunks[n][1]):
                eng.dma_start(dst, src).then_inc(self.loaded[n % RING].sem, self.loaded[n % RING].up(16))
            self.arrived[n] = self.loaded[n % RING].sent
            self.issued += 1

    def weights(self, eng, key):
        n = self.at[key]
        count = 16 * sum(len(self.chunks[m][1]) for m in range(n % RING, n + 1, RING))
        eng.wait_ge(self.loaded[n % RING].sem, count)
        return self.slot(key)

    def release(self, key, sig):
        self.freed[self.at[key]] = (sig.sem, sig.sent)


def bank_groups(c, groups, nb=8, chained=False):
    filled = c.sig("bank_filled")
    emptied = {"v": c.sig("bank_emptied_by_vector"), "a": c.sig("bank_emptied_by_scalar")}
    own = {"v": c.sig("vector_order"), "a": c.sig("scalar_order")}
    turn, seen = [], {"v": 0, "a": 0}
    for g in groups:
        seen[g[3]] += 1
        turn.append((g[3], seen[g[3]]))

    with c.nc.Block() as block:
        @block.tensor
        def _(pe):
            for n, (needs, products, releases, _, _, *after) in enumerate(groups):
                for m in after[0] if after else ():
                    pe.wait_ge(emptied[turn[m][0]].sem, emptied[turn[m][0]].at(turn[m][1]))
                if n >= nb:
                    who, count = turn[n - nb]
                    pe.wait_ge(emptied[who].sem, emptied[who].at(count))
                for key in needs:
                    c.weights(pe, key)
                products(pe, c.banks[n % nb]).then_inc(filled.sem, filled.up())
                for key in releases:
                    c.release(key, filled)

        def emptier(eng, who):
            for n, (_, _, _, w, empty, *_) in enumerate(groups):
                if w == who:
                    eng.wait_ge(filled.sem, filled.at(n + 1))
                    empty(eng, c.banks[n % nb], own[who]).then_inc(emptied[who].sem, emptied[who].up())
                    if chained:
                        eng.wait_ge(emptied[who].sem, emptied[who].sent)

        @block.vector
        def _(dve):
            emptier(dve, "v")

        @block.scalar
        def _(act):
            emptier(act, "a")

        @block.sync
        def _(sync):
            c.load_weights(sync)


def product(pairs):
    def run(pe, bank):
        for n, (lhsT, rhs) in enumerate(pairs):
            m, w = lhsT.shape[1], rhs.shape[1]
            last = pe.matmul(bank[0:m, 0:w], lhsT, rhs, start=n == 0, stop=n == len(pairs) - 1)
        return last
    return run


def turns(c, sources):
    def run(pe, bank):
        at = 0
        for s in sources:
            q, m = s.shape
            last = pe.transpose(bank[0:m, at:at + q], s, c.ident[0:q, 0:q])
            at += q
        return last
    return run


def copy_to(dst, rows=P, width=None):
    def run(eng, bank, order):
        w = dst.shape[1] if len(dst.shape) == 2 else dst.shape[1] * dst.shape[2]
        src = bank[0:dst.shape[0], 0:w]
        if len(dst.shape) == 3:
            src = src.rearrange("p (a b) -> p a b", a=dst.shape[1])
        if hasattr(eng, "activation"):
            return eng.activation(dst, src, ACT.Copy)
        return eng.tensor_copy(dst, src)
    return run


def scaled_to(dst, gain):
    def run(dve, bank, order):
        m, a, b = dst.shape
        src = bank[0:m, 0:a * b].rearrange("p (a b) -> p a b", a=a)
        return dve.tensor_tensor(dst, src, gain.unsqueeze(2).to_broadcast([m, a, b]), ALU.mult)
    return run


def inverse_rms(c, sources, eps, junk, out):
    squared, mean, root, done = (c.sig(x) for x in ("squares_summed", "mean_ready", "root_ready", "inverse_ready"))
    n = len(sources)
    width = sources[0].shape[1]
    with c.nc.Block() as block:
        @block.scalar
        def _(act):
            for i, s in enumerate(sources):
                act.activation(junk[:, 0:s.shape[1]], s, ACT.Square, accum_out=out[:, i:i + 1]).then_inc(squared.sem, squared.up())
                act.wait_ge(squared.sem, squared.sent)
            act.wait_ge(mean.sem, mean.at(n))
            act.activation(out[:, 0:n], out[:, 0:n], ACT.Sqrt).then_inc(root.sem, root.up())

        @block.vector
        def _(dve):
            dve.wait_ge(squared.sem, squared.at(n))
            for i, s in enumerate(sources):
                dve.tensor_scalar(out[:, i:i + 1], out[:, i:i + 1], 1.0 / s.shape[1], eps, ALU.mult, ALU.add).then_inc(mean.sem, mean.up())
            dve.wait_ge(root.sem, root.at(1))
            dve.reciprocal(out[:, 0:n], out[:, 0:n]).then_inc(done.sem, done.up())

        @block.sync
        def _(sync):
            c.load_weights(sync)


def load_rows(c, eng_name, pairs, also=None):
    got = c.sig("rows_loaded_" + eng_name)
    with c.nc.Block() as block:
        def issue(eng):
            for dst, src in pairs:
                eng.dma_start(dst, src, allow_slow_non_contiguous=True).then_inc(got.sem, got.up(16))
            eng.wait_ge(got.sem, got.at(16 * len(pairs)))
        {"scalar": block.scalar, "gpsimd": block.gpsimd}[eng_name](issue)


def to_features(c, source, dst, gain=None, width=D):
    groups = []
    for i in range(NT):
        for k in range(0, width // P, 4):
            m = min(4, width // P - k)
            view = dst[:, k:k + m, i * P:(i + 1) * P]
            blocks = [source(i)[:, (k + j) * P:(k + j + 1) * P] for j in range(m)]
            if gain is None:
                groups.append(((), turns(c, blocks), (), "a" if k else "v", copy_to(view)))
            else:
                groups.append(((), turns(c, blocks), (), "v", scaled_to(view, gain[:, k:k + m])))
    bank_groups(c, groups)


def layer_norm_in_place(c, x, gain, bias, eps, small, width=D):
    order, var, root, done = (c.sig(n) for n in ("vector_order", "variance_ready", "root_ready", "normed"))
    parts = -(-width // 512)
    stats = small[:, 0:NT * parts * 6].rearrange("p (i a b) -> p i a b", i=NT, a=parts)
    mv = small[:, 64:64 + 2 * NT].rearrange("p (i b) -> p i b", i=NT)
    sd = small[:, 80:80 + NT]
    with c.nc.Block() as block:
        @block.vector
        def _(dve):
            for i in range(NT):
                for a in range(parts):
                    w = min(512, width)
                    dve.bn_stats(stats[:, i, a, :], x(i)[:, a * w:(a + 1) * w]).then_inc(order.sem, order.up())
            dve.wait_ge(order.sem, order.sent)
            for i in range(NT):
                dve.bn_aggr(mv[:, i, :], stats[:, i, :, :]).then_inc(order.sem, order.up())
            dve.wait_ge(order.sem, order.sent)
            dve.tensor_scalar(sd, mv[:, :, 1], 1.0, eps, ALU.mult, ALU.add).then_inc(var.sem, var.up())
            dve.wait_ge(root.sem, root.at(1))
            dve.reciprocal(sd, sd).then_inc(order.sem, order.up())
            dve.wait_ge(order.sem, order.sent)
            for i in range(NT):
                dve.tensor_scalar(x(i), x(i), mv[:, i, 0:1], sd[:, i:i + 1], ALU.subtract, ALU.mult).then_inc(order.sem, order.up())
            for i in range(NT):
                dve.wait_ge(order.sem, order.at(order.sent - order.base - (0 if i else NT - 1)))
                dve.tensor_tensor(x(i), x(i), gain, ALU.mult).then_inc(order.sem, order.up())
            dve.wait_ge(order.sem, order.sent)
            for i in range(NT):
                dve.tensor_tensor(x(i), x(i), bias, ALU.add).then_inc(done.sem, done.up())
            dve.wait_ge(done.sem, done.at(NT))

        @block.scalar
        def _(act):
            act.wait_ge(var.sem, var.at(1))
            act.activation(sd, sd, ACT.Sqrt).then_inc(root.sem, root.up())

        @block.sync
        def _(sync):
            c.load_weights(sync)


ATT_WORK = 5 * 512 + 16
TURN_LAG, MIX_LAG = 4, 5


def attention(c, units, work):
    probs = work[:, 0:1536].rearrange("p (a b) -> p a b", a=3)
    turned = work[:, 1536:2560].rearrange("p (a b) -> p a b", a=2)
    high, total = work[:, 2560:2568], work[:, 2568:2576]
    high_of, total_of = lambda u: high[:, u % 8:u % 8 + 1], lambda u: total[:, u % 8:u % 8 + 1]
    scores, peak, exps, flipped, copied, mixed, finished = (c.sig(n) for n in (
        "scores_ready", "peak_ready", "probs_ready", "probs_turned", "turned_copied", "mixed_ready", "output_written"))
    masked, highest, inverted = c.sig("mask_added"), c.sig("maximum_ready"), c.sig("inverse_ready")
    factor_ready = {}
    N = len(units)

    def tiles(keys):
        return [(k, min(P, keys - k)) for k in range(0, keys, P)]

    with c.nc.Block() as block:
        @block.tensor
        def _(pe):
            for u in range(N + MIX_LAG):
                if u < N:
                    if u >= 4:
                        pe.wait_ge(exps.sem, exps.at(u - 3))
                    units[u]["score"](pe, c.banks[u % 4]).then_inc(scores.sem, scores.up())
                w = u - TURN_LAG
                if 0 <= w < N:
                    pe.wait_ge(exps.sem, exps.at(w + 1))
                    if w >= 2:
                        pe.wait_ge(copied.sem, copied.at(w - 1))
                    for k, m in tiles(units[w]["keys"]):
                        last = pe.transpose(c.banks[4 + w % 2][0:m, k:k + P], probs[:, w % 3, k:k + m], c.ident[:, :])
                    last.then_inc(flipped.sem, flipped.up())
                w = u - MIX_LAG
                if w >= 0:
                    pe.wait_ge(copied.sem, copied.at(w + 1))
                    if w >= 2:
                        pe.wait_ge(finished.sem, finished.at(w - 1))
                    ks, vs = tiles(units[w]["keys"]), units[w]["values"]
                    for n, (k, m) in enumerate(ks):
                        last = pe.matmul(c.banks[6 + w % 2][:, 0:vs[n].shape[1]], turned[0:m, w % 2, k:k + P], vs[n],
                                         start=n == 0, stop=n == len(ks) - 1)
                    last.then_inc(mixed.sem, mixed.up())

        @block.vector
        def _(dve):
            for u in range(N + MIX_LAG):
                w = u - MIX_LAG
                if u < N:
                    bank = c.banks[u % 4]
                    dve.wait_ge(scores.sem, scores.at(u + 1))
                    for (a, b), addend, factor in units[u]["masks"]:
                        dve.scalar_tensor_tensor(out=bank[:, a:b], in0=addend, scalar=factor, in1=bank[:, a:b],
                                                 op0=ALU.mult, op1=ALU.add).then_inc(masked.sem, masked.up())
                if 1 <= u <= N:
                    dve.wait_ge(highest.sem, highest.at(u))
                    dve.tensor_scalar(high_of(u - 1), high_of(u - 1), -units[u - 1]["scale"], None,
                                      ALU.mult).then_inc(peak.sem, peak.up())
                if 0 <= w + 1 < N:
                    dve.wait_ge(exps.sem, exps.at(w + 2))
                    dve.reciprocal(total_of(w + 1), total_of(w + 1)).then_inc(inverted.sem, inverted.up())
                if u < N:
                    dve.wait_ge(masked.sem, masked.sent)
                    if u >= 8:
                        dve.wait_ge(exps.sem, exps.at(u - 7))
                    dve.tensor_reduce(high_of(u), bank[:, 0:units[u]["keys"]], AX.X,
                                      ALU.max).then_inc(highest.sem, highest.up())
                if 0 <= w + 1 < N:
                    weight = units[w + 1].get("weight")
                    if weight is not None:
                        dve.wait_ge(inverted.sem, inverted.sent)
                        dve.tensor_tensor(total_of(w + 1), total_of(w + 1), weight,
                                          ALU.mult).then_inc(inverted.sem, inverted.up())
                    factor_ready[w + 1] = inverted.sent
                if w >= 0:
                    dve.wait_ge(inverted.sem, factor_ready[w])
                    if w >= 1:
                        dve.wait_ge(finished.sem, finished.at(w))
                    dve.wait_ge(mixed.sem, mixed.at(w + 1))
                    units[w]["finish"](dve, c.banks[6 + w % 2], total_of(w)).then_inc(finished.sem, finished.up())

        @block.scalar
        def _(act):
            for u in range(N + 3):
                w = u - 3
                if w >= 0:
                    act.wait_ge(flipped.sem, flipped.at(w + 1))
                    if w >= 2:
                        act.wait_ge(mixed.sem, mixed.at(w - 1))
                    m = min(P, units[w]["keys"])
                    n = len(tiles(units[w]["keys"])) * P
                    act.activation(turned[0:m, w % 2, 0:n], c.banks[4 + w % 2][0:m, 0:n],
                                   ACT.Copy).then_inc(copied.sem, copied.up())
                if u < N:
                    act.wait_ge(peak.sem, peak.at(u + 1))
                    if u >= 8:
                        act.wait_ge(finished.sem, finished.at(u - 7))
                    act.activation(probs[:, u % 3, 0:units[u]["keys"]], c.banks[u % 4][:, 0:units[u]["keys"]], ACT.Exp,
                                   bias=high_of(u), scale=units[u]["scale"],
                                   accum_out=total_of(u)).then_inc(exps.sem, exps.up())

        @block.sync
        def _(sync):
            c.load_weights(sync)
HEADS, NOPE, ROPE, VDIM, QR, KVR = 4, 64, 32, 64, 256, 128
EPS1 = 1e-6
TWO_PI = (6.28125, 0.0019350051879882812, 3.0199159819756e-07)


def plan_first(c, a):
    w = a["w_in"][0].rearrange("(k p) n -> p k n", p=P)
    c.plan("latents", w[:, :, 0:416])
    c.plan("gating", w[:, :, 416:928])
    c.plan("conv", w[:, :, 928:1440])
    c.plan("pool", w[:, :, 1440:1952])
    for half in range(2):
        for b in range(4):
            n = 1952 + b * D + half * 512
            c.plan(("gates", half, b), w[:, :, n:n + 512])
    w = a["w_out"][0].rearrange("(k p) n -> p k n", p=P)
    for half in range(2):
        c.plan(("out1", half), w[:, :, half * 512:(half + 1) * 512])
    w = a["w_ff1"][0].rearrange("(k p) n -> p k n", p=P)
    for n in range(8):
        c.plan(("ff1", n), w[:, :, n * 512:(n + 1) * 512])
    w = a["w_ff2"][0].rearrange("(k p) n -> p k n", p=P)
    for n in range(8):
        c.plan(("ff2", n), w[:, n * 4:(n + 1) * 4, :])


def features_from(c, key, xT, dsts, empties=None):
    groups = []
    n = len(dsts)
    for j in range(n):
        w = c.slot(key)[0]
        pairs = [(w[:, k, j * P:(j + 1) * P], xT[:, k, :]) for k in range(xT.shape[1])]
        e = empties[j] if empties else copy_to(dsts[j])
        groups.append(((key,), product(pairs), (key,) if j == n - 1 else (), "av"[j % 2] if not empties else "a", e))
    return groups


def tokens_from(c, key, xT, cols, dsts, empties=None, who=None, last=True):
    groups = []
    for i in range(NT):
        w = c.slot(key)[0]
        pairs = [(xT[:, k, i * P:(i + 1) * P], w[:, k, cols[0]:cols[1]]) for k in range(xT.shape[1])]
        e = empties[i] if empties else copy_to(dsts[i])
        groups.append(((key,), product(pairs), (key,) if last and i == NT - 1 else (),
                       who or "av"[i % 2], e))
    return groups


def setup_constants(c, a):
    nc = c.nc
    c.ident = c.sb("ident", [P, P])
    c.keep_le = c.sb("keep_le", [P, P])
    c.ones = c.sb("ones", [P, P])
    c.small = c.sb("small", [P, 128])
    rows = [c.region(11, 0, 256)[:, n * P:(n + 1) * P] for n in range(2)]
    c.columns = [c.sb(f"columns{n}", [P, P]) for n in range(2)]
    names = [
        [("gate_b", 32), ("norm_mix_pre", 8), ("q_norm", 2), ("kv_norm", 1), ("pool_scale", 2), ("conv_w", 6),
         ("norm_ffn_pre", 8), ("conv_b_2", 16), ("hg_lb_logits_3", 8), ("nsa_norm_g_3", 4), ("hg_norm_g_3", 1),
         ("lambda_q1_2", 0), ("subln_w_2", 1)],
        [("conv_w_2", 80), ("ssm_norm_w_2", 8), ("cmp_pe_k_3", 16), ("cmp_pe_v_3", 16)],
    ]
    c.col = {}
    made, set_, loaded = c.sig("constants_zeroed"), c.sig("constants_made"), c.sig("parameters_loaded")
    moves = []
    for n, group in enumerate(names):
        at = 0
        for name, count in group:
            if not count or name not in a:
                continue
            src = a[name]
            src = src.rearrange("a b n -> (a b n)") if len(src.shape) == 3 else src.rearrange("a n -> (a n)")
            moves.append((rows[n][at:at + count, :], src.rearrange("(r p) -> r p", p=P)))
            c.col[name] = c.columns[n][:, at:at + count]
            at += count
    with nc.Block() as block:
        @block.gpsimd
        def _(pool):
            pool.memset(c.ident[:, :], 0.0).then_inc(made.sem, made.up())
            pool.memset(c.keep_le[:, :], 0.0).then_inc(made.sem, made.up())
            pool.memset(c.ones[:, :], 1.0).then_inc(made.sem, made.up())
            pool.memset(c.region(11, 0, 256), 0.0).then_inc(made.sem, made.up())
            pool.wait_ge(made.sem, made.at(4))
            pool.affine_select(out=c.ident[:, :], in_=c.ident[:, :], compare_op=ALU.not_equal, fill=1.0,
                                        base=0, pattern=[[-1, P]], channel_multiplier=1).then_inc(set_.sem, set_.up())
            pool.affine_select(out=c.keep_le[:, :], in_=c.keep_le[:, :], compare_op=ALU.is_ge, fill=NEG,
                                        base=0, pattern=[[-1, P]], channel_multiplier=1).then_inc(set_.sem, set_.up())
            pool.wait_ge(set_.sem, set_.at(2))

        @block.scalar
        def _(act):
            act.wait_ge(made.sem, made.at(4))
            for dst, src in moves:
                act.dma_start(dst, src).then_inc(loaded.sem, loaded.up(16))
            act.wait_ge(loaded.sem, loaded.at(16 * len(moves)))

        @block.sync
        def _(sync):
            x = a["x"][0].rearrange("(i p) d -> p i d", p=P)
            loaded_x = c.sig("x_loaded")
            sync.dma_start(c.x, x).then_inc(loaded_x.sem, loaded_x.up(16))
            c.load_weights(sync)
            sync.wait_ge(loaded_x.sem, loaded_x.at(16))
    bank_groups(c, [((), turns(c, [rows[n]]), (), "v", copy_to(c.columns[n][:, :])) for n in range(2)])


def first_block(c, a):
    nc, x, xT = c.nc, c.x, c.xT
    small = c.small
    normed = c.region(6, 0, NT, D)
    row_inverse = small[:, 100:104]
    inverse_rms(c, [x[:, i, :] for i in range(NT)], EPS1, c.region(8, 0, D), row_inverse)

    def scale_rows(dst, src, inv, n=NT):
        done = c.sig("rows_scaled")
        with nc.Block() as block:
            @block.vector
            def _(dve):
                for i in range(n):
                    dve.tensor_scalar(dst(i), src(i), inv(i), None, ALU.mult).then_inc(done.sem, done.up())
                dve.wait_ge(done.sem, done.at(n))
    scale_rows(lambda i: normed[:, i, :], lambda i: x[:, i, :], lambda i: row_inverse[:, i:i + 1])
    to_features(c, lambda i: normed[:, i, :], xT, c.col["norm_mix_pre"])

    latents = c.region(7, 0, NT, 416)
    gating = c.region(7, 1664, NT, 512)
    convpool = c.region(6, 0, 8, S)
    groups = tokens_from(c, "latents", xT, (0, 416), [latents[:, i, :] for i in range(NT)])
    groups += tokens_from(c, "gating", xT, (0, 512), [gating[:, i, :] for i in range(NT)])
    groups += features_from(c, "conv", xT, [convpool[:, j, :] for j in range(4)])
    groups += features_from(c, "pool", xT, [convpool[:, 4 + j, :] for j in range(4)])
    bank_groups(c, groups)

    branches = c.region(10, 0, 8, S)
    latent_attention(c, a, latents, branches)
    spatial_gating(c, a, gating, branches)
    conv_and_pool(c, a, convpool, branches)

    wbr = c.region(8, 0, 8, D)
    load_rows(c, "scalar", [(wbr[:, 2 * b:2 * b + 2, :], a[n][0].rearrange("(k p) n -> p k n", p=P))
                            for b, n in enumerate(("w_br_mla", "w_br_sg", "w_br_conv", "w_br_pool"))])
    merged = c.region(11, 0, 8, S)
    gate = c.region(6, 0, 2, S)
    term = c.region(6, 2 * S, 2, S)
    filled, opened, weighed, added = (c.sig(n) for n in ("bank_filled", "gates_open", "branch_weighed", "term_added"))
    steps = [(half, b, j) for half in range(2) for b in range(4) for j in range(4)]
    with nc.Block() as block:
        @block.tensor
        def _(pe):
            for n, (half, b, j) in enumerate(steps):
                w = c.weights(pe, ("gates", half, b))[0]
                if n >= 2:
                    pe.wait_ge(opened.sem, opened.at(n - 1))
                    pe.wait_ge(weighed.sem, weighed.at(n - 1))
                for k in range(KD):
                    pe.matmul(c.banks[n % 2][:, :], w[:, k, j * P:(j + 1) * P], xT[:, k, :], start=k == 0,
                              stop=k == KD - 1)
                m = (half * 4 + j) * P
                for k in range(2):
                    last = pe.matmul(c.banks[2 + n % 2][:, :], wbr[:, 2 * b + k, m:m + P], branches[:, 2 * b + k, :],
                                     start=k == 0, stop=k == 1)
                last.then_inc(filled.sem, filled.up())
                if j == 3:
                    c.release(("gates", half, b), filled)

        @block.scalar
        def _(act):
            for n, (half, b, j) in enumerate(steps):
                act.wait_ge(filled.sem, filled.at(n + 1))
                if n >= 2:
                    act.wait_ge(weighed.sem, weighed.at(n - 1))
                col = c.col["gate_b"][:, b * 8 + half * 4 + j:b * 8 + half * 4 + j + 1]
                act.activation(gate[:, n % 2, :], c.banks[n % 2][:, :], ACT.Sigmoid, bias=col).then_inc(opened.sem, opened.up())

        @block.vector
        def _(dve):
            for n, (half, b, j) in enumerate(steps):
                dve.wait_ge(opened.sem, opened.at(n + 1))
                if n >= 2 and b:
                    dve.wait_ge(added.sem, added.sent)
                dst = merged[:, half * 4 + j, :]
                dve.tensor_tensor(dst if b == 0 else term[:, n % 2, :], gate[:, n % 2, :],
                                              c.banks[2 + n % 2][:, :], ALU.mult).then_inc(weighed.sem, weighed.up())
                if b:
                    dve.wait_ge(weighed.sem, weighed.at(n + 1))
                    dve.tensor_tensor(dst, dst, term[:, n % 2, :], ALU.add).then_inc(added.sem, added.up())
            dve.wait_ge(added.sem, added.sent)

        @block.sync
        def _(sync):
            c.load_weights(sync)

    mixed = c.region(6, 0, NT, D)
    groups = []
    for half in range(2):
        groups += tokens_from(c, ("out1", half), merged, (0, 512),
                              [mixed[:, i, half * 512:(half + 1) * 512] for i in range(NT)])
    bank_groups(c, groups)
    add_normed(c, x, mixed, a["norm_mix_post"][0], c.region(7, 0, 2, D))

    normed = c.region(6, 0, NT, D)
    inverse_rms(c, [x[:, i, :] for i in range(NT)], EPS1, c.region(8, 0, D), row_inverse)
    scale_rows(lambda i: normed[:, i, :], lambda i: x[:, i, :], lambda i: row_inverse[:, i:i + 1])
    to_features(c, lambda i: normed[:, i, :], xT, c.col["norm_ffn_pre"])
    hidden = c.region(6, 0, 32, S)

    def squared_relu(dst):
        def run(act, bank, order):
            act.activation(dst, bank[:, :], ACT.Relu).then_inc(order.sem, order.up())
            act.wait_ge(order.sem, order.sent)
            return act.activation(dst, dst, ACT.Square)
        return run
    groups = []
    for n in range(8):
        groups += features_from(c, ("ff1", n), xT, [None] * 4, [squared_relu(hidden[:, n * 4 + j, :]) for j in range(4)])
    bank_groups(c, groups)
    ffn = c.region(10, 0, NT, D)
    down_all_banks(c, [("ff2", n) for n in range(8)], hidden, lambda i, half: copy_to(ffn[:, i, half * 512:(half + 1) * 512]))
    add_normed(c, x, ffn, a["norm_ffn_post"][0], c.region(11, 0, 2, D))


def down_all_banks(c, keys, hidden, empty, all_vector=False):
    filled, emptied, emptied_a = c.sig("bank_filled"), c.sig("bank_emptied_by_vector"), c.sig("bank_emptied_by_scalar")
    order = c.sig("vector_order")
    total = hidden.shape[1]
    with c.nc.Block() as block:
        @block.tensor
        def _(pe):
            k0 = 0
            for key in keys:
                w = c.weights(pe, key)[0]
                for i in range(NT):
                    for half in range(2):
                        for k in range(w.shape[1]):
                            last = pe.matmul(c.banks[2 * i + half][:, :], hidden[:, k0 + k, i * P:(i + 1) * P],
                                             w[:, k, half * 512:(half + 1) * 512], start=k0 + k == 0,
                                             stop=k0 + k == total - 1)
                last.then_inc(filled.sem, filled.up())
                c.release(key, filled)
                k0 += w.shape[1]

        @block.vector
        def _(dve):
            dve.wait_ge(filled.sem, filled.at(len(keys)))
            for i in range(NT):
                for half in range(2 if all_vector else 1):
                    empty(i, half)(dve, c.banks[2 * i + half], order).then_inc(emptied.sem, emptied.up())

        @block.scalar
        def _(act):
            act.wait_ge(filled.sem, filled.at(len(keys)))
            for i in range(0 if all_vector else NT):
                empty(i, 1)(act, c.banks[2 * i + 1], None).then_inc(emptied_a.sem, emptied_a.up())

        @block.sync
        def _(sync):
            c.load_weights(sync)


def add_normed(c, x, y, gain_row, work):
    inv = c.small[:, 100:104]
    gain = work[:, 0, :]
    load_rows(c, "scalar", [(gain, gain_row.partition_broadcast(P))])
    inverse_rms(c, [y[:, i, :] for i in range(NT)], EPS1, work[:, 1, :], inv)
    scaled, added = c.sig("rows_scaled"), c.sig("term_added")
    with c.nc.Block() as block:
        @block.vector
        def _(dve):
            for i in range(NT):
                dve.scalar_tensor_tensor(out=y[:, i, :], in0=y[:, i, :], scalar=inv[:, i:i + 1],
                                                            in1=gain, op0=ALU.mult, op1=ALU.mult).then_inc(scaled.sem, scaled.up())
                dve.wait_ge(scaled.sem, scaled.sent)
                dve.tensor_tensor(x[:, i, :], x[:, i, :], y[:, i, :], ALU.add).then_inc(added.sem, added.up())
            dve.wait_ge(added.sem, added.at(NT))


def latent_attention(c, a, latents, branches):
    nc = c.nc
    wuq = c.region(8, 0, 2, 384)
    wukv = c.region(8, 768, 512)
    pos_i = c.small[:, 104:108].bitcast(I32)
    load_rows(c, "scalar", [(wuq, a["w_uq"][0].rearrange("(k p) n -> p k n", p=P)), (wukv, a["w_ukv"][0]),
                            (pos_i, a["positions"][0].rearrange("(i p) -> p i", p=P))])
    inv = c.small[:, 108:116]
    inverse_rms(c, [latents[:, i, 0:QR] for i in range(NT)] + [latents[:, i, QR:QR + KVR] for i in range(NT)], EPS1,
                c.region(9, 0, D), inv)
    half = ROPE // 2
    freq = c.region(8, 1280, half)
    pos = c.small[:, 116:120]
    ang = c.region(8, 1296, NT, half)
    turnsn = c.region(8, 1360, 2, NT * half)
    trig = c.region(8, 1488, 2, NT, half)
    order, ready, made = c.sig("vector_order"), c.sig("angles_ready"), c.sig("iota_made")
    sines = c.sig("sines_ready")
    with nc.Block() as block:
        @block.gpsimd
        def _(pool):
            for k in range(half):
                pool.memset(freq[:, k:k + 1], float(np.float32(10000.0) ** np.float32(-2.0 * k / ROPE))).then_inc(made.sem, made.up())

        @block.vector
        def _(dve):
            dve.tensor_copy(pos, pos_i).then_inc(order.sem, order.up())
            dve.wait_ge(order.sem, order.sent)
            dve.wait_ge(made.sem, made.at(half))
            dve.tensor_tensor(ang, pos.unsqueeze(2).to_broadcast([P, NT, half]),
                                 freq.unsqueeze(1).to_broadcast([P, NT, half]), ALU.mult).then_inc(order.sem, order.up())
            dve.wait_ge(order.sem, order.sent)
            for t, shift in enumerate((math.pi / 2, 0.0)):
                dst = trig[:, t, :, :]
                n = turnsn[:, t, :].rearrange("p (i k) -> p i k", i=NT)
                dve.tensor_scalar(n, ang, 1.0 / (2 * math.pi), shift / (2 * math.pi), ALU.mult, ALU.add).then_inc(order.sem, order.up())
                dve.wait_ge(order.sem, order.sent)
                dve.tensor_scalar(n, n, 12582912.0, None, ALU.add).then_inc(order.sem, order.up())
                dve.wait_ge(order.sem, order.sent)
                dve.tensor_scalar(n, n, -12582912.0, None, ALU.add).then_inc(order.sem, order.up())
                dve.wait_ge(order.sem, order.sent)
                dve.scalar_tensor_tensor(out=dst, in0=n, scalar=-TWO_PI[0], in1=ang, op0=ALU.mult, op1=ALU.add).then_inc(order.sem, order.up())
                dve.wait_ge(order.sem, order.sent)
                dve.scalar_tensor_tensor(out=dst, in0=n, scalar=-TWO_PI[1], in1=dst, op0=ALU.mult, op1=ALU.add).then_inc(order.sem, order.up())
                dve.wait_ge(order.sem, order.sent)
                dve.scalar_tensor_tensor(out=dst, in0=n, scalar=-TWO_PI[2], in1=dst, op0=ALU.mult, op1=ALU.add).then_inc(order.sem, order.up())
                dve.wait_ge(order.sem, order.sent)
                if shift:
                    dve.tensor_scalar(dst, dst, shift, None, ALU.add).then_inc(order.sem, order.up())
                    dve.wait_ge(order.sem, order.sent)
                dve.tensor_scalar(dst, dst, math.pi, None, ALU.min).then_inc(order.sem, order.up())
                dve.wait_ge(order.sem, order.sent)
                dve.tensor_scalar(dst, dst, -math.pi, None, ALU.max).then_inc(order.sem, order.up())
                dve.wait_ge(order.sem, order.sent)
            for i in range(NT):
                dve.tensor_scalar(latents[:, i, 0:QR], latents[:, i, 0:QR], inv[:, i:i + 1], None, ALU.mult).then_inc(order.sem, order.up())
                dve.wait_ge(order.sem, order.sent)
                dve.tensor_scalar(latents[:, i, QR:QR + KVR], latents[:, i, QR:QR + KVR], inv[:, NT + i:NT + i + 1],
                                     None, ALU.mult).then_inc(order.sem, order.up())
                dve.wait_ge(order.sem, order.sent)
            dve.tensor_copy(pos, pos).then_inc(ready.sem, ready.up())

        @block.scalar
        def _(act):
            act.wait_ge(ready.sem, ready.at(1))
            act.activation(trig, trig, ACT.Sin).then_inc(sines.sem, sines.up())
            act.wait_ge(sines.sem, sines.sent)
    latT = c.region(9, 0, 3, S)
    groups = []
    for i in range(NT):
        blocks = [latents[:, i, k * P:(k + 1) * P] for k in range(3)]
        groups.append(((), turns(c, blocks), (), "v",
                       scaled_to(latT[:, :, i * P:(i + 1) * P], c.columns[0][:, 40:43])))
    bank_groups(c, groups)
    q = c.region(8, 1616, NT, 384)
    kv = c.region(11, 0, NT, 512)
    groups = []
    for i in range(NT):
        groups.append(((), product([(latT[:, k, i * P:(i + 1) * P], wuq[:, k, :]) for k in range(2)]), (), "v",
                       copy_to(q[:, i, :])))
        groups.append(((), product([(latT[:, 2, i * P:(i + 1) * P], wukv)]), (), "a", copy_to(kv[:, i, :])))
    bank_groups(c, groups)
    keys = c.region(11, 2048, NT, 384)
    r = [c.region(9, 1536 + n * 256, NT, HEADS, half) for n in range(4)]
    rotated = c.sig("rotated")
    with nc.Block() as block:
        @block.vector
        def _(dve):
            qv = q.rearrange("p i (h e) -> p i h e", h=HEADS)
            kk = keys.rearrange("p i (h e) -> p i h e", h=HEADS)
            kvv = kv.rearrange("p i (h e) -> p i h e", h=HEADS)
            for i in range(NT):
                cos = trig[:, 0, i, :].unsqueeze(1).to_broadcast([P, HEADS, half])
                sin = trig[:, 1, i, :].unsqueeze(1).to_broadcast([P, HEADS, half])
                x1, x2 = qv[:, i, :, NOPE:NOPE + half], qv[:, i, :, NOPE + half:NOPE + ROPE]
                kr = latents[:, i, QR + KVR:QR + KVR + ROPE]
                k1 = kr[:, 0:half].unsqueeze(1).to_broadcast([P, HEADS, half])
                k2 = kr[:, half:ROPE].unsqueeze(1).to_broadcast([P, HEADS, half])
                for u1, u2, o1, o2 in ((x1, x2, x1, x2), (k1, k2, kk[:, i, :, NOPE:NOPE + half],
                                                          kk[:, i, :, NOPE + half:NOPE + ROPE])):
                    dve.tensor_tensor(r[0][:, i, :, :], u1, cos, ALU.mult).then_inc(order.sem, order.up())
                    dve.wait_ge(order.sem, order.sent)
                    dve.tensor_tensor(r[1][:, i, :, :], u2, sin, ALU.mult).then_inc(order.sem, order.up())
                    dve.wait_ge(order.sem, order.sent)
                    dve.tensor_tensor(r[2][:, i, :, :], u2, cos, ALU.mult).then_inc(order.sem, order.up())
                    dve.wait_ge(order.sem, order.sent)
                    dve.tensor_tensor(r[3][:, i, :, :], u1, sin, ALU.mult).then_inc(order.sem, order.up())
                    dve.wait_ge(order.sem, order.sent)
                    dve.tensor_tensor(o1, r[0][:, i, :, :], r[1][:, i, :, :], ALU.subtract).then_inc(order.sem, order.up())
                    dve.wait_ge(order.sem, order.sent)
                    dve.tensor_tensor(o2, r[2][:, i, :, :], r[3][:, i, :, :], ALU.add).then_inc(order.sem, order.up())
                    dve.wait_ge(order.sem, order.sent)
                dve.tensor_copy(kk[:, i, :, 0:NOPE], kvv[:, i, :, 0:NOPE]).then_inc(rotated.sem, rotated.up())
                dve.wait_ge(rotated.sem, rotated.sent)
    E = NOPE + ROPE
    qT = c.region(9, 0, HEADS, S)
    kT = c.region(9, 2048, HEADS, S)
    groups = []
    for h in range(HEADS):
        for src, dst, who in ((q, qT, "v"), (keys, kT, "a")):
            groups.append(((), turns(c, [src[:, i, h * E:(h + 1) * E] for i in range(NT)]), (), who,
                           copy_to(dst[0:E, h, :])))
    bank_groups(c, groups)
    out = c.region(8, 0, NT, HEADS * VDIM)
    units = []
    for h in range(HEADS):
        for i in range(NT):
            def score(pe, bank, h=h, i=i):
                return pe.matmul(bank[:, 0:(i + 1) * P], qT[0:E, h, i * P:(i + 1) * P], kT[0:E, h, 0:(i + 1) * P],
                                 start=True, stop=True)

            def finish(dve, bank, factor, h=h, i=i):
                return dve.tensor_scalar(out[:, i, h * VDIM:(h + 1) * VDIM], bank[:, 0:VDIM], factor, None, ALU.mult)
            units.append({"keys": (i + 1) * P, "scale": E ** -0.5, "score": score,
                          "masks": [((i * P, (i + 1) * P), c.keep_le[:, :], 1.0)],
                          "values": [kv[:, k, h * 128 + NOPE:(h + 1) * 128] for k in range(i + 1)], "finish": finish})
    attention(c, units, c.region(8, 1024, ATT_WORK))
    to_features(c, lambda i: out[:, i, :], branches[:, 0:2, :], width=256)


def spatial_gating(c, a, gating, branches):
    nc = c.nc
    gain, bias = c.region(8, 0, 2, 256)[:, 0, :], c.region(8, 0, 2, 256)[:, 1, :]
    ws = c.region(8, 512, 4, P)
    wT = c.region(8, 1024, 4, P)
    bs = c.region(8, 1536, 4)
    load_rows(c, "scalar", [(gain, a["sg_ln_g"][0].partition_broadcast(P)), (bias, a["sg_ln_b"][0].partition_broadcast(P)),
                            (ws, a["sg_w"][0].rearrange("g t s -> t g s"))])
    load_rows(c, "gpsimd", [(bs[:, g:g + 1], a["sg_b"][0, g, :].rearrange("(t o) -> t o", o=1)) for g in range(4)])
    done, picked = c.sig("gelu_ready"), c.sig("causal_weights")
    with nc.Block() as block:
        @block.scalar
        def _(act):
            act.activation(gating, gating, ACT.Gelu_apprx_tanh).then_inc(done.sem, done.up())
            act.wait_ge(done.sem, done.sent)

        @block.gpsimd
        def _(pool):
            pool.affine_select(out=ws, in_=ws, compare_op=ALU.is_ge, fill=0.0, base=0,
                                          pattern=[[0, 4], [-1, P]], channel_multiplier=1).then_inc(picked.sem, picked.up())
            pool.wait_ge(picked.sem, picked.at(1))
    layer_norm_in_place(c, lambda i: gating[:, i, 256:512], gain, bias, EPS1, c.small, width=256)
    bank_groups(c, [((), turns(c, [ws[:, g, :] for g in range(4)]), (), "v", copy_to(wT))])
    out = c.region(8, 1600, NT, 256)
    groups = []
    for i in range(NT):
        def mix(pe, bank, i=i):
            for g in range(4):
                last = pe.matmul(bank[:, g * 64:(g + 1) * 64], wT[:, g, :], gating[:, i, 256 + g * 64:256 + (g + 1) * 64],
                                 start=True, stop=True)
            return last

        def gate(dve, bank, order, i=i):
            o = out[:, i, :].rearrange("p (g e) -> p g e", g=4)
            dve.tensor_tensor(o, bank[:, 0:256].rearrange("p (g e) -> p g e", g=4),
                                     bs.unsqueeze(2).to_broadcast([P, 4, 64]), ALU.add).then_inc(order.sem, order.up())
            dve.wait_ge(order.sem, order.sent)
            return dve.tensor_tensor(out[:, i, :], out[:, i, :], gating[:, i, 0:256], ALU.mult)
        groups.append(((), mix, (), "v", gate))
    bank_groups(c, groups)
    to_features(c, lambda i: out[:, i, :], branches[:, 2:4, :], width=256)


def conv_and_pool(c, a, cp, branches):
    nc = c.nc
    order, done, made = c.sig("vector_order"), c.sig("branches_ready"), c.sig("iota_made")
    cw = c.col["conv_w"]
    count = c.region(8, 0, 2, S)
    term = c.region(8, 1024, 2, S)
    s1 = c.region(8, 2048, 2, S)
    wp = c.region(9, 0, 2, 64)
    load_rows(c, "scalar", [(wp[(g % 2) * 64:(g % 2) * 64 + 64, g // 2, :], a["pool_w"][0, g]) for g in range(4)])
    with nc.Block() as block:
        @block.gpsimd
        def _(pool):
            pool.iota(count, pattern=[[0, 2], [1, S]], base=1, channel_multiplier=0,
                               allow_small_or_imprecise_dtypes=True).then_inc(made.sem, made.up())

        @block.vector
        def _(dve):
            z, y = cp[:, 0:2, :], branches[:, 4:6, :]
            dve.tensor_tensor(z, cp[:, 4:6, :], z, ALU.mult).then_inc(order.sem, order.up())
            dve.wait_ge(order.sem, order.sent)
            for t in range(2):
                for k in (2, 1, 0):
                    lag = 2 - k
                    col = cw[:, k * 2 + t:k * 2 + t + 1]
                    if lag == 0:
                        dve.tensor_scalar(y[:, t, :], z[:, t, :], col, None, ALU.mult).then_inc(order.sem, order.up())
                        dve.wait_ge(order.sem, order.sent)
                    else:
                        dve.scalar_tensor_tensor(out=y[:, t, lag:S], in0=z[:, t, 0:S - lag], scalar=col,
                                                    in1=y[:, t, lag:S], op0=ALU.mult, op1=ALU.add).then_inc(order.sem, order.up())
                        dve.wait_ge(order.sem, order.sent)
            dve.tensor_tensor(y, y, cp[:, 2:4, :], ALU.mult).then_inc(order.sem, order.up())
            dve.wait_ge(order.sem, order.sent)
            dve.wait_ge(made.sem, made.at(1))
            p = cp[:, 6:8, :]
            a0, a1 = s1, term
            dve.tensor_copy(a0, p).then_inc(order.sem, order.up())
            dve.wait_ge(order.sem, order.sent)
            pooled = cp[:, 4:6, :]
            for n, lag in enumerate((1, 2, 4, 8)):
                dve.tensor_copy(a1[:, :, 0:lag], a0[:, :, 0:lag]).then_inc(order.sem, order.up())
                dve.wait_ge(order.sem, order.sent)
                dve.tensor_tensor(a1[:, :, lag:S], a0[:, :, lag:S], a0[:, :, 0:S - lag], ALU.add).then_inc(order.sem, order.up())
                dve.wait_ge(order.sem, order.sent)
                rows = slice((n % 2) * 64, (n % 2) * 64 + 64)
                dve.tensor_copy(pooled[rows, n // 2, :], a1[rows, n // 2, :]).then_inc(order.sem, order.up())
                dve.wait_ge(order.sem, order.sent)
                dve.tensor_scalar(count[rows, n // 2, :], count[rows, n // 2, :], float(2 ** (n + 1)), None, ALU.min).then_inc(order.sem, order.up())
                dve.wait_ge(order.sem, order.sent)
                a0, a1 = a1, a0
            dve.reciprocal(count, count).then_inc(order.sem, order.up())
            dve.wait_ge(order.sem, order.sent)
            dve.tensor_tensor(pooled, pooled, count, ALU.mult).then_inc(order.sem, order.up())
            dve.wait_ge(order.sem, order.sent)
            dve.tensor_tensor(pooled, pooled, p, ALU.subtract).then_inc(done.sem, done.up())
            dve.wait_ge(done.sem, done.sent)
    groups = []
    for t in range(2):
        def mix(pe, bank, t=t):
            for g in range(2):
                r = slice(g * 64, g * 64 + 64)
                last = pe.matmul(bank[r, :], wp[r, t, :], cp[r, 4 + t, :], start=True, stop=True)
            return last

        def scale(dve, bank, order, t=t):
            return dve.tensor_scalar(branches[:, 6 + t, :], bank[:, :], c.col["pool_scale"][:, t:t + 1], None, ALU.mult)
        groups.append(((), mix, (), "v", scale))
    bank_groups(c, groups)
AH, AHD, AVD = 8, 64, 128
LAMBDA_INIT = 0.8 - 0.6 * math.exp(0.0)
SH, SHD, SG, SN = 16, 64, 4, 128
FF2 = 2816
EPS2 = 1e-5
ALPHA = 2.0 ** 0.25


def plan_second(c, a):
    w = a["w_in_2"][0].rearrange("(k p) n -> p k n", p=P)
    for part, at in (("q2", 0), ("k2", 1024), ("v2", 2048), ("z2", 3072), ("xbc2", 4096), ("xbc2", 5120)):
        for half in range(2):
            n = at + half * 512
            c.plan((part, n), w[:, :, n:n + 512])
    c.plan("dt2", w[:, :, 6144:6160])
    w = a["w_out_2"][0].rearrange("(k p) n -> p k n", p=P)
    for n in range(4):
        c.plan(("out2", n), w[:, n * 4:(n + 1) * 4, :])
    plan_gated(c, "gu2", a["w_gate_2"][0], a["w_up_2"][0], FF2)
    w = a["w_down_2"][0].rearrange("(k p) n -> p k n", p=P)
    for n in range(0, FF2 // P, 4):
        c.plan(("down2", n), w[:, n:min(n + 4, FF2 // P), :])


def plan_gated(c, key, gate, up, width):
    g, u = (w.rearrange("(k p) n -> p k n", p=P) for w in (gate, up))
    for n in range(0, width, 256):
        c.plan((key, n), g[:, :, n:n + 256], u[:, :, n:n + 256])


def add_scaled(c, i, half):
    def run(dve, bank, order):
        dst = c.x[:, i, half * 512:(half + 1) * 512]
        return dve.scalar_tensor_tensor(out=dst, in0=dst, scalar=ALPHA, in1=bank[:, :], op0=ALU.mult, op1=ALU.add)
    return run


def post_norm(c, gain_row, bias_row, rows, eps):
    gain, bias = rows[:, 0, :], rows[:, 1, :]
    load_rows(c, "scalar", [(gain, gain_row.partition_broadcast(P)), (bias, bias_row.partition_broadcast(P))])
    layer_norm_in_place(c, lambda i: c.x[:, i, :], gain, bias, eps, c.small)


def second_block(c, a):
    nc, x, xT = c.nc, c.x, c.xT
    to_features(c, lambda i: x[:, i, :], xT)
    mixT = c.region(10, 0, 16, S)
    qT, kT = c.region(6, 0, 8, S), c.region(7, 0, 8, S)
    v = c.region(8, 0, NT, D)
    groups = []
    for n in (0, 512):
        groups += features_from(c, ("q2", n), xT, [qT[:, n // P + j, :] for j in range(4)])
    for n in (0, 512):
        groups += features_from(c, ("k2", 1024 + n), xT, [kT[:, n // P + j, :] for j in range(4)])
    for n in (0, 512):
        groups += tokens_from(c, ("v2", 2048 + n), xT, (0, 512), [v[:, i, n:n + 512] for i in range(NT)])
    bank_groups(c, groups)
    differential_attention(c, a, qT, kT, v, mixT)
    state_space(c, a, mixT)
    down_all_banks(c, [("out2", n) for n in range(4)], mixT, lambda i, half: add_scaled(c, i, half), all_vector=True)
    post_norm(c, a["ln1_g_2"][0], a["ln1_b_2"][0], c.region(9, 0, 2, D), EPS2)
    to_features(c, lambda i: x[:, i, :], xT)
    hidden = c.region(6, 0, FF2 // P, S)
    gated(c, "gu2", FF2, xT, hidden)
    down_all_banks(c, [("down2", n) for n in range(0, FF2 // P, 4)], hidden, lambda i, half: add_scaled(c, i, half),
                   all_vector=True)
    post_norm(c, a["ln2_g_2"][0], a["ln2_b_2"][0], c.region(9, 0, 2, D), EPS2)


def gated(c, key, width, xT, hidden):
    filled, opened, done = c.sig("bank_filled"), c.sig("gates_open"), c.sig("branch_weighed")
    n_tiles = width // P
    with c.nc.Block() as block:
        @block.tensor
        def _(pe):
            for n in range(n_tiles):
                g, u = c.weights(pe, (key, n // 2 * 256))
                j = n % 2
                if n >= 2:
                    pe.wait_ge(done.sem, done.at(n - 1))
                for w, bank in ((g, c.banks[n % 2]), (u, c.banks[2 + n % 2])):
                    for k in range(KD):
                        last = pe.matmul(bank[:, :], w[:, k, j * P:(j + 1) * P], xT[:, k, :], start=k == 0,
                                         stop=k == KD - 1)
                last.then_inc(filled.sem, filled.up())
                if j == 1:
                    c.release((key, n // 2 * 256), filled)

        @block.scalar
        def _(act):
            for n in range(n_tiles):
                act.wait_ge(filled.sem, filled.at(n + 1))
                act.activation(hidden[:, n, :], c.banks[n % 2][:, :], ACT.Silu).then_inc(opened.sem, opened.up())

        @block.vector
        def _(dve):
            for n in range(n_tiles):
                dve.wait_ge(opened.sem, opened.at(n + 1))
                dve.tensor_tensor(hidden[:, n, :], hidden[:, n, :], c.banks[2 + n % 2][:, :], ALU.mult).then_inc(done.sem, done.up())

        @block.sync
        def _(sync):
            c.load_weights(sync)


def differential_attention(c, a, qT, kT, v, mixT):
    nc = c.nc
    vecs = c.region(11, 0, 4, AHD)
    prod = c.region(11, 256, 2, AHD)
    lam = c.region(11, 384, 4)
    dist = c.region(11, 2600, 896)
    load_rows(c, "scalar", [(vecs[:, n, :], a[k][0].partition_broadcast(P))
                            for n, k in enumerate(("lambda_q1_2", "lambda_q2_2", "lambda_k1_2", "lambda_k2_2"))])
    made, order, powers, ready = c.sig("iota_made"), c.sig("vector_order"), c.sig("exponentials"), c.sig("lambda_ready")
    neg_lam = c.small[:, 104:105]
    gain = c.small[:, 106:107]
    with nc.Block() as block:
        @block.gpsimd
        def _(pool):
            pool.iota(dist, pattern=[[-1, 896]], base=384, channel_multiplier=1,
                               allow_small_or_imprecise_dtypes=True).then_inc(made.sem, made.up())

        @block.vector
        def _(dve):
            dve.wait_ge(made.sem, made.at(1))
            neg = c.region(11, 400, 896)
            dve.tensor_scalar(neg, dist, -1.0, None, ALU.mult).then_inc(order.sem, order.up())
            dve.wait_ge(order.sem, order.sent)
            dve.tensor_tensor(dist, dist, neg, ALU.max).then_inc(order.sem, order.up())
            dve.wait_ge(order.sem, order.sent)
            dve.tensor_tensor(prod, vecs[:, 0:2, :], vecs[:, 2:4, :], ALU.mult).then_inc(order.sem, order.up())
            dve.wait_ge(order.sem, order.sent)
            dve.tensor_reduce(lam[:, 0:2], prod, AX.X, ALU.add).then_inc(ready.sem, ready.up())
            dve.wait_ge(powers.sem, powers.at(1))
            dve.tensor_tensor(neg_lam, lam[:, 1:2], lam[:, 0:1], ALU.subtract).then_inc(order.sem, order.up())
            dve.wait_ge(order.sem, order.sent)
            dve.tensor_scalar(neg_lam, neg_lam, -LAMBDA_INIT, None, ALU.add).then_inc(order.sem, order.up())
            dve.wait_ge(order.sem, order.sent)
            dve.tensor_scalar(gain, c.col["subln_w_2"], 1.0 - LAMBDA_INIT, None, ALU.mult).then_inc(order.sem, order.up())
            dve.wait_ge(order.sem, order.sent)

        @block.scalar
        def _(act):
            act.wait_ge(ready.sem, ready.at(1))
            act.activation(lam[:, 0:2], lam[:, 0:2], ACT.Exp).then_inc(powers.sem, powers.up())
    out = c.region(9, 0, NT, D)
    units = []
    for h in range(AH):
        slope = 2.0 ** (-8.0 * (h + 1) / AH)
        for i in range(NT):
            for part in range(2):
                def score(pe, bank, h=h, i=i, part=part):
                    r = slice(part * AHD, (part + 1) * AHD)
                    return pe.matmul(bank[:, :], qT[r, h, i * P:(i + 1) * P], kT[r, h, :], start=True, stop=True)

                def finish(dve, bank, factor, h=h, i=i, part=part):
                    o = out[:, i, h * AVD:(h + 1) * AVD]
                    if part == 0:
                        return dve.tensor_scalar(o, bank[:, 0:AVD], factor, None, ALU.mult)
                    return dve.scalar_tensor_tensor(out=o, in0=bank[:, 0:AVD], scalar=factor, in1=o, op0=ALU.mult,
                                                    op1=ALU.add)
                units.append({"keys": S, "scale": AHD ** -0.5, "score": score,
                              "masks": [((0, S), dist[:, 384 - i * P:384 - i * P + S], -slope / AHD ** -0.5)],
                              "values": [v[:, k, h * AVD:(h + 1) * AVD] for k in range(NT)], "finish": finish,
                              "weight": neg_lam if part else None})
    attention(c, units, c.region(11, 0, ATT_WORK))
    group_rms(c, out, AH, EPS2, c.region(6, 0, NT, D))
    to_features(c, lambda i: out[:, i, :], mixT[:, 0:8, :], gain.to_broadcast([P, 8]))


def group_rms(c, y, groups, eps, squares):
    order, mean, root, done = (c.sig(x) for x in ("vector_order", "mean_ready", "root_ready", "inverse_ready"))
    inv = c.small[:, 0:NT * groups]
    w = y.shape[2] // groups
    with c.nc.Block() as block:
        @block.vector
        def _(dve):
            for i in range(NT):
                dve.tensor_tensor(squares[:, i, :], y[:, i, :], y[:, i, :], ALU.mult).then_inc(order.sem, order.up())
                dve.wait_ge(order.sem, order.sent)
                dve.tensor_reduce(inv[:, i * groups:(i + 1) * groups],
                                     squares[:, i, :].rearrange("p (g e) -> p g e", g=groups), AX.X, ALU.add).then_inc(order.sem, order.up())
                dve.wait_ge(order.sem, order.sent)
            dve.tensor_scalar(inv, inv, 1.0 / w, eps, ALU.mult, ALU.add).then_inc(mean.sem, mean.up())
            dve.wait_ge(root.sem, root.at(1))
            dve.reciprocal(inv, inv).then_inc(order.sem, order.up())
            dve.wait_ge(order.sem, order.sent)
            for i in range(NT):
                v = y[:, i, :].rearrange("p (g e) -> p g e", g=groups)
                g = inv[:, i * groups:(i + 1) * groups].unsqueeze(2).to_broadcast([P, groups, w])
                dve.tensor_tensor(v, v, g, ALU.mult).then_inc(done.sem, done.up())
            dve.wait_ge(done.sem, done.at(NT))

        @block.scalar
        def _(act):
            act.wait_ge(mean.sem, mean.at(1))
            act.activation(inv, inv, ACT.Sqrt).then_inc(root.sem, root.up())

        @block.sync
        def _(sync):
            c.load_weights(sync)


def state_space(c, a, mixT):
    nc, xT = c.nc, c.xT
    z = c.region(6, 0, NT, D)
    xbc = c.region(7, 0, 16, S)
    small = c.region(5, 0, 2048)
    sm = [small[:, n * 128:(n + 1) * 128].rearrange("p (d i h) -> p d i h", d=2, i=NT) for n in range(9)]
    dt, dA, acs, neg_acs, grow, tot, wdec, etot, t0 = sm
    raw = small[:, 1200:1264].rearrange("p (i h) -> p i h", i=NT)
    rows = small[:, 1264:1344].rearrange("p (n h) -> p n h", n=5)
    tri = [small[:, 1344:1472], small[:, 1472:1600]]
    neg = [small[:, 1600:1728], small[:, 1728:1856]]

    def silu_to(dst):
        return lambda act, bank, order: act.activation(dst, bank[:, :], ACT.Silu)
    groups = []
    for n in (0, 512):
        groups += tokens_from(c, ("z2", 3072 + n), xT, (0, 512), None,
                              [silu_to(z[:, i, n:n + 512]) for i in range(NT)], who="a")
    for n in range(0, 2048, 512):
        groups += features_from(c, ("xbc2", 4096 + n), xT, [xbc[:, n // P + j, :] for j in range(4)])
    groups += tokens_from(c, "dt2", xT, (0, 16), [raw[:, i, :] for i in range(NT)])
    bank_groups(c, groups)
    load_rows(c, "scalar", [(rows[:, n, :], a[k][0].partition_broadcast(P)) for n, k in enumerate(
        ("dt_bias_fwd_2", "dt_bias_bwd_2", "a_log_fwd_2", "a_log_bwd_2", "d_skip_2"))])

    term = c.region(11, 0, 2, S)
    conv, acted, made = c.sig("conv_ready"), c.sig("silu_ready"), c.sig("iota_made")
    order = c.sig("vector_order")
    with nc.Block() as block:
        @block.gpsimd
        def _(pool):
            for t in tri:
                pool.memset(t, 1.0).then_inc(made.sem, made.up())
            for t in neg:
                pool.memset(t, 0.0).then_inc(made.sem, made.up())
            pool.wait_ge(made.sem, made.at(4))
            for t, fill in ((tri, 0.0), (neg, NEG)):
                pool.affine_select(out=t[0], in_=t[0], compare_op=ALU.is_ge, fill=fill, base=0,
                                            pattern=[[1, P]], channel_multiplier=-1).then_inc(made.sem, made.up())
                pool.affine_select(out=t[1], in_=t[1], compare_op=ALU.is_ge, fill=fill, base=0,
                                            pattern=[[-1, P]], channel_multiplier=1).then_inc(made.sem, made.up())
            pool.wait_ge(made.sem, made.at(8))

        @block.vector
        def _(dve):
            for j in range(16):
                if j >= 2:
                    dve.wait_ge(acted.sem, acted.at(j - 1))
                y = term[:, j % 2, :]
                for k in (2, 0, 1, 3, 4):
                    col = c.col["conv_w_2"][:, k * 16 + j:k * 16 + j + 1]
                    lo, hi = max(0, 2 - k), min(S, S + 2 - k)
                    if k == 2:
                        ins = dve.tensor_scalar(y, xbc[:, j, :], col, None, ALU.mult)
                    else:
                        ins = dve.scalar_tensor_tensor(out=y[:, lo:hi], in0=xbc[:, j, lo - 2 + k:hi - 2 + k], scalar=col,
                                                       in1=y[:, lo:hi], op0=ALU.mult, op1=ALU.add)
                    if k == 4:
                        ins.then_inc(conv.sem, conv.up())
                    else:
                        ins.then_inc(order.sem, order.up())
                        dve.wait_ge(order.sem, order.sent)

        @block.scalar
        def _(act):
            for j in range(16):
                act.wait_ge(conv.sem, conv.at(j + 1))
                act.activation(xbc[:, j, :], term[:, j % 2, :], ACT.Silu, bias=c.col["conv_b_2"][:, j:j + 1]).then_inc(acted.sem, acted.up())

        @block.sync
        def _(sync):
            c.load_weights(sync)
    xs, Bt = xT.rearrange("p k n -> p (k n)").rearrange("p (i n) -> p i n", i=NT), c.region(9, 0, NT, 512)
    groups = []
    for i in range(NT):
        for k in range(3):
            blocks = [xbc[:, 4 * k + j, i * P:(i + 1) * P] for j in range(4)]
            dst = Bt[:, i, :] if k == 2 else xs[:, i, k * 512:(k + 1) * 512]
            groups.append(((), turns(c, blocks), (), "av"[k % 2], copy_to(dst)))
    bank_groups(c, groups)

    e1, e2 = c.sig("exponentials"), c.sig("logs_ready")
    v1 = c.sig("vector_ready")
    with nc.Block() as block:
        @block.vector
        def _(dve):
            for d in range(2):
                dve.tensor_tensor(dt[:, d, :, :], raw, rows[:, d, :].unsqueeze(1).to_broadcast([P, NT, SH]), ALU.add).then_inc(order.sem, order.up())
                dve.wait_ge(order.sem, order.sent)
            dve.tensor_scalar(t0, dt, -1.0, None, ALU.mult).then_inc(order.sem, order.up())
            dve.wait_ge(order.sem, order.sent)
            dve.tensor_tensor(t0, t0, dt, ALU.min).then_inc(v1.sem, v1.up())
            dve.wait_ge(v1.sem, v1.sent)
            dve.wait_ge(e2.sem, e2.at(1))
            dve.tensor_scalar(dt, dt, 0.0, None, ALU.max).then_inc(order.sem, order.up())
            dve.wait_ge(order.sem, order.sent)
            dve.tensor_tensor(dt, dt, t0, ALU.add).then_inc(order.sem, order.up())
            dve.wait_ge(order.sem, order.sent)
            for d in range(2):
                dve.tensor_tensor(dA[:, d, :, :], dt[:, d, :, :], rows[:, 2 + d, :].unsqueeze(1)
                                     .to_broadcast([P, NT, SH]), ALU.mult).then_inc(order.sem, order.up())
                dve.wait_ge(order.sem, order.sent)
            dve.tensor_scalar(dA, dA, -1.0, None, ALU.mult).then_inc(order.sem, order.up())
            dve.wait_ge(order.sem, order.sent)

        @block.scalar
        def _(act):
            act.wait_ge(v1.sem, v1.at(1))
            act.activation(rows[:, 2:4, :], rows[:, 2:4, :], ACT.Exp).then_inc(e1.sem, e1.up())
            act.wait_ge(e1.sem, e1.sent)
            act.activation(t0, t0, ACT.Exp).then_inc(e1.sem, e1.up())
            act.wait_ge(e1.sem, e1.sent)
            act.activation(t0, t0, ACT.Ln, bias=1.0).then_inc(e2.sem, e2.up())
    flat = lambda t, d: t[:, d, :, :].rearrange("p i h -> p (i h)")
    groups = []
    for d in range(2):
        groups.append(((), product([(tri[d], flat(dA, d))]), (), "v", copy_to(flat(acs, d))))
        groups.append(((), product([(c.ones[:, :], flat(dA, d))]), (), "v", copy_to(flat(tot, d))))
    bank_groups(c, groups)
    with nc.Block() as block:
        @block.vector
        def _(dve):
            dve.tensor_scalar(neg_acs, acs, -1.0, None, ALU.mult).then_inc(order.sem, order.up())
            dve.wait_ge(order.sem, order.sent)
            dve.tensor_tensor(t0, tot, acs, ALU.subtract).then_inc(v1.sem, v1.up())
            dve.wait_ge(e1.sem, e1.at(3 + 2))
            dve.tensor_tensor(wdec, t0, dt, ALU.mult).then_inc(order.sem, order.up())
            dve.wait_ge(order.sem, order.sent)

        @block.scalar
        def _(act):
            act.wait_ge(v1.sem, v1.at(2))
            act.activation(t0, t0, ACT.Exp).then_inc(e1.sem, e1.up())
            act.wait_ge(e1.sem, e1.sent)
            act.activation(grow, acs, ACT.Exp).then_inc(e1.sem, e1.up())
            act.wait_ge(e1.sem, e1.sent)
            act.activation(etot, tot, ACT.Exp).then_inc(e1.sem, e1.up())
            act.wait_ge(e1.sem, e1.sent)

    BT, CT = xbc[:, 8:12, :], xbc[:, 12:16, :]
    y = c.region(7, 0, NT, D)
    xdec = c.region(9, 2048, 2, D)
    state = c.region(11, 0, SG, 256)
    E = c.region(11, 1024, 4, 512)
    M = c.region(5, 2048, 2, 512)
    tmp = c.region(5, 3072, 1, 512)
    heads4 = lambda t, d, i, g, w: t[:, d, i, 4 * g:4 * g + 4].unsqueeze(2).to_broadcast([P, 4, w])
    four = lambda t: t.rearrange("p (r e) -> p r e", r=4)

    def decayed_x(d, i):
        done = c.sig("rows_scaled")
        with nc.Block() as block:
            @block.vector
            def _(dve):
                v = xdec[:, 0, :].rearrange("p (h e) -> p h e", h=SH)
                dve.tensor_tensor(v, xs[:, i, :].rearrange("p (h e) -> p h e", h=SH),
                                                   wdec[:, d, i, :].unsqueeze(2).to_broadcast([P, SH, SHD]), ALU.mult).then_inc(done.sem, done.up())
                dve.wait_ge(done.sem, done.sent)

    def update(d, i, g, first):
        def run(dve, bank, order):
            s = state[:, g, :]
            if first:
                return dve.tensor_copy(s, bank[:, 0:256])
            dve.tensor_tensor(four(s), four(s), heads4(etot, d, i, g, SHD), ALU.mult).then_inc(order.sem, order.up())
            dve.wait_ge(order.sem, order.sent)
            return dve.tensor_tensor(s, s, bank[:, 0:256], ALU.add)
        return ((), product([(Bt[:, i, g * P:(g + 1) * P], xdec[:, 0, g * 256:(g + 1) * 256])]), (), "v", run)

    for i in range(NT):
        decayed_x(0, i)
        groups, at = [], {}

        def decay_group(g, d):
            def prods(pe, bank):
                for r in range(4):
                    pe.matmul(bank[:, r * P:(r + 1) * P], dA[:, d, i, 4 * g + r:4 * g + r + 1].to_broadcast([P, P]),
                              tri[d], start=True, stop=False, skip_group_check=True)
                    last = pe.matmul(bank[:, r * P:(r + 1) * P], c.ident[:, :], neg[d], start=False, stop=True,
                                     skip_group_check=True)
                return last

            def empty(act, bank, order):
                for r in range(4):
                    last = act.activation(E[:, 2 * (g % 2) + d, r * P:(r + 1) * P], bank[:, r * P:(r + 1) * P], ACT.Exp,
                                          bias=neg_acs[:, d, i, 4 * g + r:4 * g + r + 1])
                    if r < 3:
                        last.then_inc(order.sem, order.up())
                        act.wait_ge(order.sem, order.sent)
                return last
            return ((), prods, (), "a", empty, [at["cb", g - 2]] if g >= 2 else [])

        def cb_group(g):
            def empty(dve, bank, order):
                e0, e1_, m = E[:, 2 * (g % 2), :], E[:, 2 * (g % 2) + 1, :], M[:, g % 2, :]
                dve.tensor_tensor(four(e0), four(e0), heads4(dt, 0, i, g, P), ALU.mult).then_inc(order.sem, order.up())
                dve.wait_ge(order.sem, order.sent)
                dve.tensor_tensor(four(e1_), four(e1_), heads4(dt, 1, i, g, P), ALU.mult).then_inc(order.sem, order.up())
                dve.wait_ge(order.sem, order.sent)
                dve.tensor_tensor(m, e0, e1_, ALU.add).then_inc(order.sem, order.up())
                dve.wait_ge(order.sem, order.sent)
                return dve.tensor_tensor(four(m), four(m), bank[:, 0:P].unsqueeze(1).to_broadcast([P, 4, P]), ALU.mult)
            cs = slice(i * P, (i + 1) * P)
            return ((), product([(BT[:, g, cs], CT[:, g, cs])]), (), "v", empty, [at["decay", g]])

        def y_group(g):
            def prods(pe, bank):
                for r in range(4):
                    h = 4 * g + r
                    last = pe.matmul(bank[:, r * SHD:(r + 1) * SHD], M[:, g % 2, r * P:(r + 1) * P],
                                     xs[:, i, h * SHD:(h + 1) * SHD], start=True, stop=True, skip_group_check=True)
                if i:
                    last = pe.matmul(bank[:, 256:512], CT[:, g, i * P:(i + 1) * P], state[:, g, :], start=True, stop=True,
                                     skip_group_check=True)
                return last

            def empty(dve, bank, order):
                o, cols = y[:, i, g * 256:(g + 1) * 256], slice(g * 256, (g + 1) * 256)
                dve.tensor_tensor(four(o), four(xs[:, i, cols]), rows[:, 4, 4 * g:4 * g + 4].unsqueeze(2)
                                         .to_broadcast([P, 4, SHD]), ALU.mult).then_inc(order.sem, order.up())
                dve.wait_ge(order.sem, order.sent)
                if i:
                    dve.tensor_tensor(four(tmp[:, 0, 0:256]), four(bank[:, 256:512]), heads4(grow, 0, i, g, SHD),
                                             ALU.mult).then_inc(order.sem, order.up())
                    dve.wait_ge(order.sem, order.sent)
                    dve.tensor_tensor(o, o, tmp[:, 0, 0:256], ALU.add).then_inc(order.sem, order.up())
                    dve.wait_ge(order.sem, order.sent)
                return dve.tensor_tensor(o, o, bank[:, 0:256], ALU.add)
            return ((), prods, (), "v", empty, [at["cb", g]])

        for g in range(SG + 2):
            if g < SG:
                for d in range(2):
                    groups.append(decay_group(g, d))
                at["decay", g] = len(groups) - 1
            if 1 <= g <= SG:
                groups.append(cb_group(g - 1))
                at["cb", g - 1] = len(groups) - 1
            if g >= 2:
                groups.append(y_group(g - 2))
                at["y", g - 2] = len(groups) - 1
                if i < NT - 1:
                    groups.append(update(0, i, g - 2, i == 0))
        bank_groups(c, groups, chained=True)

    for i in reversed(range(NT)):
        if i:
            decayed_x(1, i)
        groups = []
        for g in range(SG):
            if i < NT - 1:
                def empty(dve, bank, order, g=g):
                    o = y[:, i, g * 256:(g + 1) * 256]
                    dve.tensor_tensor(four(tmp[:, 0, 0:256]), four(bank[:, 0:256]), heads4(grow, 1, i, g, SHD),
                                             ALU.mult).then_inc(order.sem, order.up())
                    dve.wait_ge(order.sem, order.sent)
                    return dve.tensor_tensor(o, o, tmp[:, 0, 0:256], ALU.add)
                groups.append(((), product([(CT[:, g, i * P:(i + 1) * P], state[:, g, :])]), (), "v", empty))
            if i:
                groups.append(update(1, i, g, i == NT - 1))
        bank_groups(c, groups, chained=True)

    done = c.sig("branches_ready")
    with nc.Block() as block:
        @block.vector
        def _(dve):
            dve.tensor_tensor(y, y, z, ALU.mult).then_inc(done.sem, done.up())
            dve.wait_ge(done.sem, done.sent)

        @block.sync
        def _(sync):
            c.load_weights(sync)
    group_rms(c, y, SG, EPS2, c.region(6, 0, NT, D))
    to_features(c, lambda i: y[:, i, :], mixT[:, 8:16, :], c.col["ssm_norm_w_2"])
NH, NHD, NG = 8, 64, 2
NCMP, CSTRIDE, CBLOCK = 31, 16, 32
HH, SUB = 4, 32
NSUB = S // SUB
XH, XD, MEM = 4, 256, 256
EPS3 = 1e-6


def plan_third(c, a):
    w = a["w_in_3"][0].rearrange("(k p) n -> p k n", p=P)
    for key, lo, hi in (("nq", 0, 512), ("nkv", 512, 1024), ("nwin", 1024, 1304), ("hq", 1304, 1816),
                        ("hf", 1816, 2328), ("hi", 2328, 2840), ("hgate", 2840, 3352)):
        c.plan((key, 3), w[:, :, lo:hi])
    for k in ("cmp_w1_k_3", "cmp_w1_v_3"):
        c.plan(k, a[k][0].rearrange("(k p) n -> p k n", p=P))
    plan_square(c, a, "w_out_3")
    for k in ("xa_wq_3", "xa_wk_3", "xa_wv_3"):
        w = a[k][0].rearrange("(k p) n -> p k n", p=P)
        for n in (0, 512):
            c.plan((k, n), w[:, :, n:n + 512])
    plan_square(c, a, "xa_wo_3")
    c.plan("router", a["moe_w_group_3"][0].rearrange("(k p) n -> p k n", p=P),
           a["moe_w_expert_3"][0].rearrange("(k p) n -> p k n", p=P))


def plan_square(c, a, name):
    w = a[name][0].rearrange("(k p) n -> p k n", p=P)
    for n in (0, 4):
        c.plan((name, n), w[:, n:n + 4, :])


def third_mixers(c, a):
    nc, x, xT = c.nc, c.x, c.xT
    to_features(c, lambda i: x[:, i, :], xT)
    qT = c.region(5, 0, 4, S)
    kS, kW = c.region(5, 2048, NG, S), c.region(5, 3072, NG, S)
    kC, vC = c.region(6, 0, NG, S), c.region(6, 1024, NG, S)
    vS, vW = c.region(6, 2048, NT, 128), c.region(6, 2560, NT, 128)
    gates = c.region(6, 3072, NT, 24)
    hq, hk = c.region(7, 0, HH, S), c.region(7, 2048, HH, S)
    hf, hv = c.region(8, 0, HH, S), c.region(8, 2048, NT, 512)
    hgate = c.region(9, 0, NT, 512)
    lb, one_less = c.small[:, 104:108], c.small[:, 108:112]
    mixT = c.region(10, 0, 8, S)

    order, ready, powers = c.sig("vector_order"), c.sig("angles_ready"), c.sig("exponentials")
    with nc.Block() as block:
        @block.vector
        def _(dve):
            g = c.col["hg_lb_logits_3"]
            dve.tensor_tensor(lb, g[:, 4:8], g[:, 0:4], ALU.subtract).then_inc(ready.sem, ready.up())
            dve.wait_ge(powers.sem, powers.at(1))
            dve.tensor_scalar(lb, lb, 1.0, None, ALU.add).then_inc(order.sem, order.up())
            dve.wait_ge(order.sem, order.sent)
            dve.reciprocal(lb, lb).then_inc(order.sem, order.up())
            dve.wait_ge(order.sem, order.sent)
            dve.tensor_scalar(one_less, lb, -1.0, 1.0, ALU.mult, ALU.add).then_inc(order.sem, order.up())
            dve.wait_ge(order.sem, order.sent)

        @block.scalar
        def _(act):
            act.wait_ge(ready.sem, ready.at(1))
            act.activation(lb, lb, ACT.Exp).then_inc(powers.sem, powers.up())

    def both_halves(dst, shift=0):
        def run(dve, bank, order):
            for g in range(NG):
                rows = slice(g * 64, g * 64 + 64)
                dve.tensor_copy(dst[0:64, g, :], bank[rows, :]).then_inc(order.sem, order.up())
                dve.wait_ge(order.sem, order.sent)
                last = dve.tensor_copy(dst[64:128, g, 0:S - shift], bank[rows, shift:S])
                if g == 0:
                    last.then_inc(order.sem, order.up())
                    dve.wait_ge(order.sem, order.sent)
            return last
        return run

    def gate_parts(h):
        def run(act, bank, order):
            act.activation(hf[:, h, :], bank[:, :], ACT.Sigmoid).then_inc(order.sem, order.up())
            act.wait_ge(order.sem, order.sent)
            return act.activation(hk[:, h, :], bank[:, :], ACT.Sigmoid, scale=-1.0)
        return run

    def columns(key, lo, empty, who, release=False):
        w = c.slot(key)[0]
        return ((key,), product([(w[:, k, lo:lo + P], xT[:, k, :]) for k in range(KD)]), (key,) if release else (),
                who, empty)
    groups = features_from(c, ("nq", 3), xT, [qT[:, j, :] for j in range(4)])
    groups += [columns(("nkv", 3), 0, both_halves(kC, 1), "v"), columns(("nkv", 3), 128, both_halves(vC, 1), "v"),
               columns(("nkv", 3), 256, both_halves(kS), "v")]
    groups += tokens_from(c, ("nkv", 3), xT, (384, 512), [vS[:, i, :] for i in range(NT)])
    groups += [columns(("nwin", 3), 0, both_halves(kW), "v")]
    groups += tokens_from(c, ("nwin", 3), xT, (128, 256), [vW[:, i, :] for i in range(NT)], last=False)
    sigmoid_to = lambda dst: lambda act, bank, order: act.activation(dst, bank[:, 0:24], ACT.Sigmoid)
    groups += tokens_from(c, ("nwin", 3), xT, (256, 280), None, [sigmoid_to(gates[:, i, :]) for i in range(NT)], who="a")
    groups += features_from(c, ("hq", 3), xT, [hq[:, j, :] for j in range(4)])
    groups += features_from(c, ("hf", 3), xT, [None] * 4, [gate_parts(h) for h in range(4)])
    groups += tokens_from(c, ("hi", 3), xT, (0, 512), [hv[:, i, :] for i in range(NT)])
    silu_to = lambda dst: lambda act, bank, order: act.activation(dst, bank[:, :], ACT.Silu)
    groups += tokens_from(c, ("hgate", 3), xT, (0, 512), None, [silu_to(hgate[:, i, :]) for i in range(NT)], who="a")
    bank_groups(c, groups)

    sparse_attention(c, a, qT, kS, kW, kC, vC, vS, vW, gates, mixT)
    gated_recurrence(c, a, hq, hk, hf, hv, hgate, lb, one_less, mixT)
    down_all_banks(c, [("w_out_3", n) for n in (0, 4)], mixT, lambda i, half: add_scaled(c, i, half), all_vector=True)
    post_norm(c, a["ln1_g_3"][0], a["ln1_b_3"][0], c.region(9, 0, 2, D), EPS2)
    cross_attention(c, a)


def sparse_attention(c, a, qT, kS, kW, kC, vC, vS, vW, gates, mixT):
    nc = c.nc
    kcmp = c.region(6, 3168, NG, NCMP)
    vcmp = c.region(6, 3232, NG, NHD)
    hidden = [c.region(6, 3360, 2, NG * NCMP), c.region(6, 3490, 2, NG * NCMP)]
    w2 = [c.region(6, 3620, 2, NHD), c.region(6, 3748, 2, NHD)]
    load_rows(c, "scalar", [(w2[n], a[k][0].rearrange("(k p) n -> p k n", p=P)) for n, k in
                            enumerate(("cmp_w2_k_3", "cmp_w2_v_3"))])
    groups = []
    width = NG * NCMP
    for n, (src, pe_name, w1) in enumerate(((kC, "cmp_pe_k_3", "cmp_w1_k_3"), (vC, "cmp_pe_v_3", "cmp_w1_v_3"))):
        for m in range(2):
            def prods(pe, bank, src=src, pe_name=pe_name, w1=w1, m=m):
                w = c.slot(w1)[0]
                for k in range(CBLOCK // 2):
                    lhsT = w[:, k, m * P:(m + 1) * P]
                    tokens = src[:, :, 2 * k:2 * k + CSTRIDE * (NCMP - 1) + 1:CSTRIDE]
                    pe.matmul(bank[:, 0:width], lhsT, tokens, start=k == 0, stop=False)
                    last = pe.matmul(bank[:, 0:width], lhsT, c.col[pe_name][:, k:k + 1].to_broadcast([P, width]),
                                     start=False, stop=k == CBLOCK // 2 - 1)
                return last

            def gelu(act, bank, order, n=n, m=m):
                return act.activation(hidden[n][:, m, :], bank[:, 0:width], ACT.Gelu_apprx_tanh)
            groups.append(((w1,), prods, (w1,) if m else (), "a", gelu))

    def copy_both(dve, bank, order):
        dve.tensor_copy(kcmp[0:64, :, :], bank[0:64, 0:width].rearrange("p (g n) -> p g n", g=NG)).then_inc(order.sem, order.up())
        dve.wait_ge(order.sem, order.sent)
        return dve.tensor_copy(kcmp[64:128, :, :], bank[0:64, 0:width].rearrange("p (g n) -> p g n", g=NG))
    groups.append(((), product([(w2[0][:, m, :], hidden[0][:, m, :]) for m in range(2)]), (), "v", copy_both, [1]))
    for g in range(NG):
        groups.append(((), product([(hidden[1][:, m, g * NCMP:(g + 1) * NCMP], w2[1][:, m, :]) for m in range(2)]), (),
                       "v", copy_to(vcmp[0:NCMP, g, :]), [3]))
    bank_groups(c, groups)
    hide = c.region(11, ATT_WORK, NT, NCMP)
    seen = c.small[:, 112:113]
    made, order = c.sig("iota_made"), c.sig("vector_order")
    with nc.Block() as block:
        @block.gpsimd
        def _(pool):
            pool.memset(hide, 0.0).then_inc(made.sem, made.up())
            pool.memset(seen, 1.0).then_inc(made.sem, made.up())
            pool.wait_ge(made.sem, made.at(2))
            pool.affine_select(out=hide, in_=hide, compare_op=ALU.is_ge, fill=NEG, base=-(CBLOCK - 1),
                                        pattern=[[P, NT], [-CSTRIDE, NCMP]], channel_multiplier=1).then_inc(made.sem, made.up())
            pool.affine_select(out=seen, in_=seen, compare_op=ALU.is_ge, fill=0.0, base=-(CBLOCK - 1),
                                        pattern=[[0, 1]], channel_multiplier=1).then_inc(made.sem, made.up())

        @block.vector
        def _(dve):
            dve.wait_ge(made.sem, made.at(4))
            dve.tensor_scalar(gates[:, 0, 0:24:3], gates[:, 0, 0:24:3], seen, None, ALU.mult).then_inc(order.sem, order.up())
            dve.wait_ge(order.sem, order.sent)
    out = c.region(9, 2048, NT, 512)
    units = []
    for h in range(NH):
        for i in range(NT):
            for b in range(3):
                g, r, j = h // 4, slice((h % 2) * 64, (h % 2) * 64 + 64), h // 2
                n = NCMP if b == 0 else (i + 1) * P
                keys = kcmp[r, g, :] if b == 0 else (kS, kW)[b - 1][r, g, 0:n]

                def score(pe, bank, i=i, r=r, j=j, n=n, keys=keys):
                    return pe.matmul(bank[:, 0:n], qT[r, j, i * P:(i + 1) * P], keys, start=True, stop=True)

                def finish(dve, bank, factor, h=h, i=i, b=b):
                    o = out[:, i, h * NHD:(h + 1) * NHD]
                    if b == 0:
                        return dve.tensor_scalar(o, bank[:, 0:NHD], factor, None, ALU.mult)
                    return dve.scalar_tensor_tensor(out=o, in0=bank[:, 0:NHD], scalar=factor, in1=o, op0=ALU.mult,
                                                    op1=ALU.add)
                if b == 0:
                    masks, values = [((0, n), hide[:, i, :], 1.0)], [vcmp[0:NCMP, g, :]]
                else:
                    masks = [((i * P, n), c.keep_le[:, :], 1.0)]
                    values = [(vS, vW)[b - 1][:, k, g * NHD:(g + 1) * NHD] for k in range(i + 1)]
                units.append({"keys": n, "scale": NHD ** -0.5, "score": score, "masks": masks, "values": values,
                              "finish": finish, "weight": gates[:, i, 3 * h + b:3 * h + b + 1]})
    attention(c, units, c.region(11, 0, ATT_WORK))
    group_rms(c, out, 1, EPS3, c.region(11, 0, NT, 512))
    to_features(c, lambda i: out[:, i, :], mixT[:, 0:4, :], c.col["nsa_norm_g_3"], width=512)


def gated_recurrence(c, a, hq, hk, hf, hv, hgate, lb, one_less, mixT):
    nc = c.nc
    order, done, made = c.sig("vector_order"), c.sig("branches_ready"), c.sig("iota_made")
    N = HH * NSUB
    chunks = lambda t: t.rearrange("p h s -> p (h s)").rearrange("p (n t) -> p n t", n=N)
    f, k, q = chunks(hf), chunks(hk), chunks(hq)
    U = [c.region(5, n * 2048, N, SUB) for n in range(2)]
    G = [c.region(6, n * 2048, N, SUB) for n in range(2)]
    R = c.region(11, 2048, N, SUB)
    pick = c.region(1, 0, 2 * SUB)
    att = c.region(1, 64, HH, S)
    blocks = c.region(11, 0, NT * HH, P)
    decay = c.region(1, 2200, N)
    with nc.Block() as block:
        @block.gpsimd
        def _(pool):
            pool.memset(pick, 0.0).then_inc(made.sem, made.up())
            pool.memset(blocks, 0.0).then_inc(made.sem, made.up())
            pool.wait_ge(made.sem, made.at(2))
            pool.memset(pick[:, SUB - 1:SUB], 1.0).then_inc(made.sem, made.up())
            pool.wait_ge(made.sem, made.at(3))

        @block.vector
        def _(dve):
            for h in range(HH):
                dve.tensor_scalar(hf[:, h, :], hf[:, h, :], one_less[:, h:h + 1], lb[:, h:h + 1], ALU.mult,
                                            ALU.add).then_inc(order.sem, order.up())
                dve.tensor_scalar(hk[:, h, :], hk[:, h, :], one_less[:, h:h + 1], None, ALU.mult).then_inc(order.sem, order.up())
                dve.wait_ge(order.sem, order.sent)
    grown, keyed, added, copied = c.sig("decays_grown"), c.sig("keys_weighed"), c.sig("bank_filled"), c.sig("turned_copied")
    with nc.Block() as block:
        @block.vector
        def _(dve):
            for n, j in enumerate(reversed(range(SUB))):
                u, before = U[n % 2], U[(n + 1) % 2]
                if n >= 2:
                    dve.wait_ge(keyed.sem, keyed.at(n - 1))
                if n:
                    w = SUB - 1 - j
                    dve.tensor_tensor(u[:, :, j + 1:SUB], before[:, :, j + 1:SUB],
                                                f[:, :, j + 1:j + 2].to_broadcast([P, N, w]), ALU.mult).then_inc(order.sem, order.up())
                dve.tensor_copy(u[:, :, j:j + 1], q[:, :, j:j + 1]).then_inc(grown.sem, grown.up())
                dve.wait_ge(grown.sem, grown.at(n + 1))
                if n:
                    dve.wait_ge(order.sem, order.sent)
            dve.memset(R[:, :, SUB - 1:SUB], 1.0).then_inc(order.sem, order.up())
            dve.wait_ge(order.sem, order.sent)
            for j in reversed(range(SUB - 1)):
                dve.tensor_tensor(R[:, :, j:j + 1], R[:, :, j + 1:j + 2], f[:, :, j + 1:j + 2], ALU.mult).then_inc(order.sem, order.up())
                dve.wait_ge(order.sem, order.sent)
            dve.tensor_tensor(decay.unsqueeze(2), R[:, :, 0:1], f[:, :, 0:1], ALU.mult).then_inc(order.sem, order.up())
            dve.wait_ge(order.sem, order.sent)
            dve.wait_ge(keyed.sem, keyed.at(SUB))
            dve.tensor_tensor(k, k, R, ALU.mult).then_inc(order.sem, order.up())
            dve.wait_ge(order.sem, order.sent)
            dve.tensor_tensor(q, U[(SUB - 1) % 2], f[:, :, 0:1].to_broadcast([P, N, SUB]), ALU.mult).then_inc(order.sem, order.up())
            dve.wait_ge(order.sem, order.sent)

        @block.gpsimd
        def _(pool):
            for n, j in enumerate(reversed(range(SUB))):
                pool.wait_ge(grown.sem, grown.at(n + 1))
                if n >= 2:
                    pool.wait_ge(added.sem, added.at(n - 1))
                pool.tensor_tensor(G[n % 2][:, :, j:SUB], U[n % 2][:, :, j:SUB],
                                             k[:, :, j:j + 1].to_broadcast([P, N, SUB - j]), ALU.mult).then_inc(keyed.sem, keyed.up())

        @block.tensor
        def _(pe):
            for n, j in enumerate(reversed(range(SUB))):
                pe.wait_ge(keyed.sem, keyed.at(n + 1))
                for h in range(HH):
                    bank = c.banks[h][0:SUB, :].rearrange("p (n t) -> p n t", n=NSUB)
                    last = pe.matmul(bank[:, :, j:SUB], pick[:, SUB - 1 - j:2 * SUB - 1 - j],
                                     G[n % 2][:, h * NSUB:(h + 1) * NSUB, j:SUB], start=n == 0, stop=n == SUB - 1,
                                     skip_group_check=True)
                last.then_inc(added.sem, added.up())

        @block.scalar
        def _(act):
            act.wait_ge(added.sem, added.at(SUB))
            for h in range(HH):
                act.activation(att[0:SUB, h, :], c.banks[h][0:SUB, :], ACT.Copy).then_inc(copied.sem, copied.up())
            act.wait_ge(copied.sem, copied.at(HH))
            for quarter in range(4):
                r = slice(quarter * SUB, (quarter + 1) * SUB)
                for h in range(HH):
                    src = att[0:SUB, h, :].rearrange("p (i c t) -> p i c t", i=NT, c=4)[:, :, quarter, :]
                    dst = blocks.rearrange("p (i h) t -> p i h t", i=NT)[r, :, h, quarter * SUB:(quarter + 1) * SUB]
                    act.activation(dst, src, ACT.Copy).then_inc(copied.sem, copied.up())
            act.wait_ge(copied.sem, copied.at(5 * HH))

        @block.sync
        def _(sync):
            c.load_weights(sync)
    kt = c.region(6, 0, NT, 512)
    out = c.region(6, 2048, NT, 512)
    state = c.region(5, 0, HH, P)
    groups = []
    for i in range(NT):
        groups.append(((), turns(c, [hk[:, h, i * P:(i + 1) * P] for h in range(HH)]), (), "v", copy_to(kt[:, i, :])))

        def inside(pe, bank, i=i):
            for h in range(HH):
                last = pe.matmul(bank[:, h * P:(h + 1) * P], blocks[:, i * HH + h, :], hv[:, i, h * P:(h + 1) * P],
                                 start=True, stop=True, skip_group_check=True)
            return last
        groups.append(((), inside, (), "a", copy_to(out[:, i, :])))
    bank_groups(c, groups)
    groups = []
    for n in range(NSUB):
        i, r = n // 4, slice((n % 4) * SUB, (n % 4) * SUB + SUB)
        if n:
            def carried(pe, bank, n=n, r=r):
                for h in range(HH):
                    last = pe.matmul(bank[r, h * P:(h + 1) * P], hq[:, h, n * SUB:(n + 1) * SUB], state[:, h, :],
                                     start=True, stop=True, skip_group_check=True)
                return last

            def add(dve, bank, order, i=i, r=r):
                return dve.tensor_tensor(out[r, i, :], out[r, i, :], bank[r, :], ALU.add)
            groups.append(((), carried, (), "v", add, [len(groups) - 1]))
        if n < NSUB - 1:
            def gain(pe, bank, i=i, r=r):
                for h in range(HH):
                    last = pe.matmul(bank[:, h * P:(h + 1) * P], kt[r, i, h * P:(h + 1) * P], hv[r, i, h * P:(h + 1) * P],
                                     start=True, stop=True, skip_group_check=True)
                return last

            def update(dve, bank, order, n=n):
                b = bank[:, :].rearrange("p (h e) -> p h e", h=HH)
                if n == 0:
                    return dve.tensor_copy(state, b)
                dve.tensor_tensor(state, state, decay[:, n:N:NSUB].unsqueeze(2).to_broadcast([P, HH, P]), ALU.mult).then_inc(order.sem, order.up())
                dve.wait_ge(order.sem, order.sent)
                return dve.tensor_tensor(state, state, b, ALU.add)
            groups.append(((), gain, (), "v", update))
    bank_groups(c, groups, chained=True)
    group_rms(c, out, HH, EPS3, c.region(11, 0, NT, 512))
    with nc.Block() as block:
        @block.vector
        def _(dve):
            dve.tensor_tensor(out, out, hgate, ALU.mult).then_inc(done.sem, done.up())
            dve.wait_ge(done.sem, done.sent)
    to_features(c, lambda i: out[:, i, :], mixT[:, 4:8, :], c.col["hg_norm_g_3"].to_broadcast([P, 4]), width=512)


def cross_attention(c, a):
    x, xT = c.x, c.xT
    qT = c.region(5, 0, 8, S)
    kT, memT = c.region(6, 0, 8, MEM), c.region(6, 2048, 8, MEM)
    v, mem = c.region(7, 0, 2, D), c.region(7, 2048, 2, D)
    out, outT = c.region(8, 0, NT, D), c.region(9, 0, 8, S)
    load_rows(c, "scalar", [(mem, a["mem_3"][0].rearrange("(i p) d -> p i d", p=P))])
    to_features(c, lambda i: x[:, i, :], xT)
    groups = []
    for i in range(2):
        for k in (0, 4):
            groups.append(((), turns(c, [mem[:, i, (k + j) * P:(k + j + 1) * P] for j in range(4)]), (), "av"[k // 4],
                           copy_to(memT[:, k:k + 4, i * P:(i + 1) * P])))
    bank_groups(c, groups)
    groups = []
    for n in (0, 512):
        groups += features_from(c, ("xa_wq_3", n), xT, [qT[:, n // P + j, :] for j in range(4)])
    for n in (0, 512):
        groups += features_from(c, ("xa_wk_3", n), memT, [kT[:, n // P + j, :] for j in range(4)])
    for n in (0, 512):
        key = ("xa_wv_3", n)
        for i in range(2):
            w = c.slot(key)[0]
            groups.append(((key,), product([(memT[:, k, i * P:(i + 1) * P], w[:, k, :]) for k in range(KD)]),
                           (key,) if i else (), "av"[i], copy_to(v[:, i, n:n + 512])))
    bank_groups(c, groups)
    units = []
    for h in range(XH):
        for i in range(NT):
            def score(pe, bank, h=h, i=i):
                for j in range(2):
                    last = pe.matmul(bank[:, 0:MEM], qT[:, 2 * h + j, i * P:(i + 1) * P], kT[:, 2 * h + j, :],
                                     start=j == 0, stop=j == 1)
                return last

            def finish(dve, bank, factor, h=h, i=i):
                return dve.tensor_scalar(out[:, i, h * XD:(h + 1) * XD], bank[:, 0:XD], factor, None, ALU.mult)
            units.append({"keys": MEM, "scale": XD ** -0.5, "score": score, "masks": [],
                          "values": [v[:, k, h * XD:(h + 1) * XD] for k in range(2)], "finish": finish})
    attention(c, units, c.region(11, 0, ATT_WORK))
    to_features(c, lambda i: out[:, i, :], outT)
    down_all_banks(c, [("xa_wo_3", n) for n in (0, 4)], outT, lambda i, half: add_scaled(c, i, half), all_vector=True)
    post_norm(c, a["ln2_g_3"][0], a["ln2_b_3"][0], c.region(9, 0, 2, D), EPS2)
NE, NGR, EPG, FFE = 32, 4, 8, 512
MAX_BLOCKS = (2 * S + NE * (P - 1)) // P + 1
TABLE = (MAX_BLOCKS + 2) * P


def clear_outputs(c):
    zeros = c.sb("zeros", [P, 512])
    c.y_rows = c.nc.dram_tensor("y_rows", (MAX_BLOCKS * P, D), F32).ap()
    made, cleared = c.sig("iota_made"), c.sig("outputs_cleared")
    least = 2 * S // P
    with c.nc.Block() as block:
        @block.gpsimd
        def _(pool):
            pool.memset(zeros[:, :], 0.0).then_inc(made.sem, made.up())

        @block.scalar
        def _(act):
            act.wait_ge(made.sem, made.at(1))
            for half in range(2):
                dst = c.y_rows[least * P:, half * 512:(half + 1) * 512].rearrange("(b p) n -> p b n", p=P)
                act.dma_start(dst, zeros[:, :].unsqueeze(1).to_broadcast([P, MAX_BLOCKS - least, 512])).then_inc(cleared.sem, cleared.up(16))


def mixture_of_experts(c, a):
    nc, x, xT = c.nc, c.x, c.xT
    to_features(c, lambda i: x[:, i, :], xT)
    at = [0]

    def take(*shape):
        v = c.region(7, at[0], *shape)
        at[0] += int(np.prod(shape))
        return v
    bias, logits, padded = take(36), take(NT, 36), take(NT, 8)
    top, chosen, topi = take(NT, 8), take(NT, 8), take(NT, 8).bitcast(U32)
    etop, etopi = take(NT, 8), take(NT, 8).bitcast(U32)
    neg_top, total, group, weight = take(NT), take(NT), take(NT), take(2, NT)
    ids, onehot, both, prod = take(2, NT), take(2, NT, NE), take(NT, NE), take(NGR, EPG)
    iota, before, slots = take(64), take(P), take(2, NT)
    count, blocks, last, base = take(NE), take(NE), take(NE), take(NT, NE)
    token = take(NT).bitcast(I32)
    slot_i = take(2, NT).bitcast(I32)
    per_block = take(MAX_BLOCKS + 2)
    expert_i, trips_i = take(MAX_BLOCKS + 2).bitcast(I32), take(2).bitcast(I32)
    zero_i = take(TABLE // P).bitcast(I32)
    wide = c.region(8, 0, MAX_BLOCKS + 2, NE)
    x_rows = nc.dram_tensor("x_rows", (S, D), F32).ap()
    y_rows = c.y_rows
    cleared = c.signals["outputs_cleared"]
    table = nc.dram_tensor("token_of_slot", (TABLE, 1), I32).ap()

    stored = [c.sig("output_stored0"), c.sig("output_stored1")]
    made = c.sig("iota_made")
    load_rows(c, "scalar", [(bias[:, 0:NGR], a["moe_b_group_3"][0].partition_broadcast(P)),
                            (bias[:, NGR:36], a["moe_b_expert_3"][0].partition_broadcast(P))])
    with nc.Block() as block:
        @block.gpsimd
        def _(pool):
            pool.memset(zero_i, 0).then_inc(made.sem, made.up())
            pool.memset(padded, NEG).then_inc(made.sem, made.up())
            pool.memset(before, 1.0).then_inc(made.sem, made.up())
            pool.iota(iota, pattern=[[1, 64]], base=0, channel_multiplier=0,
                               allow_small_or_imprecise_dtypes=True).then_inc(made.sem, made.up())
            pool.iota(token, pattern=[[P, NT]], base=0, channel_multiplier=1).then_inc(made.sem, made.up())
            pool.wait_ge(made.sem, made.at(5))
            pool.affine_select(out=before, in_=before, compare_op=ALU.is_gt, fill=0.0, base=0,
                                        pattern=[[1, P]], channel_multiplier=-1).then_inc(made.sem, made.up())

        @block.sync
        def _(sync):
            sync.wait_ge(made.sem, made.at(6))
            sync.dma_start(table.rearrange("(p n) o -> p (n o)", p=P), zero_i).then_inc(stored[0].sem, stored[0].up(16))
            sync.dma_start(x_rows.rearrange("(i p) d -> p i d", p=P), x).then_inc(stored[1].sem, stored[1].up(16))
            sync.wait_ge(stored[0].sem, stored[0].at(16))
            sync.wait_ge(stored[1].sem, stored[1].at(16))
            sync.wait_ge(cleared.sem, cleared.sent)

    groups = []
    for i in range(NT):
        def prods(pe, bank, i=i):
            g, e = c.slot("router")
            for w, lo, hi in ((g, 0, NGR), (e, NGR, 36)):
                for k in range(KD):
                    last_ = pe.matmul(bank[:, lo:hi], xT[:, k, i * P:(i + 1) * P], w[:, k, :], start=k == 0,
                                      stop=k == KD - 1, skip_group_check=True)
            return last_

        def add(dve, bank, order, i=i):
            return dve.tensor_tensor(logits[:, i, :], bank[:, 0:36], bias, ALU.add)
        groups.append((("router",), prods, ("router",) if i == NT - 1 else (), "v", add))
    bank_groups(c, groups)

    order, ready, powers = c.sig("vector_order"), c.sig("peak_ready"), c.sig("exponentials")
    with nc.Block() as block:
        @block.vector
        def _(dve):
            dve.tensor_copy(padded[:, :, 0:NGR], logits[:, :, 0:NGR]).then_inc(order.sem, order.up())
            dve.wait_ge(order.sem, order.sent)
            for i in range(NT):
                dve.max(top[:, i, :], padded[:, i, :]).then_inc(order.sem, order.up())
                dve.wait_ge(order.sem, order.sent)
                dve.max_index(topi[:, i, :], top[:, i, :], padded[:, i, :]).then_inc(order.sem, order.up())
                dve.wait_ge(order.sem, order.sent)
            dve.tensor_copy(group, topi[:, :, 0]).then_inc(order.sem, order.up())
            dve.wait_ge(order.sem, order.sent)
            dve.tensor_scalar(neg_top, top[:, :, 0], -1.0, None, ALU.mult).then_inc(order.sem, order.up())
            dve.wait_ge(order.sem, order.sent)
            for i in range(NT):
                dve.tensor_scalar(chosen[:, i, 0:NGR], iota[:, 0:NGR], group[:, i:i + 1], None, ALU.is_equal).then_inc(order.sem, order.up())
                dve.wait_ge(order.sem, order.sent)
                dve.tensor_tensor(prod, logits[:, i, NGR:36].rearrange("p (g e) -> p g e", g=NGR),
                                     chosen[:, i, 0:NGR].unsqueeze(2).to_broadcast([P, NGR, EPG]), ALU.mult).then_inc(order.sem, order.up())
                dve.wait_ge(order.sem, order.sent)
                dve.tensor_reduce(chosen[:, i, :], prod.rearrange("p g e -> p e g"), AX.X, ALU.add).then_inc(order.sem, order.up())
                dve.wait_ge(order.sem, order.sent)
                dve.max(etop[:, i, :], chosen[:, i, :]).then_inc(order.sem, order.up())
                dve.wait_ge(order.sem, order.sent)
                dve.max_index(etopi[:, i, :], etop[:, i, :], chosen[:, i, :]).then_inc(order.sem, order.up())
                dve.wait_ge(order.sem, order.sent)
            for n in range(2):
                dve.tensor_copy(ids[:, n, :], etopi[:, :, n]).then_inc(order.sem, order.up())
                dve.wait_ge(order.sem, order.sent)
                dve.scalar_tensor_tensor(out=ids[:, n, :], in0=group, scalar=float(EPG), in1=ids[:, n, :],
                                            op0=ALU.mult, op1=ALU.add).then_inc(order.sem, order.up())
                dve.wait_ge(order.sem, order.sent)
                for i in range(NT):
                    dve.tensor_scalar(onehot[:, n, i, :], iota[:, 0:NE], ids[:, n, i:i + 1], None, ALU.is_equal).then_inc(order.sem, order.up())
                    dve.wait_ge(order.sem, order.sent)
            dve.tensor_tensor(both, onehot[:, 0, :, :], onehot[:, 1, :, :], ALU.add).then_inc(order.sem, order.up())
            dve.wait_ge(order.sem, order.sent)
            dve.tensor_tensor(weight[:, 1, :], etop[:, :, 1], etop[:, :, 0], ALU.subtract).then_inc(ready.sem, ready.up())
            dve.wait_ge(ready.sem, ready.sent)
            dve.wait_ge(powers.sem, powers.at(NT + 1))
            dve.tensor_scalar(weight[:, 0, :], weight[:, 1, :], 1.0, None, ALU.add).then_inc(order.sem, order.up())
            dve.wait_ge(order.sem, order.sent)
            dve.tensor_tensor(weight[:, 0, :], weight[:, 0, :], total, ALU.mult).then_inc(order.sem, order.up())
            dve.wait_ge(order.sem, order.sent)
            dve.reciprocal(weight[:, 0, :], weight[:, 0, :]).then_inc(order.sem, order.up())
            dve.wait_ge(order.sem, order.sent)
            dve.tensor_tensor(weight[:, 1, :], weight[:, 0, :], weight[:, 1, :], ALU.mult).then_inc(order.sem, order.up())
            dve.wait_ge(order.sem, order.sent)

        @block.scalar
        def _(act):
            act.wait_ge(ready.sem, ready.at(1))
            for i in range(NT):
                act.activation(padded[:, i, 0:NGR], logits[:, i, 0:NGR], ACT.Exp,
                                                  bias=neg_top[:, i:i + 1], accum_out=total[:, i:i + 1]).then_inc(powers.sem, powers.up())
                act.wait_ge(powers.sem, powers.sent)
            act.activation(weight[:, 1, :], weight[:, 1, :], ACT.Exp).then_inc(powers.sem, powers.up())
    groups = []
    for i in range(NT + 1):
        pairs = [(c.ones[:, :], both[:, j, :]) for j in range(i)] + ([(before, both[:, i, :])] if i < NT else [])
        groups.append(((), product(pairs), (), "v", copy_to(base[:, i, :] if i < NT else count)))
    bank_groups(c, groups)
    scattered = c.sig("slots_scattered")
    with nc.Block() as block:
        @block.vector
        def _(dve):
            dve.tensor_scalar(blocks, count, 0.0, None, ALU.is_gt).then_inc(order.sem, order.up())
            dve.wait_ge(order.sem, order.sent)
            for m in range(1, S // P):
                dve.scalar_tensor_tensor(out=blocks, in0=count, scalar=float(m * P), in1=blocks, op0=ALU.is_gt,
                                            op1=ALU.add).then_inc(order.sem, order.up())
                dve.wait_ge(order.sem, order.sent)
            dve.tensor_tensor_scan(last, c.ones[:, 0:NE], blocks, 0.0, ALU.mult, ALU.add).then_inc(order.sem, order.up())
            dve.wait_ge(order.sem, order.sent)
            dve.tensor_tensor(count, last, blocks, ALU.subtract).then_inc(order.sem, order.up())
            dve.wait_ge(order.sem, order.sent)
            dve.tensor_scalar(count, count, float(P), None, ALU.mult).then_inc(order.sem, order.up())
            dve.wait_ge(order.sem, order.sent)
            dve.tensor_tensor(base, base, count.unsqueeze(1).to_broadcast([P, NT, NE]), ALU.add).then_inc(order.sem, order.up())
            dve.wait_ge(order.sem, order.sent)
            for n in range(2):
                dve.tensor_tensor(onehot[:, n, :, :], onehot[:, n, :, :], base, ALU.mult).then_inc(order.sem, order.up())
                dve.wait_ge(order.sem, order.sent)
                dve.tensor_reduce(slots[:, n, :], onehot[:, n, :, :], AX.X, ALU.add).then_inc(order.sem, order.up())
                dve.wait_ge(order.sem, order.sent)
            dve.tensor_copy(slot_i, slots).then_inc(order.sem, order.up())
            dve.wait_ge(order.sem, order.sent)
            dve.tensor_tensor(wide, last.unsqueeze(1).to_broadcast([P, MAX_BLOCKS + 2, NE]),
                                 iota[:, 0:MAX_BLOCKS + 2].unsqueeze(2).to_broadcast([P, MAX_BLOCKS + 2, NE]), ALU.is_le).then_inc(order.sem, order.up())
            dve.wait_ge(order.sem, order.sent)
            dve.tensor_reduce(per_block, wide, AX.X, ALU.add).then_inc(order.sem, order.up())
            dve.wait_ge(order.sem, order.sent)
            dve.tensor_scalar(per_block, per_block, float(NE - 1), None, ALU.min).then_inc(order.sem, order.up())
            dve.wait_ge(order.sem, order.sent)
            dve.tensor_copy(expert_i, per_block).then_inc(order.sem, order.up())
            dve.wait_ge(order.sem, order.sent)
            dve.tensor_scalar(wide[:, 0, 0:MAX_BLOCKS // 2], iota[:, 0:MAX_BLOCKS:2], last[:, NE - 1:NE], None, ALU.is_lt).then_inc(order.sem, order.up())
            dve.wait_ge(order.sem, order.sent)
            dve.tensor_reduce(per_block[:, 0:1], wide[:, 0, 0:MAX_BLOCKS // 2], AX.X, ALU.add).then_inc(order.sem, order.up())
            dve.wait_ge(order.sem, order.sent)
            dve.tensor_copy(trips_i[:, 0:1], per_block[:, 0:1]).then_inc(ready.sem, ready.up())

        @block.gpsimd
        def _(pool):
            pool.wait_ge(ready.sem, ready.at(2))
            for n in range(2):
                for i in range(NT):
                    pool.indirect_dma_start(
                        out=table, out_offset=bass.IndirectOffsetOnAxis(ap=slot_i[:, n, i:i + 1], axis=0),
                        in_=token[:, i:i + 1], in_offset=None).then_inc(scattered.sem, scattered.up(16))
            pool.wait_ge(scattered.sem, scattered.at(16 * 2 * NT))
    expert_blocks(c, a, x_rows, y_rows, table, expert_i, trips_i, stored)

    gathered = c.sig("outputs_gathered")
    rows = c.region(8, 0, 2 * NT, D)
    with nc.Block() as block:
        @block.gpsimd
        def _(pool):
            for i in range(NT):
                for n in range(2):
                    pool.indirect_dma_start(
                        out=rows[:, 2 * i + n, :], out_offset=None, in_=y_rows,
                        in_offset=bass.IndirectOffsetOnAxis(ap=slot_i[:, n, i:i + 1], axis=0)).then_inc(gathered.sem, gathered.up(16))

        @block.vector
        def _(dve):
            dve.wait_ge(gathered.sem, gathered.at(16 * 2 * NT))
            for i in range(NT):
                dve.tensor_scalar(x[:, i, :], x[:, i, :], ALPHA, None, ALU.mult).then_inc(order.sem, order.up())
                dve.wait_ge(order.sem, order.sent)
                for n in range(2):
                    dve.scalar_tensor_tensor(out=x[:, i, :], in0=rows[:, 2 * i + n, :], scalar=weight[:, n, i:i + 1],
                                                in1=x[:, i, :], op0=ALU.mult, op1=ALU.add).then_inc(order.sem, order.up())
                    dve.wait_ge(order.sem, order.sent)
    post_norm(c, a["ln3_g_3"][0], a["ln3_b_3"][0], c.region(9, 0, 2, D), EPS2)


def expert_blocks(c, a, x_rows, y_rows, table, expert_i, trips_i, stored):
    nc = c.nc
    gate_w = [c.region(1 + 3 * s, 0, KD, FFE) for s in range(2)]
    up_w = [c.region(2 + 3 * s, 0, KD, FFE) for s in range(2)]
    down_w = [c.region(3 + 3 * s, 0, FFE // P, D) for s in range(2)]
    tokens = c.region(8, 0, 2, D)
    tokensT = [c.region(8, 2048 + s * 1024, KD, P) for s in range(2)]
    h, hT = c.region(9, 0, FFE), c.region(9, 512, FFE // P, P)
    out = c.region(9, 1024, 2, D)
    index = c.region(9, 3072, 2).bitcast(I32)
    filled, by_v, by_a = c.sig("bank_filled"), c.sig("bank_emptied_by_vector"), c.sig("bank_emptied_by_scalar")
    landed = [[c.sig(f"{n}_weights_landed{s}") for n in ("gate", "up", "down")] for s in range(2)]
    indexed, carried = c.sig("index_landed"), c.sig("wait_carried")
    gathered = [c.sig(f"tokens_gathered{s}") for s in range(2)]
    bF, bV, bA = filled.sent + 2, by_v.sent + 1, by_a.sent + 1

    def turn(pe, s):
        for half in range(2):
            for k in range(4):
                last = pe.transpose(c.banks[half][:, k * P:(k + 1) * P],
                                    tokens[:, s, (4 * half + k) * P:(4 * half + k + 1) * P], c.ident[:, :])
            last.then_inc(filled.sem, 1)

    with nc.Block() as block:
        @block.sync
        def _(sync):
            trips = sync.value_load(trips_i[0:1, 0:1], min_val=1, max_val=MAX_BLOCKS // 2)
            with sync.Fori(0, trips) as it:
                for s in range(2):
                    b = it * 2 + s
                    e = sync.value_load(expert_i[0:1, bass.ds(b, 1)], min_val=0, max_val=NE - 1)
                    for n, (dst, name, done) in enumerate(((gate_w[s], "moe_w_gate_3", 1), (up_w[s], "moe_w_up_3", 2),
                                                          (down_w[s], "moe_w_down_3", 7))):
                        sync.wait_ge(filled.sem, b * 7 + (bF - 14 + done))
                        src = a[name][0][bass.ds(e, 1), :, :].rearrange("o (k p) n -> p (o k) n", p=P)
                        sync.dma_start(dst, src).then_inc(landed[s][n].sem, 16)

        @block.gpsimd
        def _(pool):
            trips = pool.value_load(trips_i[0:1, 0:1], min_val=1, max_val=MAX_BLOCKS // 2)

            spare = c.region(9, 3080, 2)
            pool.memset(spare, 0.0).then_inc(carried.sem, 1)

            def gather(s, first_slot, n_index):
                pool.dma_start(index[:, s:s + 1], table[first_slot, :]).then_inc(indexed.sem, 16)
                pool.wait_ge(indexed.sem, n_index * 16)
                pool.wait_ge(carried.sem, n_index * 1)
                pool.tensor_tensor(spare[:, 0:1], spare[:, 1:2], spare[:, 1:2], ALU.add).then_inc(carried.sem, 1)
                return pool.indirect_dma_start(
                    out=tokens[:, s, :], out_offset=None, in_=x_rows,
                    in_offset=bass.IndirectOffsetOnAxis(ap=index[:, s:s + 1], axis=0))
            gather(0, slice(0, P), 1).then_inc(gathered[0].sem, 16)
            pool.wait_ge(gathered[0].sem, 16)
            with pool.Fori(0, trips) as it:
                for s in (1, 0):
                    n = it * 2 + (2 - s)
                    pool.wait_ge(filled.sem, n * 7 + (bF - 14))
                    gather(s, bass.ds(n * P, P), n + 1).then_inc(gathered[s].sem, 16)
                    pool.wait_ge(gathered[s].sem, it * 16 + (16 if s else 32))
            for s in range(2):
                pool.wait_ge(stored[s].sem, trips * 16 + stored[s].sent)

        @block.tensor
        def _(pe):
            trips = pe.value_load(trips_i[0:1, 0:1], min_val=1, max_val=MAX_BLOCKS // 2)
            pe.wait_ge(gathered[0].sem, 16)
            turn(pe, 0)
            pe.wait_ge(by_v.sem, bV)
            pe.wait_ge(by_a.sem, bA)
            with pe.Fori(0, trips) as it:
                for s in range(2):
                    b = it * 2 + s
                    pe.wait_ge(by_v.sem, b * 3 + (bV - 1))
                    pe.wait_ge(by_a.sem, b * 4 + (bA - 2))
                    for n, w in enumerate((gate_w[s], up_w[s])):
                        pe.wait_ge(landed[s][n].sem, it * 16 + 16)
                        for k in range(KD):
                            last = pe.matmul(c.banks[2 + n][:, :], tokensT[s][:, k, :], w[:, k, :], start=k == 0,
                                             stop=k == KD - 1)
                        last.then_inc(filled.sem, 1)
                    pe.wait_ge(gathered[1 - s].sem, it * 16 + (32 if s else 16))
                    turn(pe, 1 - s)
                    pe.wait_ge(by_v.sem, b * 3 + (bV + 1))
                    for k in range(FFE // P):
                        last = pe.transpose(c.banks[4][:, k * P:(k + 1) * P], h[:, k * P:(k + 1) * P], c.ident[:, :])
                    last.then_inc(filled.sem, 1)
                    pe.wait_ge(by_a.sem, b * 4 + (bA + 3))
                    pe.wait_ge(landed[s][2].sem, it * 16 + 16)
                    for half in range(2):
                        for k in range(FFE // P):
                            last = pe.matmul(c.banks[5 + half][:, :], hT[:, k, :],
                                             down_w[s][:, k, half * 512:(half + 1) * 512], start=k == 0,
                                             stop=k == FFE // P - 1)
                        last.then_inc(filled.sem, 1)

        @block.vector
        def _(dve):
            trips = dve.value_load(trips_i[0:1, 0:1], min_val=1, max_val=MAX_BLOCKS // 2)
            halfT = lambda s, half: tokensT[s][:, 4 * half:4 * half + 4, :].rearrange("p k t -> p (k t)")
            dve.wait_ge(filled.sem, bF - 1)
            dve.tensor_copy(halfT(0, 0), c.banks[0][:, :]).then_inc(by_v.sem, 1)
            with dve.Fori(0, trips) as it:
                for s in range(2):
                    b = it * 2 + s
                    dve.wait_ge(filled.sem, b * 7 + (bF + 2))
                    dve.wait_ge(by_a.sem, b * 4 + (bA + 1))
                    dve.tensor_tensor(h, h, c.banks[3][:, :], ALU.mult).then_inc(by_v.sem, 1)
                    dve.wait_ge(filled.sem, b * 7 + (bF + 3))
                    dve.tensor_copy(halfT(1 - s, 0), c.banks[0][:, :]).then_inc(by_v.sem, 1)
                    dve.wait_ge(filled.sem, b * 7 + (bF + 6))
                    dve.wait_ge(stored[s].sem, it * 16 + stored[s].sent)
                    dve.tensor_copy(out[:, s, 0:512], c.banks[5][:, :]).then_inc(by_v.sem, 1)

        @block.scalar
        def _(act):
            trips = act.value_load(trips_i[0:1, 0:1], min_val=1, max_val=MAX_BLOCKS // 2)
            halfT = lambda s, half: tokensT[s][:, 4 * half:4 * half + 4, :].rearrange("p k t -> p (k t)")
            act.wait_ge(filled.sem, bF)
            act.activation(halfT(0, 1), c.banks[1][:, :], ACT.Copy).then_inc(by_a.sem, 1)
            with act.Fori(0, trips) as it:
                for s in range(2):
                    b = it * 2 + s
                    act.wait_ge(filled.sem, b * 7 + (bF + 1))
                    act.activation(h, c.banks[2][:, :], ACT.Silu).then_inc(by_a.sem, 1)
                    act.wait_ge(filled.sem, b * 7 + (bF + 4))
                    act.activation(halfT(1 - s, 1), c.banks[1][:, :], ACT.Copy).then_inc(by_a.sem, 1)
                    act.wait_ge(filled.sem, b * 7 + (bF + 5))
                    act.activation(hT.rearrange("p k t -> p (k t)"), c.banks[4][:, :], ACT.Copy).then_inc(by_a.sem, 1)
                    act.wait_ge(filled.sem, b * 7 + (bF + 7))
                    act.wait_ge(stored[s].sem, it * 16 + stored[s].sent)
                    act.activation(out[:, s, 512:1024], c.banks[6][:, :], ACT.Copy).then_inc(by_a.sem, 1)
                    act.wait_ge(by_v.sem, b * 3 + (bV + 3))
                    act.wait_ge(by_a.sem, b * 4 + (bA + 4))
                    act.dma_start(y_rows[bass.ds(b * P, P), :], out[:, s, :]).then_inc(stored[s].sem, 16)


def block_stack(nc, a, out):
    with ExitStack() as ctx:
        c = Core(nc, ctx)
        c.x = c.region(0, 0, NT, D)
        c.xT = c.region(1, 0, KD, S)
        plan_first(c, a)
        plan_second(c, a)
        plan_third(c, a)
        setup_constants(c, a)
        clear_outputs(c)
        first_block(c, a)
        second_block(c, a)
        third_mixers(c, a)
        mixture_of_experts(c, a)
        written = c.sig("result_written")
        with nc.Block() as block:
            @block.sync
            def _(sync):
                sync.dma_start(out[0].rearrange("(i p) d -> p i d", p=P), c.x).then_inc(written.sem, written.up(16))
                sync.wait_ge(written.sem, written.at(16))


def kernel(**inputs):
    import numpy as _np
    import concourse.bacc as _bacc
    from concourse import mybir as _mybir
    from concourse.bass_utils import run_bass_kernel_spmd as _run

    nc = _bacc.Bacc("TRN2", target_bir_lowering=False, num_devices=1)
    arrays, args = {}, {}
    for name, value in inputs.items():
        v = _np.ascontiguousarray(value)
        arrays[f"in_{name}_dram"] = v
        args[name] = nc.dram_tensor(f"in_{name}_dram", v.shape, _mybir.dt.from_np(v.dtype), kind="ExternalInput").ap()
    out = nc.dram_tensor("out_0_dram", (1, S, D), F32, kind="ExternalOutput").ap()
    block_stack(nc, args, out)
    r = _run(nc, [arrays], core_ids=[0])
    return r.results[0]["out_0_dram"]
```

```python
import math
from contextlib import ExitStack

import numpy as np

import concourse.bass as bass
from concourse import mybir

F32 = mybir.dt.float32
I32 = mybir.dt.int32
U32 = mybir.dt.uint32
ALU = mybir.AluOpType
ACT = mybir.ActivationFunctionType
AX = mybir.AxisListType

P = 128
S = 512
D = 1024
NT = S // P
KD = D // P
UNIT = 4096
NEG = -1e30
RING = 3


class Signal:

    def __init__(self, sem):
        self.sem, self.base, self.sent = sem, 0, 0

    def up(self, by=1):
        self.sent += by
        return by

    def at(self, n):
        return self.base + n


class Core:

    def __init__(self, nc, ctx):
        self.nc, self.ctx = nc, ctx
        self.signals = {}
        self.arena = ctx.enter_context(nc.sbuf_tensor("arena", [P, 12 * UNIT], F32))
        self.banks = [ctx.enter_context(nc.psum_tensor(f"bank{i}", [P, 512], F32)) for i in range(8)]
        self.chunks = []
        self.at = {}
        self.loaded = [Signal(ctx.enter_context(nc.semaphore(f"weights_loaded{i}"))) for i in range(RING)]
        self.arrived = {}
        self.freed = {}
        self.issued = 0

    def sb(self, name, shape, dt=F32):
        return self.ctx.enter_context(self.nc.sbuf_tensor(name, shape, dt))

    def sig(self, name):
        if name not in self.signals:
            self.signals[name] = Signal(self.ctx.enter_context(self.nc.semaphore(name)))
        s = self.signals[name]
        s.base = s.sent
        return s

    def region(self, unit, off, *shape):
        n = int(np.prod(shape))
        v = self.arena[:, int(unit * UNIT) + off:int(unit * UNIT) + off + n]
        if len(shape) == 2:
            v = v.rearrange("p (a b) -> p a b", a=shape[0])
        if len(shape) == 3:
            v = v.rearrange("p (a b c) -> p a b c", a=shape[0], b=shape[1])
        return v

    def plan(self, key, *parts):
        self.at[key] = len(self.chunks)
        self.chunks.append((key, parts))

    def slot(self, key):
        n = self.at[key]
        out, off = [], (2 + n % RING) * UNIT
        for part in self.chunks[n][1]:
            a, b = part.shape[1], part.shape[2]
            out.append(self.arena[:, off:off + a * b].rearrange("p (a b) -> p a b", a=a))
            off += a * b
        assert off <= (3 + n % RING) * UNIT
        return out

    def load_weights(self, eng):
        while self.issued < len(self.chunks):
            n = self.issued
            if n >= RING:
                if n - RING not in self.freed:
                    return
                sem, count = self.freed[n - RING]
                eng.wait_ge(sem, count)
            for dst, src in zip(self.slot(self.chunks[n][0]), self.chunks[n][1]):
                eng.dma_start(dst, src).then_inc(self.loaded[n % RING].sem, self.loaded[n % RING].up(16))
            self.arrived[n] = self.loaded[n % RING].sent
            self.issued += 1

    def weights(self, eng, key):
        n = self.at[key]
        count = 16 * sum(len(self.chunks[m][1]) for m in range(n % RING, n + 1, RING))
        eng.wait_ge(self.loaded[n % RING].sem, count)
        return self.slot(key)

    def release(self, key, sig):
        self.freed[self.at[key]] = (sig.sem, sig.sent)


def bank_groups(c, groups, nb=8, chained=False, meanwhile=None):
    filled = c.sig("bank_filled")
    emptied = {"v": c.sig("bank_emptied_by_vector"), "a": c.sig("bank_emptied_by_scalar")}
    own = {"v": c.sig("vector_order"), "a": c.sig("scalar_order")}
    turn, seen = [], {"v": 0, "a": 0}
    for g in groups:
        seen[g[3]] += 1
        turn.append((g[3], seen[g[3]]))

    with c.nc.Block() as block:
        @block.tensor
        def _(pe):
            for n, (needs, products, releases, _, _, *after) in enumerate(groups):
                for m in after[0] if after else ():
                    pe.wait_ge(emptied[turn[m][0]].sem, emptied[turn[m][0]].at(turn[m][1]))
                if n >= nb:
                    who, count = turn[n - nb]
                    pe.wait_ge(emptied[who].sem, emptied[who].at(count))
                for key in needs:
                    c.weights(pe, key)
                products(pe, c.banks[n % nb]).then_inc(filled.sem, filled.up())
                for key in releases:
                    c.release(key, filled)

        def emptier(eng, who):
            for n, (_, _, _, w, empty, *_) in enumerate(groups):
                if w == who:
                    eng.wait_ge(filled.sem, filled.at(n + 1))
                    empty(eng, c.banks[n % nb], own[who]).then_inc(emptied[who].sem, emptied[who].up())
                    if chained:
                        eng.wait_ge(emptied[who].sem, emptied[who].sent)

        @block.vector
        def _(dve):
            emptier(dve, "v")

        @block.scalar
        def _(act):
            emptier(act, "a")

        if meanwhile:
            block.gpsimd(meanwhile)

        @block.sync
        def _(sync):
            c.load_weights(sync)


def product(pairs):
    def run(pe, bank):
        for n, (lhsT, rhs) in enumerate(pairs):
            m, w = lhsT.shape[1], rhs.shape[1]
            last = pe.matmul(bank[0:m, 0:w], lhsT, rhs, start=n == 0, stop=n == len(pairs) - 1)
        return last
    return run


def turns(c, sources):
    def run(pe, bank):
        at = 0
        for s in sources:
            q, m = s.shape
            last = pe.transpose(bank[0:m, at:at + q], s, c.ident[0:q, 0:q])
            at += q
        return last
    return run


def copy_to(dst, rows=P, width=None):
    def run(eng, bank, order):
        w = dst.shape[1] if len(dst.shape) == 2 else dst.shape[1] * dst.shape[2]
        src = bank[0:dst.shape[0], 0:w]
        if len(dst.shape) == 3:
            src = src.rearrange("p (a b) -> p a b", a=dst.shape[1])
        if hasattr(eng, "activation"):
            return eng.activation(dst, src, ACT.Copy)
        return eng.tensor_copy(dst, src)
    return run


def scaled_to(dst, gain):
    def run(dve, bank, order):
        m, a, b = dst.shape
        src = bank[0:m, 0:a * b].rearrange("p (a b) -> p a b", a=a)
        return dve.tensor_tensor(dst, src, gain.unsqueeze(2).to_broadcast([m, a, b]), ALU.mult)
    return run


def inverse_rms(c, sources, eps, junk, out):
    squared, mean, root, done = (c.sig(x) for x in ("squares_summed", "mean_ready", "root_ready", "inverse_ready"))
    n = len(sources)
    width = sources[0].shape[1]
    with c.nc.Block() as block:
        @block.scalar
        def _(act):
            for i, s in enumerate(sources):
                act.activation(junk[:, 0:s.shape[1]], s, ACT.Square, accum_out=out[:, i:i + 1]).then_inc(squared.sem, squared.up())
                act.wait_ge(squared.sem, squared.sent)
            act.wait_ge(mean.sem, mean.at(n))
            act.activation(out[:, 0:n], out[:, 0:n], ACT.Sqrt).then_inc(root.sem, root.up())

        @block.vector
        def _(dve):
            dve.wait_ge(squared.sem, squared.at(n))
            for i, s in enumerate(sources):
                dve.tensor_scalar(out[:, i:i + 1], out[:, i:i + 1], 1.0 / s.shape[1], eps, ALU.mult, ALU.add).then_inc(mean.sem, mean.up())
            dve.wait_ge(root.sem, root.at(1))
            dve.reciprocal(out[:, 0:n], out[:, 0:n]).then_inc(done.sem, done.up())

        @block.sync
        def _(sync):
            c.load_weights(sync)


def load_rows(c, eng_name, pairs, also=None):
    got = c.sig("rows_loaded_" + eng_name)
    with c.nc.Block() as block:
        def issue(eng):
            for dst, src in pairs:
                eng.dma_start(dst, src, allow_slow_non_contiguous=True).then_inc(got.sem, got.up(16))
            eng.wait_ge(got.sem, got.at(16 * len(pairs)))
        {"scalar": block.scalar, "gpsimd": block.gpsimd}[eng_name](issue)


def to_features(c, source, dst, gain=None, width=D):
    groups = []
    for i in range(NT):
        for k in range(0, width // P, 4):
            m = min(4, width // P - k)
            view = dst[:, k:k + m, i * P:(i + 1) * P]
            blocks = [source(i)[:, (k + j) * P:(k + j + 1) * P] for j in range(m)]
            if gain is None:
                groups.append(((), turns(c, blocks), (), "a" if k else "v", copy_to(view)))
            else:
                groups.append(((), turns(c, blocks), (), "v", scaled_to(view, gain[:, k:k + m])))
    bank_groups(c, groups)


def layer_norm_in_place(c, x, gain, bias, eps, small, width=D):
    order, var, root, done = (c.sig(n) for n in ("vector_order", "variance_ready", "root_ready", "normed"))
    parts = -(-width // 512)
    stats = small[:, 0:NT * parts * 6].rearrange("p (i a b) -> p i a b", i=NT, a=parts)
    mv = small[:, 64:64 + 2 * NT].rearrange("p (i b) -> p i b", i=NT)
    sd = small[:, 80:80 + NT]
    with c.nc.Block() as block:
        @block.vector
        def _(dve):
            for i in range(NT):
                for a in range(parts):
                    w = min(512, width)
                    dve.bn_stats(stats[:, i, a, :], x(i)[:, a * w:(a + 1) * w]).then_inc(order.sem, order.up())
            dve.wait_ge(order.sem, order.sent)
            for i in range(NT):
                dve.bn_aggr(mv[:, i, :], stats[:, i, :, :]).then_inc(order.sem, order.up())
            dve.wait_ge(order.sem, order.sent)
            dve.tensor_scalar(sd, mv[:, :, 1], 1.0, eps, ALU.mult, ALU.add).then_inc(var.sem, var.up())
            dve.wait_ge(root.sem, root.at(1))
            dve.reciprocal(sd, sd).then_inc(order.sem, order.up())
            dve.wait_ge(order.sem, order.sent)
            for i in range(NT):
                dve.tensor_scalar(x(i), x(i), mv[:, i, 0:1], sd[:, i:i + 1], ALU.subtract, ALU.mult).then_inc(order.sem, order.up())
            for i in range(NT):
                dve.wait_ge(order.sem, order.at(order.sent - order.base - (0 if i else NT - 1)))
                dve.tensor_tensor(x(i), x(i), gain, ALU.mult).then_inc(order.sem, order.up())
            dve.wait_ge(order.sem, order.sent)
            for i in range(NT):
                dve.tensor_tensor(x(i), x(i), bias, ALU.add).then_inc(done.sem, done.up())
            dve.wait_ge(done.sem, done.at(NT))

        @block.scalar
        def _(act):
            act.wait_ge(var.sem, var.at(1))
            act.activation(sd, sd, ACT.Sqrt).then_inc(root.sem, root.up())

        @block.sync
        def _(sync):
            c.load_weights(sync)


ATT_WORK = 5 * 512 + 16
TURN_LAG, MIX_LAG = 4, 5


def attention(c, units, work):
    probs = work[:, 0:1536].rearrange("p (a b) -> p a b", a=3)
    turned = work[:, 1536:2560].rearrange("p (a b) -> p a b", a=2)
    high, total = work[:, 2560:2568], work[:, 2568:2576]
    high_of, total_of = lambda u: high[:, u % 8:u % 8 + 1], lambda u: total[:, u % 8:u % 8 + 1]
    scores, peak, exps, flipped, copied, mixed, finished = (c.sig(n) for n in (
        "scores_ready", "peak_ready", "probs_ready", "probs_turned", "turned_copied", "mixed_ready", "output_written"))
    masked, highest, inverted = c.sig("mask_added"), c.sig("maximum_ready"), c.sig("inverse_ready")
    factor_ready = {}
    N = len(units)

    def tiles(keys):
        return [(k, min(P, keys - k)) for k in range(0, keys, P)]

    with c.nc.Block() as block:
        @block.tensor
        def _(pe):
            for u in range(N + MIX_LAG):
                if u < N:
                    if u >= 4:
                        pe.wait_ge(exps.sem, exps.at(u - 3))
                    units[u]["score"](pe, c.banks[u % 4]).then_inc(scores.sem, scores.up())
                w = u - TURN_LAG
                if 0 <= w < N:
                    pe.wait_ge(exps.sem, exps.at(w + 1))
                    if w >= 2:
                        pe.wait_ge(copied.sem, copied.at(w - 1))
                    for k, m in tiles(units[w]["keys"]):
                        last = pe.transpose(c.banks[4 + w % 2][0:m, k:k + P], probs[:, w % 3, k:k + m], c.ident[:, :])
                    last.then_inc(flipped.sem, flipped.up())
                w = u - MIX_LAG
                if w >= 0:
                    pe.wait_ge(copied.sem, copied.at(w + 1))
                    if w >= 2:
                        pe.wait_ge(finished.sem, finished.at(w - 1))
                    ks, vs = tiles(units[w]["keys"]), units[w]["values"]
                    for n, (k, m) in enumerate(ks):
                        last = pe.matmul(c.banks[6 + w % 2][:, 0:vs[n].shape[1]], turned[0:m, w % 2, k:k + P], vs[n],
                                         start=n == 0, stop=n == len(ks) - 1)
                    last.then_inc(mixed.sem, mixed.up())

        @block.vector
        def _(dve):
            for u in range(N + MIX_LAG):
                w = u - MIX_LAG
                if u < N:
                    bank = c.banks[u % 4]
                    dve.wait_ge(scores.sem, scores.at(u + 1))
                    for (a, b), addend, factor in units[u]["masks"]:
                        dve.scalar_tensor_tensor(out=bank[:, a:b], in0=addend, scalar=factor, in1=bank[:, a:b],
                                                 op0=ALU.mult, op1=ALU.add).then_inc(masked.sem, masked.up())
                if 1 <= u <= N:
                    dve.wait_ge(highest.sem, highest.at(u))
                    dve.tensor_scalar(high_of(u - 1), high_of(u - 1), -units[u - 1]["scale"], None,
                                      ALU.mult).then_inc(peak.sem, peak.up())
                if 0 <= w + 1 < N:
                    dve.wait_ge(exps.sem, exps.at(w + 2))
                    dve.reciprocal(total_of(w + 1), total_of(w + 1)).then_inc(inverted.sem, inverted.up())
                if u < N:
                    dve.wait_ge(masked.sem, masked.sent)
                    if u >= 8:
                        dve.wait_ge(exps.sem, exps.at(u - 7))
                    dve.tensor_reduce(high_of(u), bank[:, 0:units[u]["keys"]], AX.X,
                                      ALU.max).then_inc(highest.sem, highest.up())
                if 0 <= w + 1 < N:
                    weight = units[w + 1].get("weight")
                    if weight is not None:
                        dve.wait_ge(inverted.sem, inverted.sent)
                        dve.tensor_tensor(total_of(w + 1), total_of(w + 1), weight,
                                          ALU.mult).then_inc(inverted.sem, inverted.up())
                    factor_ready[w + 1] = inverted.sent
                if w >= 0:
                    dve.wait_ge(inverted.sem, factor_ready[w])
                    if w >= 1:
                        dve.wait_ge(finished.sem, finished.at(w))
                    dve.wait_ge(mixed.sem, mixed.at(w + 1))
                    units[w]["finish"](dve, c.banks[6 + w % 2], total_of(w)).then_inc(finished.sem, finished.up())

        @block.scalar
        def _(act):
            for u in range(N + 3):
                w = u - 3
                if w >= 0:
                    act.wait_ge(flipped.sem, flipped.at(w + 1))
                    if w >= 2:
                        act.wait_ge(mixed.sem, mixed.at(w - 1))
                    m = min(P, units[w]["keys"])
                    n = len(tiles(units[w]["keys"])) * P
                    act.activation(turned[0:m, w % 2, 0:n], c.banks[4 + w % 2][0:m, 0:n],
                                   ACT.Copy).then_inc(copied.sem, copied.up())
                if u < N:
                    act.wait_ge(peak.sem, peak.at(u + 1))
                    if u >= 8:
                        act.wait_ge(finished.sem, finished.at(u - 7))
                    act.activation(probs[:, u % 3, 0:units[u]["keys"]], c.banks[u % 4][:, 0:units[u]["keys"]], ACT.Exp,
                                   bias=high_of(u), scale=units[u]["scale"],
                                   accum_out=total_of(u)).then_inc(exps.sem, exps.up())

        @block.sync
        def _(sync):
            c.load_weights(sync)


def products_by_tile(c, pe, keys, hidden, tail, filled, ready, turned, source):
    total, k0 = hidden.shape[1], 0

    def add_chunk(k0, w, i):
        for half in range(2):
            for k in range(w.shape[1]):
                last = pe.matmul(c.banks[2 * i + half][:, :], hidden[:, k0 + k, i * P:(i + 1) * P],
                                 w[:, k, half * 512:(half + 1) * 512], start=k0 + k == 0, stop=k0 + k == total - 1)
        return last

    def turn_tile(i):
        signal, count = ready(i)
        pe.wait_ge(signal.sem, count)
        for half in range(2):
            for k in range(4):
                at = (4 * half + k) * P
                last = pe.transpose(c.banks[2 * i + half][:, k * P:(k + 1) * P], source(i)[:, at:at + P], c.ident[:, :])
            last.then_inc(turned.sem, turned.up())

    for key in keys[:-tail]:
        w = c.weights(pe, key)[0]
        for i in range(NT):
            last = add_chunk(k0, w, i)
        last.then_inc(filled.sem, filled.up())
        c.release(key, filled)
        k0 += w.shape[1]
    chunks = [c.weights(pe, key)[0] for key in keys[-tail:]]
    for i in range(NT):
        k = k0
        for w in chunks:
            last = add_chunk(k, w, i)
            k += w.shape[1]
        last.then_inc(filled.sem, filled.up())
        if i == NT - 1:
            for key in keys[-tail:]:
                c.release(key, filled)
        if i >= 2:
            turn_tile(i - 2)
    for i in (NT - 2, NT - 1):
        turn_tile(i)


def layer_norm_numbers(c):
    n = c.norms
    return (n[:, 0:48].rearrange("p (i a b) -> p i a b", i=NT, a=2), n[:, 48:56].rearrange("p (i b) -> p i b", i=NT),
            n[:, 56:60], n[:, 60:64])


def down_and_layer_norm(c, keys, hidden, gain_row, bias_row, rows, eps, tail=1,
                        x_rows=None, meanwhile=None):
    x, xT = c.x, c.xT
    stats, mv, sd, shift = layer_norm_numbers(c)
    gain, bias = rows[:, 0, :], rows[:, 1, :]
    filled, got, var, root, scaled, centred, gained, normed, turned, emptied = (c.sig(n) for n in (
        "bank_filled", "rows_loaded_scalar", "variance_ready", "root_ready", "scale_ready", "rows_centred",
        "gain_applied", "normed", "rows_turned", "bank_emptied_by_scalar"))
    order, emptied_v, last_normed = c.sig("vector_order"), c.sig("bank_emptied_by_vector"), c.sig("last_tile_normed")
    kept = c.sig("x_rows_stored")
    early = len(keys) - tail
    with c.nc.Block() as block:
        def ready(i):
            return (normed, normed.at(i + 1)) if i < NT - 1 else (last_normed, last_normed.at(1))

        @block.tensor
        def _(pe):
            products_by_tile(c, pe, keys, hidden, tail, filled, ready, turned, lambda i: x[:, i, :])

        def empty_turned(eng, i, half):
            eng.wait_ge(turned.sem, turned.at(2 * i + half + 1))
            src = c.banks[2 * i + half][:, :].rearrange("p (k t) -> p k t", k=4)
            return copy_to_view(eng, xT[:, 4 * half:4 * half + 4, i * P:(i + 1) * P], src)

        @block.vector
        def _(dve):
            for i in range(NT):
                dve.wait_ge(filled.sem, filled.at(early + i + 1))
                for half in range(2):
                    dst = x[:, i, half * 512:(half + 1) * 512]
                    dve.scalar_tensor_tensor(out=dst, in0=dst, scalar=ALPHA, in1=c.banks[2 * i + half][:, :],
                                             op0=ALU.mult, op1=ALU.add).then_inc(order.sem, order.up())
                for half in range(2):
                    dve.wait_ge(order.sem, order.sent - 1)
                    dve.bn_stats(stats[:, i, half, :], x[:, i, half * 512:(half + 1) * 512]).then_inc(order.sem, order.up())
                dve.wait_ge(order.sem, order.sent)
                dve.bn_aggr(mv[:, i, :], stats[:, i, :, :]).then_inc(order.sem, order.up())
                dve.wait_ge(order.sem, order.sent)
                dve.tensor_scalar(sd[:, i:i + 1], mv[:, i, 1:2], 1.0, eps, ALU.mult, ALU.add).then_inc(var.sem, var.up())
                if i >= 2:
                    empty_turned(dve, i - 2, 0).then_inc(emptied_v.sem, emptied_v.up())
                dve.wait_ge(root.sem, root.at(i + 1))
                dve.reciprocal(sd[:, i:i + 1], sd[:, i:i + 1]).then_inc(order.sem, order.up())
                dve.wait_ge(order.sem, order.sent)
                dve.scalar_tensor_tensor(out=shift[:, i:i + 1], in0=mv[:, i, 0:1], scalar=-1.0, in1=sd[:, i:i + 1],
                                         op0=ALU.mult, op1=ALU.mult).then_inc(scaled.sem, scaled.up())
                if i == 0:
                    dve.wait_ge(got.sem, got.at(32))
                dve.wait_ge(centred.sem, centred.at(i + 1))
                dve.tensor_tensor(x[:, i, :], x[:, i, :], gain, ALU.mult).then_inc(gained.sem, gained.up())
                if i == NT - 1:
                    dve.wait_ge(gained.sem, gained.at(NT))
                    dve.tensor_tensor(x[:, i, :], x[:, i, :], bias, ALU.add).then_inc(last_normed.sem, last_normed.up())
            for i in (NT - 2, NT - 1):
                empty_turned(dve, i, 0).then_inc(emptied_v.sem, emptied_v.up())

        @block.gpsimd
        def _(pool):
            if meanwhile:
                meanwhile(pool)
            pool.wait_ge(got.sem, got.at(32))
            for i in range(NT - 1):
                pool.wait_ge(gained.sem, gained.at(i + 1))
                pool.tensor_tensor(x[:, i, :], x[:, i, :], bias, ALU.add).then_inc(normed.sem, normed.up())

        @block.scalar
        def _(act):
            act.dma_start(gain, gain_row.partition_broadcast(P)).then_inc(got.sem, got.up(16))
            act.dma_start(bias, bias_row.partition_broadcast(P)).then_inc(got.sem, got.up(16))
            for i in range(NT):
                act.wait_ge(var.sem, var.at(i + 1))
                act.activation(sd[:, i:i + 1], sd[:, i:i + 1], ACT.Sqrt).then_inc(root.sem, root.up())
                act.wait_ge(scaled.sem, scaled.at(i + 1))
                act.activation(x[:, i, :], x[:, i, :], ACT.Identity, bias=shift[:, i:i + 1],
                               scale=sd[:, i:i + 1]).then_inc(centred.sem, centred.up())
                if i >= 2:
                    empty_turned(act, i - 2, 1).then_inc(emptied.sem, emptied.up())
            for i in (NT - 2, NT - 1):
                empty_turned(act, i, 1).then_inc(emptied.sem, emptied.up())

        @block.sync
        def _(sync):
            c.load_weights(sync)
            if x_rows is not None:
                for i in range(NT):
                    signal, count = ready(i)
                    sync.wait_ge(signal.sem, count)
                    sync.dma_start(x_rows[i * P:(i + 1) * P, :], x[:, i, :]).then_inc(kept.sem, kept.up(16))
                sync.wait_ge(kept.sem, kept.at(16 * NT))


def copy_to_view(eng, dst, src):
    if hasattr(eng, "activation"):
        return eng.activation(dst, src, ACT.Copy)
    return eng.tensor_copy(dst, src)


def down_and_rms_norm(c, keys, hidden, gain_row, rows, eps, next_gain=None, tail=1):
    x, xT = c.x, c.xT
    n = c.norms
    parts, inv, inv2 = n[:, 64:72].rearrange("p (i a) -> p i a", i=NT), n[:, 72:76], n[:, 76:80]
    gain, work, junk = rows[:, 0, :], rows[:, 1, :], rows[:, 2, :]
    filled, got, squared, mean, root, added, squared2, scale, normed, turned, emptied = (c.sig(n) for n in (
        "bank_filled", "rows_loaded_scalar", "squares_summed", "mean_ready", "root_ready", "term_added",
        "new_squares_summed", "scale_ready", "normed", "rows_turned", "bank_emptied_by_scalar"))
    order, emptied_v = c.sig("vector_order"), c.sig("bank_emptied_by_vector")
    early = len(keys) - tail
    again = next_gain is not None
    ready = normed if again else added
    source = (lambda i: rows[:, 3 + i, :]) if again else (lambda i: x[:, i, :])
    with c.nc.Block() as block:
        @block.tensor
        def _(pe):
            products_by_tile(c, pe, keys, hidden, tail, filled, lambda i: (ready, ready.at(i + 1)), turned, source)

        def empty_turned(eng, i, half):
            eng.wait_ge(turned.sem, turned.at(2 * i + half + 1))
            src = c.banks[2 * i + half][:, :].rearrange("p (k t) -> p k t", k=4)
            dst = xT[:, 4 * half:4 * half + 4, i * P:(i + 1) * P]
            if again:
                return eng.tensor_tensor(dst, src, next_gain[:, 4 * half:4 * half + 4].unsqueeze(2)
                                         .to_broadcast([P, 4, P]), ALU.mult)
            return copy_to_view(eng, dst, src)

        @block.vector
        def _(dve):
            dve.wait_ge(got.sem, got.at(16))
            for i in range(NT):
                dve.wait_ge(squared.sem, squared.at(2 * i + 2))
                dve.tensor_tensor(inv[:, i:i + 1], parts[:, i, 0:1], parts[:, i, 1:2], ALU.add).then_inc(order.sem, order.up())
                dve.wait_ge(order.sem, order.sent)
                dve.tensor_scalar(inv[:, i:i + 1], inv[:, i:i + 1], 1.0 / D, eps, ALU.mult, ALU.add).then_inc(mean.sem, mean.up())
                dve.wait_ge(root.sem, root.at((1 + again) * i + 1))
                dve.reciprocal(inv[:, i:i + 1], inv[:, i:i + 1]).then_inc(order.sem, order.up())
                dve.wait_ge(order.sem, order.sent)
                for half in range(2):
                    cols = slice(half * 512, (half + 1) * 512)
                    dve.scalar_tensor_tensor(out=work[:, cols], in0=c.banks[2 * i + half][:, :], scalar=inv[:, i:i + 1],
                                             in1=gain[:, cols], op0=ALU.mult, op1=ALU.mult).then_inc(order.sem, order.up())
                dve.wait_ge(order.sem, order.sent)
                dve.tensor_tensor(x[:, i, :], x[:, i, :], work, ALU.add).then_inc(added.sem, added.up())
                if i >= 2:
                    empty_turned(dve, i - 2, 0).then_inc(emptied_v.sem, emptied_v.up())
                    if again:
                        empty_turned(dve, i - 2, 1).then_inc(emptied_v.sem, emptied_v.up())
                if again:
                    dve.wait_ge(squared2.sem, squared2.at(i + 1))
                    dve.tensor_scalar(inv2[:, i:i + 1], inv2[:, i:i + 1], 1.0 / D, eps, ALU.mult,
                                      ALU.add).then_inc(mean.sem, mean.up())
                    dve.wait_ge(root.sem, root.at(2 * i + 2))
                    dve.reciprocal(inv2[:, i:i + 1], inv2[:, i:i + 1]).then_inc(scale.sem, scale.up())
            for i in (NT - 2, NT - 1):
                empty_turned(dve, i, 0).then_inc(emptied_v.sem, emptied_v.up())
                if again:
                    empty_turned(dve, i, 1).then_inc(emptied_v.sem, emptied_v.up())

        @block.scalar
        def _(act):
            act.dma_start(gain, gain_row.partition_broadcast(P)).then_inc(got.sem, got.up(16))
            for i in range(NT):
                act.wait_ge(filled.sem, filled.at(early + i + 1))
                for half in range(2):
                    act.activation(junk[:, half * 512:(half + 1) * 512], c.banks[2 * i + half][:, :], ACT.Square,
                                   accum_out=parts[:, i, half:half + 1]).then_inc(squared.sem, squared.up())
                    act.wait_ge(squared.sem, squared.sent)
                act.wait_ge(mean.sem, mean.at((1 + again) * i + 1))
                act.activation(inv[:, i:i + 1], inv[:, i:i + 1], ACT.Sqrt).then_inc(root.sem, root.up())
                if again:
                    act.wait_ge(added.sem, added.at(i + 1))
                    act.activation(junk, x[:, i, :], ACT.Square,
                                   accum_out=inv2[:, i:i + 1]).then_inc(squared2.sem, squared2.up())
                    act.wait_ge(mean.sem, mean.at(2 * i + 2))
                    act.activation(inv2[:, i:i + 1], inv2[:, i:i + 1], ACT.Sqrt).then_inc(root.sem, root.up())
                    act.wait_ge(scale.sem, scale.at(i + 1))
                    act.activation(source(i), x[:, i, :], ACT.Identity,
                                   scale=inv2[:, i:i + 1]).then_inc(normed.sem, normed.up())
                elif i >= 2:
                    empty_turned(act, i - 2, 1).then_inc(emptied.sem, emptied.up())
            if not again:
                for i in (NT - 2, NT - 1):
                    empty_turned(act, i, 1).then_inc(emptied.sem, emptied.up())

        @block.sync
        def _(sync):
            c.load_weights(sync)
HEADS, NOPE, ROPE, VDIM, QR, KVR = 4, 64, 32, 64, 256, 128
EPS1 = 1e-6
TWO_PI = (6.28125, 0.0019350051879882812, 3.0199159819756e-07)


def plan_first(c, a):
    w = a["w_in"][0].rearrange("(k p) n -> p k n", p=P)
    c.plan("latents", w[:, :, 0:416])
    c.plan("gating", w[:, :, 416:928])
    c.plan("conv", w[:, :, 928:1440])
    c.plan("pool", w[:, :, 1440:1952])
    for half in range(2):
        for b in range(4):
            n = 1952 + b * D + half * 512
            c.plan(("gates", half, b), w[:, :, n:n + 512])
    w = a["w_out"][0].rearrange("(k p) n -> p k n", p=P)
    for half in range(2):
        c.plan(("out1", half), w[:, half * 4:(half + 1) * 4, :])
    w = a["w_ff1"][0].rearrange("(k p) n -> p k n", p=P)
    for n in range(8):
        c.plan(("ff1", n), w[:, :, n * 512:(n + 1) * 512])
    w = a["w_ff2"][0].rearrange("(k p) n -> p k n", p=P)
    for n in range(8):
        c.plan(("ff2", n), w[:, n * 4:(n + 1) * 4, :])


def features_from(c, key, xT, dsts, empties=None):
    groups = []
    n = len(dsts)
    for j in range(n):
        w = c.slot(key)[0]
        pairs = [(w[:, k, j * P:(j + 1) * P], xT[:, k, :]) for k in range(xT.shape[1])]
        e = empties[j] if empties else copy_to(dsts[j])
        groups.append(((key,), product(pairs), (key,) if j == n - 1 else (), "av"[j % 2] if not empties else "a", e))
    return groups


def tokens_from(c, key, xT, cols, dsts, empties=None, who=None, last=True):
    groups = []
    for i in range(NT):
        w = c.slot(key)[0]
        pairs = [(xT[:, k, i * P:(i + 1) * P], w[:, k, cols[0]:cols[1]]) for k in range(xT.shape[1])]
        e = empties[i] if empties else copy_to(dsts[i])
        groups.append(((key,), product(pairs), (key,) if last and i == NT - 1 else (),
                       who or "av"[i % 2], e))
    return groups


def setup_constants(c, a):
    nc = c.nc
    c.ident = c.sb("ident", [P, P])
    c.keep_le = c.sb("keep_le", [P, P])
    c.ones = c.sb("ones", [P, P])
    c.small = c.sb("small", [P, 128])
    c.norms = c.sb("norm_numbers", [P, 80])
    rows = [c.region(11, 0, 256)[:, n * P:(n + 1) * P] for n in range(2)]
    c.columns = [c.sb(f"columns{n}", [P, P]) for n in range(2)]
    names = [
        [("gate_b", 32), ("norm_mix_pre", 8), ("q_norm", 2), ("kv_norm", 1), ("pool_scale", 2), ("conv_w", 6),
         ("norm_ffn_pre", 8), ("conv_b_2", 16), ("hg_lb_logits_3", 8), ("nsa_norm_g_3", 4), ("hg_norm_g_3", 1),
         ("lambda_q1_2", 0), ("subln_w_2", 1)],
        [("conv_w_2", 80), ("ssm_norm_w_2", 8), ("cmp_pe_k_3", 16), ("cmp_pe_v_3", 16)],
    ]
    c.col = {}
    made, set_, loaded = c.sig("constants_zeroed"), c.sig("constants_made"), c.sig("parameters_loaded")
    moves = []
    for n, group in enumerate(names):
        at = 0
        for name, count in group:
            if not count or name not in a:
                continue
            src = a[name]
            src = src.rearrange("a b n -> (a b n)") if len(src.shape) == 3 else src.rearrange("a n -> (a n)")
            moves.append((rows[n][at:at + count, :], src.rearrange("(r p) -> r p", p=P)))
            c.col[name] = c.columns[n][:, at:at + count]
            at += count
    with nc.Block() as block:
        @block.gpsimd
        def _(pool):
            pool.memset(c.ident[:, :], 0.0).then_inc(made.sem, made.up())
            pool.memset(c.keep_le[:, :], 0.0).then_inc(made.sem, made.up())
            pool.memset(c.ones[:, :], 1.0).then_inc(made.sem, made.up())
            pool.memset(c.region(11, 0, 256), 0.0).then_inc(made.sem, made.up())
            pool.wait_ge(made.sem, made.at(4))
            pool.affine_select(out=c.ident[:, :], in_=c.ident[:, :], compare_op=ALU.not_equal, fill=1.0,
                                        base=0, pattern=[[-1, P]], channel_multiplier=1).then_inc(set_.sem, set_.up())
            pool.affine_select(out=c.keep_le[:, :], in_=c.keep_le[:, :], compare_op=ALU.is_ge, fill=NEG,
                                        base=0, pattern=[[-1, P]], channel_multiplier=1).then_inc(set_.sem, set_.up())
            pool.wait_ge(set_.sem, set_.at(2))

        @block.scalar
        def _(act):
            act.wait_ge(made.sem, made.at(4))
            for dst, src in moves:
                act.dma_start(dst, src).then_inc(loaded.sem, loaded.up(16))
            act.wait_ge(loaded.sem, loaded.at(16 * len(moves)))

        @block.sync
        def _(sync):
            x = a["x"][0].rearrange("(i p) d -> p i d", p=P)
            loaded_x = c.sig("x_loaded")
            sync.dma_start(c.x, x).then_inc(loaded_x.sem, loaded_x.up(16))
            c.load_weights(sync)
            sync.wait_ge(loaded_x.sem, loaded_x.at(16))
    bank_groups(c, [((), turns(c, [rows[n]]), (), "v", copy_to(c.columns[n][:, :])) for n in range(2)])


def first_block(c, a):
    nc, x, xT = c.nc, c.x, c.xT
    small = c.small
    normed = c.region(6, 0, NT, D)
    row_inverse = small[:, 100:104]
    inverse_rms(c, [x[:, i, :] for i in range(NT)], EPS1, c.region(8, 0, D), row_inverse)

    def scale_rows(dst, src, inv, n=NT):
        done = c.sig("rows_scaled")
        with nc.Block() as block:
            @block.vector
            def _(dve):
                for i in range(n):
                    dve.tensor_scalar(dst(i), src(i), inv(i), None, ALU.mult).then_inc(done.sem, done.up())
                dve.wait_ge(done.sem, done.at(n))
    scale_rows(lambda i: normed[:, i, :], lambda i: x[:, i, :], lambda i: row_inverse[:, i:i + 1])
    to_features(c, lambda i: normed[:, i, :], xT, c.col["norm_mix_pre"])

    latents = c.region(7, 0, NT, 416)
    gating = c.region(7, 1664, NT, 512)
    convpool = c.region(6, 0, 8, S)
    groups = tokens_from(c, "latents", xT, (0, 416), [latents[:, i, :] for i in range(NT)])
    groups += tokens_from(c, "gating", xT, (0, 512), [gating[:, i, :] for i in range(NT)])
    groups += features_from(c, "conv", xT, [convpool[:, j, :] for j in range(4)])
    groups += features_from(c, "pool", xT, [convpool[:, 4 + j, :] for j in range(4)])
    bank_groups(c, groups)

    branches = c.region(10, 0, 8, S)
    latent_attention(c, a, latents, branches)
    spatial_gating(c, a, gating, branches)
    conv_and_pool(c, a, convpool, branches)

    wbr = c.region(8, 0, 8, D)
    load_rows(c, "scalar", [(wbr[:, 2 * b:2 * b + 2, :], a[n][0].rearrange("(k p) n -> p k n", p=P))
                            for b, n in enumerate(("w_br_mla", "w_br_sg", "w_br_conv", "w_br_pool"))])
    merged = c.region(11, 0, 8, S)
    gate = c.region(6, 0, 2, S)
    term = c.region(6, 2 * S, 2, S)
    filled, opened, weighed, added = (c.sig(n) for n in ("bank_filled", "gates_open", "branch_weighed", "term_added"))
    steps = [(half, b, j) for half in range(2) for b in range(4) for j in range(4)]
    with nc.Block() as block:
        @block.tensor
        def _(pe):
            for n, (half, b, j) in enumerate(steps):
                w = c.weights(pe, ("gates", half, b))[0]
                if n >= 2:
                    pe.wait_ge(opened.sem, opened.at(n - 1))
                    pe.wait_ge(weighed.sem, weighed.at(n - 1))
                for k in range(KD):
                    pe.matmul(c.banks[n % 2][:, :], w[:, k, j * P:(j + 1) * P], xT[:, k, :], start=k == 0,
                              stop=k == KD - 1)
                m = (half * 4 + j) * P
                for k in range(2):
                    last = pe.matmul(c.banks[2 + n % 2][:, :], wbr[:, 2 * b + k, m:m + P], branches[:, 2 * b + k, :],
                                     start=k == 0, stop=k == 1)
                last.then_inc(filled.sem, filled.up())
                if j == 3:
                    c.release(("gates", half, b), filled)

        @block.scalar
        def _(act):
            for n, (half, b, j) in enumerate(steps):
                act.wait_ge(filled.sem, filled.at(n + 1))
                if n >= 2:
                    act.wait_ge(weighed.sem, weighed.at(n - 1))
                col = c.col["gate_b"][:, b * 8 + half * 4 + j:b * 8 + half * 4 + j + 1]
                act.activation(gate[:, n % 2, :], c.banks[n % 2][:, :], ACT.Sigmoid, bias=col).then_inc(opened.sem, opened.up())

        @block.vector
        def _(dve):
            for n, (half, b, j) in enumerate(steps):
                dve.wait_ge(opened.sem, opened.at(n + 1))
                if n >= 2 and b:
                    dve.wait_ge(added.sem, added.sent)
                dst = merged[:, half * 4 + j, :]
                dve.tensor_tensor(dst if b == 0 else term[:, n % 2, :], gate[:, n % 2, :],
                                              c.banks[2 + n % 2][:, :], ALU.mult).then_inc(weighed.sem, weighed.up())
                if b:
                    dve.wait_ge(weighed.sem, weighed.at(n + 1))
                    dve.tensor_tensor(dst, dst, term[:, n % 2, :], ALU.add).then_inc(added.sem, added.up())
            dve.wait_ge(added.sem, added.sent)

        @block.sync
        def _(sync):
            c.load_weights(sync)

    down_and_rms_norm(c, [("out1", half) for half in range(2)], merged, a["norm_mix_post"][0], c.region(6, 0, 7, D), EPS1,
                      next_gain=c.col["norm_ffn_pre"])
    hidden = c.region(6, 0, 32, S)

    def squared_relu(dst):
        def run(act, bank, order):
            act.activation(dst, bank[:, :], ACT.Relu).then_inc(order.sem, order.up())
            act.wait_ge(order.sem, order.sent)
            return act.activation(dst, dst, ACT.Square)
        return run
    groups = []
    for n in range(8):
        groups += features_from(c, ("ff1", n), xT, [None] * 4, [squared_relu(hidden[:, n * 4 + j, :]) for j in range(4)])
    bank_groups(c, groups)
    down_and_rms_norm(c, [("ff2", n) for n in range(8)], hidden, a["norm_ffn_post"][0], c.region(10, 0, 3, D), EPS1)


def latent_attention(c, a, latents, branches):
    nc = c.nc
    wuq = c.region(8, 0, 2, 384)
    wukv = c.region(8, 768, 512)
    pos_i = c.small[:, 104:108].bitcast(I32)
    load_rows(c, "scalar", [(wuq, a["w_uq"][0].rearrange("(k p) n -> p k n", p=P)), (wukv, a["w_ukv"][0]),
                            (pos_i, a["positions"][0].rearrange("(i p) -> p i", p=P))])
    inv = c.small[:, 108:116]
    inverse_rms(c, [latents[:, i, 0:QR] for i in range(NT)] + [latents[:, i, QR:QR + KVR] for i in range(NT)], EPS1,
                c.region(9, 0, D), inv)
    half = ROPE // 2
    freq = c.region(8, 1280, half)
    pos = c.small[:, 116:120]
    ang = c.region(8, 1296, NT, half)
    turnsn = c.region(8, 1360, 2, NT * half)
    trig = c.region(8, 1488, 2, NT, half)
    order, ready, made = c.sig("vector_order"), c.sig("angles_ready"), c.sig("iota_made")
    sines = c.sig("sines_ready")
    with nc.Block() as block:
        @block.gpsimd
        def _(pool):
            for k in range(half):
                pool.memset(freq[:, k:k + 1], float(np.float32(10000.0) ** np.float32(-2.0 * k / ROPE))).then_inc(made.sem, made.up())

        @block.vector
        def _(dve):
            dve.tensor_copy(pos, pos_i).then_inc(order.sem, order.up())
            dve.wait_ge(order.sem, order.sent)
            dve.wait_ge(made.sem, made.at(half))
            dve.tensor_tensor(ang, pos.unsqueeze(2).to_broadcast([P, NT, half]),
                                 freq.unsqueeze(1).to_broadcast([P, NT, half]), ALU.mult).then_inc(order.sem, order.up())
            dve.wait_ge(order.sem, order.sent)
            for t, shift in enumerate((math.pi / 2, 0.0)):
                dst = trig[:, t, :, :]
                n = turnsn[:, t, :].rearrange("p (i k) -> p i k", i=NT)
                dve.tensor_scalar(n, ang, 1.0 / (2 * math.pi), shift / (2 * math.pi), ALU.mult, ALU.add).then_inc(order.sem, order.up())
                dve.wait_ge(order.sem, order.sent)
                dve.tensor_scalar(n, n, 12582912.0, None, ALU.add).then_inc(order.sem, order.up())
                dve.wait_ge(order.sem, order.sent)
                dve.tensor_scalar(n, n, -12582912.0, None, ALU.add).then_inc(order.sem, order.up())
                dve.wait_ge(order.sem, order.sent)
                dve.scalar_tensor_tensor(out=dst, in0=n, scalar=-TWO_PI[0], in1=ang, op0=ALU.mult, op1=ALU.add).then_inc(order.sem, order.up())
                dve.wait_ge(order.sem, order.sent)
                dve.scalar_tensor_tensor(out=dst, in0=n, scalar=-TWO_PI[1], in1=dst, op0=ALU.mult, op1=ALU.add).then_inc(order.sem, order.up())
                dve.wait_ge(order.sem, order.sent)
                dve.scalar_tensor_tensor(out=dst, in0=n, scalar=-TWO_PI[2], in1=dst, op0=ALU.mult, op1=ALU.add).then_inc(order.sem, order.up())
                dve.wait_ge(order.sem, order.sent)
                if shift:
                    dve.tensor_scalar(dst, dst, shift, None, ALU.add).then_inc(order.sem, order.up())
                    dve.wait_ge(order.sem, order.sent)
                dve.tensor_scalar(dst, dst, math.pi, None, ALU.min).then_inc(order.sem, order.up())
                dve.wait_ge(order.sem, order.sent)
                dve.tensor_scalar(dst, dst, -math.pi, None, ALU.max).then_inc(order.sem, order.up())
                dve.wait_ge(order.sem, order.sent)
            for i in range(NT):
                dve.tensor_scalar(latents[:, i, 0:QR], latents[:, i, 0:QR], inv[:, i:i + 1], None, ALU.mult).then_inc(order.sem, order.up())
                dve.wait_ge(order.sem, order.sent)
                dve.tensor_scalar(latents[:, i, QR:QR + KVR], latents[:, i, QR:QR + KVR], inv[:, NT + i:NT + i + 1],
                                     None, ALU.mult).then_inc(order.sem, order.up())
                dve.wait_ge(order.sem, order.sent)
            dve.tensor_copy(pos, pos).then_inc(ready.sem, ready.up())

        @block.scalar
        def _(act):
            act.wait_ge(ready.sem, ready.at(1))
            act.activation(trig, trig, ACT.Sin).then_inc(sines.sem, sines.up())
            act.wait_ge(sines.sem, sines.sent)
    latT = c.region(9, 0, 3, S)
    groups = []
    for i in range(NT):
        blocks = [latents[:, i, k * P:(k + 1) * P] for k in range(3)]
        groups.append(((), turns(c, blocks), (), "v",
                       scaled_to(latT[:, :, i * P:(i + 1) * P], c.columns[0][:, 40:43])))
    bank_groups(c, groups)
    q = c.region(8, 1616, NT, 384)
    kv = c.region(11, 0, NT, 512)
    groups = []
    for i in range(NT):
        groups.append(((), product([(latT[:, k, i * P:(i + 1) * P], wuq[:, k, :]) for k in range(2)]), (), "v",
                       copy_to(q[:, i, :])))
        groups.append(((), product([(latT[:, 2, i * P:(i + 1) * P], wukv)]), (), "a", copy_to(kv[:, i, :])))
    bank_groups(c, groups)
    keys = c.region(11, 2048, NT, 384)
    r = [c.region(9, 1536 + n * 256, NT, HEADS, half) for n in range(4)]
    rotated = c.sig("rotated")
    with nc.Block() as block:
        @block.vector
        def _(dve):
            qv = q.rearrange("p i (h e) -> p i h e", h=HEADS)
            kk = keys.rearrange("p i (h e) -> p i h e", h=HEADS)
            kvv = kv.rearrange("p i (h e) -> p i h e", h=HEADS)
            for i in range(NT):
                cos = trig[:, 0, i, :].unsqueeze(1).to_broadcast([P, HEADS, half])
                sin = trig[:, 1, i, :].unsqueeze(1).to_broadcast([P, HEADS, half])
                x1, x2 = qv[:, i, :, NOPE:NOPE + half], qv[:, i, :, NOPE + half:NOPE + ROPE]
                kr = latents[:, i, QR + KVR:QR + KVR + ROPE]
                k1 = kr[:, 0:half].unsqueeze(1).to_broadcast([P, HEADS, half])
                k2 = kr[:, half:ROPE].unsqueeze(1).to_broadcast([P, HEADS, half])
                for u1, u2, o1, o2 in ((x1, x2, x1, x2), (k1, k2, kk[:, i, :, NOPE:NOPE + half],
                                                          kk[:, i, :, NOPE + half:NOPE + ROPE])):
                    dve.tensor_tensor(r[0][:, i, :, :], u1, cos, ALU.mult).then_inc(order.sem, order.up())
                    dve.wait_ge(order.sem, order.sent)
                    dve.tensor_tensor(r[1][:, i, :, :], u2, sin, ALU.mult).then_inc(order.sem, order.up())
                    dve.wait_ge(order.sem, order.sent)
                    dve.tensor_tensor(r[2][:, i, :, :], u2, cos, ALU.mult).then_inc(order.sem, order.up())
                    dve.wait_ge(order.sem, order.sent)
                    dve.tensor_tensor(r[3][:, i, :, :], u1, sin, ALU.mult).then_inc(order.sem, order.up())
                    dve.wait_ge(order.sem, order.sent)
                    dve.tensor_tensor(o1, r[0][:, i, :, :], r[1][:, i, :, :], ALU.subtract).then_inc(order.sem, order.up())
                    dve.wait_ge(order.sem, order.sent)
                    dve.tensor_tensor(o2, r[2][:, i, :, :], r[3][:, i, :, :], ALU.add).then_inc(order.sem, order.up())
                    dve.wait_ge(order.sem, order.sent)
                dve.tensor_copy(kk[:, i, :, 0:NOPE], kvv[:, i, :, 0:NOPE]).then_inc(rotated.sem, rotated.up())
                dve.wait_ge(rotated.sem, rotated.sent)
    E = NOPE + ROPE
    qT = c.region(9, 0, HEADS, S)
    kT = c.region(9, 2048, HEADS, S)
    groups = []
    for h in range(HEADS):
        for src, dst, who in ((q, qT, "v"), (keys, kT, "a")):
            groups.append(((), turns(c, [src[:, i, h * E:(h + 1) * E] for i in range(NT)]), (), who,
                           copy_to(dst[0:E, h, :])))
    bank_groups(c, groups)
    out = c.region(8, 0, NT, HEADS * VDIM)
    units = []
    for h in range(HEADS):
        for i in range(NT):
            def score(pe, bank, h=h, i=i):
                return pe.matmul(bank[:, 0:(i + 1) * P], qT[0:E, h, i * P:(i + 1) * P], kT[0:E, h, 0:(i + 1) * P],
                                 start=True, stop=True)

            def finish(dve, bank, factor, h=h, i=i):
                return dve.tensor_scalar(out[:, i, h * VDIM:(h + 1) * VDIM], bank[:, 0:VDIM], factor, None, ALU.mult)
            units.append({"keys": (i + 1) * P, "scale": E ** -0.5, "score": score,
                          "masks": [((i * P, (i + 1) * P), c.keep_le[:, :], 1.0)],
                          "values": [kv[:, k, h * 128 + NOPE:(h + 1) * 128] for k in range(i + 1)], "finish": finish})
    attention(c, units, c.region(8, 1024, ATT_WORK))
    to_features(c, lambda i: out[:, i, :], branches[:, 0:2, :], width=256)


def spatial_gating(c, a, gating, branches):
    nc = c.nc
    gain, bias = c.region(8, 0, 2, 256)[:, 0, :], c.region(8, 0, 2, 256)[:, 1, :]
    ws = c.region(8, 512, 4, P)
    wT = c.region(8, 1024, 4, P)
    bs = c.region(8, 1536, 4)
    load_rows(c, "scalar", [(gain, a["sg_ln_g"][0].partition_broadcast(P)), (bias, a["sg_ln_b"][0].partition_broadcast(P)),
                            (ws, a["sg_w"][0].rearrange("g t s -> t g s"))])
    load_rows(c, "gpsimd", [(bs[:, g:g + 1], a["sg_b"][0, g, :].rearrange("(t o) -> t o", o=1)) for g in range(4)])
    done, picked = c.sig("gelu_ready"), c.sig("causal_weights")
    with nc.Block() as block:
        @block.scalar
        def _(act):
            act.activation(gating, gating, ACT.Gelu_apprx_tanh).then_inc(done.sem, done.up())
            act.wait_ge(done.sem, done.sent)

        @block.gpsimd
        def _(pool):
            pool.affine_select(out=ws, in_=ws, compare_op=ALU.is_ge, fill=0.0, base=0,
                                          pattern=[[0, 4], [-1, P]], channel_multiplier=1).then_inc(picked.sem, picked.up())
            pool.wait_ge(picked.sem, picked.at(1))
    layer_norm_in_place(c, lambda i: gating[:, i, 256:512], gain, bias, EPS1, c.small, width=256)
    bank_groups(c, [((), turns(c, [ws[:, g, :] for g in range(4)]), (), "v", copy_to(wT))])
    out = c.region(8, 1600, NT, 256)
    groups = []
    for i in range(NT):
        def mix(pe, bank, i=i):
            for g in range(4):
                last = pe.matmul(bank[:, g * 64:(g + 1) * 64], wT[:, g, :], gating[:, i, 256 + g * 64:256 + (g + 1) * 64],
                                 start=True, stop=True)
            return last

        def gate(dve, bank, order, i=i):
            o = out[:, i, :].rearrange("p (g e) -> p g e", g=4)
            dve.tensor_tensor(o, bank[:, 0:256].rearrange("p (g e) -> p g e", g=4),
                                     bs.unsqueeze(2).to_broadcast([P, 4, 64]), ALU.add).then_inc(order.sem, order.up())
            dve.wait_ge(order.sem, order.sent)
            return dve.tensor_tensor(out[:, i, :], out[:, i, :], gating[:, i, 0:256], ALU.mult)
        groups.append(((), mix, (), "v", gate))
    bank_groups(c, groups)
    to_features(c, lambda i: out[:, i, :], branches[:, 2:4, :], width=256)


def conv_and_pool(c, a, cp, branches):
    nc = c.nc
    order, done, made = c.sig("vector_order"), c.sig("branches_ready"), c.sig("iota_made")
    cw = c.col["conv_w"]
    count = c.region(8, 0, 2, S)
    term = c.region(8, 1024, 2, S)
    s1 = c.region(8, 2048, 2, S)
    wp = c.region(9, 0, 2, 64)
    load_rows(c, "scalar", [(wp[(g % 2) * 64:(g % 2) * 64 + 64, g // 2, :], a["pool_w"][0, g]) for g in range(4)])
    with nc.Block() as block:
        @block.gpsimd
        def _(pool):
            pool.iota(count, pattern=[[0, 2], [1, S]], base=1, channel_multiplier=0,
                               allow_small_or_imprecise_dtypes=True).then_inc(made.sem, made.up())

        @block.vector
        def _(dve):
            z, y = cp[:, 0:2, :], branches[:, 4:6, :]
            dve.tensor_tensor(z, cp[:, 4:6, :], z, ALU.mult).then_inc(order.sem, order.up())
            dve.wait_ge(order.sem, order.sent)
            for t in range(2):
                for k in (2, 1, 0):
                    lag = 2 - k
                    col = cw[:, k * 2 + t:k * 2 + t + 1]
                    if lag == 0:
                        dve.tensor_scalar(y[:, t, :], z[:, t, :], col, None, ALU.mult).then_inc(order.sem, order.up())
                        dve.wait_ge(order.sem, order.sent)
                    else:
                        dve.scalar_tensor_tensor(out=y[:, t, lag:S], in0=z[:, t, 0:S - lag], scalar=col,
                                                    in1=y[:, t, lag:S], op0=ALU.mult, op1=ALU.add).then_inc(order.sem, order.up())
                        dve.wait_ge(order.sem, order.sent)
            dve.tensor_tensor(y, y, cp[:, 2:4, :], ALU.mult).then_inc(order.sem, order.up())
            dve.wait_ge(order.sem, order.sent)
            dve.wait_ge(made.sem, made.at(1))
            p = cp[:, 6:8, :]
            a0, a1 = s1, term
            dve.tensor_copy(a0, p).then_inc(order.sem, order.up())
            dve.wait_ge(order.sem, order.sent)
            pooled = cp[:, 4:6, :]
            for n, lag in enumerate((1, 2, 4, 8)):
                dve.tensor_copy(a1[:, :, 0:lag], a0[:, :, 0:lag]).then_inc(order.sem, order.up())
                dve.wait_ge(order.sem, order.sent)
                dve.tensor_tensor(a1[:, :, lag:S], a0[:, :, lag:S], a0[:, :, 0:S - lag], ALU.add).then_inc(order.sem, order.up())
                dve.wait_ge(order.sem, order.sent)
                rows = slice((n % 2) * 64, (n % 2) * 64 + 64)
                dve.tensor_copy(pooled[rows, n // 2, :], a1[rows, n // 2, :]).then_inc(order.sem, order.up())
                dve.wait_ge(order.sem, order.sent)
                dve.tensor_scalar(count[rows, n // 2, :], count[rows, n // 2, :], float(2 ** (n + 1)), None, ALU.min).then_inc(order.sem, order.up())
                dve.wait_ge(order.sem, order.sent)
                a0, a1 = a1, a0
            dve.reciprocal(count, count).then_inc(order.sem, order.up())
            dve.wait_ge(order.sem, order.sent)
            dve.tensor_tensor(pooled, pooled, count, ALU.mult).then_inc(order.sem, order.up())
            dve.wait_ge(order.sem, order.sent)
            dve.tensor_tensor(pooled, pooled, p, ALU.subtract).then_inc(done.sem, done.up())
            dve.wait_ge(done.sem, done.sent)
    groups = []
    for t in range(2):
        def mix(pe, bank, t=t):
            for g in range(2):
                r = slice(g * 64, g * 64 + 64)
                last = pe.matmul(bank[r, :], wp[r, t, :], cp[r, 4 + t, :], start=True, stop=True)
            return last

        def scale(dve, bank, order, t=t):
            return dve.tensor_scalar(branches[:, 6 + t, :], bank[:, :], c.col["pool_scale"][:, t:t + 1], None, ALU.mult)
        groups.append(((), mix, (), "v", scale))
    bank_groups(c, groups)
AH, AHD, AVD = 8, 64, 128
LAMBDA_INIT = 0.8 - 0.6 * math.exp(0.0)
SH, SHD, SG, SN = 16, 64, 4, 128
FF2 = 2816
EPS2 = 1e-5
ALPHA = 2.0 ** 0.25


def plan_second(c, a):
    w = a["w_in_2"][0].rearrange("(k p) n -> p k n", p=P)
    for part, at in (("q2", 0), ("k2", 1024), ("v2", 2048), ("xbc2", 4096), ("xbc2", 5120), ("z2", 3072)):
        for half in range(2):
            n = at + half * 512
            c.plan((part, n), w[:, :, n:n + 512])
    c.plan("dt2", w[:, :, 6144:6160])
    w = a["w_out_2"][0].rearrange("(k p) n -> p k n", p=P)
    for n in range(4):
        c.plan(("out2", n), w[:, n * 4:(n + 1) * 4, :])
    plan_gated(c, "gu2", a["w_gate_2"][0], a["w_up_2"][0], FF2)
    w = a["w_down_2"][0].rearrange("(k p) n -> p k n", p=P)
    for n in range(0, FF2 // P, 4):
        c.plan(("down2", n), w[:, n:min(n + 4, FF2 // P), :])


def plan_gated(c, key, gate, up, width):
    g, u = (w.rearrange("(k p) n -> p k n", p=P) for w in (gate, up))
    for n in range(0, width, 256):
        c.plan((key, n), g[:, :, n:n + 256], u[:, :, n:n + 256])


def post_norm(c, gain_row, bias_row, rows, eps):
    gain, bias = rows[:, 0, :], rows[:, 1, :]
    load_rows(c, "scalar", [(gain, gain_row.partition_broadcast(P)), (bias, bias_row.partition_broadcast(P))])
    layer_norm_in_place(c, lambda i: c.x[:, i, :], gain, bias, eps, c.small)


def second_block(c, a):
    xT = c.xT
    mixT = c.region(10, 0, 16, S)
    qT, kT = c.region(6, 0, 8, S), c.region(7, 0, 8, S)
    v = c.region(8, 0, NT, D)
    groups = []
    for n in (0, 512):
        groups += features_from(c, ("q2", n), xT, [qT[:, n // P + j, :] for j in range(4)])
    for n in (0, 512):
        groups += features_from(c, ("k2", 1024 + n), xT, [kT[:, n // P + j, :] for j in range(4)])
    for n in (0, 512):
        groups += tokens_from(c, ("v2", 2048 + n), xT, (0, 512), [v[:, i, n:n + 512] for i in range(NT)])
    vecs, dist = c.region(11, 3560, 4, AHD), c.region(11, ATT_WORK, 896)
    made, got = c.sig("iota_made"), c.sig("rows_loaded_gpsimd")

    def tables(pool):
        for n, k in enumerate(("lambda_q1_2", "lambda_q2_2", "lambda_k1_2", "lambda_k2_2")):
            pool.dma_start(vecs[:, n, :], a[k][0].partition_broadcast(P)).then_inc(got.sem, got.up(16))
        pool.iota(dist, pattern=[[-1, 896]], base=384, channel_multiplier=1,
                  allow_small_or_imprecise_dtypes=True).then_inc(made.sem, made.up())
        pool.wait_ge(made.sem, made.at(1))
        pool.wait_ge(got.sem, got.at(16 * 4))
    bank_groups(c, groups, meanwhile=tables)
    differential_attention(c, qT, kT, v, vecs, dist, mixT)
    state_space(c, a, mixT)
    down_and_layer_norm(c, [("out2", n) for n in range(4)], mixT, a["ln1_g_2"][0], a["ln1_b_2"][0],
                        c.region(9, 0, 2, D), EPS2)
    hidden = c.region(6, 0, FF2 // P, S)
    gated(c, "gu2", FF2, xT, hidden)
    down_and_layer_norm(c, [("down2", n) for n in range(0, FF2 // P, 4)], hidden, a["ln2_g_2"][0], a["ln2_b_2"][0],
                        c.region(9, 0, 2, D), EPS2, tail=2)


def gated(c, key, width, xT, hidden):
    filled, opened, done = c.sig("bank_filled"), c.sig("gates_open"), c.sig("branch_weighed")
    n_tiles = width // P
    with c.nc.Block() as block:
        @block.tensor
        def _(pe):
            for n in range(n_tiles):
                g, u = c.weights(pe, (key, n // 2 * 256))
                j = n % 2
                if n >= 2:
                    pe.wait_ge(done.sem, done.at(n - 1))
                for w, bank in ((g, c.banks[n % 2]), (u, c.banks[2 + n % 2])):
                    for k in range(KD):
                        last = pe.matmul(bank[:, :], w[:, k, j * P:(j + 1) * P], xT[:, k, :], start=k == 0,
                                         stop=k == KD - 1)
                last.then_inc(filled.sem, filled.up())
                if j == 1:
                    c.release((key, n // 2 * 256), filled)

        @block.scalar
        def _(act):
            for n in range(n_tiles):
                act.wait_ge(filled.sem, filled.at(n + 1))
                act.activation(hidden[:, n, :], c.banks[n % 2][:, :], ACT.Silu).then_inc(opened.sem, opened.up())

        @block.vector
        def _(dve):
            for n in range(n_tiles):
                dve.wait_ge(opened.sem, opened.at(n + 1))
                dve.tensor_tensor(hidden[:, n, :], hidden[:, n, :], c.banks[2 + n % 2][:, :], ALU.mult).then_inc(done.sem, done.up())

        @block.sync
        def _(sync):
            c.load_weights(sync)


def differential_attention(c, qT, kT, v, vecs, dist, mixT):
    nc = c.nc
    prod = c.region(11, 256, 2, AHD)
    lam = c.region(11, 384, 4)
    order, powers, ready = c.sig("vector_order"), c.sig("exponentials"), c.sig("lambda_ready")
    neg_lam = c.small[:, 104:105]
    gain = c.small[:, 106:107]
    with nc.Block() as block:
        @block.vector
        def _(dve):
            neg = c.region(11, 400, 896)
            dve.tensor_scalar(neg, dist, -1.0, None, ALU.mult).then_inc(order.sem, order.up())
            dve.wait_ge(order.sem, order.sent)
            dve.tensor_tensor(dist, dist, neg, ALU.max).then_inc(order.sem, order.up())
            dve.wait_ge(order.sem, order.sent)
            dve.tensor_tensor(prod, vecs[:, 0:2, :], vecs[:, 2:4, :], ALU.mult).then_inc(order.sem, order.up())
            dve.wait_ge(order.sem, order.sent)
            dve.tensor_reduce(lam[:, 0:2], prod, AX.X, ALU.add).then_inc(ready.sem, ready.up())
            dve.wait_ge(powers.sem, powers.at(1))
            dve.tensor_tensor(neg_lam, lam[:, 1:2], lam[:, 0:1], ALU.subtract).then_inc(order.sem, order.up())
            dve.wait_ge(order.sem, order.sent)
            dve.tensor_scalar(neg_lam, neg_lam, -LAMBDA_INIT, None, ALU.add).then_inc(order.sem, order.up())
            dve.wait_ge(order.sem, order.sent)
            dve.tensor_scalar(gain, c.col["subln_w_2"], 1.0 - LAMBDA_INIT, None, ALU.mult).then_inc(order.sem, order.up())
            dve.wait_ge(order.sem, order.sent)

        @block.scalar
        def _(act):
            act.wait_ge(ready.sem, ready.at(1))
            act.activation(lam[:, 0:2], lam[:, 0:2], ACT.Exp).then_inc(powers.sem, powers.up())
    out = c.region(9, 0, NT, D)
    units = []
    for h in range(AH):
        slope = 2.0 ** (-8.0 * (h + 1) / AH)
        for i in range(NT):
            for part in range(2):
                def score(pe, bank, h=h, i=i, part=part):
                    r = slice(part * AHD, (part + 1) * AHD)
                    return pe.matmul(bank[:, :], qT[r, h, i * P:(i + 1) * P], kT[r, h, :], start=True, stop=True)

                def finish(dve, bank, factor, h=h, i=i, part=part):
                    o = out[:, i, h * AVD:(h + 1) * AVD]
                    if part == 0:
                        return dve.tensor_scalar(o, bank[:, 0:AVD], factor, None, ALU.mult)
                    return dve.scalar_tensor_tensor(out=o, in0=bank[:, 0:AVD], scalar=factor, in1=o, op0=ALU.mult,
                                                    op1=ALU.add)
                units.append({"keys": S, "scale": AHD ** -0.5, "score": score,
                              "masks": [((0, S), dist[:, 384 - i * P:384 - i * P + S], -slope / AHD ** -0.5)],
                              "values": [v[:, k, h * AVD:(h + 1) * AVD] for k in range(NT)], "finish": finish,
                              "weight": neg_lam if part else None})
    attention(c, units, c.region(11, 0, ATT_WORK))
    group_rms(c, out, AH, EPS2, c.region(6, 0, NT, D))
    to_features(c, lambda i: out[:, i, :], mixT[:, 0:8, :], gain.to_broadcast([P, 8]))


def group_rms(c, y, groups, eps, squares):
    order, mean, root, done = (c.sig(x) for x in ("vector_order", "mean_ready", "root_ready", "inverse_ready"))
    inv = c.small[:, 0:NT * groups]
    w = y.shape[2] // groups
    with c.nc.Block() as block:
        @block.vector
        def _(dve):
            for i in range(NT):
                dve.tensor_tensor(squares[:, i, :], y[:, i, :], y[:, i, :], ALU.mult).then_inc(order.sem, order.up())
                dve.wait_ge(order.sem, order.sent)
                dve.tensor_reduce(inv[:, i * groups:(i + 1) * groups],
                                     squares[:, i, :].rearrange("p (g e) -> p g e", g=groups), AX.X, ALU.add).then_inc(order.sem, order.up())
                dve.wait_ge(order.sem, order.sent)
            dve.tensor_scalar(inv, inv, 1.0 / w, eps, ALU.mult, ALU.add).then_inc(mean.sem, mean.up())
            dve.wait_ge(root.sem, root.at(1))
            dve.reciprocal(inv, inv).then_inc(order.sem, order.up())
            dve.wait_ge(order.sem, order.sent)
            for i in range(NT):
                v = y[:, i, :].rearrange("p (g e) -> p g e", g=groups)
                g = inv[:, i * groups:(i + 1) * groups].unsqueeze(2).to_broadcast([P, groups, w])
                dve.tensor_tensor(v, v, g, ALU.mult).then_inc(done.sem, done.up())
            dve.wait_ge(done.sem, done.at(NT))

        @block.scalar
        def _(act):
            act.wait_ge(mean.sem, mean.at(1))
            act.activation(inv, inv, ACT.Sqrt).then_inc(root.sem, root.up())

        @block.sync
        def _(sync):
            c.load_weights(sync)


def state_space(c, a, mixT):
    nc, xT = c.nc, c.xT
    z = c.region(6, 0, NT, D)
    xbc = c.region(7, 0, 16, S)
    small = c.region(5, 0, 2048)
    sm = [small[:, n * 128:(n + 1) * 128].rearrange("p (d i h) -> p d i h", d=2, i=NT) for n in range(9)]
    dt, dA, acs, neg_acs, grow, tot, wdec, etot, t0 = sm
    raw = small[:, 1200:1264].rearrange("p (i h) -> p i h", i=NT)
    rows = small[:, 1264:1344].rearrange("p (n h) -> p n h", n=5)
    tri = [small[:, 1344:1472], small[:, 1472:1600]]
    neg = [small[:, 1600:1728], small[:, 1728:1856]]

    conv, made, got = c.sig("conv_ready"), c.sig("iota_made"), c.sig("rows_loaded_gpsimd")
    order = c.sig("vector_order")

    def tables(pool):
        for n, k in enumerate(("dt_bias_fwd_2", "dt_bias_bwd_2", "a_log_fwd_2", "a_log_bwd_2", "d_skip_2")):
            pool.dma_start(rows[:, n, :], a[k][0].partition_broadcast(P)).then_inc(got.sem, got.up(16))
        for t in tri:
            pool.memset(t, 1.0).then_inc(made.sem, made.up())
        for t in neg:
            pool.memset(t, 0.0).then_inc(made.sem, made.up())
        pool.wait_ge(made.sem, made.at(4))
        for t, fill in ((tri, 0.0), (neg, NEG)):
            pool.affine_select(out=t[0], in_=t[0], compare_op=ALU.is_ge, fill=fill, base=0,
                               pattern=[[1, P]], channel_multiplier=-1).then_inc(made.sem, made.up())
            pool.affine_select(out=t[1], in_=t[1], compare_op=ALU.is_ge, fill=fill, base=0,
                               pattern=[[-1, P]], channel_multiplier=1).then_inc(made.sem, made.up())
        pool.wait_ge(made.sem, made.at(8))
        pool.wait_ge(got.sem, got.at(16 * 5))

    def convolve(j):
        def run(dve, bank, order):
            y = xbc[:, j, :]
            for k in (2, 0, 1, 3, 4):
                col = c.col["conv_w_2"][:, k * 16 + j:k * 16 + j + 1]
                lo, hi = max(0, 2 - k), min(S, S + 2 - k)
                if k == 2:
                    last = dve.tensor_scalar(y, bank[:, :], col, None, ALU.mult)
                else:
                    last = dve.scalar_tensor_tensor(out=y[:, lo:hi], in0=bank[:, lo - 2 + k:hi - 2 + k], scalar=col,
                                                    in1=y[:, lo:hi], op0=ALU.mult, op1=ALU.add)
                if k != 4:
                    last.then_inc(order.sem, order.up())
                    dve.wait_ge(order.sem, order.sent)
            return last
        return run

    def silu_z_and_conv(dst, j):
        def run(act, bank, order):
            for t in (2 * j, 2 * j + 1):
                act.activation(xbc[:, t, :], xbc[:, t, :], ACT.Silu,
                               bias=c.col["conv_b_2"][:, t:t + 1]).then_inc(conv.sem, conv.up())
            return act.activation(dst, bank[:, :], ACT.Silu)
        return run
    groups = []
    for n in range(0, 2048, 512):
        key = ("xbc2", 4096 + n)
        w = c.slot(key)[0]
        for j in range(4):
            pairs = [(w[:, k, j * P:(j + 1) * P], xT[:, k, :]) for k in range(KD)]
            groups.append(((key,), product(pairs), (key,) if j == 3 else (), "v", convolve(n // P + j)))
    for n in (0, 512):
        groups += tokens_from(c, ("z2", 3072 + n), xT, (0, 512), None,
                              [silu_z_and_conv(z[:, i, n:n + 512], n // P + i) for i in range(NT)], who="a")
    groups += tokens_from(c, "dt2", xT, (0, 16), [raw[:, i, :] for i in range(NT)])
    bank_groups(c, groups, meanwhile=tables)
    xs, Bt = xT.rearrange("p k n -> p (k n)").rearrange("p (i n) -> p i n", i=NT), c.region(9, 0, NT, 512)
    groups = []
    for i in range(NT):
        for k in range(3):
            blocks = [xbc[:, 4 * k + j, i * P:(i + 1) * P] for j in range(4)]
            dst = Bt[:, i, :] if k == 2 else xs[:, i, k * 512:(k + 1) * 512]
            groups.append(((), turns(c, blocks), (), "av"[k % 2], copy_to(dst)))
    bank_groups(c, groups)

    e1, e2 = c.sig("exponentials"), c.sig("logs_ready")
    v1 = c.sig("vector_ready")
    with nc.Block() as block:
        @block.vector
        def _(dve):
            for d in range(2):
                dve.tensor_tensor(dt[:, d, :, :], raw, rows[:, d, :].unsqueeze(1).to_broadcast([P, NT, SH]), ALU.add).then_inc(order.sem, order.up())
                dve.wait_ge(order.sem, order.sent)
            dve.tensor_scalar(t0, dt, -1.0, None, ALU.mult).then_inc(order.sem, order.up())
            dve.wait_ge(order.sem, order.sent)
            dve.tensor_tensor(t0, t0, dt, ALU.min).then_inc(v1.sem, v1.up())
            dve.wait_ge(v1.sem, v1.sent)
            dve.wait_ge(e2.sem, e2.at(1))
            dve.tensor_scalar(dt, dt, 0.0, None, ALU.max).then_inc(order.sem, order.up())
            dve.wait_ge(order.sem, order.sent)
            dve.tensor_tensor(dt, dt, t0, ALU.add).then_inc(order.sem, order.up())
            dve.wait_ge(order.sem, order.sent)
            for d in range(2):
                dve.tensor_tensor(dA[:, d, :, :], dt[:, d, :, :], rows[:, 2 + d, :].unsqueeze(1)
                                     .to_broadcast([P, NT, SH]), ALU.mult).then_inc(order.sem, order.up())
                dve.wait_ge(order.sem, order.sent)
            dve.tensor_scalar(dA, dA, -1.0, None, ALU.mult).then_inc(order.sem, order.up())
            dve.wait_ge(order.sem, order.sent)

        @block.scalar
        def _(act):
            act.wait_ge(v1.sem, v1.at(1))
            act.activation(rows[:, 2:4, :], rows[:, 2:4, :], ACT.Exp).then_inc(e1.sem, e1.up())
            act.wait_ge(e1.sem, e1.sent)
            act.activation(t0, t0, ACT.Exp).then_inc(e1.sem, e1.up())
            act.wait_ge(e1.sem, e1.sent)
            act.activation(t0, t0, ACT.Ln, bias=1.0).then_inc(e2.sem, e2.up())
    flat = lambda t, d: t[:, d, :, :].rearrange("p i h -> p (i h)")
    groups = []
    for d in range(2):
        groups.append(((), product([(tri[d], flat(dA, d))]), (), "v", copy_to(flat(acs, d))))
        groups.append(((), product([(c.ones[:, :], flat(dA, d))]), (), "v", copy_to(flat(tot, d))))
    bank_groups(c, groups)
    with nc.Block() as block:
        @block.vector
        def _(dve):
            dve.tensor_scalar(neg_acs, acs, -1.0, None, ALU.mult).then_inc(order.sem, order.up())
            dve.wait_ge(order.sem, order.sent)
            dve.tensor_tensor(t0, tot, acs, ALU.subtract).then_inc(v1.sem, v1.up())
            dve.wait_ge(e1.sem, e1.at(3 + 2))
            dve.tensor_tensor(wdec, t0, dt, ALU.mult).then_inc(order.sem, order.up())
            dve.wait_ge(order.sem, order.sent)

        @block.scalar
        def _(act):
            act.wait_ge(v1.sem, v1.at(2))
            act.activation(t0, t0, ACT.Exp).then_inc(e1.sem, e1.up())
            act.wait_ge(e1.sem, e1.sent)
            act.activation(grow, acs, ACT.Exp).then_inc(e1.sem, e1.up())
            act.wait_ge(e1.sem, e1.sent)
            act.activation(etot, tot, ACT.Exp).then_inc(e1.sem, e1.up())
            act.wait_ge(e1.sem, e1.sent)

    BT, CT = xbc[:, 8:12, :], xbc[:, 12:16, :]
    y = c.region(7, 0, NT, D)
    xdec = c.region(9, 2048, 2, D)
    state = c.region(11, 0, SG, 256)
    E = c.region(11, 1024, 4, 512)
    M = c.region(5, 2048, 2, 512)
    tmp = c.region(5, 3072, 1, 512)
    heads4 = lambda t, d, i, g, w: t[:, d, i, 4 * g:4 * g + 4].unsqueeze(2).to_broadcast([P, 4, w])
    four = lambda t: t.rearrange("p (r e) -> p r e", r=4)

    def decayed_x(d, i):
        done = c.sig("rows_scaled")
        with nc.Block() as block:
            @block.vector
            def _(dve):
                v = xdec[:, 0, :].rearrange("p (h e) -> p h e", h=SH)
                dve.tensor_tensor(v, xs[:, i, :].rearrange("p (h e) -> p h e", h=SH),
                                                   wdec[:, d, i, :].unsqueeze(2).to_broadcast([P, SH, SHD]), ALU.mult).then_inc(done.sem, done.up())
                dve.wait_ge(done.sem, done.sent)

    def update(d, i, g, first):
        def run(dve, bank, order):
            s = state[:, g, :]
            if first:
                return dve.tensor_copy(s, bank[:, 0:256])
            dve.tensor_tensor(four(s), four(s), heads4(etot, d, i, g, SHD), ALU.mult).then_inc(order.sem, order.up())
            dve.wait_ge(order.sem, order.sent)
            return dve.tensor_tensor(s, s, bank[:, 0:256], ALU.add)
        return ((), product([(Bt[:, i, g * P:(g + 1) * P], xdec[:, 0, g * 256:(g + 1) * 256])]), (), "v", run)

    for i in range(NT):
        decayed_x(0, i)
        groups, at = [], {}

        def decay_group(g, d):
            def prods(pe, bank):
                for r in range(4):
                    pe.matmul(bank[:, r * P:(r + 1) * P], dA[:, d, i, 4 * g + r:4 * g + r + 1].to_broadcast([P, P]),
                              tri[d], start=True, stop=False, skip_group_check=True)
                    last = pe.matmul(bank[:, r * P:(r + 1) * P], c.ident[:, :], neg[d], start=False, stop=True,
                                     skip_group_check=True)
                return last

            def empty(act, bank, order):
                for r in range(4):
                    last = act.activation(E[:, 2 * (g % 2) + d, r * P:(r + 1) * P], bank[:, r * P:(r + 1) * P], ACT.Exp,
                                          bias=neg_acs[:, d, i, 4 * g + r:4 * g + r + 1])
                    if r < 3:
                        last.then_inc(order.sem, order.up())
                        act.wait_ge(order.sem, order.sent)
                return last
            return ((), prods, (), "a", empty, [at["cb", g - 2]] if g >= 2 else [])

        def cb_group(g):
            def empty(dve, bank, order):
                e0, e1_, m = E[:, 2 * (g % 2), :], E[:, 2 * (g % 2) + 1, :], M[:, g % 2, :]
                dve.tensor_tensor(four(e0), four(e0), heads4(dt, 0, i, g, P), ALU.mult).then_inc(order.sem, order.up())
                dve.wait_ge(order.sem, order.sent)
                dve.tensor_tensor(four(e1_), four(e1_), heads4(dt, 1, i, g, P), ALU.mult).then_inc(order.sem, order.up())
                dve.wait_ge(order.sem, order.sent)
                dve.tensor_tensor(m, e0, e1_, ALU.add).then_inc(order.sem, order.up())
                dve.wait_ge(order.sem, order.sent)
                return dve.tensor_tensor(four(m), four(m), bank[:, 0:P].unsqueeze(1).to_broadcast([P, 4, P]), ALU.mult)
            cs = slice(i * P, (i + 1) * P)
            return ((), product([(BT[:, g, cs], CT[:, g, cs])]), (), "v", empty, [at["decay", g]])

        def y_group(g):
            def prods(pe, bank):
                for r in range(4):
                    h = 4 * g + r
                    last = pe.matmul(bank[:, r * SHD:(r + 1) * SHD], M[:, g % 2, r * P:(r + 1) * P],
                                     xs[:, i, h * SHD:(h + 1) * SHD], start=True, stop=True, skip_group_check=True)
                if i:
                    last = pe.matmul(bank[:, 256:512], CT[:, g, i * P:(i + 1) * P], state[:, g, :], start=True, stop=True,
                                     skip_group_check=True)
                return last

            def empty(dve, bank, order):
                o, cols = y[:, i, g * 256:(g + 1) * 256], slice(g * 256, (g + 1) * 256)
                dve.tensor_tensor(four(o), four(xs[:, i, cols]), rows[:, 4, 4 * g:4 * g + 4].unsqueeze(2)
                                         .to_broadcast([P, 4, SHD]), ALU.mult).then_inc(order.sem, order.up())
                dve.wait_ge(order.sem, order.sent)
                if i:
                    dve.tensor_tensor(four(tmp[:, 0, 0:256]), four(bank[:, 256:512]), heads4(grow, 0, i, g, SHD),
                                             ALU.mult).then_inc(order.sem, order.up())
                    dve.wait_ge(order.sem, order.sent)
                    dve.tensor_tensor(o, o, tmp[:, 0, 0:256], ALU.add).then_inc(order.sem, order.up())
                    dve.wait_ge(order.sem, order.sent)
                return dve.tensor_tensor(o, o, bank[:, 0:256], ALU.add)
            return ((), prods, (), "v", empty, [at["cb", g]])

        for g in range(SG + 2):
            if g < SG:
                for d in range(2):
                    groups.append(decay_group(g, d))
                at["decay", g] = len(groups) - 1
            if 1 <= g <= SG:
                groups.append(cb_group(g - 1))
                at["cb", g - 1] = len(groups) - 1
            if g >= 2:
                groups.append(y_group(g - 2))
                at["y", g - 2] = len(groups) - 1
                if i < NT - 1:
                    groups.append(update(0, i, g - 2, i == 0))
        bank_groups(c, groups, chained=True)

    for i in reversed(range(NT)):
        if i:
            decayed_x(1, i)
        groups = []
        for g in range(SG):
            if i < NT - 1:
                def empty(dve, bank, order, g=g):
                    o = y[:, i, g * 256:(g + 1) * 256]
                    dve.tensor_tensor(four(tmp[:, 0, 0:256]), four(bank[:, 0:256]), heads4(grow, 1, i, g, SHD),
                                             ALU.mult).then_inc(order.sem, order.up())
                    dve.wait_ge(order.sem, order.sent)
                    return dve.tensor_tensor(o, o, tmp[:, 0, 0:256], ALU.add)
                groups.append(((), product([(CT[:, g, i * P:(i + 1) * P], state[:, g, :])]), (), "v", empty))
            if i:
                groups.append(update(1, i, g, i == NT - 1))
        bank_groups(c, groups, chained=True)

    done = c.sig("branches_ready")
    with nc.Block() as block:
        @block.vector
        def _(dve):
            dve.tensor_tensor(y, y, z, ALU.mult).then_inc(done.sem, done.up())
            dve.wait_ge(done.sem, done.sent)

        @block.sync
        def _(sync):
            c.load_weights(sync)
    group_rms(c, y, SG, EPS2, c.region(6, 0, NT, D))
    to_features(c, lambda i: y[:, i, :], mixT[:, 8:16, :], c.col["ssm_norm_w_2"])
NH, NHD, NG = 8, 64, 2
NCMP, CSTRIDE, CBLOCK = 31, 16, 32
HH, SUB = 4, 32
NSUB = S // SUB
XH, XD, MEM = 4, 256, 256
EPS3 = 1e-6


def plan_third(c, a):
    w = a["w_in_3"][0].rearrange("(k p) n -> p k n", p=P)
    for key, lo, hi in (("nq", 0, 512), ("nkv", 512, 1024), ("nwin", 1024, 1304), ("hq", 1304, 1816),
                        ("hf", 1816, 2328), ("hi", 2328, 2840), ("hgate", 2840, 3352)):
        c.plan((key, 3), w[:, :, lo:hi])
    for k in ("cmp_w1_k_3", "cmp_w1_v_3"):
        c.plan(k, a[k][0].rearrange("(k p) n -> p k n", p=P))
    plan_square(c, a, "w_out_3")
    for k in ("xa_wq_3", "xa_wk_3", "xa_wv_3"):
        w = a[k][0].rearrange("(k p) n -> p k n", p=P)
        for n in (0, 512):
            c.plan((k, n), w[:, :, n:n + 512])
    plan_square(c, a, "xa_wo_3")


def plan_square(c, a, name):
    w = a[name][0].rearrange("(k p) n -> p k n", p=P)
    for n in (0, 4):
        c.plan((name, n), w[:, n:n + 4, :])


def third_mixers(c, a):
    nc, xT = c.nc, c.xT
    qT = c.region(5, 0, 4, S)
    kS, kW = c.region(5, 2048, NG, S), c.region(5, 3072, NG, S)
    kC, vC = c.region(6, 0, NG, S), c.region(6, 1024, NG, S)
    vS, vW = c.region(6, 2048, NT, 128), c.region(6, 2560, NT, 128)
    gates = c.region(6, 3072, NT, 24)
    hq, hk = c.region(7, 0, HH, S), c.region(7, 2048, HH, S)
    hf, hv = c.region(8, 0, HH, S), c.region(8, 2048, NT, 512)
    hgate = c.region(9, 0, NT, 512)
    lb, one_less = c.small[:, 104:108], c.small[:, 108:112]
    mixT = c.region(10, 0, 8, S)

    order, ready, powers = c.sig("vector_order"), c.sig("angles_ready"), c.sig("exponentials")
    with nc.Block() as block:
        @block.vector
        def _(dve):
            g = c.col["hg_lb_logits_3"]
            dve.tensor_tensor(lb, g[:, 4:8], g[:, 0:4], ALU.subtract).then_inc(ready.sem, ready.up())
            dve.wait_ge(powers.sem, powers.at(1))
            dve.tensor_scalar(lb, lb, 1.0, None, ALU.add).then_inc(order.sem, order.up())
            dve.wait_ge(order.sem, order.sent)
            dve.reciprocal(lb, lb).then_inc(order.sem, order.up())
            dve.wait_ge(order.sem, order.sent)
            dve.tensor_scalar(one_less, lb, -1.0, 1.0, ALU.mult, ALU.add).then_inc(order.sem, order.up())
            dve.wait_ge(order.sem, order.sent)

        @block.scalar
        def _(act):
            act.wait_ge(ready.sem, ready.at(1))
            act.activation(lb, lb, ACT.Exp).then_inc(powers.sem, powers.up())

    def both_halves(dst, shift=0):
        def run(dve, bank, order):
            for g in range(NG):
                rows = slice(g * 64, g * 64 + 64)
                dve.tensor_copy(dst[0:64, g, :], bank[rows, :]).then_inc(order.sem, order.up())
                dve.wait_ge(order.sem, order.sent)
                last = dve.tensor_copy(dst[64:128, g, 0:S - shift], bank[rows, shift:S])
                if g == 0:
                    last.then_inc(order.sem, order.up())
                    dve.wait_ge(order.sem, order.sent)
            return last
        return run

    def gate_parts(h):
        def run(act, bank, order):
            act.activation(hf[:, h, :], bank[:, :], ACT.Sigmoid).then_inc(order.sem, order.up())
            act.wait_ge(order.sem, order.sent)
            return act.activation(hk[:, h, :], bank[:, :], ACT.Sigmoid, scale=-1.0)
        return run

    def columns(key, lo, empty, who, release=False):
        w = c.slot(key)[0]
        return ((key,), product([(w[:, k, lo:lo + P], xT[:, k, :]) for k in range(KD)]), (key,) if release else (),
                who, empty)
    groups = features_from(c, ("nq", 3), xT, [qT[:, j, :] for j in range(4)])
    groups += [columns(("nkv", 3), 0, both_halves(kC, 1), "v"), columns(("nkv", 3), 128, both_halves(vC, 1), "v"),
               columns(("nkv", 3), 256, both_halves(kS), "v")]
    groups += tokens_from(c, ("nkv", 3), xT, (384, 512), [vS[:, i, :] for i in range(NT)])
    groups += [columns(("nwin", 3), 0, both_halves(kW), "v")]
    groups += tokens_from(c, ("nwin", 3), xT, (128, 256), [vW[:, i, :] for i in range(NT)], last=False)
    sigmoid_to = lambda dst: lambda act, bank, order: act.activation(dst, bank[:, 0:24], ACT.Sigmoid)
    groups += tokens_from(c, ("nwin", 3), xT, (256, 280), None, [sigmoid_to(gates[:, i, :]) for i in range(NT)], who="a")
    groups += features_from(c, ("hq", 3), xT, [hq[:, j, :] for j in range(4)])
    groups += features_from(c, ("hf", 3), xT, [None] * 4, [gate_parts(h) for h in range(4)])
    groups += tokens_from(c, ("hi", 3), xT, (0, 512), [hv[:, i, :] for i in range(NT)])
    silu_to = lambda dst: lambda act, bank, order: act.activation(dst, bank[:, :], ACT.Silu)
    groups += tokens_from(c, ("hgate", 3), xT, (0, 512), None, [silu_to(hgate[:, i, :]) for i in range(NT)], who="a")
    bank_groups(c, groups)

    sparse_attention(c, a, qT, kS, kW, kC, vC, vS, vW, gates, mixT)
    gated_recurrence(c, a, hq, hk, hf, hv, hgate, lb, one_less, mixT)
    down_and_layer_norm(c, [("w_out_3", n) for n in (0, 4)], mixT, a["ln1_g_3"][0], a["ln1_b_3"][0],
                        c.region(9, 0, 2, D), EPS2)
    return cross_attention(c, a)


def sparse_attention(c, a, qT, kS, kW, kC, vC, vS, vW, gates, mixT):
    nc = c.nc
    kcmp = c.region(6, 3168, NG, NCMP)
    vcmp = c.region(6, 3232, NG, NHD)
    hidden = [c.region(6, 3360, 2, NG * NCMP), c.region(6, 3490, 2, NG * NCMP)]
    w2 = [c.region(6, 3620, 2, NHD), c.region(6, 3748, 2, NHD)]
    load_rows(c, "scalar", [(w2[n], a[k][0].rearrange("(k p) n -> p k n", p=P)) for n, k in
                            enumerate(("cmp_w2_k_3", "cmp_w2_v_3"))])
    width = NG * NCMP
    blocks = [c.region(10, n * 1024, CBLOCK // 2, width) for n in range(2)]
    by_block = [c.region(10, 2048 + n * 256, 256) for n in range(2)]
    added = c.sig("term_added")
    with nc.Block() as block:
        @block.vector
        def _(dve):
            for n, (src, pe_name) in enumerate(((kC, "cmp_pe_k_3"), (vC, "cmp_pe_v_3"))):
                for g in range(NG):
                    for m in range(2):
                        half = slice(m * 8, m * 8 + 8)
                        tokens = src[:, g, m * CSTRIDE:m * CSTRIDE + NCMP * CSTRIDE].rearrange(
                            "p (n k two) -> p k n two", k=8, two=2)[:, :, :, 0]
                        dst = blocks[n][:, half, g * NCMP:(g + 1) * NCMP]
                        dve.tensor_tensor(dst, tokens, c.col[pe_name][:, half].unsqueeze(2).to_broadcast([P, 8, NCMP]),
                                          ALU.add).then_inc(added.sem, added.up())
            dve.wait_ge(added.sem, added.at(8))

        @block.sync
        def _(sync):
            c.load_weights(sync)
    groups = []
    for n, w1 in enumerate(("cmp_w1_k_3", "cmp_w1_v_3")):
        w = c.slot(w1)[0]

        def gelu(act, bank, order, n=n):
            return act.activation(by_block[n][0:width, :], bank[0:width, 0:256], ACT.Gelu_apprx_tanh)
        groups.append(((w1,), product([(blocks[n][:, k, :], w[:, k, :]) for k in range(CBLOCK // 2)]), (w1,), "a", gelu))
    for n in range(2):
        groups.append(((), turns(c, [by_block[n][0:width, m * P:(m + 1) * P] for m in range(2)]), (), "v",
                       copy_to(hidden[n]), [n]))

    def copy_both(dve, bank, order):
        dve.tensor_copy(kcmp[0:64, :, :], bank[0:64, 0:width].rearrange("p (g n) -> p g n", g=NG)).then_inc(order.sem, order.up())
        dve.wait_ge(order.sem, order.sent)
        return dve.tensor_copy(kcmp[64:128, :, :], bank[0:64, 0:width].rearrange("p (g n) -> p g n", g=NG))
    groups.append(((), product([(w2[0][:, m, :], hidden[0][:, m, :]) for m in range(2)]), (), "v", copy_both, [2]))
    for g in range(NG):
        groups.append(((), product([(hidden[1][:, m, g * NCMP:(g + 1) * NCMP], w2[1][:, m, :]) for m in range(2)]), (),
                       "v", copy_to(vcmp[0:NCMP, g, :]), [3]))
    bank_groups(c, groups)
    hide = c.region(11, ATT_WORK, NT, NCMP)
    seen = c.small[:, 112:113]
    made, order = c.sig("iota_made"), c.sig("vector_order")
    with nc.Block() as block:
        @block.gpsimd
        def _(pool):
            pool.memset(hide, 0.0).then_inc(made.sem, made.up())
            pool.memset(seen, 1.0).then_inc(made.sem, made.up())
            pool.wait_ge(made.sem, made.at(2))
            pool.affine_select(out=hide, in_=hide, compare_op=ALU.is_ge, fill=NEG, base=-(CBLOCK - 1),
                                        pattern=[[P, NT], [-CSTRIDE, NCMP]], channel_multiplier=1).then_inc(made.sem, made.up())
            pool.affine_select(out=seen, in_=seen, compare_op=ALU.is_ge, fill=0.0, base=-(CBLOCK - 1),
                                        pattern=[[0, 1]], channel_multiplier=1).then_inc(made.sem, made.up())

        @block.vector
        def _(dve):
            dve.wait_ge(made.sem, made.at(4))
            dve.tensor_scalar(gates[:, 0, 0:24:3], gates[:, 0, 0:24:3], seen, None, ALU.mult).then_inc(order.sem, order.up())
            dve.wait_ge(order.sem, order.sent)
    out = c.region(9, 2048, NT, 512)
    units = []
    for h in range(NH):
        for i in range(NT):
            for b in range(3):
                g, r, j = h // 4, slice((h % 2) * 64, (h % 2) * 64 + 64), h // 2
                n = NCMP if b == 0 else (i + 1) * P
                keys = kcmp[r, g, :] if b == 0 else (kS, kW)[b - 1][r, g, 0:n]

                def score(pe, bank, i=i, r=r, j=j, n=n, keys=keys):
                    return pe.matmul(bank[:, 0:n], qT[r, j, i * P:(i + 1) * P], keys, start=True, stop=True)

                def finish(dve, bank, factor, h=h, i=i, b=b):
                    o = out[:, i, h * NHD:(h + 1) * NHD]
                    if b == 0:
                        return dve.tensor_scalar(o, bank[:, 0:NHD], factor, None, ALU.mult)
                    return dve.scalar_tensor_tensor(out=o, in0=bank[:, 0:NHD], scalar=factor, in1=o, op0=ALU.mult,
                                                    op1=ALU.add)
                if b == 0:
                    masks, values = [((0, n), hide[:, i, :], 1.0)], [vcmp[0:NCMP, g, :]]
                else:
                    masks = [((i * P, n), c.keep_le[:, :], 1.0)]
                    values = [(vS, vW)[b - 1][:, k, g * NHD:(g + 1) * NHD] for k in range(i + 1)]
                units.append({"keys": n, "scale": NHD ** -0.5, "score": score, "masks": masks, "values": values,
                              "finish": finish, "weight": gates[:, i, 3 * h + b:3 * h + b + 1]})
    attention(c, units, c.region(11, 0, ATT_WORK))
    group_rms(c, out, 1, EPS3, c.region(11, 0, NT, 512))
    to_features(c, lambda i: out[:, i, :], mixT[:, 0:4, :], c.col["nsa_norm_g_3"], width=512)


def gated_recurrence(c, a, hq, hk, hf, hv, hgate, lb, one_less, mixT):
    nc = c.nc
    order, done, made = c.sig("vector_order"), c.sig("branches_ready"), c.sig("iota_made")
    N = HH * NSUB
    chunks = lambda t: t.rearrange("p h s -> p (h s)").rearrange("p (n t) -> p n t", n=N)
    f, k, q = chunks(hf), chunks(hk), chunks(hq)
    U = [c.region(5, n * 2048, N, SUB) for n in range(2)]
    G = [c.region(6, n * 2048, N, SUB) for n in range(2)]
    R = c.region(11, 2048, N, SUB)
    pick = c.region(1, 0, 2 * SUB)
    att = c.region(1, 64, HH, S)
    blocks = c.region(11, 0, NT * HH, P)
    decay = c.region(1, 2200, N)
    with nc.Block() as block:
        @block.gpsimd
        def _(pool):
            pool.memset(pick, 0.0).then_inc(made.sem, made.up())
            pool.memset(blocks, 0.0).then_inc(made.sem, made.up())
            pool.wait_ge(made.sem, made.at(2))
            pool.memset(pick[:, SUB - 1:SUB], 1.0).then_inc(made.sem, made.up())
            pool.wait_ge(made.sem, made.at(3))

        @block.vector
        def _(dve):
            for h in range(HH):
                dve.tensor_scalar(hf[:, h, :], hf[:, h, :], one_less[:, h:h + 1], lb[:, h:h + 1], ALU.mult,
                                            ALU.add).then_inc(order.sem, order.up())
                dve.tensor_scalar(hk[:, h, :], hk[:, h, :], one_less[:, h:h + 1], None, ALU.mult).then_inc(order.sem, order.up())
                dve.wait_ge(order.sem, order.sent)
    grown, keyed, added, copied = c.sig("decays_grown"), c.sig("keys_weighed"), c.sig("bank_filled"), c.sig("turned_copied")
    with nc.Block() as block:
        @block.vector
        def _(dve):
            for n, j in enumerate(reversed(range(SUB))):
                u, before = U[n % 2], U[(n + 1) % 2]
                if n >= 2:
                    dve.wait_ge(keyed.sem, keyed.at(n - 1))
                if n:
                    w = SUB - 1 - j
                    dve.tensor_tensor(u[:, :, j + 1:SUB], before[:, :, j + 1:SUB],
                                                f[:, :, j + 1:j + 2].to_broadcast([P, N, w]), ALU.mult).then_inc(order.sem, order.up())
                dve.tensor_copy(u[:, :, j:j + 1], q[:, :, j:j + 1]).then_inc(grown.sem, grown.up())
                dve.wait_ge(grown.sem, grown.at(n + 1))
                if n:
                    dve.wait_ge(order.sem, order.sent)
            dve.memset(R[:, :, SUB - 1:SUB], 1.0).then_inc(order.sem, order.up())
            dve.wait_ge(order.sem, order.sent)
            for j in reversed(range(SUB - 1)):
                dve.tensor_tensor(R[:, :, j:j + 1], R[:, :, j + 1:j + 2], f[:, :, j + 1:j + 2], ALU.mult).then_inc(order.sem, order.up())
                dve.wait_ge(order.sem, order.sent)
            dve.tensor_tensor(decay.unsqueeze(2), R[:, :, 0:1], f[:, :, 0:1], ALU.mult).then_inc(order.sem, order.up())
            dve.wait_ge(order.sem, order.sent)
            dve.wait_ge(keyed.sem, keyed.at(SUB))
            dve.tensor_tensor(k, k, R, ALU.mult).then_inc(order.sem, order.up())
            dve.wait_ge(order.sem, order.sent)
            dve.tensor_tensor(q, U[(SUB - 1) % 2], f[:, :, 0:1].to_broadcast([P, N, SUB]), ALU.mult).then_inc(order.sem, order.up())
            dve.wait_ge(order.sem, order.sent)

        @block.gpsimd
        def _(pool):
            for n, j in enumerate(reversed(range(SUB))):
                pool.wait_ge(grown.sem, grown.at(n + 1))
                if n >= 2:
                    pool.wait_ge(added.sem, added.at(n - 1))
                pool.tensor_tensor(G[n % 2][:, :, j:SUB], U[n % 2][:, :, j:SUB],
                                             k[:, :, j:j + 1].to_broadcast([P, N, SUB - j]), ALU.mult).then_inc(keyed.sem, keyed.up())

        @block.tensor
        def _(pe):
            for n, j in enumerate(reversed(range(SUB))):
                pe.wait_ge(keyed.sem, keyed.at(n + 1))
                for h in range(HH):
                    bank = c.banks[h][0:SUB, :].rearrange("p (n t) -> p n t", n=NSUB)
                    last = pe.matmul(bank[:, :, j:SUB], pick[:, SUB - 1 - j:2 * SUB - 1 - j],
                                     G[n % 2][:, h * NSUB:(h + 1) * NSUB, j:SUB], start=n == 0, stop=n == SUB - 1,
                                     skip_group_check=True)
                last.then_inc(added.sem, added.up())

        @block.scalar
        def _(act):
            act.wait_ge(added.sem, added.at(SUB))
            for h in range(HH):
                act.activation(att[0:SUB, h, :], c.banks[h][0:SUB, :], ACT.Copy).then_inc(copied.sem, copied.up())
            act.wait_ge(copied.sem, copied.at(HH))
            for quarter in range(4):
                r = slice(quarter * SUB, (quarter + 1) * SUB)
                for h in range(HH):
                    src = att[0:SUB, h, :].rearrange("p (i c t) -> p i c t", i=NT, c=4)[:, :, quarter, :]
                    dst = blocks.rearrange("p (i h) t -> p i h t", i=NT)[r, :, h, quarter * SUB:(quarter + 1) * SUB]
                    act.activation(dst, src, ACT.Copy).then_inc(copied.sem, copied.up())
            act.wait_ge(copied.sem, copied.at(5 * HH))

        @block.sync
        def _(sync):
            c.load_weights(sync)
    kt = c.region(6, 0, NT, 512)
    out = c.region(6, 2048, NT, 512)
    state = c.region(5, 0, HH, P)
    groups = []
    for i in range(NT):
        groups.append(((), turns(c, [hk[:, h, i * P:(i + 1) * P] for h in range(HH)]), (), "v", copy_to(kt[:, i, :])))

        def inside(pe, bank, i=i):
            for h in range(HH):
                last = pe.matmul(bank[:, h * P:(h + 1) * P], blocks[:, i * HH + h, :], hv[:, i, h * P:(h + 1) * P],
                                 start=True, stop=True, skip_group_check=True)
            return last
        groups.append(((), inside, (), "a", copy_to(out[:, i, :])))
    bank_groups(c, groups)
    groups = []
    for n in range(NSUB):
        i, r = n // 4, slice((n % 4) * SUB, (n % 4) * SUB + SUB)
        if n:
            def carried(pe, bank, n=n, r=r):
                for h in range(HH):
                    last = pe.matmul(bank[r, h * P:(h + 1) * P], hq[:, h, n * SUB:(n + 1) * SUB], state[:, h, :],
                                     start=True, stop=True, skip_group_check=True)
                return last

            def add(dve, bank, order, i=i, r=r):
                return dve.tensor_tensor(out[r, i, :], out[r, i, :], bank[r, :], ALU.add)
            groups.append(((), carried, (), "v", add, [len(groups) - 1]))
        if n < NSUB - 1:
            def gain(pe, bank, i=i, r=r):
                for h in range(HH):
                    last = pe.matmul(bank[:, h * P:(h + 1) * P], kt[r, i, h * P:(h + 1) * P], hv[r, i, h * P:(h + 1) * P],
                                     start=True, stop=True, skip_group_check=True)
                return last

            def update(dve, bank, order, n=n):
                b = bank[:, :].rearrange("p (h e) -> p h e", h=HH)
                if n == 0:
                    return dve.tensor_copy(state, b)
                dve.tensor_tensor(state, state, decay[:, n:N:NSUB].unsqueeze(2).to_broadcast([P, HH, P]), ALU.mult).then_inc(order.sem, order.up())
                dve.wait_ge(order.sem, order.sent)
                return dve.tensor_tensor(state, state, b, ALU.add)
            groups.append(((), gain, (), "v", update))
    bank_groups(c, groups, chained=True)
    group_rms(c, out, HH, EPS3, c.region(11, 0, NT, 512))
    with nc.Block() as block:
        @block.vector
        def _(dve):
            dve.tensor_tensor(out, out, hgate, ALU.mult).then_inc(done.sem, done.up())
            dve.wait_ge(done.sem, done.sent)
    to_features(c, lambda i: out[:, i, :], mixT[:, 4:8, :], c.col["hg_norm_g_3"].to_broadcast([P, 4]), width=512)


def cross_attention(c, a):
    xT = c.xT
    qT = c.region(5, 0, 8, S)
    kT, memT = c.region(6, 0, 8, MEM), c.region(6, 2048, 8, MEM)
    v, mem = c.region(7, 0, 2, D), c.region(7, 2048, 2, D)
    out, outT = c.region(8, 0, NT, D), c.region(9, 0, 8, S)
    load_rows(c, "scalar", [(mem, a["mem_3"][0].rearrange("(i p) d -> p i d", p=P))])
    groups = []
    for i in range(2):
        for k in (0, 4):
            groups.append(((), turns(c, [mem[:, i, (k + j) * P:(k + j + 1) * P] for j in range(4)]), (), "av"[k // 4],
                           copy_to(memT[:, k:k + 4, i * P:(i + 1) * P])))
    bank_groups(c, groups)
    groups = []
    for n in (0, 512):
        groups += features_from(c, ("xa_wq_3", n), xT, [qT[:, n // P + j, :] for j in range(4)])
    for n in (0, 512):
        groups += features_from(c, ("xa_wk_3", n), memT, [kT[:, n // P + j, :] for j in range(4)])
    for n in (0, 512):
        key = ("xa_wv_3", n)
        for i in range(2):
            w = c.slot(key)[0]
            groups.append(((key,), product([(memT[:, k, i * P:(i + 1) * P], w[:, k, :]) for k in range(KD)]),
                           (key,) if i else (), "av"[i], copy_to(v[:, i, n:n + 512])))
    bank_groups(c, groups)
    units = []
    for h in range(XH):
        for i in range(NT):
            def score(pe, bank, h=h, i=i):
                for j in range(2):
                    last = pe.matmul(bank[:, 0:MEM], qT[:, 2 * h + j, i * P:(i + 1) * P], kT[:, 2 * h + j, :],
                                     start=j == 0, stop=j == 1)
                return last

            def finish(dve, bank, factor, h=h, i=i):
                return dve.tensor_scalar(out[:, i, h * XD:(h + 1) * XD], bank[:, 0:XD], factor, None, ALU.mult)
            units.append({"keys": MEM, "scale": XD ** -0.5, "score": score, "masks": [],
                          "values": [v[:, k, h * XD:(h + 1) * XD] for k in range(2)], "finish": finish})
    attention(c, units, c.region(11, 0, ATT_WORK))
    to_features(c, lambda i: out[:, i, :], outT)
    return outT
NE, NGR, EPG, FFE = 32, 4, 8, 512
MAX_BLOCKS = (2 * S + NE * (P - 1)) // P + 1
TABLE = (MAX_BLOCKS + 2) * P


def clear_outputs(c):
    zeros = c.sb("zeros", [P, 512])
    c.y_rows = c.nc.dram_tensor("y_rows", (MAX_BLOCKS * P, D), F32).ap()
    made, cleared = c.sig("iota_made"), c.sig("outputs_cleared")
    least = 2 * S // P
    with c.nc.Block() as block:
        @block.gpsimd
        def _(pool):
            pool.memset(zeros[:, :], 0.0).then_inc(made.sem, made.up())

        @block.scalar
        def _(act):
            act.wait_ge(made.sem, made.at(1))
            for half in range(2):
                dst = c.y_rows[least * P:, half * 512:(half + 1) * 512].rearrange("(b p) n -> p b n", p=P)
                act.dma_start(dst, zeros[:, :].unsqueeze(1).to_broadcast([P, MAX_BLOCKS - least, 512])).then_inc(cleared.sem, cleared.up(16))


def mixture_of_experts(c, a, mixed, out):
    nc, x, xT = c.nc, c.x, c.xT
    at = [0]

    def take(*shape):
        v = c.region(7, at[0], *shape)
        at[0] += int(np.prod(shape))
        return v
    bias, logits, padded = take(36), take(NT, 36), take(NT, 8)
    top, chosen, topi = take(NT, 8), take(NT, 8), take(NT, 8).bitcast(U32)
    etop, etopi = take(NT, 8), take(NT, 8).bitcast(U32)
    neg_top, total, group, weight = take(NT), take(NT), take(NT), take(2, NT)
    ids, onehot, both, prod = take(2, NT), take(2, NT, NE), take(NT, NE), take(NT, NGR * EPG).rearrange("p i (g e) -> p i g e", g=NGR)
    iota, before, slots = take(64), take(P), take(2, NT)
    count, blocks, last, base = take(NE), take(NE), take(NE), take(NT, NE)
    token = take(NT).bitcast(I32)
    slot_i = take(2, NT).bitcast(I32)
    per_block = take(MAX_BLOCKS + 2)
    expert_i, trips_i = take(MAX_BLOCKS + 2).bitcast(I32), take(2).bitcast(I32)
    router, by_logit = take(KD, 36), take(S)
    zero_i = take(TABLE // P).bitcast(I32)
    wide = c.region(8, 0, MAX_BLOCKS + 2, NE)
    x_rows = nc.dram_tensor("x_rows", (S, D), F32).ap()
    y_rows = c.y_rows
    cleared = c.signals["outputs_cleared"]
    table = nc.dram_tensor("token_of_slot", (TABLE, 1), I32).ap()

    stored = [c.sig("output_stored0"), c.sig("output_stored1")]
    made, zeroed, got = c.sig("iota_made"), c.sig("table_zeroed"), c.sig("rows_loaded_gpsimd")

    def prepare(pool):
        pool.dma_start(bias[:, 0:NGR], a["moe_b_group_3"][0].partition_broadcast(P)).then_inc(got.sem, got.up(16))
        pool.dma_start(bias[:, NGR:36], a["moe_b_expert_3"][0].partition_broadcast(P)).then_inc(got.sem, got.up(16))
        for dst, name in ((router[:, :, 0:NGR], "moe_w_group_3"), (router[:, :, NGR:36], "moe_w_expert_3")):
            pool.dma_start(dst, a[name][0].rearrange("(k p) n -> p k n", p=P),
                           allow_slow_non_contiguous=True).then_inc(got.sem, got.up(16))
        pool.memset(zero_i, 0).then_inc(made.sem, made.up())
        pool.memset(padded, NEG).then_inc(made.sem, made.up())
        pool.memset(before, 1.0).then_inc(made.sem, made.up())
        pool.iota(iota, pattern=[[1, 64]], base=0, channel_multiplier=0,
                  allow_small_or_imprecise_dtypes=True).then_inc(made.sem, made.up())
        pool.iota(token, pattern=[[P, NT]], base=0, channel_multiplier=1).then_inc(made.sem, made.up())
        pool.wait_ge(made.sem, made.at(5))
        pool.affine_select(out=before, in_=before, compare_op=ALU.is_gt, fill=0.0, base=0,
                           pattern=[[1, P]], channel_multiplier=-1).then_inc(made.sem, made.up())
        pool.dma_start(table.rearrange("(p n) o -> p (n o)", p=P), zero_i).then_inc(zeroed.sem, zeroed.up(16))
        pool.wait_ge(zeroed.sem, zeroed.at(16))
        pool.wait_ge(got.sem, got.at(64))
        pool.wait_ge(cleared.sem, cleared.sent)

    down_and_layer_norm(c, [("xa_wo_3", n) for n in (0, 4)], mixed, a["ln2_g_3"][0], a["ln2_b_3"][0],
                        c.region(10, 0, 2, D), EPS2, x_rows=x_rows, meanwhile=prepare)

    def add_bias(dve, bank, order):
        return dve.tensor_tensor(logits, bank[:, 0:NT * 36].rearrange("p (i n) -> p i n", i=NT),
                                 bias.unsqueeze(1).to_broadcast([P, NT, 36]), ALU.add)
    bank_groups(c, [((), product([(router[:, k, :], xT[:, k, :]) for k in range(KD)]), (), "v", copy_to(by_logit[0:36, :])),
                    ((), turns(c, [by_logit[0:36, i * P:(i + 1) * P] for i in range(NT)]), (), "v", add_bias, [0])])

    order, ready, powers = c.sig("vector_order"), c.sig("peak_ready"), c.sig("exponentials")
    with nc.Block() as block:
        @block.vector
        def _(dve):
            dve.tensor_copy(padded[:, :, 0:NGR], logits[:, :, 0:NGR]).then_inc(order.sem, order.up())
            dve.wait_ge(order.sem, order.sent)
            for i in range(NT):
                dve.max(top[:, i, :], padded[:, i, :]).then_inc(order.sem, order.up())
                dve.wait_ge(order.sem, order.sent)
                dve.max_index(topi[:, i, :], top[:, i, :], padded[:, i, :]).then_inc(order.sem, order.up())
                dve.wait_ge(order.sem, order.sent)
            dve.tensor_copy(group, topi[:, :, 0]).then_inc(order.sem, order.up())
            dve.wait_ge(order.sem, order.sent)
            dve.tensor_scalar(neg_top, top[:, :, 0], -1.0, None, ALU.mult).then_inc(order.sem, order.up())
            dve.wait_ge(order.sem, order.sent)
            dve.tensor_tensor(chosen[:, :, 0:NGR], iota[:, 0:NGR].unsqueeze(1).to_broadcast([P, NT, NGR]),
                              group.unsqueeze(2).to_broadcast([P, NT, NGR]), ALU.is_equal).then_inc(order.sem, order.up())
            dve.wait_ge(order.sem, order.sent)
            for i in range(NT):
                dve.tensor_tensor(prod[:, i, :, :], logits[:, i, NGR:36].rearrange("p (g e) -> p g e", g=NGR),
                                  chosen[:, i, 0:NGR].unsqueeze(2).to_broadcast([P, NGR, EPG]),
                                  ALU.mult).then_inc(order.sem, order.up())
            dve.wait_ge(order.sem, order.sent)
            dve.tensor_reduce(chosen, prod.rearrange("p i g e -> p i e g"), AX.X, ALU.add).then_inc(order.sem, order.up())
            dve.wait_ge(order.sem, order.sent)
            for i in range(NT):
                dve.max(etop[:, i, :], chosen[:, i, :]).then_inc(order.sem, order.up())
                dve.wait_ge(order.sem, order.sent)
                dve.max_index(etopi[:, i, :], etop[:, i, :], chosen[:, i, :]).then_inc(order.sem, order.up())
                dve.wait_ge(order.sem, order.sent)
            for n in range(2):
                dve.tensor_copy(ids[:, n, :], etopi[:, :, n]).then_inc(order.sem, order.up())
                dve.wait_ge(order.sem, order.sent)
                dve.scalar_tensor_tensor(out=ids[:, n, :], in0=group, scalar=float(EPG), in1=ids[:, n, :],
                                            op0=ALU.mult, op1=ALU.add).then_inc(order.sem, order.up())
                dve.wait_ge(order.sem, order.sent)
                dve.tensor_tensor(onehot[:, n, :, :], iota[:, 0:NE].unsqueeze(1).to_broadcast([P, NT, NE]),
                                  ids[:, n, :].unsqueeze(2).to_broadcast([P, NT, NE]), ALU.is_equal).then_inc(order.sem, order.up())
                dve.wait_ge(order.sem, order.sent)
            dve.tensor_tensor(both, onehot[:, 0, :, :], onehot[:, 1, :, :], ALU.add).then_inc(order.sem, order.up())
            dve.wait_ge(order.sem, order.sent)
            dve.tensor_tensor(weight[:, 1, :], etop[:, :, 1], etop[:, :, 0], ALU.subtract).then_inc(ready.sem, ready.up())
            dve.wait_ge(ready.sem, ready.sent)
            dve.wait_ge(powers.sem, powers.at(NT + 1))
            dve.tensor_scalar(weight[:, 0, :], weight[:, 1, :], 1.0, None, ALU.add).then_inc(order.sem, order.up())
            dve.wait_ge(order.sem, order.sent)
            dve.tensor_tensor(weight[:, 0, :], weight[:, 0, :], total, ALU.mult).then_inc(order.sem, order.up())
            dve.wait_ge(order.sem, order.sent)
            dve.reciprocal(weight[:, 0, :], weight[:, 0, :]).then_inc(order.sem, order.up())
            dve.wait_ge(order.sem, order.sent)
            dve.tensor_tensor(weight[:, 1, :], weight[:, 0, :], weight[:, 1, :], ALU.mult).then_inc(order.sem, order.up())
            dve.wait_ge(order.sem, order.sent)

        @block.scalar
        def _(act):
            act.wait_ge(ready.sem, ready.at(1))
            for i in range(NT):
                act.activation(padded[:, i, 0:NGR], logits[:, i, 0:NGR], ACT.Exp,
                                                  bias=neg_top[:, i:i + 1], accum_out=total[:, i:i + 1]).then_inc(powers.sem, powers.up())
                act.wait_ge(powers.sem, powers.sent)
            act.activation(weight[:, 1, :], weight[:, 1, :], ACT.Exp).then_inc(powers.sem, powers.up())
    groups = []
    for i in range(NT + 1):
        pairs = [(c.ones[:, :], both[:, j, :]) for j in range(i)] + ([(before, both[:, i, :])] if i < NT else [])
        groups.append(((), product(pairs), (), "v", copy_to(base[:, i, :] if i < NT else count)))
    bank_groups(c, groups)
    with nc.Block() as block:
        @block.vector
        def _(dve):
            dve.tensor_scalar(blocks, count, 0.0, None, ALU.is_gt).then_inc(order.sem, order.up())
            dve.wait_ge(order.sem, order.sent)
            for m in range(1, S // P):
                dve.scalar_tensor_tensor(out=blocks, in0=count, scalar=float(m * P), in1=blocks, op0=ALU.is_gt,
                                            op1=ALU.add).then_inc(order.sem, order.up())
                dve.wait_ge(order.sem, order.sent)
            dve.tensor_tensor_scan(last, c.ones[:, 0:NE], blocks, 0.0, ALU.mult, ALU.add).then_inc(order.sem, order.up())
            dve.wait_ge(order.sem, order.sent)
            dve.tensor_tensor(count, last, blocks, ALU.subtract).then_inc(order.sem, order.up())
            dve.wait_ge(order.sem, order.sent)
            dve.tensor_scalar(count, count, float(P), None, ALU.mult).then_inc(order.sem, order.up())
            dve.wait_ge(order.sem, order.sent)
            dve.tensor_tensor(base, base, count.unsqueeze(1).to_broadcast([P, NT, NE]), ALU.add).then_inc(order.sem, order.up())
            dve.wait_ge(order.sem, order.sent)
            for n in range(2):
                dve.tensor_tensor(onehot[:, n, :, :], onehot[:, n, :, :], base, ALU.mult).then_inc(order.sem, order.up())
                dve.wait_ge(order.sem, order.sent)
                dve.tensor_reduce(slots[:, n, :], onehot[:, n, :, :], AX.X, ALU.add).then_inc(order.sem, order.up())
                dve.wait_ge(order.sem, order.sent)
            dve.tensor_copy(slot_i, slots).then_inc(order.sem, order.up())
            dve.wait_ge(order.sem, order.sent)
            dve.tensor_tensor(wide, last.unsqueeze(1).to_broadcast([P, MAX_BLOCKS + 2, NE]),
                                 iota[:, 0:MAX_BLOCKS + 2].unsqueeze(2).to_broadcast([P, MAX_BLOCKS + 2, NE]), ALU.is_le).then_inc(order.sem, order.up())
            dve.wait_ge(order.sem, order.sent)
            dve.tensor_reduce(per_block, wide, AX.X, ALU.add).then_inc(order.sem, order.up())
            dve.wait_ge(order.sem, order.sent)
            dve.tensor_scalar(per_block, per_block, float(NE - 1), None, ALU.min).then_inc(order.sem, order.up())
            dve.wait_ge(order.sem, order.sent)
            dve.tensor_copy(expert_i, per_block).then_inc(order.sem, order.up())
            dve.wait_ge(order.sem, order.sent)
            dve.tensor_scalar(wide[:, 0, 0:MAX_BLOCKS // 2], iota[:, 0:MAX_BLOCKS:2], last[:, NE - 1:NE], None, ALU.is_lt).then_inc(order.sem, order.up())
            dve.wait_ge(order.sem, order.sent)
            dve.tensor_reduce(per_block[:, 0:1], wide[:, 0, 0:MAX_BLOCKS // 2], AX.X, ALU.add).then_inc(order.sem, order.up())
            dve.wait_ge(order.sem, order.sent)
            dve.tensor_copy(trips_i[:, 0:1], per_block[:, 0:1]).then_inc(ready.sem, ready.up())
    expert_blocks(c, a, x_rows, y_rows, table, expert_i, trips_i, slot_i, token, stored)

    combine_and_norm(c, slot_i, weight, y_rows, a["ln3_g_3"][0], a["ln3_b_3"][0], out)


def combine_and_norm(c, slot_i, weight, y_rows, gain_row, bias_row, out):
    x = c.x
    rows = c.region(8, 0, 2 * NT, D)
    gain, bias = c.region(10, 0, 2, D)[:, 0, :], c.region(10, 0, 2, D)[:, 1, :]
    stats, mv, sd, shift = layer_norm_numbers(c)
    got, var, root, scaled, centred, gained, normed, raised, written = (c.sig(n) for n in (
        "rows_loaded_scalar", "variance_ready", "root_ready", "scale_ready", "rows_centred", "gain_applied", "normed",
        "rows_scaled", "result_written"))
    order, last_normed = c.sig("vector_order"), c.sig("last_tile_normed")
    gathered = [c.sig(f"outputs_gathered{i}") for i in range(NT)]
    with c.nc.Block() as block:
        @block.gpsimd
        def _(pool):
            for i in range(NT):
                for n in range(2):
                    pool.indirect_dma_start(
                        out=rows[:, 2 * i + n, :], out_offset=None, in_=y_rows,
                        in_offset=bass.IndirectOffsetOnAxis(ap=slot_i[:, n, i:i + 1], axis=0)).then_inc(gathered[i].sem, gathered[i].up(16))
            pool.wait_ge(got.sem, got.at(32))
            for i in range(NT - 1):
                pool.wait_ge(gained.sem, gained.at(i + 1))
                pool.tensor_tensor(x[:, i, :], x[:, i, :], bias, ALU.add).then_inc(normed.sem, normed.up())

        @block.vector
        def _(dve):
            for i in range(NT):
                dve.wait_ge(raised.sem, raised.at(i + 1))
                dve.wait_ge(gathered[i].sem, gathered[i].at(32))
                for n in range(2):
                    dve.scalar_tensor_tensor(out=x[:, i, :], in0=rows[:, 2 * i + n, :], scalar=weight[:, n, i:i + 1],
                                             in1=x[:, i, :], op0=ALU.mult, op1=ALU.add).then_inc(order.sem, order.up())
                    dve.wait_ge(order.sem, order.sent)
                for half in range(2):
                    dve.bn_stats(stats[:, i, half, :], x[:, i, half * 512:(half + 1) * 512]).then_inc(order.sem, order.up())
                dve.wait_ge(order.sem, order.sent)
                dve.bn_aggr(mv[:, i, :], stats[:, i, :, :]).then_inc(order.sem, order.up())
                dve.wait_ge(order.sem, order.sent)
                dve.tensor_scalar(sd[:, i:i + 1], mv[:, i, 1:2], 1.0, EPS2, ALU.mult, ALU.add).then_inc(var.sem, var.up())
                dve.wait_ge(root.sem, root.at(i + 1))
                dve.reciprocal(sd[:, i:i + 1], sd[:, i:i + 1]).then_inc(order.sem, order.up())
                dve.wait_ge(order.sem, order.sent)
                dve.scalar_tensor_tensor(out=shift[:, i:i + 1], in0=mv[:, i, 0:1], scalar=-1.0, in1=sd[:, i:i + 1],
                                         op0=ALU.mult, op1=ALU.mult).then_inc(scaled.sem, scaled.up())
                if i == 0:
                    dve.wait_ge(got.sem, got.at(32))
                dve.wait_ge(centred.sem, centred.at(i + 1))
                dve.tensor_tensor(x[:, i, :], x[:, i, :], gain, ALU.mult).then_inc(gained.sem, gained.up())
            dve.wait_ge(gained.sem, gained.at(NT))
            dve.tensor_tensor(x[:, NT - 1, :], x[:, NT - 1, :], bias, ALU.add).then_inc(last_normed.sem, last_normed.up())

        @block.scalar
        def _(act):
            act.dma_start(gain, gain_row.partition_broadcast(P)).then_inc(got.sem, got.up(16))
            act.dma_start(bias, bias_row.partition_broadcast(P)).then_inc(got.sem, got.up(16))
            for i in range(NT):
                act.activation(x[:, i, :], x[:, i, :], ACT.Copy, scale=ALPHA).then_inc(raised.sem, raised.up())
            for i in range(NT):
                act.wait_ge(var.sem, var.at(i + 1))
                act.activation(sd[:, i:i + 1], sd[:, i:i + 1], ACT.Sqrt).then_inc(root.sem, root.up())
                act.wait_ge(scaled.sem, scaled.at(i + 1))
                act.activation(x[:, i, :], x[:, i, :], ACT.Identity, bias=shift[:, i:i + 1],
                               scale=sd[:, i:i + 1]).then_inc(centred.sem, centred.up())

        @block.sync
        def _(sync):
            for i in range(NT):
                if i < NT - 1:
                    sync.wait_ge(normed.sem, normed.at(i + 1))
                else:
                    sync.wait_ge(last_normed.sem, last_normed.at(1))
                sync.dma_start(out[0, i * P:(i + 1) * P, :], x[:, i, :]).then_inc(written.sem, written.up(16))
            sync.wait_ge(written.sem, written.at(16 * NT))


def expert_blocks(c, a, x_rows, y_rows, table, expert_i, trips_i, slot_i, token, stored):
    nc = c.nc
    gate_w = [c.region(1 + 3 * s, 0, KD, FFE) for s in range(2)]
    up_w = [c.region(2 + 3 * s, 0, KD, FFE) for s in range(2)]
    down_w = [c.region(3 + 3 * s, 0, FFE // P, D) for s in range(2)]
    tokens = c.region(8, 0, 2, D)
    tokensT = [c.region(8, 2048 + s * 1024, KD, P) for s in range(2)]
    h, hT = c.region(9, 0, FFE), c.region(9, 512, FFE // P, P)
    out = c.region(9, 1024, 2, D)
    index = c.region(9, 3072, 2).bitcast(I32)
    filled, by_v, by_a = c.sig("bank_filled"), c.sig("bank_emptied_by_vector"), c.sig("bank_emptied_by_scalar")
    landed = [[c.sig(f"{n}_weights_landed{s}") for n in ("gate", "up", "down")] for s in range(2)]
    indexed, carried, scattered = c.sig("index_landed"), c.sig("wait_carried"), c.sig("slots_scattered")
    gathered = [c.sig(f"tokens_gathered{s}") for s in range(2)]
    bF, bV, bA = filled.sent + 2, by_v.sent + 1, by_a.sent + 1

    def turn(pe, s):
        for half in range(2):
            for k in range(4):
                last = pe.transpose(c.banks[half][:, k * P:(k + 1) * P],
                                    tokens[:, s, (4 * half + k) * P:(4 * half + k + 1) * P], c.ident[:, :])
            last.then_inc(filled.sem, 1)

    with nc.Block() as block:
        @block.sync
        def _(sync):
            trips = sync.value_load(trips_i[0:1, 0:1], min_val=1, max_val=MAX_BLOCKS // 2)
            with sync.Fori(0, trips) as it:
                for s in range(2):
                    b = it * 2 + s
                    e = sync.value_load(expert_i[0:1, bass.ds(b, 1)], min_val=0, max_val=NE - 1)
                    for n, (dst, name, done) in enumerate(((gate_w[s], "moe_w_gate_3", 1), (up_w[s], "moe_w_up_3", 2),
                                                          (down_w[s], "moe_w_down_3", 7))):
                        sync.wait_ge(filled.sem, b * 7 + (bF - 14 + done))
                        src = a[name][0][bass.ds(e, 1), :, :].rearrange("o (k p) n -> p (o k) n", p=P)
                        sync.dma_start(dst, src).then_inc(landed[s][n].sem, 16)

        @block.gpsimd
        def _(pool):
            trips = pool.value_load(trips_i[0:1, 0:1], min_val=1, max_val=MAX_BLOCKS // 2)

            for n in range(2):
                for i in range(NT):
                    pool.indirect_dma_start(
                        out=table, out_offset=bass.IndirectOffsetOnAxis(ap=slot_i[:, n, i:i + 1], axis=0),
                        in_=token[:, i:i + 1], in_offset=None).then_inc(scattered.sem, scattered.up(16))
            pool.wait_ge(scattered.sem, scattered.at(16 * 2 * NT))

            spare = c.region(9, 3080, 2)
            pool.memset(spare, 0.0).then_inc(carried.sem, 1)

            def gather(s, first_slot, n_index):
                pool.dma_start(index[:, s:s + 1], table[first_slot, :]).then_inc(indexed.sem, 16)
                pool.wait_ge(indexed.sem, n_index * 16)
                pool.wait_ge(carried.sem, n_index * 1)
                pool.tensor_tensor(spare[:, 0:1], spare[:, 1:2], spare[:, 1:2], ALU.add).then_inc(carried.sem, 1)
                return pool.indirect_dma_start(
                    out=tokens[:, s, :], out_offset=None, in_=x_rows,
                    in_offset=bass.IndirectOffsetOnAxis(ap=index[:, s:s + 1], axis=0))
            gather(0, slice(0, P), 1).then_inc(gathered[0].sem, 16)
            pool.wait_ge(gathered[0].sem, 16)
            with pool.Fori(0, trips) as it:
                for s in (1, 0):
                    n = it * 2 + (2 - s)
                    pool.wait_ge(filled.sem, n * 7 + (bF - 14))
                    gather(s, bass.ds(n * P, P), n + 1).then_inc(gathered[s].sem, 16)
                    pool.wait_ge(gathered[s].sem, it * 16 + (16 if s else 32))
            for s in range(2):
                pool.wait_ge(stored[s].sem, trips * 16 + stored[s].sent)

        @block.tensor
        def _(pe):
            trips = pe.value_load(trips_i[0:1, 0:1], min_val=1, max_val=MAX_BLOCKS // 2)
            pe.wait_ge(gathered[0].sem, 16)
            turn(pe, 0)
            pe.wait_ge(by_v.sem, bV)
            pe.wait_ge(by_a.sem, bA)
            with pe.Fori(0, trips) as it:
                for s in range(2):
                    b = it * 2 + s
                    pe.wait_ge(by_v.sem, b * 3 + (bV - 1))
                    pe.wait_ge(by_a.sem, b * 4 + (bA - 2))
                    for n, w in enumerate((gate_w[s], up_w[s])):
                        pe.wait_ge(landed[s][n].sem, it * 16 + 16)
                        for k in range(KD):
                            last = pe.matmul(c.banks[2 + n][:, :], tokensT[s][:, k, :], w[:, k, :], start=k == 0,
                                             stop=k == KD - 1)
                        last.then_inc(filled.sem, 1)
                    pe.wait_ge(gathered[1 - s].sem, it * 16 + (32 if s else 16))
                    turn(pe, 1 - s)
                    pe.wait_ge(by_v.sem, b * 3 + (bV + 1))
                    for k in range(FFE // P):
                        last = pe.transpose(c.banks[4][:, k * P:(k + 1) * P], h[:, k * P:(k + 1) * P], c.ident[:, :])
                    last.then_inc(filled.sem, 1)
                    pe.wait_ge(by_a.sem, b * 4 + (bA + 3))
                    pe.wait_ge(landed[s][2].sem, it * 16 + 16)
                    for half in range(2):
                        for k in range(FFE // P):
                            last = pe.matmul(c.banks[5 + half][:, :], hT[:, k, :],
                                             down_w[s][:, k, half * 512:(half + 1) * 512], start=k == 0,
                                             stop=k == FFE // P - 1)
                        last.then_inc(filled.sem, 1)

        @block.vector
        def _(dve):
            trips = dve.value_load(trips_i[0:1, 0:1], min_val=1, max_val=MAX_BLOCKS // 2)
            halfT = lambda s, half: tokensT[s][:, 4 * half:4 * half + 4, :].rearrange("p k t -> p (k t)")
            dve.wait_ge(filled.sem, bF - 1)
            dve.tensor_copy(halfT(0, 0), c.banks[0][:, :]).then_inc(by_v.sem, 1)
            with dve.Fori(0, trips) as it:
                for s in range(2):
                    b = it * 2 + s
                    dve.wait_ge(filled.sem, b * 7 + (bF + 2))
                    dve.wait_ge(by_a.sem, b * 4 + (bA + 1))
                    dve.tensor_tensor(h, h, c.banks[3][:, :], ALU.mult).then_inc(by_v.sem, 1)
                    dve.wait_ge(filled.sem, b * 7 + (bF + 3))
                    dve.tensor_copy(halfT(1 - s, 0), c.banks[0][:, :]).then_inc(by_v.sem, 1)
                    dve.wait_ge(filled.sem, b * 7 + (bF + 6))
                    dve.wait_ge(stored[s].sem, it * 16 + stored[s].sent)
                    dve.tensor_copy(out[:, s, 0:512], c.banks[5][:, :]).then_inc(by_v.sem, 1)

        @block.scalar
        def _(act):
            trips = act.value_load(trips_i[0:1, 0:1], min_val=1, max_val=MAX_BLOCKS // 2)
            halfT = lambda s, half: tokensT[s][:, 4 * half:4 * half + 4, :].rearrange("p k t -> p (k t)")
            act.wait_ge(filled.sem, bF)
            act.activation(halfT(0, 1), c.banks[1][:, :], ACT.Copy).then_inc(by_a.sem, 1)
            with act.Fori(0, trips) as it:
                for s in range(2):
                    b = it * 2 + s
                    act.wait_ge(filled.sem, b * 7 + (bF + 1))
                    act.activation(h, c.banks[2][:, :], ACT.Silu).then_inc(by_a.sem, 1)
                    act.wait_ge(filled.sem, b * 7 + (bF + 4))
                    act.activation(halfT(1 - s, 1), c.banks[1][:, :], ACT.Copy).then_inc(by_a.sem, 1)
                    act.wait_ge(filled.sem, b * 7 + (bF + 5))
                    act.activation(hT.rearrange("p k t -> p (k t)"), c.banks[4][:, :], ACT.Copy).then_inc(by_a.sem, 1)
                    act.wait_ge(filled.sem, b * 7 + (bF + 7))
                    act.wait_ge(stored[s].sem, it * 16 + stored[s].sent)
                    act.activation(out[:, s, 512:1024], c.banks[6][:, :], ACT.Copy).then_inc(by_a.sem, 1)
                    act.wait_ge(by_v.sem, b * 3 + (bV + 3))
                    act.wait_ge(by_a.sem, b * 4 + (bA + 4))
                    act.dma_start(y_rows[bass.ds(b * P, P), :], out[:, s, :]).then_inc(stored[s].sem, 16)


def block_stack(nc, a, out):
    with ExitStack() as ctx:
        c = Core(nc, ctx)
        c.x = c.region(0, 0, NT, D)
        c.xT = c.region(1, 0, KD, S)
        plan_first(c, a)
        plan_second(c, a)
        plan_third(c, a)
        setup_constants(c, a)
        clear_outputs(c)
        first_block(c, a)
        second_block(c, a)
        mixed = third_mixers(c, a)
        mixture_of_experts(c, a, mixed, out)


def kernel(**inputs):
    import numpy as _np
    import concourse.bacc as _bacc
    from concourse import mybir as _mybir
    from concourse.bass_utils import run_bass_kernel_spmd as _run

    nc = _bacc.Bacc("TRN2", target_bir_lowering=False, num_devices=1)
    arrays, args = {}, {}
    for name, value in inputs.items():
        v = _np.ascontiguousarray(value)
        arrays[f"in_{name}_dram"] = v
        args[name] = nc.dram_tensor(f"in_{name}_dram", v.shape, _mybir.dt.from_np(v.dtype), kind="ExternalInput").ap()
    out = nc.dram_tensor("out_0_dram", (1, S, D), F32, kind="ExternalOutput").ap()
    block_stack(nc, args, out)
    r = _run(nc, [arrays], core_ids=[0])
    return r.results[0]["out_0_dram"]
```

```python
import math
from contextlib import ExitStack

import numpy as np

import concourse.bass as bass
from concourse import mybir

F32 = mybir.dt.float32
I32 = mybir.dt.int32
U32 = mybir.dt.uint32
ALU = mybir.AluOpType
ACT = mybir.ActivationFunctionType
AX = mybir.AxisListType

P = 128
S = 512
D = 1024
NT = S // P
KD = D // P
UNIT = 4096
NEG = -1e30
RING = 3


class Signal:

    def __init__(self, sem):
        self.sem, self.base, self.sent = sem, 0, 0

    def up(self, by=1):
        self.sent += by
        return by

    def at(self, n):
        return self.base + n


class Core:

    def __init__(self, nc, ctx):
        self.nc, self.ctx = nc, ctx
        self.signals = {}
        self.arena = ctx.enter_context(nc.sbuf_tensor("arena", [P, 12 * UNIT], F32))
        self.banks = [ctx.enter_context(nc.psum_tensor(f"bank{i}", [P, 512], F32)) for i in range(8)]
        self.chunks = []
        self.at = {}
        self.loaded = [Signal(ctx.enter_context(nc.semaphore(f"weights_loaded{i}"))) for i in range(RING)]
        self.arrived = {}
        self.freed = {}
        self.issued = 0

    def sb(self, name, shape, dt=F32):
        return self.ctx.enter_context(self.nc.sbuf_tensor(name, shape, dt))

    def sig(self, name):
        if name not in self.signals:
            self.signals[name] = Signal(self.ctx.enter_context(self.nc.semaphore(name)))
        s = self.signals[name]
        s.base = s.sent
        return s

    def region(self, unit, off, *shape):
        n = int(np.prod(shape))
        v = self.arena[:, int(unit * UNIT) + off:int(unit * UNIT) + off + n]
        if len(shape) == 2:
            v = v.rearrange("p (a b) -> p a b", a=shape[0])
        if len(shape) == 3:
            v = v.rearrange("p (a b c) -> p a b c", a=shape[0], b=shape[1])
        return v

    def plan(self, key, *parts):
        self.at[key] = len(self.chunks)
        self.chunks.append((key, parts))

    def slot(self, key):
        n = self.at[key]
        out, off = [], (2 + n % RING) * UNIT
        for part in self.chunks[n][1]:
            a, b = part.shape[1], part.shape[2]
            out.append(self.arena[:, off:off + a * b].rearrange("p (a b) -> p a b", a=a))
            off += a * b
        assert off <= (3 + n % RING) * UNIT
        return out

    def load_weights(self, eng):
        while self.issued < len(self.chunks):
            n = self.issued
            if n >= RING:
                if n - RING not in self.freed:
                    return
                sem, count = self.freed[n - RING]
                eng.wait_ge(sem, count)
            for dst, src in zip(self.slot(self.chunks[n][0]), self.chunks[n][1]):
                eng.dma_start(dst, src).then_inc(self.loaded[n % RING].sem, self.loaded[n % RING].up(16))
            self.arrived[n] = self.loaded[n % RING].sent
            self.issued += 1

    def weights(self, eng, key):
        n = self.at[key]
        count = 16 * sum(len(self.chunks[m][1]) for m in range(n % RING, n + 1, RING))
        eng.wait_ge(self.loaded[n % RING].sem, count)
        return self.slot(key)

    def release(self, key, sig):
        self.freed[self.at[key]] = (sig.sem, sig.sent)


def bank_groups(c, groups, nb=8, chained=False, meanwhile=None):
    filled = c.sig("bank_filled")
    emptied = {"v": c.sig("bank_emptied_by_vector"), "a": c.sig("bank_emptied_by_scalar")}
    own = {"v": c.sig("vector_order"), "a": c.sig("scalar_order")}
    turn, seen = [], {"v": 0, "a": 0}
    for g in groups:
        seen[g[3]] += 1
        turn.append((g[3], seen[g[3]]))

    with c.nc.Block() as block:
        @block.tensor
        def _(pe):
            for n, (needs, products, releases, _, _, *after) in enumerate(groups):
                for m in after[0] if after else ():
                    pe.wait_ge(emptied[turn[m][0]].sem, emptied[turn[m][0]].at(turn[m][1]))
                if n >= nb:
                    who, count = turn[n - nb]
                    pe.wait_ge(emptied[who].sem, emptied[who].at(count))
                for key in needs:
                    c.weights(pe, key)
                products(pe, c.banks[n % nb]).then_inc(filled.sem, filled.up())
                for key in releases:
                    c.release(key, filled)

        def emptier(eng, who):
            for n, (_, _, _, w, empty, *_) in enumerate(groups):
                if w == who:
                    eng.wait_ge(filled.sem, filled.at(n + 1))
                    empty(eng, c.banks[n % nb], own[who]).then_inc(emptied[who].sem, emptied[who].up())
                    if chained:
                        eng.wait_ge(emptied[who].sem, emptied[who].sent)

        @block.vector
        def _(dve):
            emptier(dve, "v")

        @block.scalar
        def _(act):
            emptier(act, "a")

        if meanwhile:
            block.gpsimd(meanwhile)

        @block.sync
        def _(sync):
            c.load_weights(sync)


def product(pairs):
    def run(pe, bank):
        for n, (lhsT, rhs) in enumerate(pairs):
            m, w = lhsT.shape[1], rhs.shape[1]
            last = pe.matmul(bank[0:m, 0:w], lhsT, rhs, start=n == 0, stop=n == len(pairs) - 1)
        return last
    return run


def turns(c, sources):
    def run(pe, bank):
        at = 0
        for s in sources:
            q, m = s.shape
            last = pe.transpose(bank[0:m, at:at + q], s, c.ident[0:q, 0:q])
            at += q
        return last
    return run


def copy_to(dst):
    def run(eng, bank, order):
        w = dst.shape[1] if len(dst.shape) == 2 else dst.shape[1] * dst.shape[2]
        src = bank[0:dst.shape[0], 0:w]
        if len(dst.shape) == 3:
            src = src.rearrange("p (a b) -> p a b", a=dst.shape[1])
        if hasattr(eng, "activation"):
            return eng.activation(dst, src, ACT.Copy)
        return eng.tensor_copy(dst, src)
    return run


def scaled_to(dst, gain):
    def run(dve, bank, order):
        m, a, b = dst.shape
        src = bank[0:m, 0:a * b].rearrange("p (a b) -> p a b", a=a)
        return dve.tensor_tensor(dst, src, gain.unsqueeze(2).to_broadcast([m, a, b]), ALU.mult)
    return run


def inverse_rms(c, sources, eps, junk, out):
    squared, mean, root, done = (c.sig(x) for x in ("squares_summed", "mean_ready", "root_ready", "inverse_ready"))
    n = len(sources)
    width = sources[0].shape[1]
    with c.nc.Block() as block:
        @block.scalar
        def _(act):
            for i, s in enumerate(sources):
                act.activation(junk[:, 0:s.shape[1]], s, ACT.Square, accum_out=out[:,
                        i:i + 1]).then_inc(squared.sem, squared.up())
                act.wait_ge(squared.sem, squared.sent)
            act.wait_ge(mean.sem, mean.at(n))
            act.activation(out[:, 0:n], out[:, 0:n], ACT.Sqrt).then_inc(root.sem, root.up())

        @block.vector
        def _(dve):
            dve.wait_ge(squared.sem, squared.at(n))
            for i, s in enumerate(sources):
                dve.tensor_scalar(out[:, i:i + 1], out[:, i:i + 1], 1.0 / s.shape[1], eps, ALU.mult,
                                  ALU.add).then_inc(mean.sem, mean.up())
            dve.wait_ge(root.sem, root.at(1))
            dve.reciprocal(out[:, 0:n], out[:, 0:n]).then_inc(done.sem, done.up())

        @block.sync
        def _(sync):
            c.load_weights(sync)


def to_features(c, source, dst, gain=None, width=D):
    groups = []
    for i in range(NT):
        for k in range(0, width // P, 4):
            m = min(4, width // P - k)
            view = dst[:, k:k + m, i * P:(i + 1) * P]
            blocks = [source(i)[:, (k + j) * P:(k + j + 1) * P] for j in range(m)]
            if gain is None:
                groups.append(((), turns(c, blocks), (), "a" if k else "v", copy_to(view)))
            else:
                groups.append(((), turns(c, blocks), (), "v", scaled_to(view, gain[:, k:k + m])))
    bank_groups(c, groups)


def layer_norm_in_place(c, x, gain, bias, eps, small, width=D):
    order, var, root, done = (c.sig(n) for n in ("vector_order", "variance_ready", "root_ready", "normed"))
    parts = -(-width // 512)
    stats = small[:, 0:NT * parts * 6].rearrange("p (i a b) -> p i a b", i=NT, a=parts)
    mv = small[:, 64:64 + 2 * NT].rearrange("p (i b) -> p i b", i=NT)
    sd = small[:, 80:80 + NT]
    with c.nc.Block() as block:
        @block.vector
        def _(dve):
            for i in range(NT):
                for a in range(parts):
                    w = min(512, width)
                    dve.bn_stats(stats[:, i, a, :], x(i)[:, a * w:(a + 1) * w]).then_inc(order.sem, order.up())
            dve.wait_ge(order.sem, order.sent)
            for i in range(NT):
                dve.bn_aggr(mv[:, i, :], stats[:, i, :, :]).then_inc(order.sem, order.up())
            dve.wait_ge(order.sem, order.sent)
            dve.tensor_scalar(sd, mv[:, :, 1], 1.0, eps, ALU.mult, ALU.add).then_inc(var.sem, var.up())
            dve.wait_ge(root.sem, root.at(1))
            dve.reciprocal(sd, sd).then_inc(order.sem, order.up())
            dve.wait_ge(order.sem, order.sent)
            for i in range(NT):
                dve.tensor_scalar(x(i), x(i), mv[:, i, 0:1], sd[:, i:i + 1], ALU.subtract,
                                  ALU.mult).then_inc(order.sem, order.up())
            for i in range(NT):
                dve.wait_ge(order.sem, order.at(order.sent - order.base - (0 if i else NT - 1)))
                dve.tensor_tensor(x(i), x(i), gain, ALU.mult).then_inc(order.sem, order.up())
            dve.wait_ge(order.sem, order.sent)
            for i in range(NT):
                dve.tensor_tensor(x(i), x(i), bias, ALU.add).then_inc(done.sem, done.up())
            dve.wait_ge(done.sem, done.at(NT))

        @block.scalar
        def _(act):
            act.wait_ge(var.sem, var.at(1))
            act.activation(sd, sd, ACT.Sqrt).then_inc(root.sem, root.up())

        @block.sync
        def _(sync):
            c.load_weights(sync)


ATT_WORK = 5 * 512 + 16
TURN_LAG, MIX_LAG = 4, 5


def attention(c, units, work):
    probs = work[:, 0:1536].rearrange("p (a b) -> p a b", a=3)
    turned = work[:, 1536:2560].rearrange("p (a b) -> p a b", a=2)
    high, total = work[:, 2560:2568], work[:, 2568:2576]
    high_of, total_of = lambda u: high[:, u % 8:u % 8 + 1], lambda u: total[:, u % 8:u % 8 + 1]
    scores, peak, exps, flipped, copied, mixed, finished = (c.sig(n) for n in (
        "scores_ready", "peak_ready", "probs_ready", "probs_turned", "turned_copied", "mixed_ready", "output_written"))
    masked, highest, inverted = c.sig("mask_added"), c.sig("maximum_ready"), c.sig("inverse_ready")
    factor_ready = {}
    N = len(units)

    def tiles(keys):
        return [(k, min(P, keys - k)) for k in range(0, keys, P)]

    with c.nc.Block() as block:
        @block.tensor
        def _(pe):
            for u in range(N + MIX_LAG):
                if u < N:
                    if u >= 4:
                        pe.wait_ge(exps.sem, exps.at(u - 3))
                    units[u]["score"](pe, c.banks[u % 4]).then_inc(scores.sem, scores.up())
                w = u - TURN_LAG
                if 0 <= w < N:
                    pe.wait_ge(exps.sem, exps.at(w + 1))
                    if w >= 2:
                        pe.wait_ge(copied.sem, copied.at(w - 1))
                    for k, m in tiles(units[w]["keys"]):
                        last = pe.transpose(c.banks[4 + w % 2][0:m, k:k + P], probs[:, w % 3, k:k + m], c.ident[:, :])
                    last.then_inc(flipped.sem, flipped.up())
                w = u - MIX_LAG
                if w >= 0:
                    pe.wait_ge(copied.sem, copied.at(w + 1))
                    if w >= 2:
                        pe.wait_ge(finished.sem, finished.at(w - 1))
                    ks, vs = tiles(units[w]["keys"]), units[w]["values"]
                    for n, (k, m) in enumerate(ks):
                        last = pe.matmul(c.banks[6 + w % 2][:, 0:vs[n].shape[1]], turned[0:m, w % 2, k:k + P], vs[n],
                                         start=n == 0, stop=n == len(ks) - 1)
                    last.then_inc(mixed.sem, mixed.up())

        @block.vector
        def _(dve):
            for u in range(N + MIX_LAG):
                w = u - MIX_LAG
                if u < N:
                    bank = c.banks[u % 4]
                    dve.wait_ge(scores.sem, scores.at(u + 1))
                    for (a, b), addend, factor in units[u]["masks"]:
                        dve.scalar_tensor_tensor(out=bank[:, a:b], in0=addend, scalar=factor, in1=bank[:, a:b],
                                                 op0=ALU.mult, op1=ALU.add).then_inc(masked.sem, masked.up())
                if 1 <= u <= N:
                    dve.wait_ge(highest.sem, highest.at(u))
                    dve.tensor_scalar(high_of(u - 1), high_of(u - 1), -units[u - 1]["scale"], None,
                                      ALU.mult).then_inc(peak.sem, peak.up())
                if 0 <= w + 1 < N:
                    dve.wait_ge(exps.sem, exps.at(w + 2))
                    dve.reciprocal(total_of(w + 1), total_of(w + 1)).then_inc(inverted.sem, inverted.up())
                if u < N:
                    dve.wait_ge(masked.sem, masked.sent)
                    if u >= 8:
                        dve.wait_ge(exps.sem, exps.at(u - 7))
                    dve.tensor_reduce(high_of(u), bank[:, 0:units[u]["keys"]], AX.X,
                                      ALU.max).then_inc(highest.sem, highest.up())
                if 0 <= w + 1 < N:
                    weight = units[w + 1].get("weight")
                    if weight is not None:
                        dve.wait_ge(inverted.sem, inverted.sent)
                        dve.tensor_tensor(total_of(w + 1), total_of(w + 1), weight,
                                          ALU.mult).then_inc(inverted.sem, inverted.up())
                    factor_ready[w + 1] = inverted.sent
                if w >= 0:
                    dve.wait_ge(inverted.sem, factor_ready[w])
                    if w >= 1:
                        dve.wait_ge(finished.sem, finished.at(w))
                    dve.wait_ge(mixed.sem, mixed.at(w + 1))
                    units[w]["finish"](dve, c.banks[6 + w % 2], total_of(w)).then_inc(finished.sem, finished.up())

        @block.scalar
        def _(act):
            for u in range(N + 3):
                w = u - 3
                if w >= 0:
                    act.wait_ge(flipped.sem, flipped.at(w + 1))
                    if w >= 2:
                        act.wait_ge(mixed.sem, mixed.at(w - 1))
                    m = min(P, units[w]["keys"])
                    n = len(tiles(units[w]["keys"])) * P
                    act.activation(turned[0:m, w % 2, 0:n], c.banks[4 + w % 2][0:m, 0:n],
                                   ACT.Copy).then_inc(copied.sem, copied.up())
                if u < N:
                    act.wait_ge(peak.sem, peak.at(u + 1))
                    if u >= 8:
                        act.wait_ge(finished.sem, finished.at(u - 7))
                    act.activation(probs[:, u % 3, 0:units[u]["keys"]], c.banks[u % 4][:, 0:units[u]["keys"]], ACT.Exp,
                                   bias=high_of(u), scale=units[u]["scale"],
                                   accum_out=total_of(u)).then_inc(exps.sem, exps.up())

        @block.sync
        def _(sync):
            c.load_weights(sync)


def products_by_tile(c, pe, keys, hidden, tail, filled, ready, turned, source):
    total, k0 = hidden.shape[1], 0

    def add_chunk(k0, w, i):
        for half in range(2):
            for k in range(w.shape[1]):
                last = pe.matmul(c.banks[2 * i + half][:, :], hidden[:, k0 + k, i * P:(i + 1) * P],
                                 w[:, k, half * 512:(half + 1) * 512], start=k0 + k == 0, stop=k0 + k == total - 1)
        return last

    def turn_tile(i):
        signal, count = ready(i)
        pe.wait_ge(signal.sem, count)
        for half in range(2):
            for k in range(4):
                at = (4 * half + k) * P
                last = pe.transpose(c.banks[2 * i + half][:, k * P:(k + 1) * P], source(i)[:, at:at + P], c.ident[:, :])
            last.then_inc(turned.sem, turned.up())

    for key in keys[:-tail]:
        w = c.weights(pe, key)[0]
        for i in range(NT):
            last = add_chunk(k0, w, i)
        last.then_inc(filled.sem, filled.up())
        c.release(key, filled)
        k0 += w.shape[1]
    chunks = [c.weights(pe, key)[0] for key in keys[-tail:]]
    for i in range(NT):
        k = k0
        for w in chunks:
            last = add_chunk(k, w, i)
            k += w.shape[1]
        last.then_inc(filled.sem, filled.up())
        if i == NT - 1:
            for key in keys[-tail:]:
                c.release(key, filled)
        if i >= 2:
            turn_tile(i - 2)
    for i in (NT - 2, NT - 1):
        turn_tile(i)


def layer_norm_numbers(c):
    n = c.norms
    return (n[:, 0:48].rearrange("p (i a b) -> p i a b", i=NT, a=2), n[:, 48:56].rearrange("p (i b) -> p i b", i=NT),
            n[:, 56:60], n[:, 60:64])


def down_and_layer_norm(c, keys, hidden, gain_row, bias_row, rows, eps, tail=1,
                        x_rows=None, kept=None, meanwhile=None):
    x, xT = c.x, c.xT
    stats, mv, sd, shift = layer_norm_numbers(c)
    gain, bias = rows[:, 0, :], rows[:, 1, :]
    filled, got, var, root, scaled, centred, gained, normed, turned, emptied = (c.sig(n) for n in (
        "bank_filled", "rows_loaded_scalar", "variance_ready", "root_ready", "scale_ready", "rows_centred",
        "gain_applied", "normed", "rows_turned", "bank_emptied_by_scalar"))
    order, emptied_v, last_normed = c.sig("vector_order"), c.sig("bank_emptied_by_vector"), c.sig("last_tile_normed")
    early = len(keys) - tail
    with c.nc.Block() as block:
        def ready(i):
            return (normed, normed.at(i + 1)) if i < NT - 1 else (last_normed, last_normed.at(1))

        @block.tensor
        def _(pe):
            products_by_tile(c, pe, keys, hidden, tail, filled, ready, turned, lambda i: x[:, i, :])

        def empty_turned(eng, i, half):
            eng.wait_ge(turned.sem, turned.at(2 * i + half + 1))
            src = c.banks[2 * i + half][:, :].rearrange("p (k t) -> p k t", k=4)
            return copy_to_view(eng, xT[:, 4 * half:4 * half + 4, i * P:(i + 1) * P], src)

        @block.vector
        def _(dve):
            for i in range(NT):
                dve.wait_ge(filled.sem, filled.at(early + i + 1))
                for half in range(2):
                    dst = x[:, i, half * 512:(half + 1) * 512]
                    dve.scalar_tensor_tensor(out=dst, in0=dst, scalar=ALPHA, in1=c.banks[2 * i + half][:, :],
                                             op0=ALU.mult, op1=ALU.add).then_inc(order.sem, order.up())
                for half in range(2):
                    dve.wait_ge(order.sem, order.sent - 1)
                    dve.bn_stats(stats[:, i, half, :], x[:, i, half * 512:(half + 1) * 512]).then_inc(order.sem,
                                                                                                      order.up())
                dve.wait_ge(order.sem, order.sent)
                dve.bn_aggr(mv[:, i, :], stats[:, i, :, :]).then_inc(order.sem, order.up())
                dve.wait_ge(order.sem, order.sent)
                dve.tensor_scalar(sd[:, i:i + 1], mv[:, i, 1:2], 1.0, eps, ALU.mult, ALU.add).then_inc(var.sem,
                                                                                                       var.up())
                if i >= 2:
                    empty_turned(dve, i - 2, 0).then_inc(emptied_v.sem, emptied_v.up())
                dve.wait_ge(root.sem, root.at(i + 1))
                dve.reciprocal(sd[:, i:i + 1], sd[:, i:i + 1]).then_inc(order.sem, order.up())
                dve.wait_ge(order.sem, order.sent)
                dve.scalar_tensor_tensor(out=shift[:, i:i + 1], in0=mv[:, i, 0:1], scalar=-1.0, in1=sd[:, i:i + 1],
                                         op0=ALU.mult, op1=ALU.mult).then_inc(scaled.sem, scaled.up())
                if i == 0:
                    dve.wait_ge(got.sem, got.at(32))
                dve.wait_ge(centred.sem, centred.at(i + 1))
                dve.tensor_tensor(x[:, i, :], x[:, i, :], gain, ALU.mult).then_inc(gained.sem, gained.up())
                if i == NT - 1:
                    dve.wait_ge(gained.sem, gained.at(NT))
                    dve.tensor_tensor(x[:, i, :], x[:, i, :], bias, ALU.add).then_inc(last_normed.sem, last_normed.up())
            for i in (NT - 2, NT - 1):
                empty_turned(dve, i, 0).then_inc(emptied_v.sem, emptied_v.up())

        @block.gpsimd
        def _(pool):
            if meanwhile:
                meanwhile(pool)
            pool.wait_ge(got.sem, got.at(32))
            for i in range(NT - 1):
                pool.wait_ge(gained.sem, gained.at(i + 1))
                pool.tensor_tensor(x[:, i, :], x[:, i, :], bias, ALU.add).then_inc(normed.sem, normed.up())

        @block.scalar
        def _(act):
            act.dma_start(gain, gain_row.partition_broadcast(P)).then_inc(got.sem, got.up(16))
            act.dma_start(bias, bias_row.partition_broadcast(P)).then_inc(got.sem, got.up(16))
            for i in range(NT):
                act.wait_ge(var.sem, var.at(i + 1))
                act.activation(sd[:, i:i + 1], sd[:, i:i + 1], ACT.Sqrt).then_inc(root.sem, root.up())
                act.wait_ge(scaled.sem, scaled.at(i + 1))
                act.activation(x[:, i, :], x[:, i, :], ACT.Identity, bias=shift[:, i:i + 1],
                               scale=sd[:, i:i + 1]).then_inc(centred.sem, centred.up())
                if i >= 2:
                    empty_turned(act, i - 2, 1).then_inc(emptied.sem, emptied.up())
            for i in (NT - 2, NT - 1):
                empty_turned(act, i, 1).then_inc(emptied.sem, emptied.up())

        @block.sync
        def _(sync):
            c.load_weights(sync)
            if x_rows is not None:
                for i in range(NT):
                    signal, count = ready(i)
                    sync.wait_ge(signal.sem, count)
                    sync.dma_start(x_rows[i * P:(i + 1) * P, :], x[:, i, :]).then_inc(kept[i % 2].sem, kept[i % 2].up(16))
                for signal in kept:
                    sync.wait_ge(signal.sem, signal.at(16 * NT // 2))


def copy_to_view(eng, dst, src):
    if hasattr(eng, "activation"):
        return eng.activation(dst, src, ACT.Copy)
    return eng.tensor_copy(dst, src)


def down_and_rms_norm(c, keys, hidden, gain_row, rows, eps, next_gain=None, tail=1):
    x, xT = c.x, c.xT
    n = c.norms
    parts, inv, inv2 = n[:, 64:72].rearrange("p (i a) -> p i a", i=NT), n[:, 72:76], n[:, 76:80]
    gain, work, junk = rows[:, 0, :], rows[:, 1, :], rows[:, 2, :]
    filled, got, squared, mean, root, added, squared2, scale, normed, turned, emptied = (c.sig(n) for n in (
        "bank_filled", "rows_loaded_scalar", "squares_summed", "mean_ready", "root_ready", "term_added",
        "new_squares_summed", "scale_ready", "normed", "rows_turned", "bank_emptied_by_scalar"))
    order, emptied_v = c.sig("vector_order"), c.sig("bank_emptied_by_vector")
    early = len(keys) - tail
    again = next_gain is not None
    ready = normed if again else added
    source = (lambda i: rows[:, 3 + i, :]) if again else (lambda i: x[:, i, :])
    with c.nc.Block() as block:
        @block.tensor
        def _(pe):
            products_by_tile(c, pe, keys, hidden, tail, filled, lambda i: (ready, ready.at(i + 1)), turned, source)

        def empty_turned(eng, i, half):
            eng.wait_ge(turned.sem, turned.at(2 * i + half + 1))
            src = c.banks[2 * i + half][:, :].rearrange("p (k t) -> p k t", k=4)
            dst = xT[:, 4 * half:4 * half + 4, i * P:(i + 1) * P]
            if again:
                return eng.tensor_tensor(dst, src, next_gain[:, 4 * half:4 * half + 4].unsqueeze(2)
                                         .to_broadcast([P, 4, P]), ALU.mult)
            return copy_to_view(eng, dst, src)

        @block.vector
        def _(dve):
            dve.wait_ge(got.sem, got.at(16))
            for i in range(NT):
                dve.wait_ge(squared.sem, squared.at(2 * i + 2))
                dve.tensor_tensor(inv[:, i:i + 1], parts[:, i, 0:1], parts[:, i, 1:2], ALU.add).then_inc(order.sem,
                                                                                                         order.up())
                dve.wait_ge(order.sem, order.sent)
                dve.tensor_scalar(inv[:, i:i + 1], inv[:, i:i + 1], 1.0 / D, eps, ALU.mult,
                                  ALU.add).then_inc(mean.sem, mean.up())
                dve.wait_ge(root.sem, root.at((1 + again) * i + 1))
                dve.reciprocal(inv[:, i:i + 1], inv[:, i:i + 1]).then_inc(order.sem, order.up())
                dve.wait_ge(order.sem, order.sent)
                for half in range(2):
                    cols = slice(half * 512, (half + 1) * 512)
                    dve.scalar_tensor_tensor(out=work[:, cols], in0=c.banks[2 * i + half][:, :], scalar=inv[:, i:i + 1],
                                             in1=gain[:, cols], op0=ALU.mult, op1=ALU.mult).then_inc(order.sem, order.up())
                dve.wait_ge(order.sem, order.sent)
                dve.tensor_tensor(x[:, i, :], x[:, i, :], work, ALU.add).then_inc(added.sem, added.up())
                if i >= 2:
                    empty_turned(dve, i - 2, 0).then_inc(emptied_v.sem, emptied_v.up())
                    if again:
                        empty_turned(dve, i - 2, 1).then_inc(emptied_v.sem, emptied_v.up())
                if again:
                    dve.wait_ge(squared2.sem, squared2.at(i + 1))
                    dve.tensor_scalar(inv2[:, i:i + 1], inv2[:, i:i + 1], 1.0 / D, eps, ALU.mult,
                                      ALU.add).then_inc(mean.sem, mean.up())
                    dve.wait_ge(root.sem, root.at(2 * i + 2))
                    dve.reciprocal(inv2[:, i:i + 1], inv2[:, i:i + 1]).then_inc(scale.sem, scale.up())
            for i in (NT - 2, NT - 1):
                empty_turned(dve, i, 0).then_inc(emptied_v.sem, emptied_v.up())
                if again:
                    empty_turned(dve, i, 1).then_inc(emptied_v.sem, emptied_v.up())

        @block.scalar
        def _(act):
            act.dma_start(gain, gain_row.partition_broadcast(P)).then_inc(got.sem, got.up(16))
            for i in range(NT):
                act.wait_ge(filled.sem, filled.at(early + i + 1))
                for half in range(2):
                    act.activation(junk[:, half * 512:(half + 1) * 512], c.banks[2 * i + half][:, :], ACT.Square,
                                   accum_out=parts[:, i, half:half + 1]).then_inc(squared.sem, squared.up())
                    act.wait_ge(squared.sem, squared.sent)
                act.wait_ge(mean.sem, mean.at((1 + again) * i + 1))
                act.activation(inv[:, i:i + 1], inv[:, i:i + 1], ACT.Sqrt).then_inc(root.sem, root.up())
                if again:
                    act.wait_ge(added.sem, added.at(i + 1))
                    act.activation(junk, x[:, i, :], ACT.Square,
                                   accum_out=inv2[:, i:i + 1]).then_inc(squared2.sem, squared2.up())
                    act.wait_ge(mean.sem, mean.at(2 * i + 2))
                    act.activation(inv2[:, i:i + 1], inv2[:, i:i + 1], ACT.Sqrt).then_inc(root.sem, root.up())
                    act.wait_ge(scale.sem, scale.at(i + 1))
                    act.activation(source(i), x[:, i, :], ACT.Identity,
                                   scale=inv2[:, i:i + 1]).then_inc(normed.sem, normed.up())
                elif i >= 2:
                    empty_turned(act, i - 2, 1).then_inc(emptied.sem, emptied.up())
            if not again:
                for i in (NT - 2, NT - 1):
                    empty_turned(act, i, 1).then_inc(emptied.sem, emptied.up())

        @block.sync
        def _(sync):
            c.load_weights(sync)
HEADS, NOPE, ROPE, VDIM, QR, KVR = 4, 64, 32, 64, 256, 128
EPS1 = 1e-6
TWO_PI = (6.28125, 0.0019350051879882812, 3.0199159819756e-07)


def plan_first(c, a):
    w = a["w_in"][0].rearrange("(k p) n -> p k n", p=P)
    c.plan("conv", w[:, :, 928:1440])
    c.plan("pool", w[:, :, 1440:1952])
    c.plan("latents", w[:, :, 0:416])
    c.plan("gating", w[:, :, 416:928])
    for half in range(2):
        for b in range(4):
            n = 1952 + b * D + half * 512
            c.plan(("gates", half, b), w[:, :, n:n + 512])
    w = a["w_out"][0].rearrange("(k p) n -> p k n", p=P)
    for half in range(2):
        c.plan(("out1", half), w[:, half * 4:(half + 1) * 4, :])
    w = a["w_ff1"][0].rearrange("(k p) n -> p k n", p=P)
    for n in range(8):
        c.plan(("ff1", n), w[:, :, n * 512:(n + 1) * 512])
    w = a["w_ff2"][0].rearrange("(k p) n -> p k n", p=P)
    for n in range(8):
        c.plan(("ff2", n), w[:, n * 4:(n + 1) * 4, :])


def features_from(c, key, xT, dsts, empties=None):
    groups = []
    n = len(dsts)
    for j in range(n):
        w = c.slot(key)[0]
        pairs = [(w[:, k, j * P:(j + 1) * P], xT[:, k, :]) for k in range(xT.shape[1])]
        e = empties[j] if empties else copy_to(dsts[j])
        groups.append(((key,), product(pairs), (key,) if j == n - 1 else (), "av"[j % 2] if not empties else "a", e))
    return groups


def tokens_from(c, key, xT, cols, dsts, empties=None, who=None, last=True):
    groups = []
    for i in range(NT):
        w = c.slot(key)[0]
        pairs = [(xT[:, k, i * P:(i + 1) * P], w[:, k, cols[0]:cols[1]]) for k in range(xT.shape[1])]
        e = empties[i] if empties else copy_to(dsts[i])
        groups.append(((key,), product(pairs), (key,) if last and i == NT - 1 else (),
                       who or "av"[i % 2], e))
    return groups


def setup_constants(c, a):
    nc = c.nc
    c.ident = c.sb("ident", [P, P])
    c.keep_le = c.sb("keep_le", [P, P])
    c.ones = c.sb("ones", [P, P])
    c.small = c.sb("small", [P, 128])
    c.norms = c.sb("norm_numbers", [P, 80])
    rows = [c.region(11, 0, 256)[:, n * P:(n + 1) * P] for n in range(2)]
    c.columns = [c.sb(f"columns{n}", [P, P]) for n in range(2)]
    names = [
        [("gate_b", 32), ("norm_mix_pre", 8), ("q_norm", 2), ("kv_norm", 1), ("pool_scale", 2), ("conv_w", 6),
         ("norm_ffn_pre", 8), ("conv_b_2", 16), ("hg_lb_logits_3", 8), ("nsa_norm_g_3", 4), ("hg_norm_g_3", 1),
         ("lambda_q1_2", 0), ("subln_w_2", 1)],
        [("conv_w_2", 80), ("ssm_norm_w_2", 8), ("cmp_pe_k_3", 16), ("cmp_pe_v_3", 16)],
    ]
    c.col = {}
    made, set_, loaded = c.sig("constants_zeroed"), c.sig("constants_made"), c.sig("parameters_loaded")
    moves = []
    for n, group in enumerate(names):
        at = 0
        for name, count in group:
            if not count or name not in a:
                continue
            src = a[name]
            src = src.rearrange("a b n -> (a b n)") if len(src.shape) == 3 else src.rearrange("a n -> (a n)")
            moves.append((rows[n][at:at + count, :], src.rearrange("(r p) -> r p", p=P)))
            c.col[name] = c.columns[n][:, at:at + count]
            at += count
    with nc.Block() as block:
        @block.gpsimd
        def _(pool):
            pool.memset(c.ident[:, :], 0.0).then_inc(made.sem, made.up())
            pool.memset(c.keep_le[:, :], 0.0).then_inc(made.sem, made.up())
            pool.memset(c.ones[:, :], 1.0).then_inc(made.sem, made.up())
            pool.memset(c.region(11, 0, 256), 0.0).then_inc(made.sem, made.up())
            pool.wait_ge(made.sem, made.at(4))
            pool.affine_select(out=c.ident[:, :], in_=c.ident[:, :], compare_op=ALU.not_equal, fill=1.0,
                                        base=0, pattern=[[-1, P]], channel_multiplier=1).then_inc(set_.sem, set_.up())
            pool.affine_select(out=c.keep_le[:, :], in_=c.keep_le[:, :], compare_op=ALU.is_ge, fill=NEG,
                                        base=0, pattern=[[-1, P]], channel_multiplier=1).then_inc(set_.sem, set_.up())
            pool.wait_ge(set_.sem, set_.at(2))

        @block.scalar
        def _(act):
            act.wait_ge(made.sem, made.at(4))
            for dst, src in moves:
                act.dma_start(dst, src).then_inc(loaded.sem, loaded.up(16))
            act.wait_ge(loaded.sem, loaded.at(16 * len(moves)))

        @block.sync
        def _(sync):
            x = a["x"][0].rearrange("(i p) d -> p i d", p=P)
            loaded_x = c.sig("x_loaded")
            sync.dma_start(c.x, x).then_inc(loaded_x.sem, loaded_x.up(16))
            sync.wait_ge(loaded_x.sem, loaded_x.at(16))
            sync.wait_ge(loaded.sem, loaded.at(16 * len(moves)))
            c.load_weights(sync)
    bank_groups(c, [((), turns(c, [rows[n]]), (), "v", copy_to(c.columns[n][:, :])) for n in range(2)])


def first_block(c, a):
    nc, x, xT = c.nc, c.x, c.xT
    small = c.small
    normed = c.region(6, 0, NT, D)
    row_inverse = small[:, 100:104]
    inverse_rms(c, [x[:, i, :] for i in range(NT)], EPS1, c.region(8, 0, D), row_inverse)

    def scale_rows(dst, src, inv, n=NT):
        done = c.sig("rows_scaled")
        with nc.Block() as block:
            @block.vector
            def _(dve):
                for i in range(n):
                    dve.tensor_scalar(dst(i), src(i), inv(i), None, ALU.mult).then_inc(done.sem, done.up())
                dve.wait_ge(done.sem, done.at(n))
    scale_rows(lambda i: normed[:, i, :], lambda i: x[:, i, :], lambda i: row_inverse[:, i:i + 1])
    to_features(c, lambda i: normed[:, i, :], xT, c.col["norm_mix_pre"])

    latents = c.region(7, 0, NT, 416)
    gating = c.region(7, 1664, NT, 512)
    convpool = c.region(6, 0, 8, S)
    branches = c.region(10, 0, 8, S)
    small_parts = Parts()
    count = c.region(5, 2048, 2, S)
    made, got, picked = c.sig("iota_made"), c.sig("rows_loaded_gpsimd"), c.sig("causal_weights")
    counted = c.sig("counts_made")
    moves = [(small_parts.wuq(c), a["w_uq"][0].rearrange("(k p) n -> p k n", p=P)), (small_parts.wukv(c),
                                                                                     a["w_ukv"][0]),
             (small_parts.positions(c), a["positions"][0].rearrange("(i p) -> p i", p=P)),
             (small_parts.gain(c), a["sg_ln_g"][0].partition_broadcast(P)),
             (small_parts.bias(c), a["sg_ln_b"][0].partition_broadcast(P)),
             (small_parts.mix(c), a["sg_w"][0].rearrange("g t s -> t g s"))]
    moves += [(small_parts.mix_bias(c)[:, g:g + 1], a["sg_b"][0, g, :].rearrange("(t o) -> t o",
                                                                                 o=1)) for g in range(4)]
    moves += [(small_parts.pool_mix(c)[(g % 2) * 64:(g % 2) * 64 + 64, g // 2, :], a["pool_w"][0, g]) for g in range(4)]

    def tables(pool):
        pool.iota(count, pattern=[[0, 2], [1, S]], base=1, channel_multiplier=0,
                  allow_small_or_imprecise_dtypes=True).then_inc(counted.sem, counted.up())
        for dst, src in moves:
            pool.dma_start(dst, src, allow_slow_non_contiguous=True).then_inc(got.sem, got.up(16))
        for k in range(ROPE // 2):
            pool.memset(small_parts.frequencies(c)[:, k:k + 1],
                        float(np.float32(10000.0) ** np.float32(-2.0 * k / ROPE))).then_inc(made.sem, made.up())
        pool.wait_ge(made.sem, made.at(ROPE // 2))
        pool.wait_ge(got.sem, got.at(16 * len(moves)))
        ws = small_parts.mix(c)
        pool.affine_select(out=ws, in_=ws, compare_op=ALU.is_ge, fill=0.0, base=0,
                           pattern=[[0, 4], [-1, P]], channel_multiplier=1).then_inc(picked.sem, picked.up())
        pool.wait_ge(picked.sem, picked.at(1))
    groups = []
    for n, key in enumerate(("conv", "pool")):
        w = c.slot(key)[0]
        for j in range(4):
            groups.append(((key,), product([(w[:, k, j * P:(j + 1) * P], xT[:, k, :]) for k in range(KD)]),
                           (key,) if j == 3 else (), "v", copy_to(convpool[:, 4 * n + j, :])))

    def convolve_first(dve, bank, order):
        emptied = c.signals["bank_emptied_by_vector"]
        dve.wait_ge(emptied.sem, emptied.sent)
        convolve_and_pool(c, dve, convpool, branches, count, counted, order)
        return dve.tensor_copy(latents[:, 0, :], bank[:, 0:416])
    groups += tokens_from(c, "latents", xT, (0, 416), None, [convolve_first] + [copy_to(latents[:, i, :])
                                                                             for i in range(1, NT)], who="v")
    gelu_to = lambda dst: lambda act, bank, order: act.activation(dst, bank[:, :], ACT.Gelu_apprx_tanh)
    groups += tokens_from(c, "gating", xT, (0, 512), None, [gelu_to(gating[:, i, :]) for i in range(NT)], who="a")
    bank_groups(c, groups, meanwhile=tables)

    latent_attention(c, latents, branches, small_parts)
    wbr = c.region(8, 0, 8, D)
    landed = c.sig("branch_weights_landed")

    def branch_weights(sync):
        for b, n in enumerate(("w_br_mla", "w_br_sg", "w_br_conv", "w_br_pool")):
            sync.dma_start(wbr[:, 2 * b:2 * b + 2, :],
                           a[n][0].rearrange("(k p) n -> p k n", p=P)).then_inc(landed.sem, landed.up(16))
    spatial_gating(c, gating, branches, small_parts, branch_weights)
    pool_mixing(c, convpool, branches, small_parts)

    merged = c.region(11, 0, 8, S)
    gate = c.region(6, 0, 2, S)
    term = c.region(6, 2 * S, 2, S)
    filled, opened, weighed, added = (c.sig(n) for n in ("bank_filled", "gates_open", "branch_weighed", "term_added"))
    steps = [(half, b, j) for half in range(2) for b in range(4) for j in range(4)]
    with nc.Block() as block:
        @block.tensor
        def _(pe):
            pe.wait_ge(landed.sem, landed.at(16 * 4))
            for n, (half, b, j) in enumerate(steps):
                w = c.weights(pe, ("gates", half, b))[0]
                if n >= 2:
                    pe.wait_ge(opened.sem, opened.at(n - 1))
                    pe.wait_ge(weighed.sem, weighed.at(n - 1))
                for k in range(KD):
                    pe.matmul(c.banks[n % 2][:, :], w[:, k, j * P:(j + 1) * P], xT[:, k, :], start=k == 0,
                              stop=k == KD - 1)
                m = (half * 4 + j) * P
                for k in range(2):
                    last = pe.matmul(c.banks[2 + n % 2][:, :], wbr[:, 2 * b + k, m:m + P], branches[:, 2 * b + k, :],
                                     start=k == 0, stop=k == 1)
                last.then_inc(filled.sem, filled.up())
                if j == 3:
                    c.release(("gates", half, b), filled)

        @block.scalar
        def _(act):
            for n, (half, b, j) in enumerate(steps):
                act.wait_ge(filled.sem, filled.at(n + 1))
                if n >= 2:
                    act.wait_ge(weighed.sem, weighed.at(n - 1))
                col = c.col["gate_b"][:, b * 8 + half * 4 + j:b * 8 + half * 4 + j + 1]
                act.activation(gate[:, n % 2, :], c.banks[n % 2][:, :], ACT.Sigmoid, bias=col).then_inc(opened.sem,
                                                                                                        opened.up())

        @block.vector
        def _(dve):
            for n, (half, b, j) in enumerate(steps):
                dve.wait_ge(opened.sem, opened.at(n + 1))
                if n >= 2 and b:
                    dve.wait_ge(added.sem, added.sent)
                dst = merged[:, half * 4 + j, :]
                dve.tensor_tensor(dst if b == 0 else term[:, n % 2, :], gate[:, n % 2, :],
                                              c.banks[2 + n % 2][:, :], ALU.mult).then_inc(weighed.sem, weighed.up())
                if b:
                    dve.wait_ge(weighed.sem, weighed.at(n + 1))
                    dve.tensor_tensor(dst, dst, term[:, n % 2, :], ALU.add).then_inc(added.sem, added.up())
            dve.wait_ge(added.sem, added.sent)

        @block.sync
        def _(sync):
            c.load_weights(sync)

    down_and_rms_norm(c, [("out1", half) for half in range(2)], merged, a["norm_mix_post"][0], c.region(6, 0, 7, D),
                      EPS1,
                      next_gain=c.col["norm_ffn_pre"])
    hidden = c.region(6, 0, 32, S)

    def squared_relu(dst):
        def run(act, bank, order):
            act.activation(dst, bank[:, :], ACT.Relu).then_inc(order.sem, order.up())
            act.wait_ge(order.sem, order.sent)
            return act.activation(dst, dst, ACT.Square)
        return run
    groups = []
    for n in range(8):
        groups += features_from(c, ("ff1", n), xT, [None] * 4,
                                [squared_relu(hidden[:, n * 4 + j, :]) for j in range(4)])
    bank_groups(c, groups)
    down_and_rms_norm(c, [("ff2", n) for n in range(8)], hidden, a["norm_ffn_post"][0], c.region(10, 0, 3, D), EPS1)


class Parts:
    wuq = staticmethod(lambda c: c.region(8, 0, 2, 384))
    wukv = staticmethod(lambda c: c.region(8, 768, 512))
    frequencies = staticmethod(lambda c: c.region(8, 1280, ROPE // 2))
    positions = staticmethod(lambda c: c.small[:, 104:108].bitcast(I32))
    gain = staticmethod(lambda c: c.region(5, 0, 256))
    bias = staticmethod(lambda c: c.region(5, 256, 256))
    mix = staticmethod(lambda c: c.region(5, 512, 4, P))
    mix_bias = staticmethod(lambda c: c.region(5, 1536, 4))
    pool_mix = staticmethod(lambda c: c.region(5, 1540, 2, 64))


def latent_attention(c, latents, branches, parts):
    nc = c.nc
    wuq, wukv, pos_i = parts.wuq(c), parts.wukv(c), parts.positions(c)
    inv = c.small[:, 108:116]
    inverse_rms(c, [latents[:, i, 0:QR] for i in range(NT)] + [latents[:, i, QR:QR + KVR] for i in range(NT)], EPS1,
                c.region(9, 0, D), inv)
    half = ROPE // 2
    freq = parts.frequencies(c)
    pos = c.small[:, 116:120]
    ang = c.region(8, 1296, NT, half)
    turnsn = c.region(8, 1360, 2, NT * half)
    trig = c.region(8, 1488, 2, NT, half)
    order, ready = c.sig("vector_order"), c.sig("angles_ready")
    sines = c.sig("sines_ready")
    with nc.Block() as block:
        @block.vector
        def _(dve):
            dve.tensor_copy(pos, pos_i).then_inc(order.sem, order.up())
            dve.wait_ge(order.sem, order.sent)
            dve.tensor_tensor(ang, pos.unsqueeze(2).to_broadcast([P, NT, half]),
                                 freq.unsqueeze(1).to_broadcast([P, NT,
                                                                 half]), ALU.mult).then_inc(order.sem, order.up())
            dve.wait_ge(order.sem, order.sent)
            for t, shift in enumerate((math.pi / 2, 0.0)):
                dst = trig[:, t, :, :]
                n = turnsn[:, t, :].rearrange("p (i k) -> p i k", i=NT)
                dve.tensor_scalar(n, ang, 1.0 / (2 * math.pi), shift / (2 * math.pi), ALU.mult,
                                  ALU.add).then_inc(order.sem, order.up())
                dve.wait_ge(order.sem, order.sent)
                dve.tensor_scalar(n, n, 12582912.0, None, ALU.add).then_inc(order.sem, order.up())
                dve.wait_ge(order.sem, order.sent)
                dve.tensor_scalar(n, n, -12582912.0, None, ALU.add).then_inc(order.sem, order.up())
                dve.wait_ge(order.sem, order.sent)
                dve.scalar_tensor_tensor(out=dst, in0=n, scalar=-TWO_PI[0], in1=ang, op0=ALU.mult,
                                         op1=ALU.add).then_inc(order.sem, order.up())
                dve.wait_ge(order.sem, order.sent)
                dve.scalar_tensor_tensor(out=dst, in0=n, scalar=-TWO_PI[1], in1=dst, op0=ALU.mult,
                                         op1=ALU.add).then_inc(order.sem, order.up())
                dve.wait_ge(order.sem, order.sent)
                dve.scalar_tensor_tensor(out=dst, in0=n, scalar=-TWO_PI[2], in1=dst, op0=ALU.mult,
                                         op1=ALU.add).then_inc(order.sem, order.up())
                dve.wait_ge(order.sem, order.sent)
                if shift:
                    dve.tensor_scalar(dst, dst, shift, None, ALU.add).then_inc(order.sem, order.up())
                    dve.wait_ge(order.sem, order.sent)
                dve.tensor_scalar(dst, dst, math.pi, None, ALU.min).then_inc(order.sem, order.up())
                dve.wait_ge(order.sem, order.sent)
                dve.tensor_scalar(dst, dst, -math.pi, None, ALU.max).then_inc(order.sem, order.up())
                dve.wait_ge(order.sem, order.sent)
            for i in range(NT):
                dve.tensor_scalar(latents[:, i, 0:QR], latents[:, i, 0:QR], inv[:, i:i + 1], None,
                                  ALU.mult).then_inc(order.sem, order.up())
                dve.wait_ge(order.sem, order.sent)
                dve.tensor_scalar(latents[:, i, QR:QR + KVR], latents[:, i, QR:QR + KVR], inv[:, NT + i:NT + i + 1],
                                     None, ALU.mult).then_inc(order.sem, order.up())
                dve.wait_ge(order.sem, order.sent)
            dve.tensor_copy(pos, pos).then_inc(ready.sem, ready.up())

        @block.scalar
        def _(act):
            act.wait_ge(ready.sem, ready.at(1))
            act.activation(trig, trig, ACT.Sin).then_inc(sines.sem, sines.up())
            act.wait_ge(sines.sem, sines.sent)
    latT = c.region(9, 0, 3, S)
    groups = []
    for i in range(NT):
        blocks = [latents[:, i, k * P:(k + 1) * P] for k in range(3)]
        groups.append(((), turns(c, blocks), (), "v",
                       scaled_to(latT[:, :, i * P:(i + 1) * P], c.columns[0][:, 40:43])))
    bank_groups(c, groups)
    q = c.region(8, 1616, NT, 384)
    kv = c.region(11, 0, NT, 512)
    groups = []
    for i in range(NT):
        groups.append(((), product([(latT[:, k, i * P:(i + 1) * P], wuq[:, k, :]) for k in range(2)]), (), "v",
                       copy_to(q[:, i, :])))
        groups.append(((), product([(latT[:, 2, i * P:(i + 1) * P], wukv)]), (), "a", copy_to(kv[:, i, :])))
    bank_groups(c, groups)
    keys = c.region(11, 2048, NT, 384)
    r = [c.region(9, 1536 + n * 256, NT, HEADS, half) for n in range(4)]
    rotated = c.sig("rotated")
    with nc.Block() as block:
        @block.vector
        def _(dve):
            qv = q.rearrange("p i (h e) -> p i h e", h=HEADS)
            kk = keys.rearrange("p i (h e) -> p i h e", h=HEADS)
            kvv = kv.rearrange("p i (h e) -> p i h e", h=HEADS)
            cos, sin = (trig[:, t, :, :].unsqueeze(2).to_broadcast([P, NT, HEADS, half]) for t in range(2))
            x1, x2 = qv[:, :, :, NOPE:NOPE + half], qv[:, :, :, NOPE + half:NOPE + ROPE]
            kr = latents[:, :, QR + KVR:QR + KVR + ROPE]
            k1 = kr[:, :, 0:half].unsqueeze(2).to_broadcast([P, NT, HEADS, half])
            k2 = kr[:, :, half:ROPE].unsqueeze(2).to_broadcast([P, NT, HEADS, half])
            for u1, u2, o1, o2 in ((x1, x2, x1, x2), (k1, k2, kk[:, :, :, NOPE:NOPE + half],
                                                      kk[:, :, :, NOPE + half:NOPE + ROPE])):
                for t, (u, factor) in enumerate(((u1, cos), (u2, sin), (u2, cos), (u1, sin))):
                    dve.tensor_tensor(r[t], u, factor, ALU.mult).then_inc(order.sem, order.up())
                dve.wait_ge(order.sem, order.sent)
                dve.tensor_tensor(o1, r[0], r[1], ALU.subtract).then_inc(order.sem, order.up())
                dve.tensor_tensor(o2, r[2], r[3], ALU.add).then_inc(order.sem, order.up())
                dve.wait_ge(order.sem, order.sent)
            dve.tensor_copy(kk[:, :, :, 0:NOPE], kvv[:, :, :, 0:NOPE]).then_inc(rotated.sem, rotated.up())
            dve.wait_ge(rotated.sem, rotated.sent)
    E = NOPE + ROPE
    qT = c.region(9, 0, HEADS, S)
    kT = c.region(9, 2048, HEADS, S)
    groups = []
    for h in range(HEADS):
        for src, dst, who in ((q, qT, "v"), (keys, kT, "a")):
            groups.append(((), turns(c, [src[:, i, h * E:(h + 1) * E] for i in range(NT)]), (), who,
                           copy_to(dst[0:E, h, :])))
    bank_groups(c, groups)
    out = c.region(8, 0, NT, HEADS * VDIM)
    units = []
    for h in range(HEADS):
        for i in range(NT):
            def score(pe, bank, h=h, i=i):
                return pe.matmul(bank[:, 0:(i + 1) * P], qT[0:E, h, i * P:(i + 1) * P], kT[0:E, h, 0:(i + 1) * P],
                                 start=True, stop=True)

            def finish(dve, bank, factor, h=h, i=i):
                return dve.tensor_scalar(out[:, i, h * VDIM:(h + 1) * VDIM], bank[:, 0:VDIM], factor, None, ALU.mult)
            units.append({"keys": (i + 1) * P, "scale": E ** -0.5, "score": score,
                          "masks": [((i * P, (i + 1) * P), c.keep_le[:, :], 1.0)],
                          "values": [kv[:, k, h * 128 + NOPE:(h + 1) * 128] for k in range(i + 1)], "finish": finish})
    attention(c, units, c.region(8, 1024, ATT_WORK))
    to_features(c, lambda i: out[:, i, :], branches[:, 0:2, :], width=256)


def spatial_gating(c, gating, branches, parts, meanwhile):
    nc = c.nc
    gain, bias, ws, bs = parts.gain(c), parts.bias(c), parts.mix(c), parts.mix_bias(c)
    wT = c.region(5, 1024, 4, P)
    with nc.Block() as block:
        block.sync(meanwhile)
    layer_norm_in_place(c, lambda i: gating[:, i, 256:512], gain, bias, EPS1, c.small, width=256)
    bank_groups(c, [((), turns(c, [ws[:, g, :] for g in range(4)]), (), "v", copy_to(wT))])
    out = c.region(11, 0, NT, 256)
    groups = []
    for i in range(NT):
        def mix(pe, bank, i=i):
            for g in range(4):
                last = pe.matmul(bank[:, g * 64:(g + 1) * 64], wT[:, g, :], gating[:, i,
                                                                                   256 + g * 64:256 + (g + 1) * 64],
                                 start=True, stop=True)
            return last

        def gate(dve, bank, order, i=i):
            o = out[:, i, :].rearrange("p (g e) -> p g e", g=4)
            dve.tensor_tensor(o, bank[:, 0:256].rearrange("p (g e) -> p g e", g=4),
                                     bs.unsqueeze(2).to_broadcast([P, 4, 64]), ALU.add).then_inc(order.sem, order.up())
            dve.wait_ge(order.sem, order.sent)
            return dve.tensor_tensor(out[:, i, :], out[:, i, :], gating[:, i, 0:256], ALU.mult)
        groups.append(((), mix, (), "v", gate))
    bank_groups(c, groups)
    to_features(c, lambda i: out[:, i, :], branches[:, 2:4, :], width=256)


def convolve_and_pool(c, dve, cp, branches, count, counted, order):
    cw = c.col["conv_w"]
    term, s1 = c.region(11, 0, 2, S), c.region(11, 1024, 2, S)
    done = c.sig("branches_ready")
    z, y = cp[:, 0:2, :], branches[:, 4:6, :]
    dve.tensor_tensor(z, cp[:, 4:6, :], z, ALU.mult).then_inc(order.sem, order.up())
    dve.wait_ge(order.sem, order.sent)
    for t in range(2):
        for k in (2, 1, 0):
            lag = 2 - k
            col = cw[:, k * 2 + t:k * 2 + t + 1]
            if lag == 0:
                dve.tensor_scalar(y[:, t, :], z[:, t, :], col, None, ALU.mult).then_inc(order.sem, order.up())
                dve.wait_ge(order.sem, order.sent)
            else:
                dve.scalar_tensor_tensor(out=y[:, t, lag:S], in0=z[:, t, 0:S - lag], scalar=col,
                                            in1=y[:, t, lag:S], op0=ALU.mult, op1=ALU.add).then_inc(order.sem, order.up())
                dve.wait_ge(order.sem, order.sent)
    dve.tensor_tensor(y, y, cp[:, 2:4, :], ALU.mult).then_inc(order.sem, order.up())
    dve.wait_ge(order.sem, order.sent)
    dve.wait_ge(counted.sem, counted.at(1))
    p = cp[:, 6:8, :]
    a0, a1 = s1, term
    dve.tensor_copy(a0, p).then_inc(order.sem, order.up())
    dve.wait_ge(order.sem, order.sent)
    pooled = cp[:, 4:6, :]
    for n, lag in enumerate((1, 2, 4, 8)):
        dve.tensor_copy(a1[:, :, 0:lag], a0[:, :, 0:lag]).then_inc(order.sem, order.up())
        dve.wait_ge(order.sem, order.sent)
        dve.tensor_tensor(a1[:, :, lag:S], a0[:, :, lag:S], a0[:, :, 0:S - lag], ALU.add).then_inc(order.sem,
                                                                                                   order.up())
        dve.wait_ge(order.sem, order.sent)
        rows = slice((n % 2) * 64, (n % 2) * 64 + 64)
        dve.tensor_copy(pooled[rows, n // 2, :], a1[rows, n // 2, :]).then_inc(order.sem, order.up())
        dve.wait_ge(order.sem, order.sent)
        dve.tensor_scalar(count[rows, n // 2, :], count[rows, n // 2, :], float(2 ** (n + 1)), None,
                          ALU.min).then_inc(order.sem, order.up())
        dve.wait_ge(order.sem, order.sent)
        a0, a1 = a1, a0
    dve.reciprocal(count, count).then_inc(order.sem, order.up())
    dve.wait_ge(order.sem, order.sent)
    dve.tensor_tensor(pooled, pooled, count, ALU.mult).then_inc(order.sem, order.up())
    dve.wait_ge(order.sem, order.sent)
    dve.tensor_tensor(pooled, pooled, p, ALU.subtract).then_inc(done.sem, done.up())
    dve.wait_ge(done.sem, done.sent)


def pool_mixing(c, cp, branches, parts):
    wp = parts.pool_mix(c)
    groups = []
    for t in range(2):
        def mix(pe, bank, t=t):
            for g in range(2):
                r = slice(g * 64, g * 64 + 64)
                last = pe.matmul(bank[r, :], wp[r, t, :], cp[r, 4 + t, :], start=True, stop=True)
            return last

        def scale(dve, bank, order, t=t):
            return dve.tensor_scalar(branches[:, 6 + t, :], bank[:, :], c.col["pool_scale"][:, t:t + 1], None, ALU.mult)
        groups.append(((), mix, (), "v", scale))
    bank_groups(c, groups)
AH, AHD, AVD = 8, 64, 128
LAMBDA_INIT = 0.8 - 0.6 * math.exp(0.0)
SH, SHD, SG, SN = 16, 64, 4, 128
FF2 = 2816
EPS2 = 1e-5
ALPHA = 2.0 ** 0.25


def plan_second(c, a):
    w = a["w_in_2"][0].rearrange("(k p) n -> p k n", p=P)
    for part, at in (("q2", 0), ("k2", 1024), ("v2", 2048), ("xbc2", 4096), ("xbc2", 5120), ("z2", 3072)):
        for half in range(2):
            n = at + half * 512
            c.plan((part, n), w[:, :, n:n + 512])
    c.plan("dt2", w[:, :, 6144:6160])
    w = a["w_out_2"][0].rearrange("(k p) n -> p k n", p=P)
    for n in range(4):
        c.plan(("out2", n), w[:, n * 4:(n + 1) * 4, :])
    plan_gated(c, "gu2", a["w_gate_2"][0], a["w_up_2"][0], FF2)
    w = a["w_down_2"][0].rearrange("(k p) n -> p k n", p=P)
    for n in range(0, FF2 // P, 4):
        c.plan(("down2", n), w[:, n:min(n + 4, FF2 // P), :])


def plan_gated(c, key, gate, up, width):
    g, u = (w.rearrange("(k p) n -> p k n", p=P) for w in (gate, up))
    for n in range(0, width, 256):
        c.plan((key, n), g[:, :, n:n + 256], u[:, :, n:n + 256])


def second_block(c, a):
    xT = c.xT
    mixT = c.region(10, 0, 16, S)
    qT, kT = c.region(6, 0, 8, S), c.region(7, 0, 8, S)
    v = c.region(8, 0, NT, D)
    groups = []
    for n in (0, 512):
        groups += features_from(c, ("q2", n), xT, [qT[:, n // P + j, :] for j in range(4)])
    for n in (0, 512):
        groups += features_from(c, ("k2", 1024 + n), xT, [kT[:, n // P + j, :] for j in range(4)])
    for n in (0, 512):
        groups += tokens_from(c, ("v2", 2048 + n), xT, (0, 512), [v[:, i, n:n + 512] for i in range(NT)])
    vecs, dist = c.region(11, 3560, 4, AHD), c.region(11, ATT_WORK, 896)
    made, got = c.sig("iota_made"), c.sig("rows_loaded_gpsimd")

    def tables(pool):
        for n, k in enumerate(("lambda_q1_2", "lambda_q2_2", "lambda_k1_2", "lambda_k2_2")):
            pool.dma_start(vecs[:, n, :], a[k][0].partition_broadcast(P)).then_inc(got.sem, got.up(16))
        pool.iota(dist, pattern=[[-1, 896]], base=384, channel_multiplier=1,
                  allow_small_or_imprecise_dtypes=True).then_inc(made.sem, made.up())
        pool.wait_ge(made.sem, made.at(1))
        pool.wait_ge(got.sem, got.at(16 * 4))
    bank_groups(c, groups, meanwhile=tables)
    differential_attention(c, qT, kT, v, vecs, dist, mixT)
    state_space(c, a, mixT)
    down_and_layer_norm(c, [("out2", n) for n in range(4)], mixT, a["ln1_g_2"][0], a["ln1_b_2"][0],
                        c.region(9, 0, 2, D), EPS2)
    hidden = c.region(6, 0, FF2 // P, S)
    gated(c, "gu2", FF2, xT, hidden)
    down_and_layer_norm(c, [("down2", n) for n in range(0, FF2 // P, 4)], hidden, a["ln2_g_2"][0], a["ln2_b_2"][0],
                        c.region(9, 0, 2, D), EPS2, tail=2)


def gated(c, key, width, xT, hidden):
    filled, opened, done = c.sig("bank_filled"), c.sig("gates_open"), c.sig("branch_weighed")
    n_tiles = width // P
    with c.nc.Block() as block:
        @block.tensor
        def _(pe):
            for n in range(n_tiles):
                g, u = c.weights(pe, (key, n // 2 * 256))
                j = n % 2
                if n >= 2:
                    pe.wait_ge(done.sem, done.at(n - 1))
                for w, bank in ((g, c.banks[n % 2]), (u, c.banks[2 + n % 2])):
                    for k in range(KD):
                        last = pe.matmul(bank[:, :], w[:, k, j * P:(j + 1) * P], xT[:, k, :], start=k == 0,
                                         stop=k == KD - 1)
                last.then_inc(filled.sem, filled.up())
                if j == 1:
                    c.release((key, n // 2 * 256), filled)

        @block.scalar
        def _(act):
            for n in range(n_tiles):
                act.wait_ge(filled.sem, filled.at(n + 1))
                act.activation(hidden[:, n, :], c.banks[n % 2][:, :], ACT.Silu).then_inc(opened.sem, opened.up())

        @block.vector
        def _(dve):
            for n in range(n_tiles):
                dve.wait_ge(opened.sem, opened.at(n + 1))
                dve.tensor_tensor(hidden[:, n, :], hidden[:, n, :], c.banks[2 + n % 2][:, :],
                                  ALU.mult).then_inc(done.sem, done.up())

        @block.sync
        def _(sync):
            c.load_weights(sync)


def differential_attention(c, qT, kT, v, vecs, dist, mixT):
    nc = c.nc
    prod = c.region(11, 256, 2, AHD)
    lam = c.region(11, 384, 4)
    order, powers, ready = c.sig("vector_order"), c.sig("exponentials"), c.sig("lambda_ready")
    neg_lam = c.small[:, 104:105]
    gain = c.small[:, 106:107]
    with nc.Block() as block:
        @block.vector
        def _(dve):
            neg = c.region(11, 400, 896)
            dve.tensor_scalar(neg, dist, -1.0, None, ALU.mult).then_inc(order.sem, order.up())
            dve.wait_ge(order.sem, order.sent)
            dve.tensor_tensor(dist, dist, neg, ALU.max).then_inc(order.sem, order.up())
            dve.wait_ge(order.sem, order.sent)
            dve.tensor_tensor(prod, vecs[:, 0:2, :], vecs[:, 2:4, :], ALU.mult).then_inc(order.sem, order.up())
            dve.wait_ge(order.sem, order.sent)
            dve.tensor_reduce(lam[:, 0:2], prod, AX.X, ALU.add).then_inc(ready.sem, ready.up())
            dve.wait_ge(powers.sem, powers.at(1))
            dve.tensor_tensor(neg_lam, lam[:, 1:2], lam[:, 0:1], ALU.subtract).then_inc(order.sem, order.up())
            dve.wait_ge(order.sem, order.sent)
            dve.tensor_scalar(neg_lam, neg_lam, -LAMBDA_INIT, None, ALU.add).then_inc(order.sem, order.up())
            dve.wait_ge(order.sem, order.sent)
            dve.tensor_scalar(gain, c.col["subln_w_2"], 1.0 - LAMBDA_INIT, None, ALU.mult).then_inc(order.sem,
                                                                                                    order.up())
            dve.wait_ge(order.sem, order.sent)

        @block.scalar
        def _(act):
            act.wait_ge(ready.sem, ready.at(1))
            act.activation(lam[:, 0:2], lam[:, 0:2], ACT.Exp).then_inc(powers.sem, powers.up())
    out = c.region(9, 0, NT, D)
    units = []
    for h in range(AH):
        slope = 2.0 ** (-8.0 * (h + 1) / AH)
        for i in range(NT):
            for part in range(2):
                def score(pe, bank, h=h, i=i, part=part):
                    r = slice(part * AHD, (part + 1) * AHD)
                    return pe.matmul(bank[:, :], qT[r, h, i * P:(i + 1) * P], kT[r, h, :], start=True, stop=True)

                def finish(dve, bank, factor, h=h, i=i, part=part):
                    o = out[:, i, h * AVD:(h + 1) * AVD]
                    if part == 0:
                        return dve.tensor_scalar(o, bank[:, 0:AVD], factor, None, ALU.mult)
                    return dve.scalar_tensor_tensor(out=o, in0=bank[:, 0:AVD], scalar=factor, in1=o, op0=ALU.mult,
                                                    op1=ALU.add)
                units.append({"keys": S, "scale": AHD ** -0.5, "score": score,
                              "masks": [((0, S), dist[:, 384 - i * P:384 - i * P + S], -slope / AHD ** -0.5)],
                              "values": [v[:, k, h * AVD:(h + 1) * AVD] for k in range(NT)], "finish": finish,
                              "weight": neg_lam if part else None})
    attention(c, units, c.region(11, 0, ATT_WORK))
    group_rms_to_features(c, out, AH, EPS2, c.region(6, 0, NT, D), mixT[:, 0:8, :], gain)


def group_rms_to_features(c, y, groups, eps, squares, dst, gain, before=None, after=None):
    width = y.shape[2]
    w, tiles = width // groups, width // P
    inv = c.small[:, 0:NT * groups]
    of = lambda i: inv[:, i * groups:(i + 1) * groups]
    if before is not None:
        squares = before
    multiplied, squared, mean, root, normed, turned, order = (c.sig(x) for x in (
        "rows_gated", "squares_summed", "mean_ready", "root_ready", "normed", "rows_turned", "vector_order"))
    emptied = {"v": c.sig("bank_emptied_by_vector"), "a": c.sig("bank_emptied_by_scalar")}
    halves = [(k, min(4, tiles - k)) for k in range(0, tiles, 4)]
    H = len(halves)

    def empty(eng, i, h):
        k, m = halves[h]
        eng.wait_ge(turned.sem, turned.at(i * H + h + 1))
        src = c.banks[(i * H + h) % 8][:, 0:m * P].rearrange("p (k t) -> p k t", k=m)
        out = dst[:, k:k + m, i * P:(i + 1) * P]
        if gain.shape[1] == 1:
            return eng.activation(out, src, ACT.Copy, scale=gain)
        return eng.tensor_tensor(out, src, gain[:, k:k + m].unsqueeze(2).to_broadcast([P, m, P]), ALU.mult)

    with c.nc.Block() as block:
        @block.tensor
        def _(pe):
            for i in range(NT):
                pe.wait_ge(normed.sem, normed.at(i + 1))
                for h, (k, m) in enumerate(halves):
                    for j in range(m):
                        last = pe.transpose(c.banks[(i * H + h) % 8][:, j * P:(j + 1) * P],
                                            y[:, i, (k + j) * P:(k + j + 1) * P], c.ident[:, :])
                    last.then_inc(turned.sem, turned.up())

        if before is not None:
            @block.gpsimd
            def _(pool):
                for i in range(NT):
                    pool.tensor_tensor(y[:, i, :], y[:, i, :], before[:, i, :], ALU.mult).then_inc(multiplied.sem,
                                                                                                   multiplied.up())

        @block.scalar
        def _(act):
            for i in range(NT + 1):
                if i < NT:
                    if before is not None:
                        act.wait_ge(multiplied.sem, multiplied.at(i + 1))
                    act.activation(squares[:, i, :], y[:, i, :], ACT.Square).then_inc(squared.sem, squared.up())
                if i:
                    act.wait_ge(mean.sem, mean.at(i))
                    act.activation(of(i - 1), of(i - 1), ACT.Sqrt).then_inc(root.sem, root.up())
                if gain.shape[1] == 1 and i >= 2:
                    for h in range(H):
                        empty(act, i - 2, h).then_inc(emptied["a"].sem, emptied["a"].up())
            if gain.shape[1] == 1:
                for h in range(H):
                    empty(act, NT - 1, h).then_inc(emptied["a"].sem, emptied["a"].up())

        @block.vector
        def _(dve):
            for i in range(NT):
                dve.wait_ge(squared.sem, squared.at(i + 1))
                dve.tensor_reduce(of(i), squares[:, i, :].rearrange("p (g e) -> p g e", g=groups), AX.X,
                                  ALU.add).then_inc(order.sem, order.up())
                dve.wait_ge(order.sem, order.sent)
                dve.tensor_scalar(of(i), of(i), 1.0 / w, eps, ALU.mult, ALU.add).then_inc(mean.sem, mean.up())
                if i >= 2 and gain.shape[1] > 1:
                    for h in range(H):
                        empty(dve, i - 2, h).then_inc(emptied["v"].sem, emptied["v"].up())
                dve.wait_ge(root.sem, root.at(i + 1))
                dve.reciprocal(of(i), of(i)).then_inc(order.sem, order.up())
                dve.wait_ge(order.sem, order.sent)
                v = y[:, i, :].rearrange("p (g e) -> p g e", g=groups)
                last = dve.tensor_tensor(v, v, of(i).unsqueeze(2).to_broadcast([P, groups, w]), ALU.mult)
                if after is not None:
                    last.then_inc(order.sem, order.up())
                    dve.wait_ge(order.sem, order.sent)
                    last = dve.tensor_tensor(y[:, i, :], y[:, i, :], after[:, i, :], ALU.mult)
                last.then_inc(normed.sem, normed.up())
            if gain.shape[1] > 1:
                for i in (NT - 2, NT - 1):
                    for h in range(H):
                        empty(dve, i, h).then_inc(emptied["v"].sem, emptied["v"].up())

        @block.sync
        def _(sync):
            c.load_weights(sync)


def state_space(c, a, mixT):
    nc, xT = c.nc, c.xT
    z = c.region(6, 0, NT, D)
    xbc = c.region(7, 0, 16, S)
    small = c.region(5, 0, 2048)
    sm = [small[:, n * 128:(n + 1) * 128].rearrange("p (d i h) -> p d i h", d=2, i=NT) for n in range(9)]
    dt, dA, acs, neg_acs, grow, tot, wdec, etot, t0 = sm
    raw = small[:, 1200:1264].rearrange("p (i h) -> p i h", i=NT)
    rows = small[:, 1264:1344].rearrange("p (n h) -> p n h", n=5)
    tri = [small[:, 1344:1472], small[:, 1472:1600]]
    neg = [small[:, 1600:1728], small[:, 1728:1856]]

    conv, made, got = c.sig("conv_ready"), c.sig("iota_made"), c.sig("rows_loaded_gpsimd")
    order = c.sig("vector_order")

    def tables(pool):
        for n, k in enumerate(("dt_bias_fwd_2", "dt_bias_bwd_2", "a_log_fwd_2", "a_log_bwd_2", "d_skip_2")):
            pool.dma_start(rows[:, n, :], a[k][0].partition_broadcast(P)).then_inc(got.sem, got.up(16))
        for t in tri:
            pool.memset(t, 1.0).then_inc(made.sem, made.up())
        for t in neg:
            pool.memset(t, 0.0).then_inc(made.sem, made.up())
        pool.wait_ge(made.sem, made.at(4))
        for t, fill in ((tri, 0.0), (neg, NEG)):
            pool.affine_select(out=t[0], in_=t[0], compare_op=ALU.is_ge, fill=fill, base=0,
                               pattern=[[1, P]], channel_multiplier=-1).then_inc(made.sem, made.up())
            pool.affine_select(out=t[1], in_=t[1], compare_op=ALU.is_ge, fill=fill, base=0,
                               pattern=[[-1, P]], channel_multiplier=1).then_inc(made.sem, made.up())
        pool.wait_ge(made.sem, made.at(8))
        pool.wait_ge(got.sem, got.at(16 * 5))

    def convolve(j):
        def run(dve, bank, order):
            y = xbc[:, j, :]
            for k in (2, 0, 1, 3, 4):
                col = c.col["conv_w_2"][:, k * 16 + j:k * 16 + j + 1]
                lo, hi = max(0, 2 - k), min(S, S + 2 - k)
                if k == 2:
                    last = dve.tensor_scalar(y, bank[:, :], col, None, ALU.mult)
                else:
                    last = dve.scalar_tensor_tensor(out=y[:, lo:hi], in0=bank[:, lo - 2 + k:hi - 2 + k], scalar=col,
                                                    in1=y[:, lo:hi], op0=ALU.mult, op1=ALU.add)
                if k != 4:
                    last.then_inc(order.sem, order.up())
                    dve.wait_ge(order.sem, order.sent)
            return last
        return run

    def silu_z_and_conv(dst, j):
        def run(act, bank, order):
            for t in (2 * j, 2 * j + 1):
                act.activation(xbc[:, t, :], xbc[:, t, :], ACT.Silu,
                               bias=c.col["conv_b_2"][:, t:t + 1]).then_inc(conv.sem, conv.up())
            return act.activation(dst, bank[:, :], ACT.Silu)
        return run
    groups = []
    for n in range(0, 2048, 512):
        key = ("xbc2", 4096 + n)
        w = c.slot(key)[0]
        for j in range(4):
            pairs = [(w[:, k, j * P:(j + 1) * P], xT[:, k, :]) for k in range(KD)]
            groups.append(((key,), product(pairs), (key,) if j == 3 else (), "v", convolve(n // P + j)))
    for n in (0, 512):
        groups += tokens_from(c, ("z2", 3072 + n), xT, (0, 512), None,
                              [silu_z_and_conv(z[:, i, n:n + 512], n // P + i) for i in range(NT)], who="a")
    groups += tokens_from(c, "dt2", xT, (0, 16), [raw[:, i, :] for i in range(NT)])
    bank_groups(c, groups, meanwhile=tables)
    xs, Bt = xT.rearrange("p k n -> p (k n)").rearrange("p (i n) -> p i n", i=NT), c.region(9, 0, NT, 512)
    groups = []
    for i in range(NT):
        for k in range(3):
            blocks = [xbc[:, 4 * k + j, i * P:(i + 1) * P] for j in range(4)]
            dst = Bt[:, i, :] if k == 2 else xs[:, i, k * 512:(k + 1) * 512]
            groups.append(((), turns(c, blocks), (), "av"[k % 2], copy_to(dst)))
    bank_groups(c, groups)

    e1, e2 = c.sig("exponentials"), c.sig("logs_ready")
    v1 = c.sig("vector_ready")
    with nc.Block() as block:
        @block.vector
        def _(dve):
            for d in range(2):
                dve.tensor_tensor(dt[:, d, :, :], raw, rows[:, d, :].unsqueeze(1).to_broadcast([P, NT, SH]),
                                  ALU.add).then_inc(order.sem, order.up())
                dve.wait_ge(order.sem, order.sent)
            dve.tensor_scalar(t0, dt, -1.0, None, ALU.mult).then_inc(order.sem, order.up())
            dve.wait_ge(order.sem, order.sent)
            dve.tensor_tensor(t0, t0, dt, ALU.min).then_inc(v1.sem, v1.up())
            dve.wait_ge(v1.sem, v1.sent)
            dve.wait_ge(e2.sem, e2.at(1))
            dve.tensor_scalar(dt, dt, 0.0, None, ALU.max).then_inc(order.sem, order.up())
            dve.wait_ge(order.sem, order.sent)
            dve.tensor_tensor(dt, dt, t0, ALU.add).then_inc(order.sem, order.up())
            dve.wait_ge(order.sem, order.sent)
            for d in range(2):
                dve.tensor_tensor(dA[:, d, :, :], dt[:, d, :, :], rows[:, 2 + d, :].unsqueeze(1)
                                     .to_broadcast([P, NT, SH]), ALU.mult).then_inc(order.sem, order.up())
                dve.wait_ge(order.sem, order.sent)
            dve.tensor_scalar(dA, dA, -1.0, None, ALU.mult).then_inc(order.sem, order.up())
            dve.wait_ge(order.sem, order.sent)

        @block.scalar
        def _(act):
            act.wait_ge(v1.sem, v1.at(1))
            act.activation(rows[:, 2:4, :], rows[:, 2:4, :], ACT.Exp).then_inc(e1.sem, e1.up())
            act.wait_ge(e1.sem, e1.sent)
            act.activation(t0, t0, ACT.Exp).then_inc(e1.sem, e1.up())
            act.wait_ge(e1.sem, e1.sent)
            act.activation(t0, t0, ACT.Ln, bias=1.0).then_inc(e2.sem, e2.up())
    flat = lambda t, d: t[:, d, :, :].rearrange("p i h -> p (i h)")
    groups = []
    for d in range(2):
        groups.append(((), product([(tri[d], flat(dA, d))]), (), "v", copy_to(flat(acs, d))))
        groups.append(((), product([(c.ones[:, :], flat(dA, d))]), (), "v", copy_to(flat(tot, d))))
    bank_groups(c, groups)
    with nc.Block() as block:
        @block.vector
        def _(dve):
            dve.tensor_scalar(neg_acs, acs, -1.0, None, ALU.mult).then_inc(order.sem, order.up())
            dve.wait_ge(order.sem, order.sent)
            dve.tensor_tensor(t0, tot, acs, ALU.subtract).then_inc(v1.sem, v1.up())
            dve.wait_ge(e1.sem, e1.at(3 + 2))
            dve.tensor_tensor(wdec, t0, dt, ALU.mult).then_inc(order.sem, order.up())
            dve.wait_ge(order.sem, order.sent)

        @block.scalar
        def _(act):
            act.wait_ge(v1.sem, v1.at(2))
            act.activation(t0, t0, ACT.Exp).then_inc(e1.sem, e1.up())
            act.wait_ge(e1.sem, e1.sent)
            act.activation(grow, acs, ACT.Exp).then_inc(e1.sem, e1.up())
            act.wait_ge(e1.sem, e1.sent)
            act.activation(etot, tot, ACT.Exp).then_inc(e1.sem, e1.up())
            act.wait_ge(e1.sem, e1.sent)

    BT, CT = xbc[:, 8:12, :], xbc[:, 12:16, :]
    y = c.region(7, 0, NT, D)
    xdec = c.region(9, 2048, 2, D)
    state = c.region(11, 0, SG, 256)
    E = c.region(11, 1024, 6, 512)
    M = c.region(5, 2048, 2, 512)
    tmp = c.region(5, 3072, 1, 512)
    heads4 = lambda t, d, i, g, w: t[:, d, i, 4 * g:4 * g + 4].unsqueeze(2).to_broadcast([P, 4, w])
    four = lambda t: t.rearrange("p (r e) -> p r e", r=4)

    decayed = c.sig("decayed_x_ready")

    def decay_x(dve, d, i, slot):
        dve.tensor_tensor(xdec[:, slot, :].rearrange("p (h e) -> p h e", h=SH),
                          xs[:, i, :].rearrange("p (h e) -> p h e", h=SH),
                          wdec[:, d, i, :].unsqueeze(2).to_broadcast([P, SH,
                                  SHD]), ALU.mult).then_inc(decayed.sem, decayed.up())
        dve.wait_ge(decayed.sem, decayed.sent)

    skipped = c.sig("skip_ready")

    def skip(pool):
        for i in range(NT):
            pool.tensor_tensor(y[:, i, :].rearrange("p (h e) -> p h e", h=SH),
                               xs[:, i, :].rearrange("p (h e) -> p h e", h=SH),
                               rows[:, 4, :].unsqueeze(2).to_broadcast([P, SH,
                                       SHD]), ALU.mult).then_inc(skipped.sem, skipped.up())

    groups, at = [], {}

    def add_group(name, group):
        groups.append(group)
        at[name] = len(groups) - 1

    def update(d, i, g, slot, first, after):
        def run(dve, bank, order):
            s = state[:, g, :]
            if first:
                return dve.tensor_copy(s, bank[:, 0:256])
            dve.tensor_tensor(four(s), four(s), heads4(etot, d, i, g, SHD), ALU.mult).then_inc(order.sem, order.up())
            dve.wait_ge(order.sem, order.sent)
            return dve.tensor_tensor(s, s, bank[:, 0:256], ALU.add)
        return ((), product([(Bt[:, i, g * P:(g + 1) * P], xdec[:, slot, g * 256:(g + 1) * 256])]), (), "v", run, after)

    def decay_group(n, i, g, d):
        e = E[:, 2 * (n % 3) + d, :]

        def prods(pe, bank):
            for r in range(4):
                pe.matmul(bank[:, r * P:(r + 1) * P], dA[:, d, i, 4 * g + r:4 * g + r + 1].to_broadcast([P, P]),
                          tri[d], start=True, stop=False, skip_group_check=True)
                last = pe.matmul(bank[:, r * P:(r + 1) * P], c.ident[:, :], neg[d], start=False, stop=True,
                                 skip_group_check=True)
            return last

        def empty(act, bank, order):
            for r in range(4):
                act.activation(e[:, r * P:(r + 1) * P], bank[:, r * P:(r + 1) * P], ACT.Exp,
                               bias=neg_acs[:, d, i, 4 * g + r:4 * g + r + 1]).then_inc(order.sem, order.up())
            for r in range(4):
                act.wait_ge(order.sem, order.sent if r else order.sent - 3)
                last = act.activation(e[:, r * P:(r + 1) * P], e[:, r * P:(r + 1) * P], ACT.Copy,
                                      scale=dt[:, d, i, 4 * g + r:4 * g + r + 1])
                if r < 3:
                    last.then_inc(order.sem, order.up())
            return last
        return ((), prods, (), "a", empty, [at["cb", n - 3]] if n >= 3 else [])

    def cb_group(n, i, g):
        def empty(dve, bank, order):
            m = M[:, n % 2, :]
            if g == 0 and i < NT - 1:
                decay_x(dve, 0, i, i % 2)
            dve.tensor_tensor(m, E[:, 2 * (n % 3), :], E[:, 2 * (n % 3) + 1, :], ALU.add).then_inc(order.sem,
                                                                                                   order.up())
            dve.wait_ge(order.sem, order.sent)
            return dve.tensor_tensor(four(m), four(m), bank[:, 0:P].unsqueeze(1).to_broadcast([P, 4, P]), ALU.mult)
        cs = slice(i * P, (i + 1) * P)
        return ((), product([(BT[:, g, cs], CT[:, g, cs])]), (), "v", empty, [at["decay", n]])

    def y_group(n, i, g):
        def prods(pe, bank):
            for r in range(4):
                h = 4 * g + r
                last = pe.matmul(bank[:, r * SHD:(r + 1) * SHD], M[:, n % 2, r * P:(r + 1) * P],
                                 xs[:, i, h * SHD:(h + 1) * SHD], start=True, stop=True, skip_group_check=True)
            if i:
                last = pe.matmul(bank[:, 256:512], CT[:, g, i * P:(i + 1) * P], state[:, g, :], start=True, stop=True,
                                 skip_group_check=True)
            return last

        def empty(dve, bank, order):
            o = y[:, i, g * 256:(g + 1) * 256]
            if g == 0:
                dve.wait_ge(skipped.sem, skipped.at(i + 1))
            if i:
                dve.tensor_tensor(four(tmp[:, 0, 0:256]), four(bank[:, 256:512]), heads4(grow, 0, i, g, SHD),
                                  ALU.mult).then_inc(order.sem, order.up())
                dve.wait_ge(order.sem, order.sent)
                dve.tensor_tensor(o, o, tmp[:, 0, 0:256], ALU.add).then_inc(order.sem, order.up())
            if (i, g) == (NT - 1, SG - 1):
                decay_x(dve, 1, NT - 1, 1)
                decay_x(dve, 1, NT - 2, 0)
            dve.wait_ge(order.sem, order.sent)
            return dve.tensor_tensor(o, o, bank[:, 0:256], ALU.add)
        return ((), prods, (), "v", empty, [at["cb", n]] + ([at["state", i - 1, g]] if i else []))

    for n in range(NT * SG + 3):
        if n < NT * SG:
            for d in range(2):
                add_group(("decay", n), decay_group(n, n // SG, n % SG, d))
        if 2 <= n < NT * SG + 2:
            add_group(("cb", n - 2), cb_group(n - 2, (n - 2) // SG, (n - 2) % SG))
        if n >= 3:
            i, g = (n - 3) // SG, (n - 3) % SG
            add_group(("y", i, g), y_group(n - 3, i, g))
            if i < NT - 1:
                add_group(("state", i, g), update(0, i, g, i % 2, i == 0, [at["cb", i * SG]]))
    turned_back = at["y", NT - 1, SG - 1]
    for i in reversed(range(NT)):
        for g in range(SG):
            if i < NT - 1:
                def empty(dve, bank, order, i=i, g=g):
                    o = y[:, i, g * 256:(g + 1) * 256]
                    dve.tensor_tensor(four(tmp[:, 0, 0:256]), four(bank[:, 0:256]), heads4(grow, 1, i, g, SHD),
                                      ALU.mult).then_inc(order.sem, order.up())
                    dve.wait_ge(order.sem, order.sent)
                    if (i, g) == (NT - 2, SG - 1):
                        decay_x(dve, 1, NT - 3, 1)
                    return dve.tensor_tensor(o, o, tmp[:, 0, 0:256], ALU.add)
                add_group(("back", i, g), ((), product([(CT[:, g, i * P:(i + 1) * P], state[:, g, :])]), (), "v", empty,
                                           [at["right", i + 1, g]]))
            if i:
                ready = turned_back if i >= NT - 2 else at["back", NT - 2, SG - 1]
                add_group(("right", i, g), update(1, i, g, 1 if i != NT - 2 else 0, i == NT - 1, [ready]))
    bank_groups(c, groups, chained=True, meanwhile=skip)

    group_rms_to_features(c, y, SG, EPS2, None, mixT[:, 8:16, :], c.col["ssm_norm_w_2"], before=z)
NH, NHD, NG = 8, 64, 2
NCMP, CSTRIDE, CBLOCK = 31, 16, 32
HH, SUB = 4, 32
NSUB = S // SUB
XH, XD, MEM = 4, 256, 256
EPS3 = 1e-6


def plan_third(c, a):
    w = a["w_in_3"][0].rearrange("(k p) n -> p k n", p=P)
    for key, lo, hi in (("nq", 0, 512), ("nkv", 512, 1024), ("nwin", 1024, 1304), ("hq", 1304, 1816),
                        ("hf", 1816, 2328), ("hi", 2328, 2840), ("hgate", 2840, 3352)):
        c.plan((key, 3), w[:, :, lo:hi])
    for k in ("cmp_w1_k_3", "cmp_w1_v_3"):
        c.plan(k, a[k][0].rearrange("(k p) n -> p k n", p=P))
    plan_square(c, a, "w_out_3")
    for k in ("xa_wq_3", "xa_wk_3", "xa_wv_3"):
        w = a[k][0].rearrange("(k p) n -> p k n", p=P)
        for n in (0, 512):
            c.plan((k, n), w[:, :, n:n + 512])
    plan_square(c, a, "xa_wo_3")


def plan_square(c, a, name):
    w = a[name][0].rearrange("(k p) n -> p k n", p=P)
    for n in (0, 4):
        c.plan((name, n), w[:, n:n + 4, :])


def third_mixers(c, a):
    nc, xT = c.nc, c.xT
    qT = c.region(5, 0, 4, S)
    kS, kW = c.region(5, 2048, NG, S), c.region(5, 3072, NG, S)
    kC, vC = c.region(6, 0, NG, S), c.region(6, 1024, NG, S)
    vS, vW = c.region(6, 2048, NT, 128), c.region(6, 2560, NT, 128)
    gates = c.region(6, 3072, NT, 24)
    hq, hk = c.region(7, 0, HH, S), c.region(7, 2048, HH, S)
    hf, hv = c.region(8, 0, HH, S), c.region(8, 2048, NT, 512)
    hgate = c.region(9, 0, NT, 512)
    lb, one_less = c.small[:, 104:108], c.small[:, 108:112]
    mixT = c.region(10, 0, 8, S)

    order, ready, powers = c.sig("vector_order"), c.sig("angles_ready"), c.sig("exponentials")
    with nc.Block() as block:
        @block.vector
        def _(dve):
            g = c.col["hg_lb_logits_3"]
            dve.tensor_tensor(lb, g[:, 4:8], g[:, 0:4], ALU.subtract).then_inc(ready.sem, ready.up())
            dve.wait_ge(powers.sem, powers.at(1))
            dve.tensor_scalar(lb, lb, 1.0, None, ALU.add).then_inc(order.sem, order.up())
            dve.wait_ge(order.sem, order.sent)
            dve.reciprocal(lb, lb).then_inc(order.sem, order.up())
            dve.wait_ge(order.sem, order.sent)
            dve.tensor_scalar(one_less, lb, -1.0, 1.0, ALU.mult, ALU.add).then_inc(order.sem, order.up())
            dve.wait_ge(order.sem, order.sent)

        @block.scalar
        def _(act):
            act.wait_ge(ready.sem, ready.at(1))
            act.activation(lb, lb, ACT.Exp).then_inc(powers.sem, powers.up())

    def both_halves(dst, shift=0):
        def run(dve, bank, order):
            for g in range(NG):
                rows = slice(g * 64, g * 64 + 64)
                dve.tensor_copy(dst[0:64, g, :], bank[rows, :]).then_inc(order.sem, order.up())
                dve.wait_ge(order.sem, order.sent)
                last = dve.tensor_copy(dst[64:128, g, 0:S - shift], bank[rows, shift:S])
                if g == 0:
                    last.then_inc(order.sem, order.up())
                    dve.wait_ge(order.sem, order.sent)
            return last
        return run

    def gate_parts(h):
        def run(act, bank, order):
            act.activation(hf[:, h, :], bank[:, :], ACT.Sigmoid).then_inc(order.sem, order.up())
            act.wait_ge(order.sem, order.sent)
            return act.activation(hk[:, h, :], bank[:, :], ACT.Sigmoid, scale=-1.0)
        return run

    def columns(key, lo, empty, who, release=False):
        w = c.slot(key)[0]
        return ((key,), product([(w[:, k, lo:lo + P], xT[:, k, :]) for k in range(KD)]), (key,) if release else (),
                who, empty)
    groups = features_from(c, ("nq", 3), xT, [qT[:, j, :] for j in range(4)])
    groups += [columns(("nkv", 3), 0, both_halves(kC, 1), "v"), columns(("nkv", 3), 128, both_halves(vC, 1), "v"),
               columns(("nkv", 3), 256, both_halves(kS), "v")]
    groups += tokens_from(c, ("nkv", 3), xT, (384, 512), [vS[:, i, :] for i in range(NT)])
    groups += [columns(("nwin", 3), 0, both_halves(kW), "v")]
    groups += tokens_from(c, ("nwin", 3), xT, (128, 256), [vW[:, i, :] for i in range(NT)], last=False)
    sigmoid_to = lambda dst: lambda act, bank, order: act.activation(dst, bank[:, 0:24], ACT.Sigmoid)
    groups += tokens_from(c, ("nwin", 3), xT, (256, 280), None, [sigmoid_to(gates[:, i, :]) for i in range(NT)],
                          who="a")
    groups += features_from(c, ("hq", 3), xT, [hq[:, j, :] for j in range(4)])
    groups += features_from(c, ("hf", 3), xT, [None] * 4, [gate_parts(h) for h in range(4)])
    groups += tokens_from(c, ("hi", 3), xT, (0, 512), [hv[:, i, :] for i in range(NT)])
    silu_to = lambda dst: lambda act, bank, order: act.activation(dst, bank[:, :], ACT.Silu)
    groups += tokens_from(c, ("hgate", 3), xT, (0, 512), None, [silu_to(hgate[:, i, :]) for i in range(NT)], who="a")
    w2 = [c.region(6, 3620, 2, NHD), c.region(6, 3748, 2, NHD)]
    got = c.sig("rows_loaded_gpsimd")

    def second_weights(pool):
        for n, k in enumerate(("cmp_w2_k_3", "cmp_w2_v_3")):
            pool.dma_start(w2[n], a[k][0].rearrange("(k p) n -> p k n", p=P)).then_inc(got.sem, got.up(16))
        pool.wait_ge(got.sem, got.at(32))
    bank_groups(c, groups, meanwhile=second_weights)

    sparse_attention(c, a, w2, qT, kS, kW, kC, vC, vS, vW, gates, mixT)
    gated_recurrence(c, a, hq, hk, hf, hv, hgate, lb, one_less, mixT)
    mem, remembered = c.region(7, 2048, 2, D), c.sig("memory_landed")

    def load_memory(pool):
        pool.dma_start(mem, a["mem_3"][0].rearrange("(i p) d -> p i d", p=P)).then_inc(remembered.sem,
                                                                                       remembered.up(16))
        pool.wait_ge(remembered.sem, remembered.at(16))
    down_and_layer_norm(c, [("w_out_3", n) for n in (0, 4)], mixT, a["ln1_g_3"][0], a["ln1_b_3"][0],
                        c.region(9, 0, 2, D), EPS2, meanwhile=load_memory)
    return cross_attention(c, mem)


def sparse_attention(c, a, w2, qT, kS, kW, kC, vC, vS, vW, gates, mixT):
    nc = c.nc
    kcmp = c.region(6, 3168, NG, NCMP)
    vcmp = c.region(6, 3232, NG, NHD)
    hidden = [c.region(6, 3360, 2, NG * NCMP), c.region(6, 3490, 2, NG * NCMP)]
    width = NG * NCMP
    blocks = [c.region(10, n * 1024, CBLOCK // 2, width) for n in range(2)]
    by_block = [c.region(10, 2048 + n * 256, 256) for n in range(2)]
    added = c.sig("term_added")
    with nc.Block() as block:
        @block.vector
        def _(dve):
            for n, (src, pe_name) in enumerate(((kC, "cmp_pe_k_3"), (vC, "cmp_pe_v_3"))):
                for g in range(NG):
                    for m in range(2):
                        half = slice(m * 8, m * 8 + 8)
                        tokens = src[:, g, m * CSTRIDE:m * CSTRIDE + NCMP * CSTRIDE].rearrange(
                            "p (n k two) -> p k n two", k=8, two=2)[:, :, :, 0]
                        dst = blocks[n][:, half, g * NCMP:(g + 1) * NCMP]
                        dve.tensor_tensor(dst, tokens, c.col[pe_name][:, half].unsqueeze(2).to_broadcast([P, 8, NCMP]),
                                          ALU.add).then_inc(added.sem, added.up())
            dve.wait_ge(added.sem, added.at(8))

        @block.sync
        def _(sync):
            c.load_weights(sync)
    groups = []
    for n, w1 in enumerate(("cmp_w1_k_3", "cmp_w1_v_3")):
        w = c.slot(w1)[0]

        def gelu(act, bank, order, n=n):
            return act.activation(by_block[n][0:width, :], bank[0:width, 0:256], ACT.Gelu_apprx_tanh)
        groups.append(((w1,), product([(blocks[n][:, k, :], w[:, k, :]) for k in range(CBLOCK // 2)]), (w1,), "a",
                       gelu))
    for n in range(2):
        groups.append(((), turns(c, [by_block[n][0:width, m * P:(m + 1) * P] for m in range(2)]), (), "v",
                       copy_to(hidden[n]), [n]))

    def copy_both(dve, bank, order):
        dve.tensor_copy(kcmp[0:64, :, :], bank[0:64, 0:width].rearrange("p (g n) -> p g n",
                                                                        g=NG)).then_inc(order.sem, order.up())
        dve.wait_ge(order.sem, order.sent)
        return dve.tensor_copy(kcmp[64:128, :, :], bank[0:64, 0:width].rearrange("p (g n) -> p g n", g=NG))
    groups.append(((), product([(w2[0][:, m, :], hidden[0][:, m, :]) for m in range(2)]), (), "v", copy_both, [2]))
    for g in range(NG):
        groups.append(((), product([(hidden[1][:, m, g * NCMP:(g + 1) * NCMP], w2[1][:, m, :]) for m in range(2)]), (),
                       "v", copy_to(vcmp[0:NCMP, g, :]), [3]))
    bank_groups(c, groups)
    hide = c.region(11, ATT_WORK, NT, NCMP)
    seen = c.small[:, 112:113]
    made, order = c.sig("iota_made"), c.sig("vector_order")
    with nc.Block() as block:
        @block.gpsimd
        def _(pool):
            pool.memset(hide, 0.0).then_inc(made.sem, made.up())
            pool.memset(seen, 1.0).then_inc(made.sem, made.up())
            pool.wait_ge(made.sem, made.at(2))
            pool.affine_select(out=hide, in_=hide, compare_op=ALU.is_ge, fill=NEG, base=-(CBLOCK - 1),
                                        pattern=[[P, NT], [-CSTRIDE,
                                                           NCMP]], channel_multiplier=1).then_inc(made.sem, made.up())
            pool.affine_select(out=seen, in_=seen, compare_op=ALU.is_ge, fill=0.0, base=-(CBLOCK - 1),
                                        pattern=[[0, 1]], channel_multiplier=1).then_inc(made.sem, made.up())

        @block.vector
        def _(dve):
            dve.wait_ge(made.sem, made.at(4))
            dve.tensor_scalar(gates[:, 0, 0:24:3], gates[:, 0, 0:24:3], seen, None, ALU.mult).then_inc(order.sem,
                                                                                                       order.up())
            dve.wait_ge(order.sem, order.sent)
    out = c.region(9, 2048, NT, 512)
    units = []
    for h in range(NH):
        for i in range(NT):
            for b in range(3):
                g, r, j = h // 4, slice((h % 2) * 64, (h % 2) * 64 + 64), h // 2
                n = NCMP if b == 0 else (i + 1) * P
                keys = kcmp[r, g, :] if b == 0 else (kS, kW)[b - 1][r, g, 0:n]

                def score(pe, bank, i=i, r=r, j=j, n=n, keys=keys):
                    return pe.matmul(bank[:, 0:n], qT[r, j, i * P:(i + 1) * P], keys, start=True, stop=True)

                def finish(dve, bank, factor, h=h, i=i, b=b):
                    o = out[:, i, h * NHD:(h + 1) * NHD]
                    if b == 0:
                        return dve.tensor_scalar(o, bank[:, 0:NHD], factor, None, ALU.mult)
                    return dve.scalar_tensor_tensor(out=o, in0=bank[:, 0:NHD], scalar=factor, in1=o, op0=ALU.mult,
                                                    op1=ALU.add)
                if b == 0:
                    masks, values = [((0, n), hide[:, i, :], 1.0)], [vcmp[0:NCMP, g, :]]
                else:
                    masks = [((i * P, n), c.keep_le[:, :], 1.0)]
                    values = [(vS, vW)[b - 1][:, k, g * NHD:(g + 1) * NHD] for k in range(i + 1)]
                units.append({"keys": n, "scale": NHD ** -0.5, "score": score, "masks": masks, "values": values,
                              "finish": finish, "weight": gates[:, i, 3 * h + b:3 * h + b + 1]})
    attention(c, units, c.region(11, 0, ATT_WORK))
    group_rms_to_features(c, out, 1, EPS3, c.region(11, 0, NT, 512), mixT[:, 0:4, :], c.col["nsa_norm_g_3"])


def gated_recurrence(c, a, hq, hk, hf, hv, hgate, lb, one_less, mixT):
    nc = c.nc
    order, made = c.sig("vector_order"), c.sig("iota_made")
    N = HH * NSUB
    chunks = lambda t: t.rearrange("p h s -> p (h s)").rearrange("p (n t) -> p n t", n=N)
    f, k, q = chunks(hf), chunks(hk), chunks(hq)
    U = [c.region(5, n * 2048, N, SUB) for n in range(2)]
    G = [c.region(6, n * 2048, N, SUB) for n in range(2)]
    R = c.region(11, 2048, N, SUB)
    pick = c.region(1, 0, 2 * SUB)
    att = c.region(1, 64, HH, S)
    blocks = c.region(11, 0, NT * HH, P)
    decay = c.region(1, 2200, N)
    with nc.Block() as block:
        @block.gpsimd
        def _(pool):
            pool.memset(pick, 0.0).then_inc(made.sem, made.up())
            pool.memset(blocks, 0.0).then_inc(made.sem, made.up())
            pool.wait_ge(made.sem, made.at(2))
            pool.memset(pick[:, SUB - 1:SUB], 1.0).then_inc(made.sem, made.up())
            pool.wait_ge(made.sem, made.at(3))

        @block.vector
        def _(dve):
            for h in range(HH):
                dve.tensor_scalar(hf[:, h, :], hf[:, h, :], one_less[:, h:h + 1], lb[:, h:h + 1], ALU.mult,
                                            ALU.add).then_inc(order.sem, order.up())
                dve.tensor_scalar(hk[:, h, :], hk[:, h, :], one_less[:, h:h + 1], None,
                                  ALU.mult).then_inc(order.sem, order.up())
                dve.wait_ge(order.sem, order.sent)
    grown, keyed, added, copied = c.sig("decays_grown"), c.sig("keys_weighed"), c.sig("bank_filled"), c.sig("turned_copied")
    with nc.Block() as block:
        @block.vector
        def _(dve):
            for n, j in enumerate(reversed(range(SUB))):
                u, before = U[n % 2], U[(n + 1) % 2]
                if n >= 2:
                    dve.wait_ge(keyed.sem, keyed.at(n - 1))
                if n:
                    w = SUB - 1 - j
                    dve.tensor_tensor(u[:, :, j + 1:SUB], before[:, :, j + 1:SUB],
                                                f[:, :, j + 1:j + 2].to_broadcast([P, N,
                                                        w]), ALU.mult).then_inc(order.sem, order.up())
                dve.tensor_copy(u[:, :, j:j + 1], q[:, :, j:j + 1]).then_inc(grown.sem, grown.up())
                dve.wait_ge(grown.sem, grown.at(n + 1))
                if n:
                    dve.wait_ge(order.sem, order.sent)
            dve.memset(R[:, :, SUB - 1:SUB], 1.0).then_inc(order.sem, order.up())
            dve.wait_ge(order.sem, order.sent)
            for j in reversed(range(SUB - 1)):
                dve.tensor_tensor(R[:, :, j:j + 1], R[:, :, j + 1:j + 2], f[:, :, j + 1:j + 2],
                                  ALU.mult).then_inc(order.sem, order.up())
                dve.wait_ge(order.sem, order.sent)
            dve.tensor_tensor(decay.unsqueeze(2), R[:, :, 0:1], f[:, :, 0:1], ALU.mult).then_inc(order.sem, order.up())
            dve.wait_ge(order.sem, order.sent)
            dve.wait_ge(keyed.sem, keyed.at(SUB))
            dve.tensor_tensor(k, k, R, ALU.mult).then_inc(order.sem, order.up())
            dve.wait_ge(order.sem, order.sent)
            dve.tensor_tensor(q, U[(SUB - 1) % 2], f[:, :, 0:1].to_broadcast([P, N, SUB]),
                              ALU.mult).then_inc(order.sem, order.up())
            dve.wait_ge(order.sem, order.sent)

        @block.gpsimd
        def _(pool):
            for n, j in enumerate(reversed(range(SUB))):
                pool.wait_ge(grown.sem, grown.at(n + 1))
                if n >= 2:
                    pool.wait_ge(added.sem, added.at(n - 1))
                pool.tensor_tensor(G[n % 2][:, :, j:SUB], U[n % 2][:, :, j:SUB],
                                             k[:, :, j:j + 1].to_broadcast([P, N,
                                                     SUB - j]), ALU.mult).then_inc(keyed.sem, keyed.up())

        @block.tensor
        def _(pe):
            for n, j in enumerate(reversed(range(SUB))):
                pe.wait_ge(keyed.sem, keyed.at(n + 1))
                for h in range(HH):
                    bank = c.banks[h][0:SUB, :].rearrange("p (n t) -> p n t", n=NSUB)
                    last = pe.matmul(bank[:, :, j:SUB], pick[:, SUB - 1 - j:2 * SUB - 1 - j],
                                     G[n % 2][:, h * NSUB:(h + 1) * NSUB, j:SUB], start=n == 0, stop=n == SUB - 1,
                                     skip_group_check=True)
                last.then_inc(added.sem, added.up())

        @block.scalar
        def _(act):
            act.wait_ge(added.sem, added.at(SUB))
            for h in range(HH):
                act.activation(att[0:SUB, h, :], c.banks[h][0:SUB, :], ACT.Copy).then_inc(copied.sem, copied.up())
            act.wait_ge(copied.sem, copied.at(HH))
            for quarter in range(4):
                r = slice(quarter * SUB, (quarter + 1) * SUB)
                for h in range(HH):
                    src = att[0:SUB, h, :].rearrange("p (i c t) -> p i c t", i=NT, c=4)[:, :, quarter, :]
                    dst = blocks.rearrange("p (i h) t -> p i h t", i=NT)[r, :, h, quarter * SUB:(quarter + 1) * SUB]
                    act.activation(dst, src, ACT.Copy).then_inc(copied.sem, copied.up())
            act.wait_ge(copied.sem, copied.at(5 * HH))

        @block.sync
        def _(sync):
            c.load_weights(sync)
    kt = c.region(6, 0, NT, 512)
    out = c.region(6, 2048, NT, 512)
    state = [c.region(5, m * HH * P, HH, P) for m in range(2)]
    groups = []
    for i in range(NT):
        groups.append(((), turns(c, [hk[:, h, i * P:(i + 1) * P] for h in range(HH)]), (), "v", copy_to(kt[:, i, :])))

        def inside(pe, bank, i=i):
            for h in range(HH):
                last = pe.matmul(bank[:, h * P:(h + 1) * P], blocks[:, i * HH + h, :], hv[:, i, h * P:(h + 1) * P],
                                 start=True, stop=True, skip_group_check=True)
            return last
        groups.append(((), inside, (), "a", copy_to(out[:, i, :])))
    bank_groups(c, groups)
    groups, at = [], {}

    def gain_group(n):
        i, r = n // 4, slice((n % 4) * SUB, (n % 4) * SUB + SUB)

        def gain(pe, bank):
            for h in range(HH):
                last = pe.matmul(bank[:, h * P:(h + 1) * P], kt[r, i, h * P:(h + 1) * P], hv[r, i, h * P:(h + 1) * P],
                                 start=True, stop=True, skip_group_check=True)
            return last

        def update(dve, bank, order):
            b = bank[:, :].rearrange("p (h e) -> p h e", h=HH)
            if n == 0:
                return dve.tensor_copy(state[0], b)
            dve.tensor_tensor(state[n % 2], state[(n - 1) % 2], decay[:, n:N:NSUB].unsqueeze(2).to_broadcast([P, HH,
                                                                                                              P]),
                              ALU.mult).then_inc(order.sem, order.up())
            dve.wait_ge(order.sem, order.sent)
            return dve.tensor_tensor(state[n % 2], state[n % 2], b, ALU.add)
        at[n] = len(groups)
        groups.append(((), gain, (), "v", update))

    def carried_group(n):
        i, r = n // 4, slice((n % 4) * SUB, (n % 4) * SUB + SUB)

        def carried(pe, bank):
            for h in range(HH):
                last = pe.matmul(bank[r, h * P:(h + 1) * P], hq[:, h, n * SUB:(n + 1) * SUB], state[(n - 1) % 2][:,
                                                                                                                 h, :],
                                 start=True, stop=True, skip_group_check=True)
            return last

        def add(dve, bank, order):
            return dve.tensor_tensor(out[r, i, :], out[r, i, :], bank[r, :], ALU.add)
        groups.append(((), carried, (), "v", add, [at[n - 1]]))
    gain_group(0)
    for n in range(1, NSUB):
        if n < NSUB - 1:
            gain_group(n)
        carried_group(n)
    bank_groups(c, groups, chained=True)
    group_rms_to_features(c, out, HH, EPS3, c.region(11, 0, NT, 512), mixT[:, 4:8, :], c.col["hg_norm_g_3"],
                          after=hgate)


def cross_attention(c, mem):
    xT = c.xT
    qT = c.region(5, 0, 8, S)
    kT, memT = c.region(6, 0, 8, MEM), c.region(6, 2048, 8, MEM)
    v = c.region(7, 0, 2, D)
    out, outT = c.region(8, 0, NT, D), c.region(9, 0, 8, S)
    groups = []
    for i in range(2):
        for k in (0, 4):
            groups.append(((), turns(c, [mem[:, i, (k + j) * P:(k + j + 1) * P] for j in range(4)]), (), "av"[k // 4],
                           copy_to(memT[:, k:k + 4, i * P:(i + 1) * P])))
    bank_groups(c, groups)
    groups = []
    for n in (0, 512):
        groups += features_from(c, ("xa_wq_3", n), xT, [qT[:, n // P + j, :] for j in range(4)])
    for n in (0, 512):
        groups += features_from(c, ("xa_wk_3", n), memT, [kT[:, n // P + j, :] for j in range(4)])
    for n in (0, 512):
        key = ("xa_wv_3", n)
        for i in range(2):
            w = c.slot(key)[0]
            groups.append(((key,), product([(memT[:, k, i * P:(i + 1) * P], w[:, k, :]) for k in range(KD)]),
                           (key,) if i else (), "av"[i], copy_to(v[:, i, n:n + 512])))
    bank_groups(c, groups)
    units = []
    for h in range(XH):
        for i in range(NT):
            def score(pe, bank, h=h, i=i):
                for j in range(2):
                    last = pe.matmul(bank[:, 0:MEM], qT[:, 2 * h + j, i * P:(i + 1) * P], kT[:, 2 * h + j, :],
                                     start=j == 0, stop=j == 1)
                return last

            def finish(dve, bank, factor, h=h, i=i):
                return dve.tensor_scalar(out[:, i, h * XD:(h + 1) * XD], bank[:, 0:XD], factor, None, ALU.mult)
            units.append({"keys": MEM, "scale": XD ** -0.5, "score": score, "masks": [],
                          "values": [v[:, k, h * XD:(h + 1) * XD] for k in range(2)], "finish": finish})
    attention(c, units, c.region(11, 0, ATT_WORK))
    to_features(c, lambda i: out[:, i, :], outT)
    return outT
NE, NGR, EPG, FFE = 32, 4, 8, 512
MAX_BLOCKS = (2 * S + NE * (P - 1)) // P + 1
TABLE = (MAX_BLOCKS + 2) * P


def clear_outputs(c):
    zeros = c.sb("zeros", [P, 512])
    c.y_rows = c.nc.dram_tensor("y_rows", (MAX_BLOCKS * P, D), F32).ap()
    made, cleared = c.sig("iota_made"), c.sig("outputs_cleared")
    least = 2 * S // P
    with c.nc.Block() as block:
        @block.gpsimd
        def _(pool):
            pool.memset(zeros[:, :], 0.0).then_inc(made.sem, made.up())

        @block.scalar
        def _(act):
            act.wait_ge(made.sem, made.at(1))
            for half in range(2):
                dst = c.y_rows[least * P:, half * 512:(half + 1) * 512].rearrange("(b p) n -> p b n", p=P)
                act.dma_start(dst, zeros[:, :].unsqueeze(1).to_broadcast([P, MAX_BLOCKS - least,
                                                                          512])).then_inc(cleared.sem, cleared.up(16))


def mixture_of_experts(c, a, mixed, out):
    nc, x, xT = c.nc, c.x, c.xT
    at = [0]

    def take(*shape):
        v = c.region(7, at[0], *shape)
        at[0] += int(np.prod(shape))
        return v
    bias, logits, padded = take(36), take(NT, 36), take(NT, 8)
    top, chosen, topi = take(NT, 8), take(NT, 8), take(NT, 8).bitcast(U32)
    etop, etopi = take(NT, 8), take(NT, 8).bitcast(U32)
    neg_top, total, group, weight = take(NT), take(NT), take(NT), take(2, NT)
    ids, onehot, both, prod = take(2, NT), take(2, NT, NE), take(NT, NE), take(NT,
            NGR * EPG).rearrange("p i (g e) -> p i g e", g=NGR)
    iota, before, slots = take(64), take(P), take(2, NT)
    count, blocks, last, base = take(NE), take(NE), take(NE), take(NT, NE)
    token = take(NT).bitcast(I32)
    slot_i = take(2, NT).bitcast(I32)
    per_block = take(MAX_BLOCKS + 2)
    expert_i, trips_i = take(MAX_BLOCKS + 2).bitcast(I32), take(2).bitcast(I32)
    router, by_logit = take(KD, 36), take(S)
    zero_i = take(TABLE // P).bitcast(I32)
    wide = c.region(8, 0, MAX_BLOCKS + 2, NE)
    x_rows = nc.dram_tensor("x_rows", (S, D), F32).ap()
    y_rows = c.y_rows
    cleared = c.signals["outputs_cleared"]
    table = nc.dram_tensor("token_of_slot", (TABLE, 1), I32).ap()

    stored = [c.sig("rows_stored0"), c.sig("rows_stored1")]
    made, zeroed, got = c.sig("iota_made"), c.sig("table_zeroed"), c.sig("rows_loaded_gpsimd")

    def prepare(pool):
        pool.dma_start(bias[:, 0:NGR], a["moe_b_group_3"][0].partition_broadcast(P)).then_inc(got.sem, got.up(16))
        pool.dma_start(bias[:, NGR:36], a["moe_b_expert_3"][0].partition_broadcast(P)).then_inc(got.sem, got.up(16))
        for dst, name in ((router[:, :, 0:NGR], "moe_w_group_3"), (router[:, :, NGR:36], "moe_w_expert_3")):
            pool.dma_start(dst, a[name][0].rearrange("(k p) n -> p k n", p=P),
                           allow_slow_non_contiguous=True).then_inc(got.sem, got.up(16))
        pool.memset(zero_i, 0).then_inc(made.sem, made.up())
        pool.memset(padded, NEG).then_inc(made.sem, made.up())
        pool.memset(before, 1.0).then_inc(made.sem, made.up())
        pool.iota(iota, pattern=[[1, 64]], base=0, channel_multiplier=0,
                  allow_small_or_imprecise_dtypes=True).then_inc(made.sem, made.up())
        pool.iota(token, pattern=[[P, NT]], base=0, channel_multiplier=1).then_inc(made.sem, made.up())
        pool.wait_ge(made.sem, made.at(5))
        pool.affine_select(out=before, in_=before, compare_op=ALU.is_gt, fill=0.0, base=0,
                           pattern=[[1, P]], channel_multiplier=-1).then_inc(made.sem, made.up())
        pool.dma_start(table.rearrange("(p n) o -> p (n o)", p=P), zero_i).then_inc(zeroed.sem, zeroed.up(16))
        pool.wait_ge(zeroed.sem, zeroed.at(16))
        pool.wait_ge(got.sem, got.at(64))
        pool.wait_ge(cleared.sem, cleared.sent)

    down_and_layer_norm(c, [("xa_wo_3", n) for n in (0, 4)], mixed, a["ln2_g_3"][0], a["ln2_b_3"][0],
                        c.region(10, 0, 2, D), EPS2, x_rows=x_rows, kept=stored, meanwhile=prepare)

    def add_bias(dve, bank, order):
        return dve.tensor_tensor(logits, bank[:, 0:NT * 36].rearrange("p (i n) -> p i n", i=NT),
                                 bias.unsqueeze(1).to_broadcast([P, NT, 36]), ALU.add)
    bank_groups(c, [((), product([(router[:, k, :], xT[:, k, :]) for k in range(KD)]), (), "v", copy_to(by_logit[0:36, :])),
                    ((), turns(c, [by_logit[0:36, i * P:(i + 1) * P] for i in range(NT)]), (), "v", add_bias, [0])])

    order, ready, powers = c.sig("vector_order"), c.sig("peak_ready"), c.sig("exponentials")
    with nc.Block() as block:
        @block.vector
        def _(dve):
            dve.tensor_copy(padded[:, :, 0:NGR], logits[:, :, 0:NGR]).then_inc(order.sem, order.up())
            dve.wait_ge(order.sem, order.sent)
            for i in range(NT):
                dve.max(top[:, i, :], padded[:, i, :]).then_inc(order.sem, order.up())
                dve.wait_ge(order.sem, order.sent)
                dve.max_index(topi[:, i, :], top[:, i, :], padded[:, i, :]).then_inc(order.sem, order.up())
                dve.wait_ge(order.sem, order.sent)
            dve.tensor_copy(group, topi[:, :, 0]).then_inc(order.sem, order.up())
            dve.wait_ge(order.sem, order.sent)
            dve.tensor_scalar(neg_top, top[:, :, 0], -1.0, None, ALU.mult).then_inc(order.sem, order.up())
            dve.wait_ge(order.sem, order.sent)
            dve.tensor_tensor(chosen[:, :, 0:NGR], iota[:, 0:NGR].unsqueeze(1).to_broadcast([P, NT, NGR]),
                              group.unsqueeze(2).to_broadcast([P, NT,
                                                               NGR]), ALU.is_equal).then_inc(order.sem, order.up())
            dve.wait_ge(order.sem, order.sent)
            for i in range(NT):
                dve.tensor_tensor(prod[:, i, :, :], logits[:, i, NGR:36].rearrange("p (g e) -> p g e", g=NGR),
                                  chosen[:, i, 0:NGR].unsqueeze(2).to_broadcast([P, NGR, EPG]),
                                  ALU.mult).then_inc(order.sem, order.up())
            dve.wait_ge(order.sem, order.sent)
            dve.tensor_reduce(chosen, prod.rearrange("p i g e -> p i e g"), AX.X, ALU.add).then_inc(order.sem,
                                                                                                    order.up())
            dve.wait_ge(order.sem, order.sent)
            for i in range(NT):
                dve.max(etop[:, i, :], chosen[:, i, :]).then_inc(order.sem, order.up())
                dve.wait_ge(order.sem, order.sent)
                dve.max_index(etopi[:, i, :], etop[:, i, :], chosen[:, i, :]).then_inc(order.sem, order.up())
                dve.wait_ge(order.sem, order.sent)
            for n in range(2):
                dve.tensor_copy(ids[:, n, :], etopi[:, :, n]).then_inc(order.sem, order.up())
                dve.wait_ge(order.sem, order.sent)
                dve.scalar_tensor_tensor(out=ids[:, n, :], in0=group, scalar=float(EPG), in1=ids[:, n, :],
                                            op0=ALU.mult, op1=ALU.add).then_inc(order.sem, order.up())
                dve.wait_ge(order.sem, order.sent)
                dve.tensor_tensor(onehot[:, n, :, :], iota[:, 0:NE].unsqueeze(1).to_broadcast([P, NT, NE]),
                                  ids[:, n, :].unsqueeze(2).to_broadcast([P, NT,
                                          NE]), ALU.is_equal).then_inc(order.sem, order.up())
                dve.wait_ge(order.sem, order.sent)
            dve.tensor_tensor(both, onehot[:, 0, :, :], onehot[:, 1, :, :], ALU.add).then_inc(order.sem, order.up())
            dve.wait_ge(order.sem, order.sent)
            dve.tensor_tensor(weight[:, 1, :], etop[:, :, 1], etop[:, :, 0], ALU.subtract).then_inc(ready.sem,
                                                                                                    ready.up())
            dve.wait_ge(ready.sem, ready.sent)
            dve.wait_ge(powers.sem, powers.at(NT + 1))
            dve.tensor_scalar(weight[:, 0, :], weight[:, 1, :], 1.0, None, ALU.add).then_inc(order.sem, order.up())
            dve.wait_ge(order.sem, order.sent)
            dve.tensor_tensor(weight[:, 0, :], weight[:, 0, :], total, ALU.mult).then_inc(order.sem, order.up())
            dve.wait_ge(order.sem, order.sent)
            dve.reciprocal(weight[:, 0, :], weight[:, 0, :]).then_inc(order.sem, order.up())
            dve.wait_ge(order.sem, order.sent)
            dve.tensor_tensor(weight[:, 1, :], weight[:, 0, :], weight[:, 1, :], ALU.mult).then_inc(order.sem,
                                                                                                    order.up())
            dve.wait_ge(order.sem, order.sent)

        @block.scalar
        def _(act):
            act.wait_ge(ready.sem, ready.at(1))
            for i in range(NT):
                act.activation(padded[:, i, 0:NGR], logits[:, i, 0:NGR], ACT.Exp,
                                                  bias=neg_top[:, i:i + 1], accum_out=total[:,
                                                          i:i + 1]).then_inc(powers.sem, powers.up())
                act.wait_ge(powers.sem, powers.sent)
            act.activation(weight[:, 1, :], weight[:, 1, :], ACT.Exp).then_inc(powers.sem, powers.up())
    groups = []
    for i in range(NT + 1):
        pairs = [(c.ones[:, :], both[:, j, :]) for j in range(i)] + ([(before, both[:, i, :])] if i < NT else [])
        groups.append(((), product(pairs), (), "v", copy_to(base[:, i, :] if i < NT else count)))
    bank_groups(c, groups)
    with nc.Block() as block:
        @block.vector
        def _(dve):
            dve.tensor_scalar(blocks, count, 0.0, None, ALU.is_gt).then_inc(order.sem, order.up())
            dve.wait_ge(order.sem, order.sent)
            for m in range(1, S // P):
                dve.scalar_tensor_tensor(out=blocks, in0=count, scalar=float(m * P), in1=blocks, op0=ALU.is_gt,
                                            op1=ALU.add).then_inc(order.sem, order.up())
                dve.wait_ge(order.sem, order.sent)
            dve.tensor_tensor_scan(last, c.ones[:, 0:NE], blocks, 0.0, ALU.mult, ALU.add).then_inc(order.sem,
                                                                                                   order.up())
            dve.wait_ge(order.sem, order.sent)
            dve.tensor_tensor(count, last, blocks, ALU.subtract).then_inc(order.sem, order.up())
            dve.wait_ge(order.sem, order.sent)
            dve.tensor_scalar(count, count, float(P), None, ALU.mult).then_inc(order.sem, order.up())
            dve.wait_ge(order.sem, order.sent)
            dve.tensor_tensor(base, base, count.unsqueeze(1).to_broadcast([P, NT, NE]), ALU.add).then_inc(order.sem,
                                                                                                          order.up())
            dve.wait_ge(order.sem, order.sent)
            for n in range(2):
                dve.tensor_tensor(onehot[:, n, :, :], onehot[:, n, :, :], base, ALU.mult).then_inc(order.sem,
                                                                                                   order.up())
                dve.wait_ge(order.sem, order.sent)
                dve.tensor_reduce(slots[:, n, :], onehot[:, n, :, :], AX.X, ALU.add).then_inc(order.sem, order.up())
                dve.wait_ge(order.sem, order.sent)
            dve.tensor_copy(slot_i, slots).then_inc(order.sem, order.up())
            dve.wait_ge(order.sem, order.sent)
            dve.tensor_tensor(wide, last.unsqueeze(1).to_broadcast([P, MAX_BLOCKS + 2, NE]),
                                 iota[:, 0:MAX_BLOCKS + 2].unsqueeze(2).to_broadcast([P, MAX_BLOCKS + 2,
                                         NE]), ALU.is_le).then_inc(order.sem, order.up())
            dve.wait_ge(order.sem, order.sent)
            dve.tensor_reduce(per_block, wide, AX.X, ALU.add).then_inc(order.sem, order.up())
            dve.wait_ge(order.sem, order.sent)
            dve.tensor_scalar(per_block, per_block, float(NE - 1), None, ALU.min).then_inc(order.sem, order.up())
            dve.wait_ge(order.sem, order.sent)
            dve.tensor_copy(expert_i, per_block).then_inc(order.sem, order.up())
            dve.wait_ge(order.sem, order.sent)
            dve.tensor_scalar(wide[:, 0, 0:MAX_BLOCKS // 2], iota[:, 0:MAX_BLOCKS:2], last[:, NE - 1:NE], None,
                              ALU.is_lt).then_inc(order.sem, order.up())
            dve.wait_ge(order.sem, order.sent)
            dve.tensor_reduce(per_block[:, 0:1], wide[:, 0, 0:MAX_BLOCKS // 2], AX.X, ALU.add).then_inc(order.sem,
                                                                                                        order.up())
            dve.wait_ge(order.sem, order.sent)
            dve.tensor_copy(trips_i[:, 0:1], per_block[:, 0:1]).then_inc(ready.sem, ready.up())
    expert_blocks(c, a, x_rows, y_rows, table, expert_i, trips_i, slot_i, token, stored)

    combine_and_norm(c, slot_i, weight, y_rows, a["ln3_g_3"][0], a["ln3_b_3"][0], out)


def combine_and_norm(c, slot_i, weight, y_rows, gain_row, bias_row, out):
    x = c.x
    rows = c.region(8, 0, 2 * NT, D)
    gain, bias = c.region(10, 0, 2, D)[:, 0, :], c.region(10, 0, 2, D)[:, 1, :]
    stats, mv, sd, shift = layer_norm_numbers(c)
    got, var, root, scaled, centred, gained, normed, raised, written = (c.sig(n) for n in (
        "rows_loaded_scalar", "variance_ready", "root_ready", "scale_ready", "rows_centred", "gain_applied", "normed",
        "rows_scaled", "result_written"))
    order, last_normed = c.sig("vector_order"), c.sig("last_tile_normed")
    gathered = [c.sig(f"outputs_gathered{i}") for i in range(NT)]

    def apply_gain(dve, i):
        if i == 0:
            dve.wait_ge(got.sem, got.at(32))
        dve.wait_ge(centred.sem, centred.at(i + 1))
        dve.tensor_tensor(x[:, i, :], x[:, i, :], gain, ALU.mult).then_inc(gained.sem, gained.up())

    with c.nc.Block() as block:
        @block.gpsimd
        def _(pool):
            for i in range(NT):
                for n in range(2):
                    pool.indirect_dma_start(
                        out=rows[:, 2 * i + n, :], out_offset=None, in_=y_rows,
                        in_offset=bass.IndirectOffsetOnAxis(ap=slot_i[:, n, i:i + 1],
                                                            axis=0)).then_inc(gathered[i].sem, gathered[i].up(16))
            pool.wait_ge(got.sem, got.at(32))
            for i in range(NT - 1):
                pool.wait_ge(gained.sem, gained.at(i + 1))
                pool.tensor_tensor(x[:, i, :], x[:, i, :], bias, ALU.add).then_inc(normed.sem, normed.up())

        @block.vector
        def _(dve):
            for i in range(NT):
                dve.wait_ge(raised.sem, raised.at(i + 1))
                dve.wait_ge(gathered[i].sem, gathered[i].at(32))
                for n in range(2):
                    dve.scalar_tensor_tensor(out=x[:, i, :], in0=rows[:, 2 * i + n, :], scalar=weight[:, n, i:i + 1],
                                             in1=x[:, i, :], op0=ALU.mult, op1=ALU.add).then_inc(order.sem, order.up())
                    dve.wait_ge(order.sem, order.sent)
                for half in range(2):
                    dve.bn_stats(stats[:, i, half, :], x[:, i, half * 512:(half + 1) * 512]).then_inc(order.sem,
                                                                                                      order.up())
                dve.wait_ge(order.sem, order.sent)
                dve.bn_aggr(mv[:, i, :], stats[:, i, :, :]).then_inc(order.sem, order.up())
                dve.wait_ge(order.sem, order.sent)
                dve.tensor_scalar(sd[:, i:i + 1], mv[:, i, 1:2], 1.0, EPS2, ALU.mult, ALU.add).then_inc(var.sem,
                                                                                                        var.up())
                if i:
                    apply_gain(dve, i - 1)
                dve.wait_ge(root.sem, root.at(i + 1))
                dve.reciprocal(sd[:, i:i + 1], sd[:, i:i + 1]).then_inc(order.sem, order.up())
                dve.wait_ge(order.sem, order.sent)
                dve.scalar_tensor_tensor(out=shift[:, i:i + 1], in0=mv[:, i, 0:1], scalar=-1.0, in1=sd[:, i:i + 1],
                                         op0=ALU.mult, op1=ALU.mult).then_inc(scaled.sem, scaled.up())
            apply_gain(dve, NT - 1)
            dve.wait_ge(gained.sem, gained.at(NT))
            dve.tensor_tensor(x[:, NT - 1, :], x[:, NT - 1, :], bias, ALU.add).then_inc(last_normed.sem,
                                                                                        last_normed.up())

        @block.scalar
        def _(act):
            act.dma_start(gain, gain_row.partition_broadcast(P)).then_inc(got.sem, got.up(16))
            act.dma_start(bias, bias_row.partition_broadcast(P)).then_inc(got.sem, got.up(16))
            for i in range(NT):
                act.activation(x[:, i, :], x[:, i, :], ACT.Copy, scale=ALPHA).then_inc(raised.sem, raised.up())
            for i in range(NT):
                act.wait_ge(var.sem, var.at(i + 1))
                act.activation(sd[:, i:i + 1], sd[:, i:i + 1], ACT.Sqrt).then_inc(root.sem, root.up())
                act.wait_ge(scaled.sem, scaled.at(i + 1))
                act.activation(x[:, i, :], x[:, i, :], ACT.Identity, bias=shift[:, i:i + 1],
                               scale=sd[:, i:i + 1]).then_inc(centred.sem, centred.up())

        @block.sync
        def _(sync):
            for i in range(NT):
                if i < NT - 1:
                    sync.wait_ge(normed.sem, normed.at(i + 1))
                else:
                    sync.wait_ge(last_normed.sem, last_normed.at(1))
                sync.dma_start(out[0, i * P:(i + 1) * P, :], x[:, i, :]).then_inc(written.sem, written.up(16))
            sync.wait_ge(written.sem, written.at(16 * NT))


def expert_blocks(c, a, x_rows, y_rows, table, expert_i, trips_i, slot_i, token, stored):
    nc = c.nc
    gate_w = [c.region(1 + 3 * s, 0, KD, FFE) for s in range(2)]
    up_w = [c.region(2 + 3 * s, 0, KD, FFE) for s in range(2)]
    down_w = [c.region(3 + 3 * s, 0, FFE // P, D) for s in range(2)]
    tokens = c.region(8, 0, 2, D)
    tokensT = [c.region(8, 2048 + s * 1024, KD, P) for s in range(2)]
    h, hT = c.region(9, 0, FFE), c.region(9, 512, FFE // P, P)
    out = c.region(9, 1024, 2, D)
    index = c.region(9, 3072, 2).bitcast(I32)
    filled, by_v, by_a = c.sig("bank_filled"), c.sig("bank_emptied_by_vector"), c.sig("bank_emptied_by_scalar")
    landed = [[c.sig(f"{n}_weights_landed{s}") for n in ("gate", "up", "down")] for s in range(2)]
    indexed, carried, scattered = c.sig("index_landed"), c.sig("wait_carried"), c.sig("slots_scattered")
    gathered = [c.sig(f"tokens_gathered{s}") for s in range(2)]
    bF, bV, bA = filled.sent + 2, by_v.sent + 1, by_a.sent + 1

    def turn(pe, s):
        for half in range(2):
            for k in range(4):
                last = pe.transpose(c.banks[half][:, k * P:(k + 1) * P],
                                    tokens[:, s, (4 * half + k) * P:(4 * half + k + 1) * P], c.ident[:, :])
            last.then_inc(filled.sem, 1)

    with nc.Block() as block:
        @block.sync
        def _(sync):
            trips = sync.value_load(trips_i[0:1, 0:1], min_val=1, max_val=MAX_BLOCKS // 2)
            with sync.Fori(0, trips) as it:
                for s in range(2):
                    b = it * 2 + s
                    e = sync.value_load(expert_i[0:1, bass.ds(b, 1)], min_val=0, max_val=NE - 1)
                    for n, (dst, name, done) in enumerate(((gate_w[s], "moe_w_gate_3", 1), (up_w[s], "moe_w_up_3", 2),
                                                          (down_w[s], "moe_w_down_3", 7))):
                        if s == 0 and n == 1:
                            sync.wait_ge(gathered[0].sem, 16)
                        if s == 0 and n == 2:
                            sync.wait_ge(gathered[1].sem, 16)
                        sync.wait_ge(filled.sem, b * 7 + (bF - 14 + done))
                        src = a[name][0][bass.ds(e, 1), :, :].rearrange("o (k p) n -> p (o k) n", p=P)
                        sync.dma_start(dst, src).then_inc(landed[s][n].sem, 16)

        @block.gpsimd
        def _(pool):
            trips = pool.value_load(trips_i[0:1, 0:1], min_val=1, max_val=MAX_BLOCKS // 2)

            for n in range(2):
                for i in range(NT):
                    pool.indirect_dma_start(
                        out=table, out_offset=bass.IndirectOffsetOnAxis(ap=slot_i[:, n, i:i + 1], axis=0),
                        in_=token[:, i:i + 1], in_offset=None).then_inc(scattered.sem, scattered.up(16))
            pool.wait_ge(scattered.sem, scattered.at(16 * 2 * NT))

            spare = c.region(9, 3080, 2)
            pool.memset(spare, 0.0).then_inc(carried.sem, 1)

            def gather(s, first_slot, n_index):
                pool.dma_start(index[:, s:s + 1], table[first_slot, :]).then_inc(indexed.sem, 16)
                pool.wait_ge(indexed.sem, n_index * 16)
                pool.wait_ge(carried.sem, n_index * 1)
                pool.tensor_tensor(spare[:, 0:1], spare[:, 1:2], spare[:, 1:2], ALU.add).then_inc(carried.sem, 1)
                return pool.indirect_dma_start(
                    out=tokens[:, s, :], out_offset=None, in_=x_rows,
                    in_offset=bass.IndirectOffsetOnAxis(ap=index[:, s:s + 1], axis=0))
            gather(0, slice(0, P), 1).then_inc(gathered[0].sem, 16)
            pool.wait_ge(gathered[0].sem, 16)
            with pool.Fori(0, trips) as it:
                for s in (1, 0):
                    n = it * 2 + (2 - s)
                    pool.wait_ge(filled.sem, n * 7 + (bF - 14))
                    gather(s, bass.ds(n * P, P), n + 1).then_inc(gathered[s].sem, 16)
                    pool.wait_ge(gathered[s].sem, it * 16 + (16 if s else 32))
            for s in range(2):
                pool.wait_ge(stored[s].sem, trips * 16 + stored[s].sent)

        @block.tensor
        def _(pe):
            trips = pe.value_load(trips_i[0:1, 0:1], min_val=1, max_val=MAX_BLOCKS // 2)
            pe.wait_ge(gathered[0].sem, 16)
            turn(pe, 0)
            pe.wait_ge(by_v.sem, bV)
            pe.wait_ge(by_a.sem, bA)
            with pe.Fori(0, trips) as it:
                for s in range(2):
                    b = it * 2 + s
                    pe.wait_ge(by_v.sem, b * 3 + (bV - 1))
                    pe.wait_ge(by_a.sem, b * 4 + (bA - 2))
                    for n, w in enumerate((gate_w[s], up_w[s])):
                        pe.wait_ge(landed[s][n].sem, it * 16 + 16)
                        for k in range(KD):
                            last = pe.matmul(c.banks[2 + n][:, :], tokensT[s][:, k, :], w[:, k, :], start=k == 0,
                                             stop=k == KD - 1)
                        last.then_inc(filled.sem, 1)
                    pe.wait_ge(gathered[1 - s].sem, it * 16 + (32 if s else 16))
                    turn(pe, 1 - s)
                    pe.wait_ge(by_v.sem, b * 3 + (bV + 1))
                    for k in range(FFE // P):
                        last = pe.transpose(c.banks[4][:, k * P:(k + 1) * P], h[:, k * P:(k + 1) * P], c.ident[:, :])
                    last.then_inc(filled.sem, 1)
                    pe.wait_ge(by_a.sem, b * 4 + (bA + 3))
                    pe.wait_ge(landed[s][2].sem, it * 16 + 16)
                    for half in range(2):
                        for k in range(FFE // P):
                            last = pe.matmul(c.banks[5 + half][:, :], hT[:, k, :],
                                             down_w[s][:, k, half * 512:(half + 1) * 512], start=k == 0,
                                             stop=k == FFE // P - 1)
                        last.then_inc(filled.sem, 1)

        @block.vector
        def _(dve):
            trips = dve.value_load(trips_i[0:1, 0:1], min_val=1, max_val=MAX_BLOCKS // 2)
            halfT = lambda s, half: tokensT[s][:, 4 * half:4 * half + 4, :].rearrange("p k t -> p (k t)")
            dve.wait_ge(filled.sem, bF - 1)
            dve.tensor_copy(halfT(0, 0), c.banks[0][:, :]).then_inc(by_v.sem, 1)
            with dve.Fori(0, trips) as it:
                for s in range(2):
                    b = it * 2 + s
                    dve.wait_ge(filled.sem, b * 7 + (bF + 2))
                    dve.wait_ge(by_a.sem, b * 4 + (bA + 1))
                    dve.tensor_tensor(h, h, c.banks[3][:, :], ALU.mult).then_inc(by_v.sem, 1)
                    dve.wait_ge(filled.sem, b * 7 + (bF + 3))
                    dve.tensor_copy(halfT(1 - s, 0), c.banks[0][:, :]).then_inc(by_v.sem, 1)
                    dve.wait_ge(filled.sem, b * 7 + (bF + 6))
                    dve.wait_ge(stored[s].sem, it * 16 + stored[s].sent)
                    dve.tensor_copy(out[:, s, 0:512], c.banks[5][:, :]).then_inc(by_v.sem, 1)

        @block.scalar
        def _(act):
            trips = act.value_load(trips_i[0:1, 0:1], min_val=1, max_val=MAX_BLOCKS // 2)
            halfT = lambda s, half: tokensT[s][:, 4 * half:4 * half + 4, :].rearrange("p k t -> p (k t)")
            act.wait_ge(filled.sem, bF)
            act.activation(halfT(0, 1), c.banks[1][:, :], ACT.Copy).then_inc(by_a.sem, 1)
            with act.Fori(0, trips) as it:
                for s in range(2):
                    b = it * 2 + s
                    act.wait_ge(filled.sem, b * 7 + (bF + 1))
                    act.activation(h, c.banks[2][:, :], ACT.Silu).then_inc(by_a.sem, 1)
                    act.wait_ge(filled.sem, b * 7 + (bF + 4))
                    act.activation(halfT(1 - s, 1), c.banks[1][:, :], ACT.Copy).then_inc(by_a.sem, 1)
                    act.wait_ge(filled.sem, b * 7 + (bF + 5))
                    act.activation(hT.rearrange("p k t -> p (k t)"), c.banks[4][:, :], ACT.Copy).then_inc(by_a.sem, 1)
                    act.wait_ge(filled.sem, b * 7 + (bF + 7))
                    act.wait_ge(stored[s].sem, it * 16 + stored[s].sent)
                    act.activation(out[:, s, 512:1024], c.banks[6][:, :], ACT.Copy).then_inc(by_a.sem, 1)
                    act.wait_ge(by_v.sem, b * 3 + (bV + 3))
                    act.wait_ge(by_a.sem, b * 4 + (bA + 4))
                    act.dma_start(y_rows[bass.ds(b * P, P), :], out[:, s, :]).then_inc(stored[s].sem, 16)


def block_stack(nc, a, out):
    with ExitStack() as ctx:
        c = Core(nc, ctx)
        c.x = c.region(0, 0, NT, D)
        c.xT = c.region(1, 0, KD, S)
        plan_first(c, a)
        plan_second(c, a)
        plan_third(c, a)
        setup_constants(c, a)
        clear_outputs(c)
        first_block(c, a)
        second_block(c, a)
        mixed = third_mixers(c, a)
        mixture_of_experts(c, a, mixed, out)


def kernel(**inputs):
    import numpy as _np
    import concourse.bacc as _bacc
    from concourse import mybir as _mybir
    from concourse.bass_utils import run_bass_kernel_spmd as _run

    nc = _bacc.Bacc("TRN2", target_bir_lowering=False, num_devices=1)
    arrays, args = {}, {}
    for name, value in inputs.items():
        v = _np.ascontiguousarray(value)
        arrays[f"in_{name}_dram"] = v
        args[name] = nc.dram_tensor(f"in_{name}_dram", v.shape, _mybir.dt.from_np(v.dtype), kind="ExternalInput").ap()
    out = nc.dram_tensor("out_0_dram", (1, S, D), F32, kind="ExternalOutput").ap()
    block_stack(nc, args, out)
    r = _run(nc, [arrays], core_ids=[0])
    return r.results[0]["out_0_dram"]
```
